# Optimizing a Trainium2 kernel written in Bass

```python
import math
import jax, jax.numpy as jnp
from jax import lax
import numpy as np

D_MODEL = 1024
BATCH = 1
SEQ = 256
DEPTH = 2

N_MIXERS = 2
D_FF = 2816
HG_HEADS = 8
HG_KEY = D_MODEL // HG_HEADS
HG_VAL = D_MODEL // HG_HEADS
HG_CHUNK = 64
FOX_HEADS = 16
FOX_HEAD_DIM = D_MODEL // FOX_HEADS
Q_BLOCK = 128
N_HG_LAYERS = (DEPTH + 1) // 2
N_FOX_LAYERS = DEPTH // 2
EPS = 1e-6
MASK_VALUE = -1e30
MIN_GATE = 1e-30


def rmsnorm(x, g):
    x32 = x.astype(jnp.float32)
    y = x32 * lax.rsqrt(jnp.mean(x32 * x32, axis=-1, keepdims=True) + EPS)
    return (y * g.astype(jnp.float32)).astype(x.dtype)

def swiglu(h, w_in, w_out):
    gate, up = jnp.split(h @ w_in, 2, axis=-1)
    return (jax.nn.silu(gate) * up) @ w_out

def hgrn2_mixer(h, w_in, lb, out_norm_g, w_out):
    B, T, _ = h.shape
    C = HG_CHUNK
    n = T // C
    q, z_f, i, g = jnp.split(h @ w_in, 4, axis=-1)
    z32 = z_f.astype(jnp.float32)
    lb = lb.astype(jnp.float32)
    f = lb + (1.0 - lb) * jax.nn.sigmoid(z32)
    log_f = jnp.log(jnp.maximum(f, MIN_GATE))
    k = (1.0 - lb) * jax.nn.sigmoid(-z32)
    q = jax.nn.silu(q.astype(jnp.float32))
    v = i.astype(jnp.float32)

    def to_chunks(a, d):
        return a.reshape(B, n, C, HG_HEADS, d).transpose(1, 0, 3, 2, 4)

    qc, kc, lfc = to_chunks(q, HG_KEY), to_chunks(k, HG_KEY), to_chunks(log_f, HG_KEY)
    vc = to_chunks(v, HG_VAL)
    causal = jnp.tril(jnp.ones((C, C), dtype=bool))[:, :, None]

    def step(S, inp):
        qb, kb, vb, lb_c = inp
        b = jnp.cumsum(lb_c, axis=2)
        o_inter = jnp.einsum('bhtk,bhkv->bhtv', qb * jnp.exp(b), S)
        diff = b[:, :, :, None, :] - b[:, :, None, :, :]
        decay = jnp.where(causal, jnp.exp(jnp.where(causal, diff, 0.0)), 0.0)
        scores = jnp.einsum('bhtk,bhtsk,bhsk->bhts', qb, decay, kb)
        o_intra = jnp.einsum('bhts,bhsv->bhtv', scores, vb)
        b_last = b[:, :, -1:, :]
        k_dec = kb * jnp.exp(b_last - b)
        S_new = jnp.exp(b_last[:, :, 0, :])[..., None] * S + jnp.einsum('bhsk,bhsv->bhkv', k_dec, vb)
        return S_new, o_inter + o_intra

    S0 = jnp.zeros((B, HG_HEADS, HG_KEY, HG_VAL), jnp.float32)
    _, o = lax.scan(step, S0, (qc, kc, vc, lfc))
    o = o.transpose(1, 0, 3, 2, 4).reshape(B, T, HG_HEADS, HG_VAL)
    o = rmsnorm(o, out_norm_g).reshape(B, T, D_MODEL)
    o = o * jax.nn.silu(g.astype(jnp.float32))
    return o.astype(h.dtype) @ w_out

def fox_mixer(h, w_in, b_f, q_norm_g, k_norm_g, w_out):
    B, T, _ = h.shape
    H, Dh = FOX_HEADS, FOX_HEAD_DIM
    nb = T // Q_BLOCK
    D = D_MODEL
    proj = h @ w_in
    q, k, v, g, z_f = jnp.split(proj, [D, 2 * D, 3 * D, 4 * D], axis=-1)
    q = rmsnorm(q.reshape(B, T, H, Dh), q_norm_g).transpose(0, 2, 1, 3)
    k = rmsnorm(k.reshape(B, T, H, Dh), k_norm_g).transpose(0, 2, 1, 3)
    v = v.reshape(B, T, H, Dh).transpose(0, 2, 1, 3)
    log_f = jax.nn.log_sigmoid(z_f.astype(jnp.float32) + b_f.astype(jnp.float32))
    c = jnp.cumsum(log_f, axis=1).transpose(0, 2, 1)
    qb = q.reshape(B, H, nb, Q_BLOCK, Dh).transpose(2, 0, 1, 3, 4)
    cq = c.reshape(B, H, nb, Q_BLOCK).transpose(2, 0, 1, 3)
    scale = 1.0 / math.sqrt(Dh)
    key_pos = jnp.arange(T)

    def block(args):
        qi, cqi, start = args
        s = jnp.einsum('bhqd,bhkd->bhqk', qi, k).astype(jnp.float32) * scale
        s = s + cqi[..., None] - c[:, :, None, :]
        qpos = start + jnp.arange(Q_BLOCK)
        s = jnp.where(key_pos[None, :] <= qpos[:, None], s, MASK_VALUE)
        p = jax.nn.softmax(s, axis=-1)
        return jnp.einsum('bhqk,bhkd->bhqd', p.astype(v.dtype), v)

    o = lax.map(block, (qb, cq, jnp.arange(nb) * Q_BLOCK))
    o = o.transpose(1, 0, 3, 2, 4).reshape(B, T, D)
    o = o * jax.nn.sigmoid(g)
    return o @ w_out

def first_inputs(seed: int = 0) -> dict:
    key = jax.random.key(seed)
    ks = jax.random.split(key, 16)
    f32 = jnp.float32
    D = D_MODEL

    def w(k, shape, fan_in):
        return jax.random.normal(k, shape, f32) * (fan_in ** -0.5)

    return {
        "x": jax.random.normal(ks[0], (BATCH, SEQ, D), f32),
        "norm_g": 1.0 + 0.05 * jax.random.normal(ks[1], (DEPTH, 3, D), f32),
        "ffn_w_in": w(ks[2], (DEPTH, 2, D, 2 * D_FF), D),
        "ffn_w_out": w(ks[3], (DEPTH, 2, D_FF, D), D_FF),
        "hg_w_in": w(ks[4], (N_HG_LAYERS, D, 4 * D), D),
        "hg_lb_logits": 0.5 * jax.random.normal(ks[5], (N_HG_LAYERS, HG_HEADS * HG_KEY), f32),
        "hg_out_norm_g": 1.0 + 0.05 * jax.random.normal(ks[6], (N_HG_LAYERS, HG_VAL), f32),
        "hg_w_out": w(ks[7], (N_HG_LAYERS, D, D), D),
        "fox_w_in": w(ks[8], (N_FOX_LAYERS, D, 4 * D + FOX_HEADS), D),
        "fox_b_f": 2.0 + 0.5 * jax.random.normal(ks[9], (N_FOX_LAYERS, FOX_HEADS), f32),
        "fox_q_norm_g": 1.0 + 0.05 * jax.random.normal(ks[10], (N_FOX_LAYERS, FOX_HEAD_DIM), f32),
        "fox_k_norm_g": 1.0 + 0.05 * jax.random.normal(ks[11], (N_FOX_LAYERS, FOX_HEAD_DIM), f32),
        "fox_w_out": w(ks[12], (N_FOX_LAYERS, D, D), D),
    }

def first_block(x, norm_g, ffn_w_in, ffn_w_out, hg_w_in, hg_lb_logits, hg_out_norm_g, hg_w_out,
              fox_w_in, fox_b_f, fox_q_norm_g, fox_k_norm_g, fox_w_out):
    p = jax.nn.softmax(hg_lb_logits.astype(jnp.float32), axis=0)
    lbs = jnp.cumsum(p, axis=0) - p[0]
    for layer in range(DEPTH):
        j = layer // N_MIXERS
        x = x + 0.5 * swiglu(rmsnorm(x, norm_g[layer, 0]), ffn_w_in[layer, 0], ffn_w_out[layer, 0])
        hn = rmsnorm(x, norm_g[layer, 1])
        if layer % N_MIXERS == 0:
            x = x + hgrn2_mixer(hn, hg_w_in[j], lbs[j], hg_out_norm_g[j], hg_w_out[j])
        else:
            x = x + fox_mixer(hn, fox_w_in[j], fox_b_f[j], fox_q_norm_g[j], fox_k_norm_g[j], fox_w_out[j])
        x = x + 0.5 * swiglu(rmsnorm(x, norm_g[layer, 2]), ffn_w_in[layer, 1], ffn_w_out[layer, 1])
    return x


N_MEM = 256
N_MIXERS_2 = 3
HEAD_DIM = 64
MIX_HEADS = 12
MIX_WIDTH = MIX_HEADS * HEAD_DIM
XA_HEADS = 4
XA_WIDTH = XA_HEADS * HEAD_DIM
OUT_IN = MIX_WIDTH + XA_WIDTH
ROPE_THETA = 500000.0
ROT_DIM = HEAD_DIM // 4
LN_EPS = 1e-5
RMS_EPS = 1e-6
DEEPNORM_ALPHA = (2.0 * DEPTH) ** 0.25
DEEPNORM_BETA = (8.0 * DEPTH) ** -0.25

NSA_KV_HEADS = 4
NSA_GROUP = MIX_HEADS // NSA_KV_HEADS
NSA_KV_WIDTH = NSA_KV_HEADS * HEAD_DIM
CMP_LEN = 32
CMP_STRIDE = 16
CMP_HIDDEN = 128
SEL_BLOCK = 64
SEL_TOPK = 16
WINDOW = 512
NSA_QBLOCK = 32
NSA_IN = MIX_WIDTH + 6 * NSA_KV_WIDTH + 3 * MIX_HEADS + XA_WIDTH

MLA_Q_RANK = 256
MLA_KV_RANK = 128
MLA_NOPE = 64
MLA_ROPE = 32
MLA_V = 64
MLA_THETA = 10000.0
MLA_QBLOCK = 128
MLA_IN = MLA_Q_RANK + MLA_KV_RANK + MLA_ROPE + XA_WIDTH

CONV_CH = MIX_WIDTH
CONV_WIDTH = 31
CONV_IN = 2 * CONV_CH + XA_WIDTH

N_GROUPS = 4
EXPERTS_PER_GROUP = 4
N_EXPERTS = N_GROUPS * EXPERTS_PER_GROUP
EXPERT_FF = 512
TOPK_IN_GROUP = 2


def layer_norm(x, g, b):
    xf = x.astype(jnp.float32)
    mu = jnp.mean(xf, -1, keepdims=True)
    var = jnp.mean(jnp.square(xf - mu), -1, keepdims=True)
    y = (xf - mu) * lax.rsqrt(var + LN_EPS) * g.astype(jnp.float32) + b.astype(jnp.float32)
    return y.astype(x.dtype)

def rms_norm(x, g):
    xf = x.astype(jnp.float32)
    y = xf * lax.rsqrt(jnp.mean(xf * xf, -1, keepdims=True) + RMS_EPS) * g.astype(jnp.float32)
    return y.astype(x.dtype)

def rope_tables(positions, dim, theta):
    inv = theta ** (-jnp.arange(0, dim, 2, dtype=jnp.float32) / dim)
    ang = positions.astype(jnp.float32)[..., None] * inv
    return jnp.cos(ang), jnp.sin(ang)

def apply_rope(x, cos, sin):
    r = cos.shape[-1]
    x1, x2 = x[..., :r], x[..., r:]
    c, s = cos[:, :, None, :], sin[:, :, None, :]
    return jnp.concatenate([x1 * c - x2 * s, x1 * s + x2 * c], -1).astype(x.dtype)

def partial_rope(x, cos, sin):
    return jnp.concatenate([apply_rope(x[..., :ROT_DIM], cos, sin), x[..., ROT_DIM:]], -1)

def masked_softmax(s, mask):
    s = jnp.where(mask, s.astype(jnp.float32), -jnp.inf)
    m = jnp.max(s, -1, keepdims=True)
    m = jnp.where(jnp.isfinite(m), m, 0.0)
    e = jnp.where(mask, jnp.exp(s - m), 0.0)
    return e / jnp.maximum(jnp.sum(e, -1, keepdims=True), 1e-30)

def nsa_mixer(mix_cols, cmp_pe, cmp_w1, cmp_w2, cos_n, sin_n):
    B, S, _ = mix_cols.shape
    H, K, G, Dh = MIX_HEADS, NSA_KV_HEADS, NSA_GROUP, HEAD_DIM
    offs = np.cumsum([MIX_WIDTH] + [NSA_KV_WIDTH] * 6).tolist()
    q, kc, vc, ks, vs, kw, vw, gate_logits = jnp.split(mix_cols, offs, axis=-1)
    dt = mix_cols.dtype
    q = partial_rope(q.reshape(B, S, H, Dh), cos_n, sin_n)
    ks = partial_rope(ks.reshape(B, S, K, Dh), cos_n, sin_n)
    kw = partial_rope(kw.reshape(B, S, K, Dh), cos_n, sin_n)
    vs, vw = vs.reshape(B, S, K, Dh), vw.reshape(B, S, K, Dh)
    kc, vc = kc.reshape(B, S, K, Dh), vc.reshape(B, S, K, Dh)
    gates = jax.nn.sigmoid(gate_logits.astype(jnp.float32)).astype(dt).reshape(B, S, H, 3)

    n_cmp = (S - CMP_LEN) // CMP_STRIDE + 1
    starts = np.arange(n_cmp) * CMP_STRIDE
    tok_idx = starts[:, None] + np.arange(CMP_LEN)[None, :]
    end_idx = starts + CMP_LEN - 1

    def compress(t, pe, w1, w2):
        blk = t[:, tok_idx] + pe[None, None, :, None, :]
        blk = blk.transpose(0, 1, 3, 2, 4).reshape(B, n_cmp, K, CMP_LEN * Dh)
        return jax.nn.silu(blk @ w1) @ w2

    k_cmp = compress(kc, cmp_pe[0], cmp_w1[0], cmp_w2[0])
    v_cmp = compress(vc, cmp_pe[1], cmp_w1[1], cmp_w2[1])
    k_cmp = partial_rope(k_cmp, cos_n[:, end_idx], sin_n[:, end_idx])

    n_sel = S // SEL_BLOCK
    top_n = min(SEL_TOPK, n_sel)
    sel_start = np.arange(n_sel) * SEL_BLOCK
    overlap = ((starts[:, None] < sel_start[None, :] + SEL_BLOCK)
               & (starts[:, None] + CMP_LEN > sel_start[None, :])).astype(np.float32)
    overlap = jnp.asarray(overlap)
    ksb = ks.reshape(B, n_sel, SEL_BLOCK, K, Dh).transpose(0, 3, 1, 2, 4)
    vsb = vs.reshape(B, n_sel, SEL_BLOCK, K, Dh).transpose(0, 3, 1, 2, 4)
    kwp = jnp.pad(kw, ((0, 0), (WINDOW, 0), (0, 0), (0, 0)))
    vwp = jnp.pad(vw, ((0, 0), (WINDOW, 0), (0, 0), (0, 0)))
    qg = q.reshape(B, S, K, G, Dh)
    scale = 1.0 / math.sqrt(Dh)
    C = NSA_QBLOCK
    bi = jnp.arange(B)[:, None, None, None]
    ki = jnp.arange(K)[None, :, None, None]
    blk_id = jnp.arange(n_sel)

    def block(i):
        t0 = i * C
        qb = lax.dynamic_slice_in_dim(qg, t0, C, axis=1)
        t = t0 + jnp.arange(C)
        s_c = jnp.einsum('bckgd,bnkd->bkgcn', qb, k_cmp) * scale
        p_c = masked_softmax(s_c, end_idx[None, :] <= t[:, None])
        o_c = jnp.einsum('bkgcn,bnkd->bckgd', p_c.astype(dt), v_cmp)
        imp = jnp.einsum('bkgcn,nj->bkcj', p_c, overlap)
        cur = t // SEL_BLOCK
        valid = blk_id[None, :] <= cur[:, None]
        forced = (blk_id[None, :] == 0) | (blk_id[None, :] == cur[:, None]) | (blk_id[None, :] == cur[:, None] - 1)
        imp = jnp.where(valid & forced, jnp.inf, jnp.where(valid, imp, -jnp.inf))
        _, sel = lax.top_k(imp, top_n)
        k_sel = ksb[bi, ki, sel]
        v_sel = vsb[bi, ki, sel]
        s_s = jnp.einsum('bckgd,bkcnld->bkgcnl', qb, k_sel) * scale
        key_pos = sel[..., None] * SEL_BLOCK + jnp.arange(SEL_BLOCK)
        mask_s = (key_pos <= t[None, None, :, None, None]).reshape(B, K, 1, C, top_n * SEL_BLOCK)
        p_s = masked_softmax(s_s.reshape(B, K, G, C, top_n * SEL_BLOCK), mask_s)
        o_s = jnp.einsum('bkgcm,bkcmd->bckgd', p_s.astype(dt),
                         v_sel.reshape(B, K, C, top_n * SEL_BLOCK, Dh))
        kwb = lax.dynamic_slice_in_dim(kwp, t0, WINDOW + C, axis=1)
        vwb = lax.dynamic_slice_in_dim(vwp, t0, WINDOW + C, axis=1)
        s_w = jnp.einsum('bckgd,bjkd->bkgcj', qb, kwb) * scale
        kp = t0 - WINDOW + jnp.arange(WINDOW + C)
        diff = t[:, None] - kp[None, :]
        p_w = masked_softmax(s_w, (diff >= 0) & (diff < WINDOW) & (kp[None, :] >= 0))
        o_w = jnp.einsum('bkgcj,bjkd->bckgd', p_w.astype(dt), vwb)
        gb = lax.dynamic_slice_in_dim(gates, t0, C, axis=1).reshape(B, C, K, G, 3)
        o = gb[..., 0:1] * o_c + gb[..., 1:2] * o_s + gb[..., 2:3] * o_w
        return o.reshape(B, C, H * Dh)

    out = lax.map(block, jnp.arange(S // C))
    return out.transpose(1, 0, 2, 3).reshape(B, S, MIX_WIDTH)

def mla_mixer(mix_cols, q_norm, w_uq, kv_norm, w_ukv, cos_m, sin_m):
    B, S, _ = mix_cols.shape
    H = MIX_HEADS
    dt = mix_cols.dtype
    c_q = mix_cols[..., :MLA_Q_RANK]
    c_kv = mix_cols[..., MLA_Q_RANK:MLA_Q_RANK + MLA_KV_RANK]
    k_rope = mix_cols[..., MLA_Q_RANK + MLA_KV_RANK:]
    q = (rms_norm(c_q, q_norm) @ w_uq).reshape(B, S, H, MLA_NOPE + MLA_ROPE)
    q = jnp.concatenate([q[..., :MLA_NOPE], apply_rope(q[..., MLA_NOPE:], cos_m, sin_m)], -1)
    kv = (rms_norm(c_kv, kv_norm) @ w_ukv).reshape(B, S, H, MLA_NOPE + MLA_V)
    k_nope, v = kv[..., :MLA_NOPE], kv[..., MLA_NOPE:]
    k_rope = apply_rope(k_rope[:, :, None, :], cos_m, sin_m)
    k = jnp.concatenate([k_nope, jnp.broadcast_to(k_rope, (B, S, H, MLA_ROPE))], -1)
    scale = 1.0 / math.sqrt(MLA_NOPE + MLA_ROPE)
    key_idx = jnp.arange(S)

    def block(i):
        t0 = i * MLA_QBLOCK
        qb = lax.dynamic_slice_in_dim(q, t0, MLA_QBLOCK, axis=1)
        s = jnp.einsum('bqhd,bkhd->bhqk', qb, k) * scale
        mask = (t0 + jnp.arange(MLA_QBLOCK))[:, None] >= key_idx[None, :]
        p = masked_softmax(s, mask)
        return jnp.einsum('bhqk,bkhd->bqhd', p.astype(dt), v).reshape(B, MLA_QBLOCK, H * MLA_V)

    out = lax.map(block, jnp.arange(S // MLA_QBLOCK))
    return out.transpose(1, 0, 2, 3).reshape(B, S, H * MLA_V)

def conv_mixer(mix_cols, b_in, dw_w, dw_b, ln_g, ln_b):
    a = mix_cols + b_in
    u = a[..., :CONV_CH] * jax.nn.sigmoid(a[..., CONV_CH:])
    y = lax.conv_general_dilated(u, dw_w[:, None, :], window_strides=(1,),
                                 padding=[(CONV_WIDTH - 1, 0)],
                                 dimension_numbers=('NWC', 'WIO', 'NWC'),
                                 feature_group_count=CONV_CH) + dw_b
    return jax.nn.silu(layer_norm(y, ln_g, ln_b))

def memory_cross_attention(q, mem_k, mem_v):
    s = jnp.einsum('bshd,bmhd->bhsm', q, mem_k) * (1.0 / math.sqrt(HEAD_DIM))
    p = jax.nn.softmax(s.astype(jnp.float32), -1).astype(q.dtype)
    return jnp.einsum('bhsm,bmhd->bshd', p, mem_v)

def hier_moe(x, w_grp, b_grp, w_exp, b_exp, w_gate, w_up, w_down):
    def per_seq(xs):
        S = xs.shape[0]
        pg = jax.nn.softmax((xs @ w_grp + b_grp).astype(jnp.float32), -1)
        g_sel = jnp.argmax(pg, -1)
        g_prob = jnp.max(pg, -1)
        le = (xs @ w_exp + b_exp).astype(jnp.float32).reshape(S, N_GROUPS, EXPERTS_PER_GROUP)
        le = le[jnp.arange(S), g_sel]
        pe = jax.nn.softmax(le, -1)
        top_p, top_i = lax.top_k(pe, TOPK_IN_GROUP)
        top_p = top_p / jnp.sum(top_p, -1, keepdims=True)
        eid = g_sel[:, None] * EXPERTS_PER_GROUP + top_i
        gate = jnp.sum(jax.nn.one_hot(eid, N_EXPERTS, dtype=jnp.float32)
                       * (g_prob[:, None] * top_p)[..., None], axis=1)
        hdn = jax.nn.silu(jnp.einsum('sd,edf->sef', xs, w_gate)) * jnp.einsum('sd,edf->sef', xs, w_up)
        hdn = hdn * gate[..., None].astype(hdn.dtype)
        return jnp.einsum('sef,efd->sd', hdn, w_down)
    return lax.map(per_seq, x)

def second_inputs(seed: int = 0) -> dict:
    key = jax.random.key(seed)
    ks = iter(jax.random.split(key, 40))
    nA = len(range(0, DEPTH, N_MIXERS_2))
    nB = len(range(1, DEPTH, N_MIXERS_2))
    nC = len(range(2, DEPTH, N_MIXERS_2))
    f32 = jnp.float32

    def nrm(shape, scale):
        return jax.random.normal(next(ks), shape, f32) * scale

    def gain(shape):
        return 1.0 + nrm(shape, 0.02)

    positions = (jax.random.randint(next(ks), (BATCH, 1), 0, 2048, dtype=jnp.int32)
                 + jnp.arange(SEQ, dtype=jnp.int32)[None, :])
    return {
        'x': nrm((BATCH, SEQ, D_MODEL), 1.0),
        'mem': nrm((BATCH, N_MEM, D_MODEL), 1.0),
        'positions': positions,
        'nsa_w_in': nrm((nA, D_MODEL, NSA_IN), D_MODEL ** -0.5),
        'nsa_cmp_pe': nrm((nA, 2, CMP_LEN, HEAD_DIM), 0.1),
        'nsa_cmp_w1': nrm((nA, 2, CMP_LEN * HEAD_DIM, CMP_HIDDEN), (CMP_LEN * HEAD_DIM) ** -0.5),
        'nsa_cmp_w2': nrm((nA, 2, CMP_HIDDEN, HEAD_DIM), CMP_HIDDEN ** -0.5),
        'mla_w_in': nrm((nB, D_MODEL, MLA_IN), D_MODEL ** -0.5),
        'mla_q_norm': gain((nB, MLA_Q_RANK)),
        'mla_w_uq': nrm((nB, MLA_Q_RANK, MIX_HEADS * (MLA_NOPE + MLA_ROPE)), MLA_Q_RANK ** -0.5),
        'mla_kv_norm': gain((nB, MLA_KV_RANK)),
        'mla_w_ukv': nrm((nB, MLA_KV_RANK, MIX_HEADS * (MLA_NOPE + MLA_V)), MLA_KV_RANK ** -0.5),
        'conv_w_in': nrm((nC, D_MODEL, CONV_IN), D_MODEL ** -0.5),
        'conv_b_in': nrm((nC, 2 * CONV_CH), 0.02),
        'conv_dw_w': nrm((nC, CONV_WIDTH, CONV_CH), CONV_WIDTH ** -0.5),
        'conv_dw_b': nrm((nC, CONV_CH), 0.02),
        'conv_ln_g': gain((nC, CONV_CH)),
        'conv_ln_b': nrm((nC, CONV_CH), 0.02),
        'mem_w_kv': nrm((DEPTH, D_MODEL, 2 * XA_WIDTH), D_MODEL ** -0.5),
        'w_out': nrm((DEPTH, OUT_IN, D_MODEL), OUT_IN ** -0.5 * DEEPNORM_BETA),
        'ln_g': gain((DEPTH, 2, D_MODEL)),
        'ln_b': nrm((DEPTH, 2, D_MODEL), 0.02),
        'moe_w_grp': nrm((DEPTH, D_MODEL, N_GROUPS), D_MODEL ** -0.5),
        'moe_b_grp': nrm((DEPTH, N_GROUPS), 0.01),
        'moe_w_exp': nrm((DEPTH, D_MODEL, N_EXPERTS), D_MODEL ** -0.5),
        'moe_b_exp': nrm((DEPTH, N_EXPERTS), 0.01),
        'moe_w_gate': nrm((DEPTH, N_EXPERTS, D_MODEL, EXPERT_FF), D_MODEL ** -0.5),
        'moe_w_up': nrm((DEPTH, N_EXPERTS, D_MODEL, EXPERT_FF), D_MODEL ** -0.5),
        'moe_w_down': nrm((DEPTH, N_EXPERTS, EXPERT_FF, D_MODEL), EXPERT_FF ** -0.5 * DEEPNORM_BETA),
    }

def second_block(x, mem, positions, nsa_w_in, nsa_cmp_pe, nsa_cmp_w1, nsa_cmp_w2,
              mla_w_in, mla_q_norm, mla_w_uq, mla_kv_norm, mla_w_ukv,
              conv_w_in, conv_b_in, conv_dw_w, conv_dw_b, conv_ln_g, conv_ln_b,
              mem_w_kv, w_out, ln_g, ln_b,
              moe_w_grp, moe_b_grp, moe_w_exp, moe_b_exp, moe_w_gate, moe_w_up, moe_w_down):
    B, S, _ = x.shape
    cos_n, sin_n = rope_tables(positions, ROT_DIM, ROPE_THETA)
    cos_m, sin_m = rope_tables(positions, MLA_ROPE, MLA_THETA)
    for i in range(DEPTH):
        kind = i % N_MIXERS_2
        j = i // N_MIXERS_2
        if kind == 0:
            proj = x @ nsa_w_in[j]
            mix = nsa_mixer(proj[..., :-XA_WIDTH], nsa_cmp_pe[j], nsa_cmp_w1[j], nsa_cmp_w2[j], cos_n, sin_n)
        elif kind == 1:
            proj = x @ mla_w_in[j]
            mix = mla_mixer(proj[..., :-XA_WIDTH], mla_q_norm[j], mla_w_uq[j],
                            mla_kv_norm[j], mla_w_ukv[j], cos_m, sin_m)
        else:
            proj = x @ conv_w_in[j]
            mix = conv_mixer(proj[..., :-XA_WIDTH], conv_b_in[j], conv_dw_w[j], conv_dw_b[j],
                             conv_ln_g[j], conv_ln_b[j])
        xq = proj[..., -XA_WIDTH:].reshape(B, S, XA_HEADS, HEAD_DIM)
        mkv = mem @ mem_w_kv[i]
        mk = mkv[..., :XA_WIDTH].reshape(B, N_MEM, XA_HEADS, HEAD_DIM)
        mv = mkv[..., XA_WIDTH:].reshape(B, N_MEM, XA_HEADS, HEAD_DIM)
        xa = memory_cross_attention(xq, mk, mv).reshape(B, S, XA_WIDTH)
        y = jnp.concatenate([mix, xa], -1) @ w_out[i]
        x = layer_norm(DEEPNORM_ALPHA * x + y, ln_g[i, 0], ln_b[i, 0])
        f = hier_moe(x, moe_w_grp[i], moe_b_grp[i], moe_w_exp[i], moe_b_exp[i],
                     moe_w_gate[i], moe_w_up[i], moe_w_down[i])
        x = layer_norm(DEEPNORM_ALPHA * x + f, ln_g[i, 1], ln_b[i, 1])
    return x


def setup_inputs(seed=0):
    out = dict(first_inputs(seed))
    for name, value in second_inputs(seed + 1).items():
        if name != "x":
            out[name + "_2"] = value
    return out


def reference(
    x, norm_g, ffn_w_in, ffn_w_out, hg_w_in, hg_lb_logits, hg_out_norm_g, hg_w_out, fox_w_in,
    fox_b_f, fox_q_norm_g, fox_k_norm_g, fox_w_out, mem_2, positions_2, nsa_w_in_2,
    nsa_cmp_pe_2, nsa_cmp_w1_2, nsa_cmp_w2_2, mla_w_in_2, mla_q_norm_2, mla_w_uq_2,
    mla_kv_norm_2, mla_w_ukv_2, conv_w_in_2, conv_b_in_2, conv_dw_w_2, conv_dw_b_2, conv_ln_g_2,
    conv_ln_b_2, mem_w_kv_2, w_out_2, ln_g_2, ln_b_2, moe_w_grp_2, moe_b_grp_2, moe_w_exp_2,
    moe_b_exp_2, moe_w_gate_2, moe_w_up_2, moe_w_down_2,
):
    x = first_block(
        x, norm_g, ffn_w_in, ffn_w_out, hg_w_in, hg_lb_logits, hg_out_norm_g, hg_w_out,
        fox_w_in, fox_b_f, fox_q_norm_g, fox_k_norm_g, fox_w_out,
    )
    return second_block(
        x, mem_2, positions_2, nsa_w_in_2, nsa_cmp_pe_2, nsa_cmp_w1_2, nsa_cmp_w2_2, mla_w_in_2,
        mla_q_norm_2, mla_w_uq_2, mla_kv_norm_2, mla_w_ukv_2, conv_w_in_2, conv_b_in_2,
        conv_dw_w_2, conv_dw_b_2, conv_ln_g_2, conv_ln_b_2, mem_w_kv_2, w_out_2, ln_g_2, ln_b_2,
        moe_w_grp_2, moe_b_grp_2, moe_w_exp_2, moe_b_exp_2, moe_w_gate_2, moe_w_up_2,
        moe_w_down_2,
    )


_drawn_inputs = setup_inputs


def setup_inputs(seed=0):
    import zlib

    import numpy as np

    out = dict(_drawn_inputs(seed))
    spreads = {}
    factors = {'fox_q_norm_g': 6.041,
     'fox_k_norm_g': 5.54,
     'nsa_cmp_pe_2': 7.529,
     'mla_q_norm_2': 8.0,
     'mla_kv_norm_2': 8.0,
     'moe_b_grp_2': 8.0,
     'moe_b_exp_2': 8.0}
    for name, (base, spread) in spreads.items():
        noise = np.random.default_rng([zlib.crc32(name.encode()), seed]).standard_normal(out[name].shape)
        drawn = base * np.exp(spread * noise) if base else spread * noise
        out[name] = __import__('jax').numpy.asarray(drawn.astype(out[name].dtype))
    for name, factor in factors.items():
        out[name] = (out[name] * factor).astype(out[name].dtype)
    return out
```

```python
from contextlib import ExitStack

import numpy as np

import concourse.bass as bass
from concourse import mybir

F32 = mybir.dt.float32
F32R = mybir.dt.float32r
BF16 = mybir.dt.bfloat16
I32 = mybir.dt.int32
U32 = mybir.dt.uint32
ALU = mybir.AluOpType
ACT = mybir.ActivationFunctionType
X_AXIS = mybir.AxisListType.X
ds = bass.ds

P = 128
D = 1024
KD = D // P
T = 256
TT = T // P
FF = 2816
HG_H, HG_CHUNK = 8, 64
FOX_H, HD = 16, 64
NSA_H, NSA_KV, GROUP = 12, 4, 3
N_CMP, CMP_STRIDE, CMP_LEN = 15, 16, 32
XA_H = 4
MLA_H, MLA_K, MLA_NOPE, MLA_ROPE = 12, 96, 64, 32
E_N, E_FF, G_N, E_G = 16, 512, 4, 4
EPS = 1e-6
LN_EPS = 1e-5
ALPHA = (2.0 * 2) ** 0.25
MASKED = -1e30
NEG_BIG = -3e38

SLOTS = 3
SLOT = 6144
ARENA = 17408

NSA_ROT, NSA_THETA = 16, 500000.0
MLA_THETA = 10000.0
C_IDENT, C_ONES, C_BLK, C_ROTN, C_ROTM = 0, 128, 256, 384, 512
C_CAUSAL = 640
C_CMPADD, C_CMPMUL = 1024, 1054
C_LEVEL = 1084
C_RESET = C_LEVEL + 1024
C_INVN, C_INVM = C_RESET + 256, C_RESET + 257
C_FIRST = C_RESET + 258
C_EPS, C_LNEPS = C_FIRST + 4, C_FIRST + 5
N_CONST = C_LNEPS + 1


def constants():
    c = np.zeros((P, N_CONST), np.float32)
    i = np.arange(P)
    c[:, C_IDENT:C_IDENT + P] = np.eye(P)
    c[:, C_ONES:C_ONES + P] = 1.0
    c[:, C_BLK:C_BLK + P] = (i[:, None] // HD == i[None, :] // HD)
    for first, half, at in [(0, 8, C_ROTN), (64, 8, C_ROTN), (64, 16, C_ROTM)]:
        for d in range(half):
            c[first + half + d, at + first + d] = -1.0
            c[first + d, at + first + half + d] = 1.0
    t = np.arange(P)
    c[:, C_CAUSAL + 256:C_CAUSAL + 384] = np.where(t[None, :] <= t[:, None], 0.0, MASKED)
    for q in range(TT):
        seen = (np.arange(N_CMP)[None, :] * CMP_STRIDE + CMP_LEN - 1) <= (q * P + t)[:, None]
        c[:, C_CMPADD + q * N_CMP:C_CMPADD + (q + 1) * N_CMP] = np.where(seen, 0.0, MASKED)
        c[:, C_CMPMUL + q * N_CMP:C_CMPMUL + (q + 1) * N_CMP] = seen
    for n in range(7):
        L = 1 << n
        s, u = t[:, None], t[None, :]
        c[:, C_LEVEL + n * P:C_LEVEL + (n + 1) * P] = (
            (s // (2 * L) == u // (2 * L)) & (s // L % 2 == 0) & (u // L % 2 == 1))
    c[:, C_LEVEL + 7 * P:C_LEVEL + 8 * P] = np.eye(P)
    c[:, C_RESET:C_RESET + T] = (np.arange(T) % HG_CHUNK != 0)
    inv = lambda theta, dim: np.float32(theta) ** (-np.arange(0, dim, 2, dtype=np.float32) / np.float32(dim))
    for first in (0, 64):
        c[first:first + NSA_ROT, C_INVN] = np.tile(inv(NSA_THETA, NSA_ROT), 2)
    c[64:64 + MLA_ROPE, C_INVM] = np.tile(inv(MLA_THETA, MLA_ROPE), 2)
    c[:, C_FIRST:C_FIRST + 4] = [4, 3, 2, 1]
    c[:, C_EPS], c[:, C_LNEPS] = EPS, LN_EPS
    return c


class Counted:

    def __init__(self, sem):
        self.sem, self.n = sem, 0

    def inc(self, ins):
        ins.then_inc(self.sem, 1)
        self.n += 1
        return self.n

    def wait(self, eng, n=None):
        eng.wait_ge(self.sem, self.n if n is None else n)


class Ring:

    def __init__(self, ctx, nc, slots):
        self.slots = slots
        self.full = [ctx.enter_context(nc.semaphore(f"slot_full_{s}")) for s in range(SLOTS)]
        self.free = [ctx.enter_context(nc.semaphore(f"slot_free_{s}")) for s in range(SLOTS)]
        self.targets, self.landed = [], [0] * SLOTS

    def plan(self, dmas):
        n = len(self.targets)
        self.landed[n % SLOTS] += 16 * dmas
        self.targets.append(self.landed[n % SLOTS])
        return n

    def slot(self, n):
        return self.slots[:, n % SLOTS, :]

    def wait_free(self, eng, n, turns=0):
        eng.wait_ge(self.free[n % SLOTS], n // SLOTS + 1 + turns)

    def wait_full(self, eng, n, more=0):
        eng.wait_ge(self.full[n % SLOTS], self.targets[n] + more)


class Banks:

    def __init__(self, ctx, nc, psum):
        self.psum = psum
        self.ready = [ctx.enter_context(nc.semaphore(f"bank_ready_{b}")) for b in range(4)]
        self.free = [ctx.enter_context(nc.semaphore(f"bank_free_{b}")) for b in range(4)]
        self.number = {}

    def plan(self, *names):
        for name in names:
            assert name not in self.number, name
            self.number[name] = len(self.number)

    def at(self, name):
        return self.psum[:, 4 + self.number[name] % 4, :]

    def claim(self, pe, name):
        n = self.number[name]
        if n >= 4:
            pe.wait_ge(self.free[n % 4], n // 4)
        return self.at(name)

    def filled(self, ins, name):
        ins.then_inc(self.ready[self.number[name] % 4], 1)

    def wait(self, eng, name):
        n = self.number[name]
        eng.wait_ge(self.ready[n % 4], n // 4 + 1)
        return self.at(name)

    def read(self, ins, name):
        ins.then_inc(self.free[self.number[name] % 4], 1)

    def release(self, eng, name):
        eng.sem_inc(self.free[self.number[name] % 4], 1)

    def wait_read(self, eng, name):
        n = self.number[name]
        eng.wait_ge(self.free[n % 4], n // 4 + 1)


R_NORM, R_LB, R_HGN, R_LNG, R_LNB, R_FQ, R_FK, R_MQ, R_MKV, N_ROWS = 0, 48, 56, 57, 89, 121, 122, 123, 125, 126


class Core:

    def __init__(self, ctx, nc, a):
        self.ctx, self.nc, self.a = ctx, nc, a
        f32 = lambda n, s, d=F32: ctx.enter_context(nc.sbuf_tensor(n, s, d))
        self.ring = Ring(ctx, nc, f32("weight_ring", [P, SLOTS, SLOT]))
        with ExitStack() as split:
            fr = lambda n, s: split.enter_context(nc.sbuf_tensor(n, s, F32R))
            self.w_hi, self.w_lo = fr("w_hi", [P, 2, SLOT // 2]), fr("w_lo", [P, 2, SLOT // 2])
            self.x_hi, self.x_lo = fr("x_hi", [P, KD, T]), fr("x_lo", [P, KD, T])
            self.h_hi, self.h_lo = fr("h_hi", [P, 2, T]), fr("h_lo", [P, 2, T])
        self.arena = f32("arena", [P, ARENA])
        self.x = f32("x_res", [P, KD, T])
        self.wide = f32("wide", [P, 2, KD, T])
        self.xn, self.cat = self.wide[:, 0], self.wide[:, 1]
        self.gate_b = self.wide[:].rearrange("p a k t -> p (a k) t")
        self.sq = f32("squares", [P, KD, T])
        self.sg = f32("silu_gate", [P, 2, T])
        self.h32 = f32("hidden", [P, 2, T])
        self.hraw = f32("hidden_ungated", [P, 2, T])
        self.std, self.rstd = f32("std", [P, T]), f32("rstd", [P, T])
        self.c = f32("consts", [P, N_CONST])
        self.param = f32("params", [P, P])
        self.pe_cols = f32("cmp_pe_cols", [P, 32])
        self.lb, self.omlb, self.lb_e, self.lb_r, self.ends01 = (f32(n, [P, 8]) for n in ("lb", "omlb", "lb_e", "lb_r", "ends01"))
        self.zeros = f32("zeros", [P, 512], BF16)
        self.psum = ctx.enter_context(nc.psum_tensor("banks", [P, 8, 512], F32))
        self.acc = self.psum[:, 0:4, :].rearrange("p b (h t) -> p (b h) t", h=2)
        self.banks = Banks(ctx, nc, self.psum)
        s = lambda n: ctx.enter_context(nc.semaphore(n))
        self.s = s
        self.const_ready, self.zero_ready, self.rows_ready = s("const_ready"), s("zero_ready"), s("rows_ready")
        self.x_ready = s("x_ready")
        self.x_turns = 0
        self.norm_sq, self.xn_ready, self.norm_rstd = s("norm_sq"), s("xn_ready"), s("norm_rstd")
        self.xs_hi, self.xs_lo = s("xs_hi"), s("xs_lo")
        self.norms, self.splits = 0, 0
        self.gu_hi, self.gu_lo, self.out_hi, self.out_lo = s("gu_hi"), s("gu_lo"), s("out_hi"), s("out_lo")
        self.gu_ready, self.out_used, self.h_ready = s("gu_ready"), s("out_used"), s("h_ready")
        self.sg_ready, self.h_prod, self.h_raw = s("sg_ready"), s("h_prod"), s("h_raw")
        self.steps, self.raws = 0, 0
        self.att_max, self.att_exp, self.att_sum, self.att_norm, self.att_out = (
            s("att_" + n) for n in ("max", "exp", "sum", "norm", "out"))
        self.att_units = 0
        self.att_cols = f32("att_cols", [P, 3, 8])
        self.ln_sq, self.ln_centred, self.ln_rstd, self.ln_scaled = (s("ln_" + n) for n in ("sq", "centred", "rstd", "scaled"))
        self.layer_norms = 0
        self.rope = f32("rope", [P, 2, 2, T])
        self.rope_ready = s("rope_ready")
        self.pos = f32("positions", [P, T], I32)
        self.cmp_w2 = f32("cmp_w2", [P, 2, HD])
        self.w_route = f32("w_route", [P, 2, KD, G_N + E_N])
        self.b_route = f32("b_route", [P, 2, G_N + E_N])
        self.wz, self.bf = f32("fox_w_z", [P, KD, FOX_H]), f32("fox_b_f", [FOX_H, 1])
        self.small_ready = s("small_ready")
        self.small_loads()
        self.act_seq, self.dve_seq, self.pool_seq = Counted(s("act_seq")), Counted(s("dve_seq")), Counted(s("pool_seq"))

    def small_loads(self):
        a = self.a
        loads = [
            (self.wz[:], a["fox_w_in"][0][:, 4 * D:4 * D + FOX_H].rearrange("(k p) n -> p k n", p=P)),
            (self.bf[:], a["fox_b_f"].rearrange("o h -> h o")),
            (self.pos[:], a["positions_2"].partition_broadcast(P)),
            (self.cmp_w2[:], a["nsa_cmp_w2_2"][0].rearrange("v p n -> p v n")),
        ]
        for layer in range(2):
            loads += [
                (self.w_route[:, layer, :, 0:G_N], a["moe_w_grp_2"][layer].rearrange("(k p) n -> p k n", p=P)),
                (self.w_route[:, layer, :, G_N:G_N + E_N], a["moe_w_exp_2"][layer].rearrange("(k p) n -> p k n", p=P)),
                (self.b_route[:, layer, 0:G_N], a["moe_b_grp_2"][layer:layer + 1, :].partition_broadcast(P)),
                (self.b_route[:, layer, G_N:G_N + E_N], a["moe_b_exp_2"][layer:layer + 1, :].partition_broadcast(P)),
            ]
        loads += [
        ]
        self.small_all = 16 * len(loads)
        return loads

    def const(self, at, n, p=P):
        return self.c[0:p, at:at + n]

    @property
    def ident(self):
        return self.const(C_IDENT, P)

    @property
    def ones(self):
        return self.const(C_ONES, P)


class Start:

    def __init__(self, k):
        self.k = k
        self.fill = k.ring.plan(1)
        self.rows = k.sq[:].rearrange("p k t -> p (k t)")[:, 0:P]
        self.pe_rows = k.sq[:].rearrange("p k t -> p (k t)")[0:32, P:2 * P]
        k.banks.plan("params", "x0", "x1", "x2", "x3")
        self.turn = k.x_turns
        k.x_turns += 1

    def sp(self, eng):
        k, r = self.k, self.k.ring
        r.wait_free(eng, self.fill)
        xt = r.slot(self.fill)[:, 0:TT * D].rearrange("p (t d) -> p t d", t=TT)
        eng.dma_start(xt, k.a["x"].rearrange("o (t p) d -> p (o t) d", p=P)).then_inc(r.full[self.fill % SLOTS], 16)

    def act_dma(self, eng):
        k, a = self.k, self.k.a
        eng.dma_start(k.c[:], a["consts"]).then_inc(k.const_ready, 16)
        rows = self.rows
        for at, n, src in [
            (R_NORM, 48, a["norm_g"].rearrange("l n (k p) -> (l n k) p", p=P)),
            (R_LB, 8, a["hg_lb_logits"].rearrange("l (k p) -> (l k) p", p=P)),
            (R_HGN, 1, a["hg_out_norm_g"]),
            (R_LNG, 32, a["ln_g_2"].rearrange("l n (k p) -> (l n k) p", p=P)),
            (R_LNB, 32, a["ln_b_2"].rearrange("l n (k p) -> (l n k) p", p=P)),
            (R_MQ, 2, a["mla_q_norm_2"].rearrange("l (k p) -> (l k) p", p=P)),
            (R_MKV, 1, a["mla_kv_norm_2"]),
        ]:
            eng.dma_start(rows[at:at + n, :], src).then_inc(k.rows_ready, 16)
        for half in (0, HD):
            eng.dma_start(rows[R_FQ:R_FQ + 1, half:half + HD], a["fox_q_norm_g"]).then_inc(k.rows_ready, 16)
            eng.dma_start(rows[R_FK:R_FK + 1, half:half + HD], a["fox_k_norm_g"]).then_inc(k.rows_ready, 16)
        eng.dma_start(self.pe_rows, a["nsa_cmp_pe_2"].rearrange("o v (l e) d -> (o v l) (e d)", e=2)).then_inc(k.rows_ready, 16)

        for dst, src in k.small_loads():
            eng.dma_start(dst, src, allow_slow_non_contiguous=True).then_inc(k.small_ready, 16)

    def pool(self, eng):
        k = self.k
        eng.memset(k.zeros[:], 0.0).then_inc(k.zero_ready, 1)

    def pe(self, pe):
        k, b = self.k, self.k.banks
        pe.wait_ge(k.const_ready, 16)
        k.ring.wait_full(pe, self.fill)
        xt = k.ring.slot(self.fill)
        for q in range(4):
            out = b.claim(pe, f"x{q}") if q else None
            if q == 0:
                pe.wait_ge(k.rows_ready, 12 * 16)
                out = b.claim(pe, "params")
                pe.transpose(out[:, 0:N_ROWS], self.rows[0:N_ROWS, :], k.ident[0:N_ROWS, 0:N_ROWS])
                b.filled(pe.transpose(out[:, P:P + 32], self.pe_rows, k.ident[0:32, 0:32]), "params")
                out = b.claim(pe, "x0")
            for n in range(4):
                kk, t = 2 * q + n // 2, n % 2
                last = pe.transpose(out[:, n * P:(n + 1) * P], xt[:, t * D + kk * P:t * D + (kk + 1) * P], k.ident)
            b.filled(last, f"x{q}")

    def dve(self, dve):
        k, b = self.k, self.k.banks
        src = b.wait(dve, "params")
        dve.tensor_copy(k.param[:, 0:N_ROWS], src[:, 0:N_ROWS])
        b.read(dve.tensor_copy(k.pe_cols[:], src[:, P:P + 32]), "params")
        for q in range(4):
            src = b.wait(dve, f"x{q}")
            ins = dve.tensor_copy(k.x[:, 2 * q:2 * q + 2, :].rearrange("p k t -> p (k t)"), src)
            ins.then_inc(k.x_ready, 1)
        dve.wait_ge(k.x_ready, 4)
        for q in range(4):
            b.release(dve, f"x{q}")
        dve.sem_inc(k.ring.free[self.fill % SLOTS], 1)


class RmsNorm:

    def __init__(self, k, row):
        self.k, self.row, self.i, self.turn = k, row, k.norms, k.x_turns
        k.norms += 1
        k.banks.plan(f"norm{self.i}")

    def act_squares(self, act):
        k = self.k
        for c in range(4):
            act.wait_ge(k.x_ready, 4 * (self.turn - 1) + c + 1)
            act.activation(k.sq[:, 2 * c:2 * c + 2], k.x[:, 2 * c:2 * c + 2], ACT.Square).then_inc(k.norm_sq, 1)

    def pe(self, pe):
        k = self.k
        out = k.banks.claim(pe, f"norm{self.i}")[:, 0:T]
        for kk in range(KD):
            if kk % 2 == 0:
                pe.wait_ge(k.norm_sq, 4 * self.i + kk // 2 + 1)
            last = pe.matmul(out, k.ones, k.sq[:, kk], start=kk == 0, stop=kk == KD - 1)
        k.banks.filled(last, f"norm{self.i}")

    def act_std(self, act):
        k = self.k
        src = k.banks.wait(act, f"norm{self.i}")[:, 0:T]
        k.banks.read(act.activation(k.std[:], src, ACT.Sqrt, bias=k.const(C_EPS, 1), scale=1.0 / D), f"norm{self.i}")

    def dve(self, dve):
        k = self.k
        k.banks.wait_read(dve, f"norm{self.i}")
        dve.reciprocal(k.rstd[:], k.std[:]).then_inc(k.norm_rstd, 1)
        dve.wait_ge(k.norm_rstd, self.i + 1)
        for kk in range(KD):
            g = k.param[:, R_NORM + self.row * KD + kk:R_NORM + self.row * KD + kk + 1]
            dve.scalar_tensor_tensor(out=k.xn[:, kk], in0=k.x[:, kk], scalar=g, in1=k.rstd[:],
                                     op0=ALU.mult, op1=ALU.mult).then_inc(k.xn_ready, 1)

    def wait_xn(self, eng, tiles=KD):
        eng.wait_ge(self.k.xn_ready, KD * self.i + tiles)


class Ffn:

    PARTS = 3

    def __init__(self, k, steps, sources, norm=None, gated=False):
        self.k, self.steps, self.sources, self.norm, self.gated = k, steps, sources, norm, gated
        self.j0, self.r0, self.split = k.steps, k.raws, k.splits
        k.steps += steps
        k.raws += steps if gated else 0
        k.splits += 1
        self.fills = [k.ring.plan(3) for _ in range(steps // 2)]
        self.body = 12 if gated else 6
        self.turns = (steps - 1) // self.body
        self.rest = steps - 1 - self.turns * self.body
        if norm is not None:
            self.turn = k.x_turns
            k.x_turns += 1

    def fill_more(self, i):
        return i * (48 * self.body // 6)

    def sp(self, eng):
        k, r, half = self.k, self.k.ring, self.body // 2
        turns = (self.steps // 2) // half

        def load(f, i, more):
            n = self.fills[f]
            r.wait_free(eng, n, more)
            slot, full = r.slot(n), r.full[n % SLOTS]
            wg, wu, wd = self.sources(i, f)
            for at, src in ((0, wg), (1, wu)):
                eng.dma_start(slot[:, at * 2048:(at + 1) * 2048].rearrange("p (k n) -> p k n", k=KD),
                              src).then_inc(full, 16)
            eng.dma_start(slot[:, 4096:6144].rearrange("p (j n) -> p j n", j=2), wd).then_inc(full, 16)

        with eng.Fori(0, turns) as i:
            for f in range(half):
                load(f, i, i * (half // SLOTS))
        for f in range(turns * half, self.steps // 2):
            load(f, 0, 0)

    def act_split(self, act, j, base, more):
        k, n = self.k, self.fills[j // 2]
        b, jj, raw = j % 2, j % 2, k.ring.slot(n)
        k.ring.wait_full(act, n, more)
        act.wait_ge(k.gu_ready, base + 1)
        act.activation(k.w_hi[:, b, 0:2048].rearrange("p (k n) -> p k n", n=P),
                       raw[:, 0:4096].rearrange("p (k n) -> p k n", n=256)[:, :, jj * P:(jj + 1) * P],
                       ACT.Copy).then_inc(k.gu_hi, 1)
        act.wait_ge(k.out_used, base + 1)
        act.activation(k.w_hi[:, b, 2048:3072], raw[:, 4096 + jj * D:4096 + (jj + 1) * D],
                       ACT.Copy).then_inc(k.out_hi, 1)

    def dve_split(self, dve, j, base):
        k, n = self.k, self.fills[j // 2]
        b, jj, raw = j % 2, j % 2, k.ring.slot(n)
        dve.wait_ge(k.gu_hi, base + 1)
        dve.tensor_tensor(k.w_lo[:, b, 0:2048].rearrange("p (k n) -> p k n", n=P),
                          raw[:, 0:4096].rearrange("p (k n) -> p k n", n=256)[:, :, jj * P:(jj + 1) * P],
                          k.w_hi[:, b, 0:2048].bitcast(F32).rearrange("p (k n) -> p k n", n=P),
                          ALU.subtract).then_inc(k.gu_lo, 1)
        dve.wait_ge(k.out_hi, base + 1)
        dve.tensor_tensor(k.w_lo[:, b, 2048:3072], raw[:, 4096 + jj * D:4096 + (jj + 1) * D],
                          k.w_hi[:, b, 2048:3072].bitcast(F32), ALU.subtract).then_inc(k.out_lo, 1)

    def dve_release(self, dve, j, base):
        if j % 2 == 1:
            dve.wait_ge(self.k.out_lo, base + 1)
            dve.sem_inc(self.k.ring.free[self.fills[j // 2] % SLOTS], 1)

    def act_silu(self, act, j, base):
        k, b = self.k, j % 2
        act.wait_ge(k.h_ready, base + 1)
        act.wait_ge(k.gu_ready, base + 3)
        act.activation(k.sg[:, b], k.psum[:, 4 + b, 0:T], ACT.Silu).then_inc(k.sg_ready, 1)

    def dve_hidden(self, dve, j, base, raw_base, expert):
        k, b = self.k, j % 2
        dve.wait_ge(k.sg_ready, base + 1)
        left, right = k.sg[:, b], k.psum[:, 4 + b, T:2 * T]
        if self.gated:
            dve.tensor_tensor(k.hraw[:, b], left, right, ALU.mult).then_inc(k.h_raw, 1)
            dve.wait_ge(k.h_raw, raw_base + 1)
            left = k.hraw[:, b]
            right = k.gate_b[:, expert, :] if isinstance(expert, int) else k.gate_b[:, ds(expert, 1), :].rearrange("p o t -> p (o t)")
        dve.tensor_tensor(k.h32[:, b], left, right, ALU.mult).then_inc(k.h_prod, 1)
        dve.wait_ge(k.out_used, base + 1)
        dve.tensor_tensor(k.h_hi[:, b], left, right, ALU.mult).then_inc(k.h_prod, 1)
        dve.wait_ge(k.h_prod, 2 * base + 2)
        dve.tensor_tensor(k.h_lo[:, b], k.h32[:, b], k.h_hi[:, b].bitcast(F32), ALU.subtract).then_inc(k.h_ready, 1)

    def pool(self, pool):
        pass

    def pe_three(self, pe, out, w_hi, w_lo, m_hi, m_lo, start, stop):
        pe.matmul(out, w_hi, m_hi, start=start, stop=False, skip_group_check=True)
        pe.matmul(out, w_hi, m_lo, start=False, stop=False, skip_group_check=True)
        return pe.matmul(out, w_lo, m_hi, start=False, stop=stop, skip_group_check=True)

    def pe_gate_up(self, pe, b, base):
        k = self.k
        pe.wait_ge(k.gu_lo, base + 1)
        pe.wait_ge(k.h_ready, base + 1)
        for part in range(2):
            for kk in range(KD):
                at = (part * KD + kk) * P
                last = self.pe_three(pe, k.psum[:, 4 + b, part * T:(part + 1) * T],
                                     k.w_hi[:, b, at:at + P], k.w_lo[:, b, at:at + P],
                                     k.x_hi[:, kk], k.x_lo[:, kk], kk == 0, kk == KD - 1)
        last.then_inc(k.gu_ready, 1)

    def pe_down(self, pe, b, base):
        k = self.k
        pe.wait_ge(k.out_lo, base + 1)
        pe.wait_ge(k.h_ready, base + 3)
        for n in range(KD):
            at = 2048 + n * P
            last = self.pe_three(pe, k.acc[:, n], k.w_hi[:, b, at:at + P], k.w_lo[:, b, at:at + P],
                                 k.h_hi[:, b], k.h_lo[:, b], False, True)
        last.then_inc(k.out_used, 1)

    def pe(self, pe):
        k = self.k
        self.pe_before(pe)
        pe.wait_ge(k.xs_lo, 4 * self.split + 4)
        for bank in range(4):
            pe.matmul(k.psum[:, bank, :], k.zeros[:, 0:P], k.zeros[:], start=True, stop=True, skip_group_check=True)
        self.pe_gate_up(pe, 0, self.j0)
        turns, rest = divmod(self.steps - 1, 2)
        with pe.Fori(0, turns) as i:
            for t in range(2):
                self.pe_gate_up(pe, (t + 1) % 2, i * 2 + (self.j0 + t + 1))
                self.pe_down(pe, t % 2, i * 2 + (self.j0 + t))
        for j in range(2 * turns, self.steps - 1):
            self.pe_gate_up(pe, (j + 1) % 2, self.j0 + j + 1)
            self.pe_down(pe, j % 2, self.j0 + j)
        self.pe_down(pe, (self.steps - 1) % 2, self.j0 + self.steps - 1)

    def act_input(self, act):
        k, src = self.k, self.k.xn if self.norm is not None else self.k.x
        for c in range(4):
            if self.norm is not None:
                self.norm.wait_xn(act, 2 * c + 2)
            act.activation(k.x_hi[:, 2 * c:2 * c + 2], src[:, 2 * c:2 * c + 2], ACT.Copy).then_inc(k.xs_hi, 1)

    def dve_input(self, dve):
        k, src = self.k, self.k.xn if self.norm is not None else self.k.x
        for c in range(4):
            dve.wait_ge(k.xs_hi, 4 * self.split + c + 1)
            dve.tensor_tensor(k.x_lo[:, 2 * c:2 * c + 2], src[:, 2 * c:2 * c + 2],
                              k.x_hi[:, 2 * c:2 * c + 2].bitcast(F32), ALU.subtract).then_inc(k.xs_lo, 1)

    def pe_before(self, pe):
        self.norm.pe(pe)

    def act_before(self, act):
        self.norm.act_squares(act)
        self.act_split(act, 0, self.j0, 0)
        self.norm.act_std(act)

    def act_after(self, act):
        pass

    def dve_before(self, dve):
        self.dve_split(dve, 0, self.j0)
        self.norm.dve(dve)

    def dve_after(self, dve):
        pass

    def act(self, act):
        self.act_before(act)
        self.act_input(act)
        self.act_after(act)
        with act.Fori(0, self.turns) as i:
            for t in range(self.body):
                self.act_split(act, t + 1, i * self.body + (self.j0 + t + 1), self.fill_more(i))
                self.act_silu(act, t, i * self.body + (self.j0 + t))
        for j in range(self.turns * self.body, self.steps - 1):
            self.act_split(act, j + 1, self.j0 + j + 1, 0)
            self.act_silu(act, j, self.j0 + j)
        self.act_silu(act, self.steps - 1, self.j0 + self.steps - 1)

    def dve(self, dve):
        k = self.k
        self.dve_before(dve)
        self.dve_input(dve)
        self.dve_after(dve)
        with dve.Fori(0, self.turns) as i:
            for t in range(self.body):
                base = i * self.body + self.j0
                self.dve_split(dve, t + 1, base + (t + 1))
                self.dve_hidden(dve, t, base + t, i * self.body + (self.r0 + t), i * (self.body // 4) + t // 4)
                self.dve_release(dve, t + 1, base + (t + 1))
        for j in range(self.turns * self.body, self.steps - 1):
            self.dve_split(dve, j + 1, self.j0 + j + 1)
            self.dve_hidden(dve, j, self.j0 + j, self.r0 + j, j // 4)
            self.dve_release(dve, j + 1, self.j0 + j + 1)
        j = self.steps - 1
        self.dve_hidden(dve, j, self.j0 + j, self.r0 + j, j // 4)
        dve.wait_ge(k.out_used, self.j0 + self.steps + 2)
        self.dve_residual(dve)

    def dve_residual(self, dve):
        k = self.k
        for c in range(4):
            dve.scalar_tensor_tensor(out=k.x[:, 2 * c:2 * c + 2], in0=k.acc[:, 2 * c:2 * c + 2], scalar=0.5,
                                     in1=k.x[:, 2 * c:2 * c + 2], op0=ALU.mult, op1=ALU.add).then_inc(k.x_ready, 1)


def swiglu_sources(a, layer, half):
    w_in, w_out = a["ffn_w_in"][layer, half], a["ffn_w_out"][layer, half]

    def sources(i, f):
        p = i * 3 + f
        cols = lambda at: w_in[:, ds(p * 256 + at, 256)].rearrange("(k q) n -> q k n", q=P)
        return cols(0), cols(FF), w_out[ds(p * 256, 256), :].rearrange("(j q) n -> q j n", q=P)
    return sources


class Finish:

    def __init__(self, k):
        self.k = k
        self.turn = k.x_turns
        k.banks.plan("y0", "y1", "y2", "y3")
        self.stored, self.turned = k.s("stored"), k.s("turned")
        self.y = k.arena[:, 0:TT * D].rearrange("p (t d) -> p t d", t=TT)

    def pe(self, pe):
        k, b = self.k, self.k.banks
        pe.wait_ge(k.x_ready, 4 * self.turn)
        for q in range(4):
            out = b.claim(pe, f"y{q}")
            for n in range(4):
                t, kk = q // 2, (q % 2) * 4 + n
                last = pe.transpose(out[:, n * P:(n + 1) * P], k.x[:, kk, t * P:(t + 1) * P], k.ident)
            b.filled(last, f"y{q}")

    def dve(self, dve):
        k, b = self.k, self.k.banks
        for q in range(4):
            src = b.wait(dve, f"y{q}")
            b.read(dve.tensor_copy(self.y[:, q // 2, (q % 2) * 512:(q % 2 + 1) * 512], src), f"y{q}")

    def sp(self, eng):
        k, b = self.k, self.k.banks
        for q in range(4):
            b.wait_read(eng, f"y{q}")
            eng.dma_start(k.a["out"][0, (q // 2) * P:(q // 2 + 1) * P, (q % 2) * 512:(q % 2 + 1) * 512],
                          self.y[:, q // 2, (q % 2) * 512:(q % 2 + 1) * 512]).then_inc(self.stored, 16)
        eng.wait_ge(self.stored, 64)


class Mixer:

    def plan_blocks(self, blocks, per_fill=3):
        self.block_fill = {}
        for at in range(0, len(blocks), per_fill):
            some = blocks[at:at + per_fill]
            n = self.k.ring.plan(len(some))
            for i, (name, src) in enumerate(some):
                self.block_fill[name] = (n, i, src)

    def sp_blocks(self, eng):
        k, last = self.k, None
        for n, i, src in self.block_fill.values():
            if n != last:
                k.ring.wait_free(eng, n)
                last = n
            width = src.shape[1]
            eng.dma_start(k.ring.slot(n)[:, i * 2048:i * 2048 + KD * width].rearrange("p (k n) -> p k n", k=KD),
                          src.rearrange("(k p) n -> p k n", p=P)).then_inc(k.ring.full[n % SLOTS], 16)

    def block(self, name):
        n, i, src = self.block_fill[name]
        width = src.shape[1]
        return n, self.k.ring.slot(n)[:, i * 2048:i * 2048 + KD * width].rearrange("p (k n) -> p k n", k=KD)

    def project(self, pe, out, w, moving, start=True):
        for kk in range(KD):
            last = pe.matmul(out, w(kk), moving[:, kk], start=kk == 0, stop=kk == KD - 1)
        return last

    def release(self, eng, fill):
        eng.sem_inc(self.k.ring.free[fill % SLOTS], 1)

    def plan_out(self, name, w_out):
        k = self.k
        self.w_out, self.out_fills = w_out, [k.ring.plan(1), k.ring.plan(1)]
        self.out_ready = k.s(name + "_out_ready")
        self.turn = k.x_turns
        k.x_turns += 1

    def sp_out(self, eng):
        k = self.k
        for half, n in enumerate(self.out_fills):
            k.ring.wait_free(eng, n)
            eng.dma_start(k.ring.slot(n)[:, 0:4096].rearrange("p (k n) -> p k n", k=KD),
                          self.w_out[:, half * 512:(half + 1) * 512].rearrange("(k p) n -> p k n", p=P)
                          ).then_inc(k.ring.full[n % SLOTS], 16)

    def pe_out(self, pe):
        k = self.k
        for n in range(KD):
            fill = self.out_fills[n // 4]
            if n % 4 == 0:
                k.ring.wait_full(pe, fill)
            w = k.ring.slot(fill)
            last = self.project(pe, k.acc[:, n], lambda kk: w[:, kk * 512 + (n % 4) * P:kk * 512 + (n % 4 + 1) * P], k.cat)
            if n % 2:
                last.then_inc(self.out_ready, 1)

    def dve_out(self, dve, scale=1.0):
        k = self.k
        for c in range(4):
            dve.wait_ge(self.out_ready, c + 1)
            if c % 2:
                self.release(dve, self.out_fills[c // 2])
            dve.scalar_tensor_tensor(out=k.x[:, 2 * c:2 * c + 2], in0=k.x[:, 2 * c:2 * c + 2], scalar=scale,
                                     in1=k.acc[:, 2 * c:2 * c + 2], op0=ALU.mult, op1=ALU.add).then_inc(k.x_ready, 1)


class Hgrn2(Mixer):

    def __init__(self, k, norm):
        self.k, self.norm = k, norm
        a = k.a
        w = a["hg_w_in"][0]
        cols = lambda part, n: w[:, part * D + n * 256:part * D + (n + 1) * 256]
        self.plan_blocks([(f"z{n}", cols(1, n)) for n in range(4)] + [(f"q{n}", cols(0, n)) for n in range(4)]
                         + [(f"g{n}", cols(3, n)) for n in range(4)])
        self.v_fills = [k.ring.plan(1), k.ring.plan(1)]
        self.plan_out("hg", a["hg_w_out"][0])
        k.banks.plan(*[f"hg_{p}{n}" for p in "zqg" for n in range(4)])
        k.banks.plan(*[f"hg_v{h}{t}" for h in range(2) for t in range(TT)])
        k.banks.plan(*[f"hg_s{n}_{g}" for n in [7, 0, 1, 2, 3, 4, 5, 6] for g in range(4)], "hg_x0", "hg_x1")
        k.banks.plan(*[f"hg_n{n}" for n in range(4)])
        ar = k.arena
        part = lambda n: ar[:, n * 2048:(n + 1) * 2048].rearrange("p (h t) -> p h t", h=HG_H)
        self.q, self.kk, self.b, self.g, self.e = part(0), part(1), part(2), part(3), [part(4), part(5)]
        self.v = ar[:, 6 * 2048:7 * 2048].rearrange("p (t d) -> p t d", t=TT)
        self.score = ar[:, 7 * 2048:7 * 2048 + 2048].rearrange("p (m t) -> p m t", m=16)
        self.cross = ar[:, 8 * 2048:8 * 2048 + 1024].rearrange("p (h t) -> p h t", h=HG_H)
        self.std = self.e[0]
        s = lambda n: k.s("hg_" + n)
        self.sig, self.qg, self.f_ready, self.ln_ready, self.b_ready = s("sig"), s("qg"), s("f"), s("ln"), s("b")
        self.diff, self.exped, self.scaled = s("diff"), s("exped"), s("scaled")
        self.o_ready, self.o_sq, self.o_rstd, self.o_normed, self.cat_ready = s("o"), s("o_sq"), s("o_rstd"), s("o_normed"), s("cat")

    def sp(self, eng):
        k = self.k
        self.sp_blocks(eng)
        for half, n in enumerate(self.v_fills):
            k.ring.wait_free(eng, n)
            eng.dma_start(k.ring.slot(n)[:, 0:4096].rearrange("p (k n) -> p k n", k=KD),
                          k.a["hg_w_in"][0][:, 2 * D + half * 512:2 * D + (half + 1) * 512].rearrange("(k p) n -> p k n", p=P)
                          ).then_inc(k.ring.full[n % SLOTS], 16)
        self.sp_out(eng)

    def pe(self, pe):
        k, b = self.k, self.k.banks
        self.norm.pe(pe)
        self.norm.wait_xn(pe)
        for part in "zqg":
            for n in range(4):
                fill, w = self.block(f"{part}{n}")
                k.ring.wait_full(pe, fill)
                out = b.claim(pe, f"hg_{part}{n}")
                for h in range(2):
                    last = self.project(pe, out[:, h * T:(h + 1) * T], lambda kk: w[:, kk, h * P:(h + 1) * P], k.xn)
                b.filled(last, f"hg_{part}{n}")
        for half, n in enumerate(self.v_fills):
            k.ring.wait_full(pe, n)
            w = k.ring.slot(n)[:, 0:4096].rearrange("p (k n) -> p k n", k=KD)
            for t in range(TT):
                out = b.claim(pe, f"hg_v{half}{t}")
                b.filled(self.project(pe, out, lambda kk: k.xn[:, kk, t * P:(t + 1) * P], w), f"hg_v{half}{t}")
        for i, n in enumerate([7, 0, 1, 2, 3, 4, 5, 6]):
            if n == 7:
                pe.wait_ge(self.qg, 4)
            else:
                pe.wait_ge(self.scaled, 2 * (n + 1))
            e = self.e[n % 2]
            for g in range(4):
                out = b.claim(pe, f"hg_s{n}_{g}")
                for m in range(4 * g, 4 * g + 4):
                    h, t = m // 2, slice(m % 2 * P, (m % 2 + 1) * P)
                    left, right = (self.kk, self.q) if n == 7 else (e, e)
                    last = pe.matmul(out[:, (m % 4) * P:(m % 4 + 1) * P], left[:, h, t], right[:, h, t], start=True, stop=True)
                b.filled(last, f"hg_s{n}_{g}")
        pe.wait_ge(self.scaled, 16)
        for g in range(2):
            out = b.claim(pe, f"hg_x{g}")
            for h in range(4 * g, 4 * g + 4):
                last = pe.matmul(out[:, (h % 4) * P:(h % 4 + 1) * P], self.e[1][:, h, 0:P], self.e[1][:, h, P:T], start=True, stop=True)
            b.filled(last, f"hg_x{g}")
        b.wait_read(pe, "hg_v11")
        b.wait_read(pe, "hg_s6_3")
        b.wait_read(pe, "hg_x1")
        for h in range(HG_H):
            v = [self.v[:, t, h * P:(h + 1) * P] for t in range(TT)]
            pe.matmul(k.acc[:, h, 0:P], v[0], self.score[:, 2 * h], start=True, stop=True)
            pe.matmul(k.acc[:, h, P:T], v[0], self.cross[:, h], start=True, stop=False)
            last = pe.matmul(k.acc[:, h, P:T], v[1], self.score[:, 2 * h + 1], start=False, stop=True)
            if h % 2:
                last.then_inc(self.o_ready, 1)
        for n in range(4):
            pe.wait_ge(self.o_sq, n + 1)
            out = b.claim(pe, f"hg_n{n}")
            b.filled(pe.matmul(out, k.ones, k.sq[:, 2 * n:2 * n + 2], start=True, stop=True), f"hg_n{n}")
        pe.wait_ge(self.cat_ready, 4)
        self.pe_out(pe)

    def act(self, act):
        k, b = self.k, self.k.banks
        self.norm.act_squares(act)
        self.norm.act_std(act)
        for n in range(4):
            src = b.wait(act, f"hg_z{n}").rearrange("p (h t) -> p h t", h=2)
            act.activation(self.b[:, 2 * n:2 * n + 2], src, ACT.Sigmoid).then_inc(self.sig, 1)
            b.read(act.activation(self.kk[:, 2 * n:2 * n + 2], src, ACT.Sigmoid, scale=-1.0), f"hg_z{n}")
        for part, to in (("q", self.q), ("g", self.g)):
            for n in range(4):
                src = b.wait(act, f"hg_{part}{n}").rearrange("p (h t) -> p h t", h=2)
                act.activation(to[:, 2 * n:2 * n + 2], src, ACT.Sigmoid).then_inc(self.sig, 1)
        act.wait_ge(self.f_ready, 4)
        act.activation(self.e[0], self.e[0], ACT.Ln).then_inc(self.ln_ready, 1)
        for half in range(2):
            for t in range(TT):
                src = b.wait(act, f"hg_v{half}{t}")
                b.read(act.activation(self.v[:, t, half * 512:(half + 1) * 512], src, ACT.Copy), f"hg_v{half}{t}")
            self.release(act, self.v_fills[half])
        for n in range(8):
            act.wait_ge(self.diff, self.diffs[n])
            act.activation(self.e[n % 2], self.e[n % 2], ACT.Exp).then_inc(self.exped, 1)
        for g in range(2):
            src = b.wait(act, f"hg_x{g}").rearrange("p (h t) -> p h t", h=4)
            b.read(act.activation(self.cross[:, 4 * g:4 * g + 4], src, ACT.Copy), f"hg_x{g}")
        for n in range(4):
            act.wait_ge(self.o_ready, n + 1)
            act.activation(k.sq[:, 2 * n:2 * n + 2], k.acc[:, 2 * n:2 * n + 2], ACT.Square).then_inc(self.o_sq, 1)
        for n in range(4):
            src = b.wait(act, f"hg_n{n}").rearrange("p (h t) -> p h t", h=2)
            b.read(act.activation(self.std[:, 2 * n:2 * n + 2], src, ACT.Sqrt, bias=k.const(C_EPS, 1), scale=1.0 / P), f"hg_n{n}")

    def level(self, t, L):
        return t.rearrange("p h t -> p (h t)").rearrange("p (n a l) -> p n a l", a=2, l=L)

    diffs = [2, 4, 6, 8, 10, 12, 14, 18]

    def pool(self, pool):
        k, b, seq = self.k, self.k.banks, self.k.pool_seq
        ends = self.b.rearrange("p h (c l) -> p h c l", l=HG_CHUNK)[:, :, :, HG_CHUNK - 1]
        pool.wait_ge(self.b_ready, 8)
        seq.inc(pool.tensor_tensor(k.ends01[:], ends[:, :, 0], ends[:, :, 1], ALU.add))
        for n in range(7):
            L = 1 << n
            if n >= 2:
                b.wait(pool, f"hg_s{n - 2}_3")
            e, c = self.level(self.e[n % 2], L), self.level(self.b, L)
            mid = c[:, :, 0, L - 1:L].to_broadcast([P, c.shape[1], L])
            pool.tensor_tensor(e[:, :, 0, :], mid, c[:, :, 0, :], ALU.subtract).then_inc(self.diff, 1)
            if L < HG_CHUNK:
                pool.tensor_tensor(e[:, :, 1, :], c[:, :, 1, :], mid, ALU.subtract).then_inc(self.diff, 1)
            else:
                pool.tensor_copy(e[:, :, 1, :], c[:, :, 1, :]).then_inc(self.diff, 1)
        b.wait(pool, "hg_s5_3")
        seq.wait(pool)
        chunk = lambda t, c: t[:, :, c * HG_CHUNK:(c + 1) * HG_CHUNK]
        wide = lambda col: col.to_broadcast([P, HG_H, HG_CHUNK])
        e, c = self.e[1], self.b
        pool.tensor_tensor(chunk(e, 0), wide(k.ends01[:].unsqueeze(2)), chunk(c, 0), ALU.subtract).then_inc(self.diff, 1)
        pool.tensor_tensor(chunk(e, 1), wide(c[:, :, 127:128]), chunk(c, 1), ALU.subtract).then_inc(self.diff, 1)
        pool.tensor_copy(chunk(e, 2), chunk(c, 2)).then_inc(self.diff, 1)
        pool.tensor_tensor(chunk(e, 3), chunk(c, 3), wide(c[:, :, 191:192]), ALU.add).then_inc(self.diff, 1)

    def dve(self, dve):
        k, b, seq = self.k, self.k.banks, self.k.dve_seq
        l, w, r = k.param[:, R_LB:R_LB + 8], k.lb_e[:], k.lb_r[:]
        for ins in (lambda: dve.tensor_tensor(w, l, l, ALU.subtract),
                    lambda: dve.tensor_scalar(w, w, 1.0, None, ALU.add),
                    lambda: dve.reciprocal(r, w),
                    lambda: dve.tensor_tensor(r, w, r, ALU.mult),
                    lambda: dve.tensor_tensor(k.lb[:], r, r, ALU.subtract),
                    lambda: dve.tensor_scalar(k.omlb[:], k.lb[:], -1.0, 1.0, ALU.mult, ALU.add)):
            seq.inc(ins())
            seq.wait(dve)
        self.norm.dve(dve)
        seq.inc(dve.memset(self.score, 0.0))
        f, up, off = self.b, self.e[0], self.e[1]
        for h in range(HG_H):
            if h % 2 == 0:
                b.wait_read(dve, f"hg_z{h // 2}")
            if h == 4:
                self.release(dve, self.block_fill["z2"][0])
            seq.inc(dve.tensor_scalar(f[:, h], f[:, h], k.omlb[:, h:h + 1], k.lb[:, h:h + 1], ALU.mult, ALU.add))
            seq.inc(dve.tensor_scalar(self.kk[:, h], self.kk[:, h], k.omlb[:, h:h + 1], None, ALU.mult))
        seq.wait(dve)
        seq.inc(dve.tensor_scalar(f, f, 1e-30, None, ALU.max))
        seq.wait(dve)
        small = 2.0 ** -60
        seq.inc(dve.tensor_scalar(up, f, small, 2.0 ** 36 - 1.0, ALU.is_lt, ALU.mult))
        seq.inc(dve.tensor_scalar(off, f, small, 36.0 * float(np.log(2.0)), ALU.is_lt, ALU.mult))
        seq.wait(dve)
        for c in range(4):
            hs = slice(2 * c, 2 * c + 2)
            dve.scalar_tensor_tensor(out=up[:, hs], in0=up[:, hs], scalar=1.0, in1=f[:, hs], op0=ALU.add, op1=ALU.mult).then_inc(self.f_ready, 1)
        for part, to, at, last in (("q", self.q, 4, "q1"), ("g", self.g, 8, "g0")):
            for n in range(4):
                dve.wait_ge(self.sig, at + n + 1)
                if f"{part}{n}" in ("q1", "g0", "g3"):
                    self.release(dve, self.block_fill[f"{part}{n}"][0])
                src = b.at(f"hg_{part}{n}").rearrange("p (h t) -> p h t", h=2)
                dve.tensor_tensor(to[:, 2 * n:2 * n + 2], to[:, 2 * n:2 * n + 2], src, ALU.mult).then_inc(self.qg, 1)
                if n:
                    dve.wait_ge(self.qg, at - 4 + n)
                    b.release(dve, f"hg_{part}{n - 1}")
            dve.wait_ge(self.qg, at)
            b.release(dve, f"hg_{part}3")
        dve.wait_ge(self.ln_ready, 1)
        seq.inc(dve.tensor_tensor(up, up, off, ALU.subtract))
        seq.wait(dve)
        for h in range(HG_H):
            dve.tensor_tensor_scan(f[:, h], k.const(C_RESET, T), up[:, h], 0.0, ALU.mult, ALU.add).then_inc(self.b_ready, 1)

        def place(n):
            mask = k.const(C_LEVEL + n * P, P).bitcast(U32).unsqueeze(1).to_broadcast([P, 4, P])
            for g in range(4):
                src = b.wait(dve, f"hg_s{n}_{g}").rearrange("p (m t) -> p m t", m=4)
                b.read(dve.copy_predicated(self.score[:, 4 * g:4 * g + 4], mask, src), f"hg_s{n}_{g}")

        for n in range(8):
            dve.wait_ge(self.exped, n + 1)
            e = self.level(self.e[n % 2], 1 << n)
            for half, by in enumerate((self.kk, self.q)):
                dve.tensor_tensor(e[:, :, half, :], e[:, :, half, :], self.level(by, 1 << n)[:, :, half, :],
                                  ALU.mult).then_inc(self.scaled, 1)
            place(n - 1 if n else 7)
        for n in range(4):
            hs = slice(2 * n, 2 * n + 2)
            b.wait_read(dve, f"hg_n{n}")
            dve.reciprocal(self.std[:, hs], self.std[:, hs]).then_inc(self.o_rstd, 1)
            dve.wait_ge(self.o_rstd, n + 1)
            dve.scalar_tensor_tensor(out=self.e[1][:, hs], in0=k.acc[:, hs], scalar=k.param[:, R_HGN:R_HGN + 1],
                                     in1=self.std[:, hs], op0=ALU.mult, op1=ALU.mult).then_inc(self.o_normed, 1)
            dve.wait_ge(self.o_normed, n + 1)
            dve.tensor_tensor(k.cat[:, hs], self.e[1][:, hs], self.g[:, hs], ALU.mult).then_inc(self.cat_ready, 1)
        self.dve_out(dve)


class Attention(Mixer):

    def plan_units(self, name, units, at):
        k = self.k
        self.units, self.u0, self.name = units, k.att_units, name
        k.att_units += len(units)
        n = len(units)
        for i in range(n + 3):
            if i < n:
                k.banks.plan(f"{name}_s{i}")
            if 2 <= i < n + 2:
                k.banks.plan(f"{name}_t{i - 2}")
        part = lambda j: at[:, j * 768:(j + 1) * 768].rearrange("p (r t) -> p r t", r=3)
        self.sc, self.pr, self.pt = part(0), part(1), part(2)
        self.acc_out = {}
        for i, u in enumerate(units):
            self.acc_out[u["out"][0]] = self.u0 + i + 1

    def pe_unit(self, pe, i):
        k, b, n = self.k, self.k.banks, len(self.units)
        if i < n:
            u = self.units[i]
            out = b.claim(pe, f"{self.name}_s{i}")[:, 0:u["n"]]
            pairs = [(u["q"], u["keys"])] + u.get("bias", [])
            for m, (left, right) in enumerate(pairs):
                last = pe.matmul(out, left, right, start=m == 0, stop=m == len(pairs) - 1)
            b.filled(last, f"{self.name}_s{i}")
        if 2 <= i < n + 2:
            u, j = self.units[i - 2], i - 2
            pe.wait_ge(k.att_norm, self.u0 + j + 1)
            out = b.claim(pe, f"{self.name}_t{j}")
            for m, (rows, _) in enumerate(u["values"]):
                last = pe.transpose(out[0:rows, m * P:(m + 1) * P], self.pr[:, j % 3, m * P:m * P + rows], k.ident)
            b.filled(last, f"{self.name}_t{j}")
        if i >= 3:
            u, j = self.units[i - 3], i - 3
            b.wait_read(pe, f"{self.name}_t{j}")
            pair, half, qt = u["out"]
            out = k.acc[half * HD:(half + 1) * HD, pair, qt * P:(qt + 1) * P]
            for m, (rows, v) in enumerate(u["values"]):
                last = pe.matmul(out, v, self.pt[0:rows, j % 3, m * P:(m + 1) * P],
                                 start=u["first"] and m == 0, stop=u["last"] and m == len(u["values"]) - 1)
            last.then_inc(k.att_out, 1)

    def act_unit(self, act, i):
        k, b, n = self.k, self.k.banks, len(self.units)
        if i < n:
            u, c = self.units[i], (self.u0 + i) % 8
            act.wait_ge(k.att_max, self.u0 + i + 1)
            act.activation(self.pr[:, i % 3, 0:u["n"]], self.sc[:, i % 3, 0:u["n"]], ACT.Exp, scale=-1.0,
                           bias=k.att_cols[:, 0, c:c + 1], accum_out=k.att_cols[:, 1, c:c + 1]).then_inc(k.att_exp, 1)
        if 2 <= i < n + 2:
            u, j = self.units[i - 2], i - 2
            src = b.wait(act, f"{self.name}_t{j}")
            if self.u0 + j >= 3:
                act.wait_ge(k.att_out, self.u0 + j - 2)
            rows, w = u["values"][0][0], len(u["values"]) * P
            b.read(act.activation(self.pt[0:rows, j % 3, 0:w], src[0:rows, 0:w], ACT.Copy), f"{self.name}_t{j}")

    def dve_unit(self, dve, i):
        k, b, seq, n = self.k, self.k.banks, self.k.dve_seq, len(self.units)
        if i < n:
            u, c = self.units[i], (self.u0 + i) % 8
            if self.u0 + i >= 3:
                dve.wait_ge(k.att_exp, self.u0 + i - 2)
            src = b.wait(dve, f"{self.name}_s{i}")[:, 0:u["n"]]
            dve.tensor_tensor_reduce(self.sc[:, i % 3, 0:u["n"]], src, u["mask"], -u["scale"], -NEG_BIG, ALU.add, ALU.min,
                                     k.att_cols[:, 0, c:c + 1]).then_inc(k.att_max, 1)
            dve.wait_ge(k.att_max, self.u0 + i + 1)
            b.release(dve, f"{self.name}_s{i}")
        if i >= 1 and i - 1 < n:
            u, j = self.units[i - 1], i - 1
            c = (self.u0 + j) % 8
            total, weight = k.att_cols[:, 1, c:c + 1], k.att_cols[:, 2, c:c + 1]
            dve.wait_ge(k.att_exp, self.u0 + j + 1)
            if u["seen"] is not None:
                pr = self.pr[:, j % 3, 0:u["n"]]
                seq.inc(dve.tensor_tensor_reduce(pr, pr, u["seen"], 1.0, 0.0, ALU.mult, ALU.add, total))
                seq.wait(dve)
                seq.inc(dve.tensor_scalar(total, total, 1e-30, None, ALU.max))
                seq.wait(dve)
            if u["gate"] is None:
                dve.reciprocal(weight, total).then_inc(k.att_sum, 1)
            else:
                seq.inc(dve.reciprocal(total, total))
                seq.wait(dve)
                dve.tensor_tensor(weight, total, u["gate"], ALU.mult).then_inc(k.att_sum, 1)

    def pool_units(self, pool):
        k = self.k
        for j, u in enumerate(self.units):
            c, pr = (self.u0 + j) % 8, self.pr[:, j % 3, 0:u["n"]]
            pool.wait_ge(k.att_sum, self.u0 + j + 1)
            pool.tensor_scalar(pr, pr, k.att_cols[:, 2, c:c + 1], None, ALU.mult).then_inc(k.att_norm, 1)

    def run(self, eng, unit):
        for i in range(len(self.units) + 3):
            unit(eng, i)


class Fox(Attention):

    def __init__(self, k, norm):
        self.k, self.norm = k, norm
        a, ar, b = k.a, k.arena, k.banks
        w = a["fox_w_in"][0]
        cols = lambda part, n: w[:, part * D + n * 256:part * D + (n + 1) * 256]
        self.normed = [f"k{n}" for n in range(4)] + [f"q{n}" for n in range(4)]
        self.plan_blocks([(f"k{n}", cols(1, n)) for n in range(4)] + [(f"q{n}", cols(0, n)) for n in range(4)]
                         + [(f"g{n}", cols(3, n)) for n in range(4)])
        self.v_fills = [k.ring.plan(1), k.ring.plan(1)]
        self.plan_out("fox", a["fox_w_out"][0])
        b.plan("fox_z")
        for i, name in enumerate(self.normed):
            b.plan("fox_" + name)
            if i:
                b.plan("fox_n" + self.normed[i - 1])
        b.plan("fox_n" + self.normed[-1])
        b.plan(*[f"fox_g{n}" for n in range(4)], *[f"fox_v{h}{t}" for h in range(2) for t in range(TT)])
        part = lambda n: ar[:, n * 2048:(n + 1) * 2048].rearrange("p (h t) -> p h t", h=8)
        self.q, self.kk, self.g, self.bq, self.bk = part(0), part(1), part(2), part(4), part(5)
        self.v = ar[:, 3 * 2048:4 * 2048].rearrange("p (t d) -> p t d", t=TT)
        self.std = ar[:, 14592:15616].rearrange("p (r h t) -> p r h t", r=2, h=2)
        self.zb, self.ez, self.lf, self.cc, self.nc_ = (ar[0:FOX_H, 15616 + n * T:15616 + (n + 1) * T] for n in range(5))
        s = lambda n: k.s("fox_" + n)
        self.sq_ready, self.rstd_ready, self.gate_ready = s("sq"), s("rstd"), s("gate")
        self.z_step, self.c_ready, self.bias_ready, self.bias_rows, self.cat_ready = s("z"), s("c"), s("bias"), s("bias_rows"), s("cat")
        units = []
        for h in range(FOX_H):
            pair, half = divmod(h, 2)
            at = slice(half * HD, (half + 1) * HD)
            for t in range(TT):
                n, tok = (t + 1) * P, slice(t * P, (t + 1) * P)
                units.append(dict(
                    q=self.q[at, pair, tok], keys=self.kk[at, pair, 0:n], bias=[(self.bq[at, pair, tok], self.bk[at, pair, 0:n])],
                    n=n, mask=k.const(C_CAUSAL + 384 - n, n), seen=None, scale=HD ** -0.5, gate=None,
                    values=[(P, self.v[:, m, h * HD:(h + 1) * HD]) for m in range(t + 1)],
                    out=(pair, half, t), first=True, last=True))
        self.plan_units("fox", units, ar[:, 12288:14592])

    def sp(self, eng):
        k = self.k
        self.sp_blocks(eng)
        for half, n in enumerate(self.v_fills):
            k.ring.wait_free(eng, n)
            eng.dma_start(k.ring.slot(n)[:, 0:4096].rearrange("p (k n) -> p k n", k=KD),
                          k.a["fox_w_in"][0][:, 2 * D + half * 512:2 * D + (half + 1) * 512].rearrange("(k p) n -> p k n", p=P)
                          ).then_inc(k.ring.full[n % SLOTS], 16)
        self.sp_out(eng)

    def pe(self, pe):
        k, b = self.k, self.k.banks
        self.norm.pe(pe)
        self.norm.wait_xn(pe)
        pe.wait_ge(k.small_ready, k.small_all)
        b.filled(self.project(pe, b.claim(pe, "fox_z")[0:FOX_H, 0:T], lambda kk: k.wz[:, kk], k.xn), "fox_z")

        def blocks(name):
            fill, w = self.block(name)
            k.ring.wait_full(pe, fill)
            out = b.claim(pe, "fox_" + name)
            for h in range(2):
                last = self.project(pe, out[:, h * T:(h + 1) * T], lambda kk: w[:, kk, h * P:(h + 1) * P], k.xn)
            b.filled(last, "fox_" + name)

        def stat(i):
            pe.wait_ge(self.sq_ready, i + 1)
            at = 2 * (i % 4)
            b.filled(pe.matmul(b.claim(pe, "fox_n" + self.normed[i]), k.const(C_BLK, P), k.sq[:, at:at + 2],
                               start=True, stop=True), "fox_n" + self.normed[i])

        for i, name in enumerate(self.normed):
            blocks(name)
            if i:
                stat(i - 1)
        stat(len(self.normed) - 1)
        for n in range(4):
            blocks(f"g{n}")
        for half, n in enumerate(self.v_fills):
            k.ring.wait_full(pe, n)
            w = k.ring.slot(n)[:, 0:4096].rearrange("p (k n) -> p k n", k=KD)
            for t in range(TT):
                out = b.claim(pe, f"fox_v{half}{t}")
                b.filled(self.project(pe, out, lambda kk: k.xn[:, kk, t * P:(t + 1) * P], w), f"fox_v{half}{t}")
        b.wait_read(pe, "fox_q3")
        b.wait_read(pe, "fox_v11")
        pe.wait_ge(self.bias_ready, 4)
        pe.wait_ge(self.bias_rows, 64)
        self.run(pe, self.pe_unit)
        pe.wait_ge(self.cat_ready, 4)
        self.pe_out(pe)

    def act(self, act):
        k, b = self.k, self.k.banks
        self.norm.act_squares(act)
        self.norm.act_std(act)

        def square(i):
            src = b.wait(act, "fox_" + self.normed[i]).rearrange("p (h t) -> p h t", h=2)
            at = 2 * (i % 4)
            act.activation(k.sq[:, at:at + 2], src, ACT.Square).then_inc(self.sq_ready, 1)

        def root(i):
            name = "fox_n" + self.normed[i]
            src = b.wait(act, name).rearrange("p (h t) -> p h t", h=2)
            if i >= 2:
                b.wait_read(act, "fox_" + self.normed[i - 2])
            b.read(act.activation(self.std[:, i % 2], src, ACT.Sqrt, bias=k.const(C_EPS, 1), scale=1.0 / HD), name)

        for i in range(len(self.normed)):
            square(i)
            if i:
                root(i - 1)
        root(len(self.normed) - 1)
        act.wait_ge(self.z_step, 1)
        act.activation(self.ez, self.zb, ACT.Abs).then_inc(self.z_step, 1)
        act.wait_ge(self.z_step, 2)
        act.activation(self.ez, self.ez, ACT.Exp, scale=-1.0).then_inc(self.z_step, 1)
        act.wait_ge(self.z_step, 3)
        act.activation(self.ez, self.ez, ACT.Ln, bias=k.const(C_ONES, 1, FOX_H)).then_inc(self.z_step, 1)
        for n in range(4):
            src = b.wait(act, f"fox_g{n}").rearrange("p (h t) -> p h t", h=2)
            if n in (0, 3):
                self.release(act, self.block_fill[f"g{n}"][0])
            b.read(act.activation(self.g[:, 2 * n:2 * n + 2], src, ACT.Sigmoid), f"fox_g{n}")
        for half in range(2):
            for t in range(TT):
                src = b.wait(act, f"fox_v{half}{t}")
                b.read(act.activation(self.v[:, t, half * 512:(half + 1) * 512], src, ACT.Copy), f"fox_v{half}{t}")
            self.release(act, self.v_fills[half])
        act.wait_ge(self.c_ready, 2)
        act.wait_ge(self.bias_ready, 4)
        for half in range(2):
            act.dma_start(self.bq[half * HD:half * HD + 1], self.cc[half:FOX_H:2, :]).then_inc(self.bias_rows, 16)
            act.dma_start(self.bk[half * HD + 32:half * HD + 33], self.nc_[half:FOX_H:2, :]).then_inc(self.bias_rows, 16)
        self.run(act, self.act_unit)

    def dve(self, dve):
        k, b, seq = self.k, self.k.banks, self.k.dve_seq
        self.norm.dve(dve)
        src = b.wait(dve, "fox_z")[0:FOX_H, 0:T]
        dve.tensor_scalar(self.zb, src, k.bf[0:FOX_H, 0:1], None, ALU.add).then_inc(self.z_step, 1)
        dve.wait_ge(self.z_step, 1)
        b.release(dve, "fox_z")
        for i, name in enumerate(self.normed):
            std = self.std[:, i % 2]
            b.wait_read(dve, "fox_n" + name)
            if name in ("k2", "q1"):
                self.release(dve, self.block_fill[name][0])
            dve.reciprocal(std, std).then_inc(self.rstd_ready, 1)
            dve.wait_ge(self.rstd_ready, i + 1)
            to, row = (self.kk, R_FK) if name[0] == "k" else (self.q, R_FQ)
            n = int(name[1])
            src = b.at("fox_" + name).rearrange("p (h t) -> p h t", h=2)
            b.read(dve.scalar_tensor_tensor(out=to[:, 2 * n:2 * n + 2], in0=src, scalar=k.param[:, row:row + 1], in1=std,
                                            op0=ALU.mult, op1=ALU.mult), "fox_" + name)
        dve.wait_ge(self.z_step, 4)
        seq.inc(dve.scalar_tensor_tensor(out=self.lf, in0=self.zb, scalar=0.0, in1=self.ez, op0=ALU.min, op1=ALU.subtract))
        seq.wait(dve)
        seq.inc(dve.tensor_scalar(self.lf, self.lf, HD ** 0.5, None, ALU.mult))
        seq.wait(dve)
        dve.tensor_tensor_scan(self.cc, k.const(C_CAUSAL, T, FOX_H), self.lf, 0.0, ALU.add, ALU.add).then_inc(self.c_ready, 1)
        dve.wait_ge(self.c_ready, 1)
        dve.tensor_scalar(self.nc_, self.cc, -1.0, None, ALU.mult).then_inc(self.c_ready, 1)
        n_units = len(self.units)
        for i in range(n_units + 3):
            self.dve_unit(dve, i)
            if i >= 12 and (i - 12) % 8 == 0:
                self.dve_gate(dve, (i - 12) // 8)
        self.dve_gate(dve, 3)
        self.dve_out(dve)

    def dve_gate(self, dve, bank):
        k, pairs = self.k, slice(2 * bank, 2 * bank + 2)
        dve.wait_ge(k.att_out, self.acc_out[2 * bank + 1])
        dve.tensor_tensor(k.cat[:, pairs], k.acc[:, pairs], self.g[:, pairs], ALU.mult).then_inc(self.cat_ready, 1)

    def pool(self, pool):
        k, seq = self.k, self.k.pool_seq
        self.norm.wait_xn(pool)
        seq.inc(pool.memset(self.bq, 0.0))
        seq.inc(pool.memset(self.bk, 0.0))
        seq.wait(pool)
        for half in range(2):
            pool.memset(self.bq[half * HD + 32:half * HD + 33], 1.0).then_inc(self.bias_ready, 1)
            pool.memset(self.bk[half * HD:half * HD + 1], 1.0).then_inc(self.bias_ready, 1)
        self.pool_units(pool)


class Rope:

    C1, MAGIC = 6.28125, 12582912.0
    C2 = 2 * float(np.pi) - C1

    def __init__(self, k):
        self.k, self.turn = k, k.x_turns
        self.sined = k.s("rope_sined")
        self.angle, self.turns, self.half = (k.arena[:, n * 512:(n + 1) * 512].rearrange("p (r t) -> p r t", r=2) for n in range(3))
        self.reduced = k.s("rope_reduced")

    def sp(self, eng):
        pass

    def pool(self, pool):
        pass

    def pe(self, pe):
        pass

    def act(self, act):
        k = self.k
        act.wait_ge(self.reduced, 1)
        act.activation(k.rope[:, 1], self.angle, ACT.Sin).then_inc(self.sined, 1)
        act.activation(self.half, self.angle, ACT.Sin, scale=0.5).then_inc(self.sined, 1)

    def dve(self, dve):
        k, seq = self.k, self.k.dve_seq
        dve.wait_ge(k.small_ready, k.small_all)
        dve.wait_ge(k.x_ready, 4 * self.turn)
        seq.inc(dve.tensor_copy(self.turns[:, 0], k.pos[:]))
        seq.wait(dve)
        for r, col in ((0, C_INVN), (1, C_INVM)):
            seq.inc(dve.tensor_scalar(self.angle[:, r], self.turns[:, 0], k.const(col, 1), None, ALU.mult))
        seq.wait(dve)
        steps = [
            lambda: dve.tensor_scalar(self.turns, self.angle, 1.0 / (2 * float(np.pi)), self.MAGIC, ALU.mult, ALU.add),
            lambda: dve.tensor_scalar(self.turns, self.turns, self.MAGIC, None, ALU.subtract),
            lambda: dve.scalar_tensor_tensor(out=self.angle, in0=self.turns, scalar=-self.C1, in1=self.angle, op0=ALU.mult, op1=ALU.add),
            lambda: dve.scalar_tensor_tensor(out=self.angle, in0=self.turns, scalar=-self.C2, in1=self.angle, op0=ALU.mult, op1=ALU.add),
        ]
        for step in steps:
            seq.inc(step())
            seq.wait(dve)
        dve.tensor_scalar(self.angle, self.angle, 3.1415925, -3.1415925, ALU.min, ALU.max).then_inc(self.reduced, 1)
        dve.wait_ge(self.sined, 2)
        seq.inc(dve.tensor_tensor(self.half, self.half, self.half, ALU.mult))
        seq.wait(dve)
        dve.tensor_scalar(k.rope[:, 0], self.half, -2.0, 1.0, ALU.mult, ALU.add).then_inc(k.rope_ready, 1)


class LayerNorm:

    def __init__(self, k, row):
        self.k, self.row, self.i = k, row, k.layer_norms
        k.layer_norms += 1
        self.before = k.x_turns
        k.x_turns += 1
        k.banks.plan(f"ln_m{self.i}", f"ln_v{self.i}")

    def sp(self, eng):
        pass

    def pool(self, pool):
        pass

    def pe(self, pe):
        k, b, i = self.k, self.k.banks, self.i
        out = b.claim(pe, f"ln_m{i}")[:, 0:T]
        for kk in range(KD):
            if kk % 2 == 0:
                pe.wait_ge(k.x_ready, 4 * (self.before - 1) + kk // 2 + 1)
            last = pe.matmul(out, k.ones, k.x[:, kk], start=kk == 0, stop=kk == KD - 1)
        b.filled(last, f"ln_m{i}")
        out = b.claim(pe, f"ln_v{i}")[:, 0:T]
        for kk in range(KD):
            if kk % 2 == 0:
                pe.wait_ge(k.ln_sq, 4 * i + kk // 2 + 1)
            last = pe.matmul(out, k.ones, k.sq[:, kk], start=kk == 0, stop=kk == KD - 1)
        b.filled(last, f"ln_v{i}")

    def act(self, act):
        k, b, i = self.k, self.k.banks, self.i
        for c in range(4):
            act.wait_ge(k.ln_centred, 4 * i + c + 1)
            act.activation(k.sq[:, 2 * c:2 * c + 2], k.xn[:, 2 * c:2 * c + 2], ACT.Square).then_inc(k.ln_sq, 1)
        src = b.wait(act, f"ln_v{i}")[:, 0:T]
        b.read(act.activation(k.std[:], src, ACT.Sqrt, bias=k.const(C_LNEPS, 1), scale=1.0 / D), f"ln_v{i}")

    def dve(self, dve):
        k, b, i = self.k, self.k.banks, self.i
        total = b.wait(dve, f"ln_m{i}")[:, 0:T].unsqueeze(1).to_broadcast([P, 2, T])
        for c in range(4):
            cs = slice(2 * c, 2 * c + 2)
            dve.scalar_tensor_tensor(out=k.xn[:, cs], in0=total, scalar=-1.0 / D, in1=k.x[:, cs],
                                     op0=ALU.mult, op1=ALU.add).then_inc(k.ln_centred, 1)
        dve.wait_ge(k.ln_centred, 4 * i + 4)
        b.release(dve, f"ln_m{i}")
        b.wait_read(dve, f"ln_v{i}")
        dve.reciprocal(k.rstd[:], k.std[:]).then_inc(k.ln_rstd, 1)
        dve.wait_ge(k.ln_rstd, i + 1)
        for c in range(4):
            cs = slice(2 * c, 2 * c + 2)
            dve.tensor_tensor(k.xn[:, cs], k.xn[:, cs], k.rstd[:].unsqueeze(1).to_broadcast([P, 2, T]), ALU.mult).then_inc(k.ln_scaled, 1)
        for c in range(4):
            dve.wait_ge(k.ln_scaled, 4 * i + c + 1)
            for kk in (2 * c, 2 * c + 1):
                g = k.param[:, R_LNG + self.row * KD + kk:R_LNG + self.row * KD + kk + 1]
                bb = k.param[:, R_LNB + self.row * KD + kk:R_LNB + self.row * KD + kk + 1]
                ins = dve.tensor_scalar(k.x[:, kk], k.xn[:, kk], g, bb, ALU.mult, ALU.add)
            ins.then_inc(k.x_ready, 1)


class Memory(Attention):

    def plan_memory(self, layer, name, xq, mk, mv, mem_t):
        self.mem_name, self.xq, self.mk, self.mv, self.mem_t = name, xq, mk, mv, mem_t
        self.mem_layer = layer
        self.mem_fill = self.k.ring.plan(2)
        self.k.banks.plan(*[f"{name}_mt{n}" for n in range(4)], f"{name}_mk", f"{name}_mv")

    def sp_memory(self, eng):
        k, n = self.k, self.mem_fill
        k.ring.wait_free(eng, n)
        slot, full = k.ring.slot(n), k.ring.full[n % SLOTS]
        eng.dma_start(slot[:, 0:2048].rearrange("p (t d) -> p t d", t=TT), k.a["mem_2"].rearrange("o (t p) d -> p (o t) d", p=P)).then_inc(full, 16)
        eng.dma_start(slot[:, 2048:6144].rearrange("p (k n) -> p k n", k=KD),
                      k.a["mem_w_kv_2"][self.mem_layer].rearrange("(k p) n -> p k n", p=P)).then_inc(full, 16)

    def pe_memory(self, pe):
        k, b, name = self.k, self.k.banks, self.mem_name
        k.ring.wait_full(pe, self.mem_fill)
        slot = k.ring.slot(self.mem_fill)
        w = slot[:, 2048:6144].rearrange("p (k n) -> p k n", k=KD)
        for q in range(4):
            out = b.claim(pe, f"{name}_mt{q}")
            for n in range(4):
                kk, t = 2 * q + n // 2, n % 2
                last = pe.transpose(out[:, n * P:(n + 1) * P], slot[:, t * D + kk * P:t * D + (kk + 1) * P], k.ident)
            b.filled(last, f"{name}_mt{q}")
        for q in range(4):
            b.wait_read(pe, f"{name}_mt{q}")
        out = b.claim(pe, f"{name}_mk")
        for h in range(2):
            last = self.project(pe, out[:, h * T:(h + 1) * T], lambda kk: w[:, kk, h * P:(h + 1) * P], self.mem_t)
        b.filled(last, f"{name}_mk")
        out = b.claim(pe, f"{name}_mv")
        for t in range(TT):
            last = self.project(pe, out[:, t * T:(t + 1) * T], lambda kk: self.mem_t[:, kk, t * P:(t + 1) * P], w[:, :, 256:512])
        b.filled(last, f"{name}_mv")

    def act_memory(self, act):
        k, b, name = self.k, self.k.banks, self.mem_name
        for q in range(4):
            src = b.wait(act, f"{name}_mt{q}").rearrange("p (k t) -> p k t", k=2)
            b.read(act.activation(self.mem_t[:, 2 * q:2 * q + 2], src, ACT.Copy), f"{name}_mt{q}")
        for part, to in (("mk", self.mk), ("mv", self.mv)):
            src = b.wait(act, f"{name}_{part}").rearrange("p (k t) -> p k t", k=2)
            b.read(act.activation(to, src, ACT.Copy), f"{name}_{part}")
        self.release(act, self.mem_fill)

    def memory_units(self):
        k, units = self.k, []
        for h in range(XA_H):
            pair, half = divmod(h, 2)
            at = slice(half * HD, (half + 1) * HD)
            for t in range(TT):
                units.append(dict(
                    q=self.xq[at, pair, t * P:(t + 1) * P], keys=self.mk[at, pair, :], n=T, mask=k.const(C_CAUSAL, T),
                    seen=None, scale=HD ** -0.5, gate=None, values=[(P, self.mv[:, m, h * HD:(h + 1) * HD]) for m in range(TT)],
                    out=(6 + pair, half, t), first=True, last=True))
        return units

    def dve_collect(self, dve, bank):
        k, pairs = self.k, slice(2 * bank, 2 * bank + 2)
        dve.wait_ge(k.att_out, self.acc_out[2 * bank + 1])
        dve.tensor_copy(k.cat[:, pairs], k.acc[:, pairs]).then_inc(self.cat_ready, 1)

    def dve_units(self, dve):
        bank = 0
        for i in range(len(self.units) + 3):
            self.dve_unit(dve, i)
            while bank < 3 and self.u0 + i - 4 >= self.acc_out[2 * bank + 1]:
                self.dve_collect(dve, bank)
                bank += 1
        while bank < 4:
            self.dve_collect(dve, bank)
            bank += 1

    def pe_rotate(self, pe, name, raw, matrix, shape):
        k, b = self.k, self.k.banks
        b.wait_read(pe, name)
        out = b.claim(pe, name + "_r")
        b.filled(pe.matmul(out[0:shape[0], 0:shape[1]], matrix, raw, start=True, stop=True), name + "_r")

    def dve_rotate(self, dve, name, raw, out, cos, sin, shape):
        k, b, seq = self.k, self.k.banks, self.k.dve_seq
        wide = lambda t: t.unsqueeze(1).to_broadcast(list(shape))
        rot = b.wait(dve, name + "_r")[raw.start_partition():raw.start_partition() + shape[0], 0:shape[1] * shape[2]]
        rot = rot.rearrange("p (m n) -> p m n", m=shape[1])
        seq.inc(dve.tensor_tensor(out, rot, wide(sin), ALU.mult))
        first = seq.n
        seq.inc(dve.tensor_tensor(raw, raw, wide(cos), ALU.mult))
        seq.wait(dve)
        b.read(dve.tensor_tensor(out, out, raw, ALU.add), name + "_r")


class Nsa(Memory):

    def __init__(self, k):
        self.k = k
        a, ar, b = k.a, k.arena, k.banks
        w = a["nsa_w_in_2"][0]
        offs = dict(q0=0, q1=256, q2=512, kc=768, vc=1024, ks=1280, vs=1536, kw=1792, vw=2048)
        col = lambda at, n=256: w[:, at:at + n]
        cut = lambda at, p, *s: ar[:p, at:at + int(np.prod(s))].rearrange(
            "p (a b) -> p a b", a=s[0])
        self.q, self.ks, self.kw = cut(0, P, 6, T), cut(1536, P, 4, T), cut(2560, P, 4, T)
        self.kc2, self.vc2 = cut(3584, P, 4, T), cut(4608, P, 4, T)
        self.vs, self.vw = cut(5632, P, 2, T), cut(6144, P, 2, T)
        self.kc, self.vc, self.ks_once, self.kw_once = (cut(10240 + n * 512, P, 2, T) for n in range(4))
        self.raw = [cut(12544 + n * 512, P, 2, T) for n in range(3)]
        self.hid = [cut(14080 + n * 64, P, 4, N_CMP) for n in range(2)]
        self.kcmp, self.kcmp_raw = cut(14208, P, 4, N_CMP), cut(14272, P, 4, N_CMP)
        self.vcmp = ar[0:N_CMP, 14336:14336 + T]
        self.gates = cut(14592, P, 2, 36)
        self.pe_bias = ar[:, 14664:14666]
        self.plan_memory(0, "nsa", cut(6656, P, 2, T), cut(7168, P, 2, T), cut(7680, P, 2, T), cut(8192, P, 8, T))
        self.plan_blocks([(n, col(offs[n])) for n in ("kc", "vc", "ks", "kw", "vs", "vw", "q0", "q1", "q2")]
                         + [("xq", col(2340)), ("gt", col(2304, 36))])
        self.w1_fill = k.ring.plan(1)
        self.plan_out("nsa", a["w_out_2"][0])
        b.plan("nsa_kc", "nsa_vc")
        self.rotated = ["ks", "kw", "q0", "q1", "q2"]
        for i, n in enumerate(self.rotated):
            b.plan("nsa_" + n)
            if i:
                b.plan("nsa_" + self.rotated[i - 1] + "_r")
            if n == "kw":
                b.plan("nsa_vs", "nsa_vw")
        b.plan("nsa_q2_r", "nsa_xq", "nsa_gt", "nsa_hk", "nsa_hv", "nsa_kcmp", "nsa_vcmp", "nsa_kcmp_r")
        s = lambda n: k.s("nsa_" + n)
        self.cat_ready, self.pe_ready, self.hid_ready = s("cat"), s("pe"), s("hid")
        self.pairs_placed, self.keys_placed = s("pairs_placed"), s("keys_placed")
        units = []
        for h in range(NSA_H):
            pair, half, kv = h // 2, h % 2, h // GROUP
            at = slice(half * HD, (half + 1) * HD)
            vcol = slice(kv * HD, (kv + 1) * HD)
            for t in range(TT):
                n = (t + 1) * P
                base = dict(q=self.q[at, pair, t * P:(t + 1) * P], scale=HD ** -0.5, out=(pair, half, t))
                gate = lambda j: self.gates[:, t, 3 * h + j:3 * h + j + 1]
                units.append(dict(base, keys=self.kcmp[at, kv, :], n=N_CMP, mask=k.const(C_CMPADD + t * N_CMP, N_CMP),
                                  seen=k.const(C_CMPMUL + t * N_CMP, N_CMP), gate=gate(0),
                                  values=[(N_CMP, self.vcmp[:, vcol])], first=True, last=False))
                for j, keys, v in ((1, self.ks, self.vs), (2, self.kw, self.vw)):
                    units.append(dict(base, keys=keys[at, kv, 0:n], n=n, mask=k.const(C_CAUSAL + 384 - n, n), seen=None,
                                      gate=gate(j), values=[(P, v[:, m, vcol]) for m in range(t + 1)], first=False, last=j == 2))
        self.plan_units("nsa", units + self.memory_units(), ar[:, 10240:12544])

    def sp(self, eng):
        k = self.k
        self.sp_memory(eng)
        self.sp_blocks(eng)
        n = self.w1_fill
        k.ring.wait_free(eng, n)
        eng.dma_start(k.ring.slot(n)[:, 0:4096].rearrange("p (v l n) -> p v l n", v=2, l=16),
                      k.a["nsa_cmp_w1_2"][0].rearrange("v (l p) n -> p v l n", p=P)).then_inc(k.ring.full[n % SLOTS], 16)
        self.sp_out(eng)

    def pe(self, pe):
        k, b = self.k, self.k.banks
        pe.wait_ge(k.x_ready, 4 * self.turn)
        pe.wait_ge(k.rope_ready, 1)
        self.pe_memory(pe)

        def tiles(name):
            fill, w = self.block(name)
            k.ring.wait_full(pe, fill)
            out = b.claim(pe, "nsa_" + name)
            for h in range(2):
                last = self.project(pe, out[:, h * T:(h + 1) * T], lambda kk: w[:, kk, h * P:(h + 1) * P], k.x)
            b.filled(last, "nsa_" + name)

        def rows(name, n):
            fill, w = self.block(name)
            k.ring.wait_full(pe, fill)
            out = b.claim(pe, "nsa_" + name)
            for t in range(TT):
                last = self.project(pe, out[:, t * n:(t + 1) * n], lambda kk: k.x[:, kk, t * P:(t + 1) * P], w)
            b.filled(last, "nsa_" + name)

        for name in ("kc", "vc"):
            tiles(name)
        for i, name in enumerate(self.rotated):
            tiles(name)
            if i:
                self.rotate(pe, i - 1)
            if name == "kw":
                rows("vs", T)
                rows("vw", T)
        self.rotate(pe, len(self.rotated) - 1)
        tiles("xq")
        rows("gt", 36)
        k.ring.wait_full(pe, self.w1_fill)
        w1 = k.ring.slot(self.w1_fill)[:, 0:4096].rearrange("p (v l n) -> p v l n", v=2, l=16)
        pe.wait_ge(self.pairs_placed, 128)
        for v, (name, src) in enumerate((("nsa_hk", self.kc2), ("nsa_hv", self.vc2))):
            out = b.claim(pe, name)
            for l in range(16):
                pe.matmul(out[:, 64:65], w1[:, v, l], k.pe_cols[:, v * 16 + l:v * 16 + l + 1], start=l == 0, stop=l == 15)
            for l in range(16):
                last = pe.matmul(out[:, 0:4 * N_CMP], w1[:, v, l], src[:, :, 2 * l:2 * l + 225:CMP_STRIDE], start=l == 0, stop=l == 15)
            b.filled(last, name)
        pe.wait_ge(self.hid_ready, 1)
        pe.wait_ge(k.small_ready, k.small_all)
        flat = lambda t: t.rearrange("p h n -> p (h n)")
        out = b.claim(pe, "nsa_kcmp")
        for half in range(2):
            last = pe.matmul(out[half * HD:(half + 1) * HD, 0:4 * N_CMP], k.cmp_w2[:, 0], flat(self.hid[0]), start=True, stop=True)
        b.filled(last, "nsa_kcmp")
        pe.wait_ge(self.hid_ready, 2)
        out = b.claim(pe, "nsa_vcmp")
        for h in range(NSA_KV):
            last = pe.matmul(out[0:N_CMP, h * HD:(h + 1) * HD], self.hid[1][:, h], k.cmp_w2[:, 1], start=True, stop=True)
        b.filled(last, "nsa_vcmp")
        self.pe_rotate(pe, "nsa_kcmp", flat(self.kcmp_raw), k.const(C_ROTN, P), (P, 4 * N_CMP))
        b.wait_read(pe, "nsa_q2_r")
        b.wait_read(pe, "nsa_gt")
        b.wait_read(pe, "nsa_vcmp")
        b.wait_read(pe, "nsa_kcmp_r")
        pe.wait_ge(self.keys_placed, 128)
        self.run(pe, self.pe_unit)
        pe.wait_ge(self.cat_ready, 4)
        self.pe_out(pe)

    def rotate(self, pe, i):
        k = self.k
        raw = self.raw[i % 3].rearrange("p m t -> p (m t)")
        self.pe_rotate(pe, "nsa_" + self.rotated[i], raw, k.const(C_ROTN, P), (P, 2 * T))

    def act(self, act):
        k, b = self.k, self.k.banks
        act.wait_ge(k.x_ready, 4 * self.turn)
        act.wait_ge(k.rope_ready, 1)
        self.act_memory(act)
        for name, once, pairs in (("kc", self.kc, self.kc2), ("vc", self.vc, self.vc2)):
            src = b.wait(act, "nsa_" + name).rearrange("p (m t) -> p m t", m=2)
            b.read(act.activation(once, src, ACT.Copy), "nsa_" + name)
            b.wait_read(act, "nsa_" + name)
            for j in range(2):
                src = once[j * HD:(j + 1) * HD]
                act.dma_start(pairs[0:HD, j:NSA_KV:2], src).then_inc(self.pairs_placed, 16)
                act.dma_start(pairs[HD:P, j:NSA_KV:2, 0:T - 1], src[:, :, 1:T]).then_inc(self.pairs_placed, 16)
        copies = {"vs": self.vs, "vw": self.vw}
        for i, name in enumerate(self.rotated):
            if i >= 3:
                b.wait_read(act, "nsa_" + self.rotated[i - 3] + "_r")
            src = b.wait(act, "nsa_" + name).rearrange("p (m t) -> p m t", m=2)
            if name in ("ks", "q2"):
                self.release(act, self.block_fill[name][0])
            b.read(act.activation(self.raw[i % 3], src, ACT.Copy), "nsa_" + name)
            if name == "kw":
                for n, to in copies.items():
                    src = b.wait(act, "nsa_" + n).rearrange("p (m t) -> p m t", m=2)
                    b.read(act.activation(to, src, ACT.Copy), "nsa_" + n)
                self.release(act, self.block_fill["vw"][0])
        for name, once, keys in (("ks", self.ks_once, self.ks), ("kw", self.kw_once, self.kw)):
            b.wait_read(act, f"nsa_{name}_r")
            for j in range(2):
                for half in range(2):
                    act.dma_start(keys[half * HD:(half + 1) * HD, j:NSA_KV:2], once[j * HD:(j + 1) * HD]).then_inc(self.keys_placed, 16)
        src = b.wait(act, "nsa_xq").rearrange("p (m t) -> p m t", m=2)
        b.read(act.activation(self.xq, src, ACT.Copy), "nsa_xq")
        src = b.wait(act, "nsa_gt")[:, 0:72].rearrange("p (m t) -> p m t", m=2)
        self.release(act, self.block_fill["gt"][0])
        b.read(act.activation(self.gates, src, ACT.Sigmoid), "nsa_gt")
        for v, name in enumerate(("nsa_hk", "nsa_hv")):
            act.wait_ge(self.pe_ready, v + 1)
            src = b.at(name)[:, 0:4 * N_CMP].rearrange("p (h n) -> p h n", h=4)
            act.activation(self.hid[v], src, ACT.Silu, bias=self.pe_bias[:, v:v + 1]).then_inc(self.hid_ready, 1)
            act.wait_ge(self.hid_ready, v + 1)
            b.release(act, name)
        self.release(act, self.w1_fill)
        src = b.wait(act, "nsa_kcmp")[:, 0:4 * N_CMP].rearrange("p (h n) -> p h n", h=4)
        b.read(act.activation(self.kcmp_raw, src, ACT.Copy), "nsa_kcmp")
        src = b.wait(act, "nsa_vcmp")[0:N_CMP, 0:T]
        b.read(act.activation(self.vcmp, src, ACT.Copy), "nsa_vcmp")
        self.run(act, self.act_unit)

    def dve(self, dve):
        k, b = self.k, self.k.banks
        cos, sin = k.rope[:, 0, 0, :], k.rope[:, 1, 0, :]
        outs = [self.ks_once, self.kw_once] + [self.q[:, 2 * n:2 * n + 2] for n in range(3)]
        for i, name in enumerate(self.rotated):
            self.dve_rotate(dve, "nsa_" + name, self.raw[i % 3], outs[i], cos, sin, (P, 2, T))
        for v, name in enumerate(("nsa_hk", "nsa_hv")):
            src = b.wait(dve, name)
            dve.tensor_copy(self.pe_bias[:, v:v + 1], src[:, 64:65]).then_inc(self.pe_ready, 1)
        ends = slice(CMP_LEN - 1, T, CMP_STRIDE)
        self.dve_rotate(dve, "nsa_kcmp", self.kcmp_raw, self.kcmp, cos[:, ends], sin[:, ends], (P, 4, N_CMP))
        self.dve_units(dve)
        self.dve_out(dve, ALPHA)

    def pool(self, pool):
        self.pool_units(pool)


class Mla(Memory):

    def __init__(self, k):
        self.k = k
        a, ar, b = k.a, k.arena, k.banks
        cut = lambda at, p, *s: ar[:p, at:at + int(np.prod(s))].rearrange("p (a b) -> p a b", a=s[0])
        self.q, self.kk, self.v = cut(0, P, MLA_H, T), cut(3072, P, MLA_H, T), cut(6144, P, TT, MLA_H * HD)
        self.cq, self.ckv = cut(7680, P, 2, T), ar[:, 8192:8192 + T]
        self.kr_raw, self.kr = cut(8448, MLA_K, 1, T), cut(8704, MLA_K, 1, T)
        self.raw = [cut(8960 + n * 512, MLA_K, 2, T) for n in range(3)]
        self.std = cut(10496, P, 2, T)
        self.plan_memory(1, "mla", cut(11008, P, 2, T), cut(11520, P, 2, T), cut(12032, P, 2, T), cut(12544, P, 8, T))
        self.in_fill, self.up_fill = k.ring.plan(1), k.ring.plan(2)
        self.plan_out("mla", a["w_out_2"][1])
        b.plan("mla_cq", "mla_ckv", "mla_xq", "mla_n", "mla_kr_r")
        for i in range(6):
            b.plan(f"mla_q{i}", f"mla_k{i}")
            if i:
                b.plan(f"mla_q{i - 1}_r")
        b.plan("mla_q5_r", *[f"mla_v{t}{half}" for t in range(TT) for half in range(2)])
        s = lambda n: k.s("mla_" + n)
        self.sq_ready, self.std_ready, self.rstd_ready = s("sq"), s("std"), s("rstd")
        self.kr_copied, self.kr_ready, self.kr_placed = s("kr_copied"), s("kr"), s("kr_placed")
        self.latent_ready, self.cat_ready = s("latent"), s("cat")
        units = []
        for h in range(MLA_H):
            for t in range(TT):
                n = (t + 1) * P
                units.append(dict(
                    q=self.q[0:MLA_K, h, t * P:n], keys=self.kk[0:MLA_K, h, 0:n], n=n, mask=k.const(C_CAUSAL + 384 - n, n),
                    seen=None, scale=MLA_K ** -0.5, gate=None, out=(h // 2, h % 2, t), first=True, last=True,
                    values=[(P, self.v[:, m, h * HD:(h + 1) * HD]) for m in range(t + 1)]))
        self.plan_units("mla", units + self.memory_units(), ar[:, 14592:16896])

    def sp(self, eng):
        k, r, a = self.k, self.k.ring, self.k.a
        self.sp_memory(eng)
        r.wait_free(eng, self.in_fill)
        eng.dma_start(r.slot(self.in_fill)[:, 0:KD * 672].rearrange("p (k n) -> p k n", k=KD),
                      a["mla_w_in_2"][0].rearrange("(k p) n -> p k n", p=P)).then_inc(r.full[self.in_fill % SLOTS], 16)
        r.wait_free(eng, self.up_fill)
        slot, full = r.slot(self.up_fill), r.full[self.up_fill % SLOTS]
        eng.dma_start(slot[:, 0:2304].rearrange("p (k n) -> p k n", k=2),
                      a["mla_w_uq_2"][0].rearrange("(k p) n -> p k n", p=P)).then_inc(full, 16)
        eng.dma_start(slot[:, 2304:3840], a["mla_w_ukv_2"][0]).then_inc(full, 16)
        self.sp_out(eng)

    def pe(self, pe):
        k, b = self.k, self.k.banks
        pe.wait_ge(k.x_ready, 4 * self.turn)
        self.pe_memory(pe)
        k.ring.wait_full(pe, self.in_fill)
        w = k.ring.slot(self.in_fill)[:, 0:KD * 672].rearrange("p (k n) -> p k n", k=KD)

        def columns(out, at, n):
            return self.project(pe, out, lambda kk: w[:, kk, at:at + n], k.x)

        out = b.claim(pe, "mla_cq")
        columns(out[:, 0:T], 0, P)
        b.filled(columns(out[:, T:2 * T], P, P), "mla_cq")
        out = b.claim(pe, "mla_ckv")
        columns(out[:, 0:T], 256, P)
        b.filled(columns(out[0:MLA_K, T:2 * T], 320, MLA_K), "mla_ckv")
        out = b.claim(pe, "mla_xq")
        columns(out[:, 0:T], 416, P)
        b.filled(columns(out[:, T:2 * T], 416 + P, P), "mla_xq")
        pe.wait_ge(self.sq_ready, 2)
        out = b.claim(pe, "mla_n")
        pe.matmul(out[:, 0:T], k.ones, k.sq[:, 0], start=True, stop=False)
        pe.matmul(out[:, 0:T], k.ones, k.sq[:, 1], start=False, stop=True)
        b.filled(pe.matmul(out[:, T:2 * T], k.ones, k.sq[:, 2], start=True, stop=True), "mla_n")
        rot = k.c[0:MLA_K, C_ROTM:C_ROTM + MLA_K]
        pe.wait_ge(self.kr_copied, 1)
        b.filled(pe.matmul(b.claim(pe, "mla_kr_r")[0:MLA_K, 0:T], rot, self.kr_raw[:, 0], start=True, stop=True), "mla_kr_r")
        k.ring.wait_full(pe, self.up_fill)
        slot = k.ring.slot(self.up_fill)
        uq = slot[:, 0:2304].rearrange("p (k n) -> p k n", k=2)
        ukv = slot[:, 2304:3840].rearrange("p (h n) -> p h n", h=MLA_H)
        pe.wait_ge(self.latent_ready, 3)

        def rotate(i):
            self.pe_rotate(pe, f"mla_q{i}", self.raw[i % 3].rearrange("p m t -> p (m t)"), rot, (MLA_K, 2 * T))

        for i in range(6):
            out = b.claim(pe, f"mla_q{i}")
            for j in range(2):
                at = (2 * i + j) * MLA_K
                for kk in range(2):
                    last = pe.matmul(out[0:MLA_K, j * T:(j + 1) * T], uq[:, kk, at:at + MLA_K], self.cq[:, kk], start=kk == 0, stop=kk == 1)
            b.filled(last, f"mla_q{i}")
            out = b.claim(pe, f"mla_k{i}")
            for j in range(2):
                last = pe.matmul(out[0:HD, j * T:(j + 1) * T], ukv[:, 2 * i + j, 0:HD], self.ckv, start=True, stop=True)
            b.filled(last, f"mla_k{i}")
            if i:
                rotate(i - 1)
        rotate(5)
        for t in range(TT):
            for half in range(2):
                out = b.claim(pe, f"mla_v{t}{half}")[:, 0:6 * HD]
                b.filled(pe.matmul(out.rearrange("p (h n) -> p h n", h=6), self.ckv[:, t * P:(t + 1) * P],
                                   ukv[:, 6 * half:6 * half + 6, HD:2 * HD], start=True, stop=True), f"mla_v{t}{half}")
        b.wait_read(pe, "mla_q5_r")
        b.wait_read(pe, "mla_v11")
        pe.wait_ge(self.kr_placed, 1)
        self.run(pe, self.pe_unit)
        pe.wait_ge(self.cat_ready, 4)
        self.pe_out(pe)

    def act(self, act):
        k, b = self.k, self.k.banks
        act.wait_ge(k.x_ready, 4 * self.turn)
        self.act_memory(act)
        src = b.wait(act, "mla_cq").rearrange("p (m t) -> p m t", m=2)
        act.activation(k.sq[:, 0:2], src, ACT.Square).then_inc(self.sq_ready, 1)
        src = b.wait(act, "mla_ckv")
        act.activation(k.sq[:, 2], src[:, 0:T], ACT.Square).then_inc(self.sq_ready, 1)
        act.activation(self.kr_raw[:, 0], src[0:MLA_K, T:2 * T], ACT.Copy).then_inc(self.kr_copied, 1)
        src = b.wait(act, "mla_xq").rearrange("p (m t) -> p m t", m=2)
        self.release(act, self.in_fill)
        b.read(act.activation(self.xq, src, ACT.Copy), "mla_xq")
        src = b.wait(act, "mla_n")
        act.activation(self.std[:, 0], src[:, 0:T], ACT.Sqrt, bias=k.const(C_EPS, 1), scale=1.0 / 256).then_inc(self.std_ready, 1)
        act.activation(self.std[:, 1], src[:, T:2 * T], ACT.Sqrt, bias=k.const(C_EPS, 1), scale=1.0 / P).then_inc(self.std_ready, 1)
        act.wait_ge(self.std_ready, 2)
        b.release(act, "mla_n")
        for i in range(6):
            if i >= 3:
                b.wait_read(act, f"mla_q{i - 3}_r")
            src = b.wait(act, f"mla_q{i}")[0:MLA_K].rearrange("p (m t) -> p m t", m=2)
            b.read(act.activation(self.raw[i % 3], src, ACT.Copy), f"mla_q{i}")
            src = b.wait(act, f"mla_k{i}")[0:HD].rearrange("p (m t) -> p m t", m=2)
            b.read(act.activation(self.kk[0:HD, 2 * i:2 * i + 2], src, ACT.Copy), f"mla_k{i}")
        for t in range(TT):
            for half in range(2):
                src = b.wait(act, f"mla_v{t}{half}")[:, 0:6 * HD]
                b.read(act.activation(self.v[:, t, half * 384:(half + 1) * 384], src, ACT.Copy), f"mla_v{t}{half}")
        self.release(act, self.up_fill)
        self.run(act, self.act_unit)

    def dve(self, dve):
        k, b = self.k, self.k.banks
        cos, sin = k.rope[0:MLA_K, 0, 1, :], k.rope[0:MLA_K, 1, 1, :]
        dve.wait_ge(self.std_ready, 2)
        dve.reciprocal(self.std, self.std).then_inc(self.rstd_ready, 1)
        dve.wait_ge(self.rstd_ready, 1)
        cq, ckv = b.at("mla_cq"), b.at("mla_ckv")
        for out, src, row, std in ((self.cq[:, 0], cq[:, 0:T], R_MQ, 0), (self.cq[:, 1], cq[:, T:2 * T], R_MQ + 1, 0),
                                   (self.ckv, ckv[:, 0:T], R_MKV, 1)):
            dve.scalar_tensor_tensor(out=out, in0=src, scalar=k.param[:, row:row + 1], in1=self.std[:, std],
                                     op0=ALU.mult, op1=ALU.mult).then_inc(self.latent_ready, 1)
        dve.wait_ge(self.latent_ready, 3)
        b.release(dve, "mla_cq")
        b.release(dve, "mla_ckv")
        self.dve_rotate(dve, "mla_kr", self.kr_raw, self.kr, cos, sin, (MLA_K, 1, T))
        b.wait_read(dve, "mla_kr_r")
        dve.sem_inc(self.kr_ready, 1)
        for i in range(6):
            self.dve_rotate(dve, f"mla_q{i}", self.raw[i % 3], self.q[0:MLA_K, 2 * i:2 * i + 2], cos, sin, (MLA_K, 2, T))
        self.dve_units(dve)
        self.dve_out(dve, ALPHA)

    def pool(self, pool):
        pool.wait_ge(self.kr_ready, 1)
        pool.tensor_copy(self.kk[HD:MLA_K], self.kr[HD:MLA_K].to_broadcast([MLA_ROPE, MLA_H, T])).then_inc(self.kr_placed, 1)
        self.pool_units(pool)


class Moe(Ffn):

    def __init__(self, k, layer):
        a = k.a
        gate, up, down = a["moe_w_gate_2"][layer], a["moe_w_up_2"][layer], a["moe_w_down_2"][layer]

        def sources(i, f):
            e, half = ds(i * 3 + f // 2, 1), f % 2
            cols = lambda w: w[e, :, half * 256:(half + 1) * 256].rearrange("o (k q) n -> q (o k) n", q=P)
            return cols(gate), cols(up), down[e, half * 256:(half + 1) * 256, :].rearrange("o (j q) n -> q (o j) n", q=P)

        Ffn.__init__(self, k, E_N * E_FF // P, sources, None, True)
        self.layer, self.name, self.turn = layer, f"moe{layer}", k.x_turns
        k.x_turns += 1
        k.banks.plan(self.name + "_lg", self.name + "_gt", *[f"{self.name}_gb{n}" for n in range(8)])
        s = lambda n: k.s(f"{self.name}_{n}")
        self.shifted, self.exped, self.gates_ready, self.turned = s("shifted"), s("exped"), s("gates"), s("turned")
        sq = k.sq[:].rearrange("p k t -> p (k t)")
        cut = lambda at, n: sq[:, at:at + 2 * n].rearrange("p (t n) -> p t n", t=2)
        self.logits, self.group, self.chosen, self.first = cut(0, 20), cut(64, 4), cut(96, 4), cut(128, 4)
        self.exp_g, self.exp_e, self.best = cut(160, 4), cut(192, 4), cut(224, 4)
        self.picked = sq[:, 256:288].rearrange("p (t g j) -> p t g j", t=2, g=4)
        self.gates = sq[:, 320:352].rearrange("p (t g j) -> p t g j", t=2, g=4)
        self.cols = [cut(384 + 8 * n, 1) for n in range(8)]
        self.gates_t = sq[0:E_N, 512:512 + T]

    def pe_before(self, pe):
        k, b, name = self.k, self.k.banks, self.name
        pe.wait_ge(k.x_ready, 4 * self.turn)
        pe.wait_ge(k.small_ready, k.small_all)
        out = b.claim(pe, name + "_lg")
        for t in range(TT):
            for kk in range(KD):
                last = pe.matmul(out[:, t * 20:(t + 1) * 20], k.x[:, kk, t * P:(t + 1) * P], k.w_route[:, self.layer, kk],
                                 start=kk == 0, stop=kk == KD - 1)
        b.filled(last, name + "_lg")
        pe.wait_ge(self.gates_ready, 1)
        out = b.claim(pe, name + "_gt")
        for t in range(TT):
            last = pe.transpose(out[0:E_N, t * P:(t + 1) * P], self.gates[:, t].rearrange("p g j -> p (g j)"), k.ident)
        b.filled(last, name + "_gt")
        b.wait_read(pe, name + "_gt")
        for n in range(8):
            out = b.claim(pe, f"{name}_gb{n}")
            for j in range(2):
                e = 2 * n + j
                last = pe.matmul(out[:, j * T:(j + 1) * T], k.c[0:E_N, C_IDENT + e:C_IDENT + e + 1].to_broadcast([E_N, P]),
                                 self.gates_t, start=True, stop=True)
            b.filled(last, f"{name}_gb{n}")
        for n in range(4, 8):
            b.wait_read(pe, f"{name}_gb{n}")

    def act_before(self, act):
        act.wait_ge(self.k.x_ready, 4 * self.turn)
        self.act_split(act, 0, self.j0, 0)

    def act_after(self, act):
        k, b = self.k, self.k.banks
        for i, to in enumerate((self.exp_g, self.exp_e)):
            act.wait_ge(self.shifted, i + 1)
            act.activation(to, to, ACT.Exp).then_inc(self.exped, 1)
        src = b.wait(act, self.name + "_gt")[0:E_N, 0:T]
        b.read(act.activation(self.gates_t, src, ACT.Copy), self.name + "_gt")
        for n in range(8):
            src = b.wait(act, f"{self.name}_gb{n}").rearrange("p (e t) -> p e t", e=2)
            b.read(act.activation(k.gate_b[:, 2 * n:2 * n + 2], src, ACT.Copy), f"{self.name}_gb{n}")

    def dve_before(self, dve):
        self.dve_split(dve, 0, self.j0)

    def dve_after(self, dve):
        k, b, seq = self.k, self.k.banks, self.k.dve_seq

        def do(ins):
            seq.inc(ins)
            seq.wait(dve)

        def best(of, top, onehot):
            wide = lambda t: t.to_broadcast([P, TT, 4])
            do(dve.tensor_reduce(top, of, X_AXIS, ALU.max))
            do(dve.tensor_tensor(self.first, of, wide(top), ALU.is_equal))
            do(dve.tensor_tensor(self.first, self.first, k.const(C_FIRST, 4).unsqueeze(1).to_broadcast([P, TT, 4]), ALU.mult))
            do(dve.tensor_reduce(self.cols[7], self.first, X_AXIS, ALU.max))
            do(dve.tensor_tensor(onehot, self.first, wide(self.cols[7]), ALU.is_equal))

        top, total, top_e, one, two, both = self.cols[0:6]
        wide = lambda t: t.to_broadcast([P, TT, 4])
        src = b.wait(dve, self.name + "_lg")[:, 0:40].rearrange("p (t n) -> p t n", t=2)
        do(dve.tensor_tensor(self.logits, src, k.b_route[:, self.layer].unsqueeze(1).to_broadcast([P, TT, 20]), ALU.add))
        b.release(dve, self.name + "_lg")
        groups = self.logits[:, :, 0:4]
        best(groups, top, self.group)
        dve.tensor_tensor(self.exp_g, groups, wide(top), ALU.subtract).then_inc(self.shifted, 1)
        experts = self.logits[:, :, 4:20].rearrange("p t (g j) -> p t g j", g=4)
        do(dve.tensor_tensor(self.picked, experts, self.group.unsqueeze(3).to_broadcast([P, TT, 4, 4]), ALU.mult))
        do(dve.tensor_reduce(self.chosen, self.picked.rearrange("p t g j -> p t j g"), X_AXIS, ALU.add))
        do(dve.tensor_reduce(top_e, self.chosen, X_AXIS, ALU.max))
        dve.tensor_tensor(self.exp_e, self.chosen, wide(top_e), ALU.subtract).then_inc(self.shifted, 1)
        dve.wait_ge(self.exped, 2)
        do(dve.tensor_reduce(total, self.exp_g, X_AXIS, ALU.add))
        best(self.exp_e, one, self.best)
        do(dve.scalar_tensor_tensor(out=self.chosen, in0=self.best, scalar=-2.0, in1=self.exp_e, op0=ALU.mult, op1=ALU.add))
        best(self.chosen, two, self.first)
        do(dve.tensor_tensor(self.best, self.best, self.first, ALU.add))
        do(dve.tensor_tensor(self.best, self.best, self.exp_e, ALU.mult))
        do(dve.tensor_tensor(both, one, two, ALU.add))
        do(dve.tensor_tensor(both, both, total, ALU.mult))
        do(dve.reciprocal(both, both))
        do(dve.tensor_tensor(self.best, self.best, wide(both), ALU.mult))
        dve.tensor_tensor(self.gates, self.group.unsqueeze(3).to_broadcast([P, TT, 4, 4]),
                          self.best.unsqueeze(2).to_broadcast([P, TT, 4, 4]), ALU.mult).then_inc(self.gates_ready, 1)

    def dve_residual(self, dve):
        k = self.k
        for c in range(4):
            cs = slice(2 * c, 2 * c + 2)
            dve.scalar_tensor_tensor(out=k.x[:, cs], in0=k.x[:, cs], scalar=ALPHA, in1=k.acc[:, cs],
                                     op0=ALU.mult, op1=ALU.add).then_inc(k.x_ready, 1)


def make_stages(k, stages):
    a = k.a
    made = []
    order = [
        lambda: Ffn(k, FF // P, swiglu_sources(a, 0, 0), RmsNorm(k, 0)),
        lambda: Hgrn2(k, RmsNorm(k, 1)),
        lambda: Ffn(k, FF // P, swiglu_sources(a, 0, 1), RmsNorm(k, 2)),
        lambda: Ffn(k, FF // P, swiglu_sources(a, 1, 0), RmsNorm(k, 3)),
        lambda: Fox(k, RmsNorm(k, 4)),
        lambda: Ffn(k, FF // P, swiglu_sources(a, 1, 1), RmsNorm(k, 5)),
        lambda: Rope(k),
        lambda: Nsa(k),
        lambda: LayerNorm(k, 0),
        lambda: Moe(k, 0),
        lambda: LayerNorm(k, 1),
        lambda: Mla(k),
        lambda: LayerNorm(k, 2),
        lambda: Moe(k, 1),
        lambda: LayerNorm(k, 3),
    ]
    for n, make in enumerate(order[:stages]):
        made.append(make())
    return made


NAMES = ['x', 'norm_g', 'ffn_w_in', 'ffn_w_out', 'hg_w_in', 'hg_lb_logits', 'hg_out_norm_g', 'hg_w_out', 'fox_w_in',
         'fox_b_f', 'fox_q_norm_g', 'fox_k_norm_g', 'fox_w_out', 'mem_2', 'positions_2', 'nsa_w_in_2',
         'nsa_cmp_pe_2', 'nsa_cmp_w1_2', 'nsa_cmp_w2_2', 'mla_w_in_2', 'mla_q_norm_2', 'mla_w_uq_2',
         'mla_kv_norm_2', 'mla_w_ukv_2', 'mem_w_kv_2', 'w_out_2', 'ln_g_2', 'ln_b_2', 'moe_w_grp_2', 'moe_b_grp_2',
         'moe_w_exp_2', 'moe_b_exp_2', 'moe_w_gate_2', 'moe_w_up_2', 'moe_w_down_2']


def build(nc, a, stages=99):
    with ExitStack() as ctx:
        k = Core(ctx, nc, a)
        start = Start(k)
        made = make_stages(k, stages)
        finish = Finish(k)
        block = ctx.enter_context(nc.Block())

        @block.sync
        def _(sp):
            start.sp(sp)
            for stage in made:
                stage.sp(sp)
            finish.sp(sp)

        @block.scalar
        def _(act):
            start.act_dma(act)
            act.wait_ge(k.const_ready, 16)
            for stage in made:
                stage.act(act)

        @block.vector
        def _(dve):
            for sem in k.ring.free:
                dve.sem_inc(sem, 1)
            dve.sem_inc(k.gu_ready, 2)
            dve.sem_inc(k.out_used, 2)
            dve.sem_inc(k.h_ready, 2)
            start.dve(dve)
            for stage in made:
                stage.dve(dve)
            finish.dve(dve)

        @block.gpsimd
        def _(pool):
            start.pool(pool)
            for stage in made:
                stage.pool(pool)

        @block.tensor
        def _(pe):
            pe.wait_ge(k.zero_ready, 1)
            start.pe(pe)
            for stage in made:
                stage.pe(pe)
            finish.pe(pe)


def kernel(**inputs):
    import concourse.bacc as bacc
    from concourse.bass_utils import run_bass_kernel_spmd

    nc = bacc.Bacc("TRN2", target_bir_lowering=False, num_devices=1)
    arrays = {"in_" + n: np.ascontiguousarray(inputs[n]) for n in NAMES}
    arrays["in_consts"] = constants()
    a = {n[3:]: nc.dram_tensor(n, v.shape, mybir.dt.from_np(v.dtype), kind="ExternalInput").ap()
         for n, v in arrays.items()}
    a["out"] = nc.dram_tensor("out_x", (1, T, D), F32, kind="ExternalOutput").ap()
    build(nc, a)
    return run_bass_kernel_spmd(nc, [arrays], core_ids=[0]).results[0]["out_x"]
```

```python
from contextlib import ExitStack

import numpy as np

import concourse.bass as bass
from concourse import mybir

F32 = mybir.dt.float32
F32R = mybir.dt.float32r
BF16 = mybir.dt.bfloat16
I32 = mybir.dt.int32
U32 = mybir.dt.uint32
ALU = mybir.AluOpType
ACT = mybir.ActivationFunctionType
X_AXIS = mybir.AxisListType.X
ds = bass.ds

P = 128
D = 1024
KD = D // P
T = 256
TT = T // P
FF = 2816
HG_H, HG_CHUNK = 8, 64
FOX_H, HD = 16, 64
NSA_H, NSA_KV, GROUP = 12, 4, 3
N_CMP, CMP_STRIDE, CMP_LEN = 15, 16, 32
XA_H = 4
MLA_H, MLA_K, MLA_NOPE, MLA_ROPE = 12, 96, 64, 32
E_N, E_FF, G_N, E_G = 16, 512, 4, 4
EPS = 1e-6
LN_EPS = 1e-5
ALPHA = (2.0 * 2) ** 0.25
MASKED = -1e30
NEG_BIG = -3e38

SLOTS = 3
SLOT = 6144
ARENA = 17408

NSA_ROT, NSA_THETA = 16, 500000.0
MLA_THETA = 10000.0
C_IDENT, C_ONES, C_BLK, C_ROTN, C_ROTM = 0, 128, 256, 384, 512
C_CAUSAL = 640
C_CMPADD, C_CMPMUL = 1024, 1054
C_LEVEL = 1084
C_RESET = C_LEVEL + 1024
C_INVN, C_INVM = C_RESET + 256, C_RESET + 257
C_FIRST = C_RESET + 258
C_EPS, C_LNEPS = C_FIRST + 4, C_FIRST + 5
C_BEFORE, C_IOTA = C_LNEPS + 1, C_LNEPS + 1 + P
N_CONST = C_IOTA + P


def constants():
    c = np.zeros((P, N_CONST), np.float32)
    i = np.arange(P)
    c[:, C_IDENT:C_IDENT + P] = np.eye(P)
    c[:, C_ONES:C_ONES + P] = 1.0
    c[:, C_BLK:C_BLK + P] = (i[:, None] // HD == i[None, :] // HD)
    for first, half, at in [(0, 8, C_ROTN), (64, 8, C_ROTN), (64, 16, C_ROTM)]:
        for d in range(half):
            c[first + half + d, at + first + d] = -1.0
            c[first + d, at + first + half + d] = 1.0
    t = np.arange(P)
    c[:, C_CAUSAL + 256:C_CAUSAL + 384] = np.where(t[None, :] <= t[:, None], 0.0, MASKED)
    for q in range(TT):
        seen = (np.arange(N_CMP)[None, :] * CMP_STRIDE + CMP_LEN - 1) <= (q * P + t)[:, None]
        c[:, C_CMPADD + q * N_CMP:C_CMPADD + (q + 1) * N_CMP] = np.where(seen, 0.0, MASKED)
        c[:, C_CMPMUL + q * N_CMP:C_CMPMUL + (q + 1) * N_CMP] = seen
    for n in range(7):
        L = 1 << n
        s, u = t[:, None], t[None, :]
        c[:, C_LEVEL + n * P:C_LEVEL + (n + 1) * P] = (
            (s // (2 * L) == u // (2 * L)) & (s // L % 2 == 0) & (u // L % 2 == 1))
    c[:, C_LEVEL + 7 * P:C_LEVEL + 8 * P] = np.eye(P)
    c[:, C_RESET:C_RESET + T] = (np.arange(T) % HG_CHUNK != 0)
    inv = lambda theta, dim: np.float32(theta) ** (-np.arange(0, dim, 2, dtype=np.float32) / np.float32(dim))
    for first in (0, 64):
        c[first:first + NSA_ROT, C_INVN] = np.tile(inv(NSA_THETA, NSA_ROT), 2)
    c[64:64 + MLA_ROPE, C_INVM] = np.tile(inv(MLA_THETA, MLA_ROPE), 2)
    c[:, C_FIRST:C_FIRST + 4] = [4, 3, 2, 1]
    c[:, C_EPS], c[:, C_LNEPS] = EPS, LN_EPS
    c[:, C_BEFORE:C_BEFORE + P] = i[:, None] < i[None, :]
    c[:, C_IOTA:C_IOTA + P] = i[None, :]
    return c


class Counted:

    def __init__(self, sem):
        self.sem, self.n = sem, 0

    def inc(self, ins):
        ins.then_inc(self.sem, 1)
        self.n += 1
        return self.n

    def wait(self, eng, n=None):
        eng.wait_ge(self.sem, self.n if n is None else n)


class Ring:

    def __init__(self, ctx, nc, slots):
        self.slots = slots
        self.full = [ctx.enter_context(nc.semaphore(f"slot_full_{s}")) for s in range(SLOTS)]
        self.free = [ctx.enter_context(nc.semaphore(f"slot_free_{s}")) for s in range(SLOTS)]
        self.targets, self.landed = [], [0] * SLOTS

    def plan(self, dmas):
        n = len(self.targets)
        self.landed[n % SLOTS] += 16 * dmas
        self.targets.append(self.landed[n % SLOTS])
        return n

    def slot(self, n):
        return self.slots[:, n % SLOTS, :]

    def wait_free(self, eng, n, turns=0):
        eng.wait_ge(self.free[n % SLOTS], n // SLOTS + 1 + turns)

    def wait_full(self, eng, n, more=0):
        eng.wait_ge(self.full[n % SLOTS], self.targets[n] + more)


class Banks:

    def __init__(self, ctx, nc, psum):
        self.psum = psum
        self.ready = [ctx.enter_context(nc.semaphore(f"bank_ready_{b}")) for b in range(4)]
        self.free = [ctx.enter_context(nc.semaphore(f"bank_free_{b}")) for b in range(4)]
        self.number = {}

    def plan(self, *names):
        for name in names:
            assert name not in self.number, name
            self.number[name] = len(self.number)

    def at(self, name):
        return self.psum[:, 4 + self.number[name] % 4, :]

    def claim(self, pe, name):
        n = self.number[name]
        if n >= 4:
            pe.wait_ge(self.free[n % 4], n // 4)
        return self.at(name)

    def filled(self, ins, name):
        ins.then_inc(self.ready[self.number[name] % 4], 1)

    def wait(self, eng, name):
        n = self.number[name]
        eng.wait_ge(self.ready[n % 4], n // 4 + 1)
        return self.at(name)

    def read(self, ins, name):
        ins.then_inc(self.free[self.number[name] % 4], 1)

    def release(self, eng, name):
        eng.sem_inc(self.free[self.number[name] % 4], 1)

    def wait_read(self, eng, name):
        n = self.number[name]
        eng.wait_ge(self.free[n % 4], n // 4 + 1)


R_NORM, R_LB, R_HGN, R_LNG, R_LNB, R_FQ, R_FK, R_MQ, R_MKV, N_ROWS = 0, 48, 56, 57, 89, 121, 122, 123, 125, 126


class Core:

    def __init__(self, ctx, nc, a):
        self.ctx, self.nc, self.a = ctx, nc, a
        f32 = lambda n, s, d=F32: ctx.enter_context(nc.sbuf_tensor(n, s, d))
        self.ring = Ring(ctx, nc, f32("weight_ring", [P, SLOTS, SLOT]))
        with ExitStack() as split:
            fr = lambda n, s: split.enter_context(nc.sbuf_tensor(n, s, F32R))
            self.w_hi, self.w_lo = fr("w_hi", [P, 2, SLOT // 2]), fr("w_lo", [P, 2, SLOT // 2])
            self.x_hi, self.x_lo = fr("x_hi", [P, KD, T]), fr("x_lo", [P, KD, T])
            self.h_hi, self.h_lo = fr("h_hi", [P, 2, T]), fr("h_lo", [P, 2, T])
        self.arena = f32("arena", [P, ARENA])
        self.x = f32("x_res", [P, KD, T])
        self.wide = f32("wide", [P, 2, KD, T])
        self.xn, self.cat = self.wide[:, 0], self.wide[:, 1]
        self.sq = f32("squares", [P, KD, T])
        self.sg = f32("silu_gate", [P, 2, T])
        self.h32 = f32("hidden", [P, 2, T])
        self.y = f32("slot_out", [P, D])
        self.plan = f32("moe_plan", [1, 2], I32)
        self.std, self.rstd = f32("std", [P, T]), f32("rstd", [P, T])
        self.c = f32("consts", [P, N_CONST])
        self.param = f32("params", [P, P])
        self.pe_cols = f32("cmp_pe_cols", [P, 32])
        self.lb, self.omlb, self.lb_e, self.lb_r, self.ends01 = (f32(n, [P, 8]) for n in ("lb", "omlb", "lb_e", "lb_r", "ends01"))
        self.zeros = f32("zeros", [P, 512], BF16)
        self.psum = ctx.enter_context(nc.psum_tensor("banks", [P, 8, 512], F32))
        self.acc = self.psum[:, 0:4, :].rearrange("p b (h t) -> p (b h) t", h=2)
        self.banks = Banks(ctx, nc, self.psum)
        s = lambda n: ctx.enter_context(nc.semaphore(n))
        self.s = s
        self.const_ready, self.zero_ready, self.rows_ready = s("const_ready"), s("zero_ready"), s("rows_ready")
        self.x_ready = s("x_ready")
        self.x_turns = 0
        self.norm_sq, self.xn_ready, self.norm_rstd = s("norm_sq"), s("xn_ready"), s("norm_rstd")
        self.xs_hi, self.xs_lo = s("xs_hi"), s("xs_lo")
        self.norms, self.splits = 0, 0
        self.gu_hi, self.gu_lo, self.out_hi, self.out_lo = s("gu_hi"), s("gu_lo"), s("out_hi"), s("out_lo")
        self.gu_ready, self.out_used, self.h_ready = s("gu_ready"), s("out_used"), s("h_ready")
        self.sg_ready, self.h_prod = s("sg_ready"), s("h_prod")
        self.steps = 0
        self.att_max, self.att_exp, self.att_sum, self.att_norm, self.att_out = (
            s("att_" + n) for n in ("max", "exp", "sum", "norm", "out"))
        self.att_units = 0
        self.att_cols = f32("att_cols", [P, 3, 8])
        self.ln_sq, self.ln_centred, self.ln_rstd, self.ln_scaled = (s("ln_" + n) for n in ("sq", "centred", "rstd", "scaled"))
        self.layer_norms = 0
        self.rope = f32("rope", [P, 2, 2, T])
        self.rope_ready = s("rope_ready")
        self.pos = f32("positions", [P, T], I32)
        self.cmp_w2 = f32("cmp_w2", [P, 2, HD])
        self.w_route = f32("w_route", [P, 2, KD, G_N + E_N])
        self.b_route = f32("b_route", [P, 2, G_N + E_N])
        self.wz, self.bf = f32("fox_w_z", [P, KD, FOX_H]), f32("fox_b_f", [FOX_H, 1])
        self.small_ready = s("small_ready")
        self.small_loads()
        self.act_seq, self.dve_seq, self.pool_seq = Counted(s("act_seq")), Counted(s("dve_seq")), Counted(s("pool_seq"))

    def small_loads(self):
        a = self.a
        loads = [
            (self.wz[:], a["fox_w_in"][0][:, 4 * D:4 * D + FOX_H].rearrange("(k p) n -> p k n", p=P)),
            (self.bf[:], a["fox_b_f"].rearrange("o h -> h o")),
            (self.pos[:], a["positions_2"].partition_broadcast(P)),
            (self.cmp_w2[:], a["nsa_cmp_w2_2"][0].rearrange("v p n -> p v n")),
        ]
        for layer in range(2):
            loads += [
                (self.w_route[:, layer, :, 0:G_N], a["moe_w_grp_2"][layer].rearrange("(k p) n -> p k n", p=P)),
                (self.w_route[:, layer, :, G_N:G_N + E_N], a["moe_w_exp_2"][layer].rearrange("(k p) n -> p k n", p=P)),
                (self.b_route[:, layer, 0:G_N], a["moe_b_grp_2"][layer:layer + 1, :].partition_broadcast(P)),
                (self.b_route[:, layer, G_N:G_N + E_N], a["moe_b_exp_2"][layer:layer + 1, :].partition_broadcast(P)),
            ]
        loads += [
        ]
        self.small_all = 16 * len(loads)
        return loads

    def const(self, at, n, p=P):
        return self.c[0:p, at:at + n]

    @property
    def ident(self):
        return self.const(C_IDENT, P)

    @property
    def ones(self):
        return self.const(C_ONES, P)


class Start:

    def __init__(self, k):
        self.k = k
        self.fill = k.ring.plan(1)
        self.rows = k.sq[:].rearrange("p k t -> p (k t)")[:, 0:P]
        self.pe_rows = k.sq[:].rearrange("p k t -> p (k t)")[0:32, P:2 * P]
        k.banks.plan("params", "x0", "x1", "x2", "x3")
        self.turn = k.x_turns
        k.x_turns += 1

    def sp(self, eng):
        k, r = self.k, self.k.ring
        r.wait_free(eng, self.fill)
        xt = r.slot(self.fill)[:, 0:TT * D].rearrange("p (t d) -> p t d", t=TT)
        eng.dma_start(xt, k.a["x"].rearrange("o (t p) d -> p (o t) d", p=P)).then_inc(r.full[self.fill % SLOTS], 16)

    def act_dma(self, eng):
        k, a = self.k, self.k.a
        eng.dma_start(k.c[:], a["consts"]).then_inc(k.const_ready, 16)
        rows = self.rows
        for at, n, src in [
            (R_NORM, 48, a["norm_g"].rearrange("l n (k p) -> (l n k) p", p=P)),
            (R_LB, 8, a["hg_lb_logits"].rearrange("l (k p) -> (l k) p", p=P)),
            (R_HGN, 1, a["hg_out_norm_g"]),
            (R_LNG, 32, a["ln_g_2"].rearrange("l n (k p) -> (l n k) p", p=P)),
            (R_LNB, 32, a["ln_b_2"].rearrange("l n (k p) -> (l n k) p", p=P)),
            (R_MQ, 2, a["mla_q_norm_2"].rearrange("l (k p) -> (l k) p", p=P)),
            (R_MKV, 1, a["mla_kv_norm_2"]),
        ]:
            eng.dma_start(rows[at:at + n, :], src).then_inc(k.rows_ready, 16)
        for half in (0, HD):
            eng.dma_start(rows[R_FQ:R_FQ + 1, half:half + HD], a["fox_q_norm_g"]).then_inc(k.rows_ready, 16)
            eng.dma_start(rows[R_FK:R_FK + 1, half:half + HD], a["fox_k_norm_g"]).then_inc(k.rows_ready, 16)
        eng.dma_start(self.pe_rows, a["nsa_cmp_pe_2"].rearrange("o v (l e) d -> (o v l) (e d)", e=2)).then_inc(k.rows_ready, 16)

        for dst, src in k.small_loads():
            eng.dma_start(dst, src, allow_slow_non_contiguous=True).then_inc(k.small_ready, 16)

    def pool(self, eng):
        k = self.k
        eng.memset(k.zeros[:], 0.0).then_inc(k.zero_ready, 1)

    def pe(self, pe):
        k, b = self.k, self.k.banks
        pe.wait_ge(k.const_ready, 16)
        k.ring.wait_full(pe, self.fill)
        xt = k.ring.slot(self.fill)
        for q in range(4):
            out = b.claim(pe, f"x{q}") if q else None
            if q == 0:
                pe.wait_ge(k.rows_ready, 12 * 16)
                out = b.claim(pe, "params")
                pe.transpose(out[:, 0:N_ROWS], self.rows[0:N_ROWS, :], k.ident[0:N_ROWS, 0:N_ROWS])
                b.filled(pe.transpose(out[:, P:P + 32], self.pe_rows, k.ident[0:32, 0:32]), "params")
                out = b.claim(pe, "x0")
            for n in range(4):
                kk, t = 2 * q + n // 2, n % 2
                last = pe.transpose(out[:, n * P:(n + 1) * P], xt[:, t * D + kk * P:t * D + (kk + 1) * P], k.ident)
            b.filled(last, f"x{q}")

    def dve(self, dve):
        k, b = self.k, self.k.banks
        src = b.wait(dve, "params")
        dve.tensor_copy(k.param[:, 0:N_ROWS], src[:, 0:N_ROWS])
        b.read(dve.tensor_copy(k.pe_cols[:], src[:, P:P + 32]), "params")
        for q in range(4):
            src = b.wait(dve, f"x{q}")
            ins = dve.tensor_copy(k.x[:, 2 * q:2 * q + 2, :].rearrange("p k t -> p (k t)"), src)
            ins.then_inc(k.x_ready, 1)
        dve.wait_ge(k.x_ready, 4)
        for q in range(4):
            b.release(dve, f"x{q}")
        dve.sem_inc(k.ring.free[self.fill % SLOTS], 1)


class RmsNorm:

    def __init__(self, k, row):
        self.k, self.row, self.i, self.turn = k, row, k.norms, k.x_turns
        k.norms += 1
        k.banks.plan(f"norm{self.i}")

    def act_squares(self, act):
        k = self.k
        for c in range(4):
            act.wait_ge(k.x_ready, 4 * (self.turn - 1) + c + 1)
            act.activation(k.sq[:, 2 * c:2 * c + 2], k.x[:, 2 * c:2 * c + 2], ACT.Square).then_inc(k.norm_sq, 1)

    def pe(self, pe):
        k = self.k
        out = k.banks.claim(pe, f"norm{self.i}")[:, 0:T]
        for kk in range(KD):
            if kk % 2 == 0:
                pe.wait_ge(k.norm_sq, 4 * self.i + kk // 2 + 1)
            last = pe.matmul(out, k.ones, k.sq[:, kk], start=kk == 0, stop=kk == KD - 1)
        k.banks.filled(last, f"norm{self.i}")

    def act_std(self, act):
        k = self.k
        src = k.banks.wait(act, f"norm{self.i}")[:, 0:T]
        k.banks.read(act.activation(k.std[:], src, ACT.Sqrt, bias=k.const(C_EPS, 1), scale=1.0 / D), f"norm{self.i}")

    def dve(self, dve):
        k = self.k
        k.banks.wait_read(dve, f"norm{self.i}")
        dve.reciprocal(k.rstd[:], k.std[:]).then_inc(k.norm_rstd, 1)
        dve.wait_ge(k.norm_rstd, self.i + 1)
        for kk in range(KD):
            g = k.param[:, R_NORM + self.row * KD + kk:R_NORM + self.row * KD + kk + 1]
            dve.scalar_tensor_tensor(out=k.xn[:, kk], in0=k.x[:, kk], scalar=g, in1=k.rstd[:],
                                     op0=ALU.mult, op1=ALU.mult).then_inc(k.xn_ready, 1)

    def wait_xn(self, eng, tiles=KD):
        eng.wait_ge(self.k.xn_ready, KD * self.i + tiles)


class Ffn:

    PARTS = 3

    def __init__(self, k, steps, sources, norm):
        self.k, self.steps, self.sources, self.norm = k, steps, sources, norm
        self.j0, self.split = k.steps, k.splits
        k.steps += steps
        k.splits += 1
        self.fills = [k.ring.plan(3) for _ in range(steps // 2)]
        self.body = 2 * SLOTS
        self.turns = (steps - 1) // self.body
        self.rest = steps - 1 - self.turns * self.body
        k.x_turns += 1

    def fill_more(self, i):
        return i * (48 * self.body // 6)

    def sp(self, eng):
        k, r, half = self.k, self.k.ring, self.body // 2
        turns = (self.steps // 2) // half

        def load(f, i, more):
            n = self.fills[f]
            r.wait_free(eng, n, more)
            slot, full = r.slot(n), r.full[n % SLOTS]
            wg, wu, wd = self.sources(i, f)
            for at, src in ((0, wg), (1, wu)):
                eng.dma_start(slot[:, at * 2048:(at + 1) * 2048].rearrange("p (k n) -> p k n", k=KD),
                              src).then_inc(full, 16)
            eng.dma_start(slot[:, 4096:6144].rearrange("p (j n) -> p j n", j=2), wd).then_inc(full, 16)

        with eng.Fori(0, turns) as i:
            for f in range(half):
                load(f, i, i * (half // SLOTS))
        for f in range(turns * half, self.steps // 2):
            load(f, 0, 0)

    def act_split(self, act, j, base, more):
        k, n = self.k, self.fills[j // 2]
        b, jj, raw = j % 2, j % 2, k.ring.slot(n)
        k.ring.wait_full(act, n, more)
        act.wait_ge(k.gu_ready, base + 1)
        act.activation(k.w_hi[:, b, 0:2048].rearrange("p (k n) -> p k n", n=P),
                       raw[:, 0:4096].rearrange("p (k n) -> p k n", n=256)[:, :, jj * P:(jj + 1) * P],
                       ACT.Copy).then_inc(k.gu_hi, 1)
        act.wait_ge(k.out_used, base + 1)
        act.activation(k.w_hi[:, b, 2048:3072], raw[:, 4096 + jj * D:4096 + (jj + 1) * D],
                       ACT.Copy).then_inc(k.out_hi, 1)

    def dve_split(self, dve, j, base):
        k, n = self.k, self.fills[j // 2]
        b, jj, raw = j % 2, j % 2, k.ring.slot(n)
        dve.wait_ge(k.gu_hi, base + 1)
        dve.tensor_tensor(k.w_lo[:, b, 0:2048].rearrange("p (k n) -> p k n", n=P),
                          raw[:, 0:4096].rearrange("p (k n) -> p k n", n=256)[:, :, jj * P:(jj + 1) * P],
                          k.w_hi[:, b, 0:2048].bitcast(F32).rearrange("p (k n) -> p k n", n=P),
                          ALU.subtract).then_inc(k.gu_lo, 1)
        dve.wait_ge(k.out_hi, base + 1)
        dve.tensor_tensor(k.w_lo[:, b, 2048:3072], raw[:, 4096 + jj * D:4096 + (jj + 1) * D],
                          k.w_hi[:, b, 2048:3072].bitcast(F32), ALU.subtract).then_inc(k.out_lo, 1)

    def dve_release(self, dve, j, base):
        if j % 2 == 1:
            dve.wait_ge(self.k.out_lo, base + 1)
            dve.sem_inc(self.k.ring.free[self.fills[j // 2] % SLOTS], 1)

    def act_silu(self, act, j, base):
        k, b = self.k, j % 2
        act.wait_ge(k.h_ready, base + 1)
        act.wait_ge(k.gu_ready, base + 3)
        act.activation(k.sg[:, b], k.psum[:, 4 + b, 0:T], ACT.Silu).then_inc(k.sg_ready, 1)

    def dve_hidden(self, dve, j, base):
        k, b = self.k, j % 2
        dve.wait_ge(k.sg_ready, base + 1)
        left, right = k.sg[:, b], k.psum[:, 4 + b, T:2 * T]
        dve.tensor_tensor(k.h32[:, b], left, right, ALU.mult).then_inc(k.h_prod, 1)
        dve.wait_ge(k.out_used, base + 1)
        dve.tensor_tensor(k.h_hi[:, b], left, right, ALU.mult).then_inc(k.h_prod, 1)
        dve.wait_ge(k.h_prod, 2 * base + 2)
        dve.tensor_tensor(k.h_lo[:, b], k.h32[:, b], k.h_hi[:, b].bitcast(F32), ALU.subtract).then_inc(k.h_ready, 1)

    def pool(self, pool):
        pass

    def pe_three(self, pe, out, w_hi, w_lo, m_hi, m_lo, start, stop):
        pe.matmul(out, w_hi, m_hi, start=start, stop=False, skip_group_check=True)
        pe.matmul(out, w_hi, m_lo, start=False, stop=False, skip_group_check=True)
        return pe.matmul(out, w_lo, m_hi, start=False, stop=stop, skip_group_check=True)

    def pe_gate_up(self, pe, b, base):
        k = self.k
        pe.wait_ge(k.gu_lo, base + 1)
        pe.wait_ge(k.h_ready, base + 1)
        for part in range(2):
            for kk in range(KD):
                at = (part * KD + kk) * P
                last = self.pe_three(pe, k.psum[:, 4 + b, part * T:(part + 1) * T],
                                     k.w_hi[:, b, at:at + P], k.w_lo[:, b, at:at + P],
                                     k.x_hi[:, kk], k.x_lo[:, kk], kk == 0, kk == KD - 1)
        last.then_inc(k.gu_ready, 1)

    def pe_down(self, pe, b, base):
        k = self.k
        pe.wait_ge(k.out_lo, base + 1)
        pe.wait_ge(k.h_ready, base + 3)
        for n in range(KD):
            at = 2048 + n * P
            last = self.pe_three(pe, k.acc[:, n], k.w_hi[:, b, at:at + P], k.w_lo[:, b, at:at + P],
                                 k.h_hi[:, b], k.h_lo[:, b], False, True)
        last.then_inc(k.out_used, 1)

    def pe(self, pe):
        k = self.k
        self.norm.pe(pe)
        pe.wait_ge(k.xs_lo, 4 * self.split + 4)
        for bank in range(4):
            pe.matmul(k.psum[:, bank, :], k.zeros[:, 0:P], k.zeros[:], start=True, stop=True, skip_group_check=True)
        self.pe_gate_up(pe, 0, self.j0)
        turns, rest = divmod(self.steps - 1, 2)
        with pe.Fori(0, turns) as i:
            for t in range(2):
                self.pe_gate_up(pe, (t + 1) % 2, i * 2 + (self.j0 + t + 1))
                self.pe_down(pe, t % 2, i * 2 + (self.j0 + t))
        for j in range(2 * turns, self.steps - 1):
            self.pe_gate_up(pe, (j + 1) % 2, self.j0 + j + 1)
            self.pe_down(pe, j % 2, self.j0 + j)
        self.pe_down(pe, (self.steps - 1) % 2, self.j0 + self.steps - 1)

    def act_input(self, act):
        k, src = self.k, self.k.xn
        for c in range(4):
            self.norm.wait_xn(act, 2 * c + 2)
            act.activation(k.x_hi[:, 2 * c:2 * c + 2], src[:, 2 * c:2 * c + 2], ACT.Copy).then_inc(k.xs_hi, 1)

    def dve_input(self, dve):
        k, src = self.k, self.k.xn
        for c in range(4):
            dve.wait_ge(k.xs_hi, 4 * self.split + c + 1)
            dve.tensor_tensor(k.x_lo[:, 2 * c:2 * c + 2], src[:, 2 * c:2 * c + 2],
                              k.x_hi[:, 2 * c:2 * c + 2].bitcast(F32), ALU.subtract).then_inc(k.xs_lo, 1)

    def act(self, act):
        self.norm.act_squares(act)
        self.act_split(act, 0, self.j0, 0)
        self.norm.act_std(act)
        self.act_input(act)
        with act.Fori(0, self.turns) as i:
            for t in range(self.body):
                self.act_split(act, t + 1, i * self.body + (self.j0 + t + 1), self.fill_more(i))
                self.act_silu(act, t, i * self.body + (self.j0 + t))
        for j in range(self.turns * self.body, self.steps - 1):
            self.act_split(act, j + 1, self.j0 + j + 1, 0)
            self.act_silu(act, j, self.j0 + j)
        self.act_silu(act, self.steps - 1, self.j0 + self.steps - 1)

    def dve(self, dve):
        k = self.k
        self.dve_split(dve, 0, self.j0)
        self.norm.dve(dve)
        self.dve_input(dve)
        with dve.Fori(0, self.turns) as i:
            for t in range(self.body):
                base = i * self.body + self.j0
                self.dve_split(dve, t + 1, base + (t + 1))
                self.dve_hidden(dve, t, base + t)
                self.dve_release(dve, t + 1, base + (t + 1))
        for j in range(self.turns * self.body, self.steps - 1):
            self.dve_split(dve, j + 1, self.j0 + j + 1)
            self.dve_hidden(dve, j, self.j0 + j)
            self.dve_release(dve, j + 1, self.j0 + j + 1)
        j = self.steps - 1
        self.dve_hidden(dve, j, self.j0 + j)
        dve.wait_ge(k.out_used, self.j0 + self.steps + 2)
        self.dve_residual(dve)

    def dve_residual(self, dve):
        k = self.k
        for c in range(4):
            dve.scalar_tensor_tensor(out=k.x[:, 2 * c:2 * c + 2], in0=k.acc[:, 2 * c:2 * c + 2], scalar=0.5,
                                     in1=k.x[:, 2 * c:2 * c + 2], op0=ALU.mult, op1=ALU.add).then_inc(k.x_ready, 1)


def swiglu_sources(a, layer, half):
    w_in, w_out = a["ffn_w_in"][layer, half], a["ffn_w_out"][layer, half]

    def sources(i, f):
        p = i * 3 + f
        cols = lambda at: w_in[:, ds(p * 256 + at, 256)].rearrange("(k q) n -> q k n", q=P)
        return cols(0), cols(FF), w_out[ds(p * 256, 256), :].rearrange("(j q) n -> q j n", q=P)
    return sources


class Finish:

    def __init__(self, k):
        self.k = k
        self.turn = k.x_turns
        k.banks.plan("y0", "y1", "y2", "y3")
        self.stored, self.turned = k.s("stored"), k.s("turned")
        self.y = k.arena[:, 0:TT * D].rearrange("p (t d) -> p t d", t=TT)

    def pe(self, pe):
        k, b = self.k, self.k.banks
        pe.wait_ge(k.x_ready, 4 * self.turn)
        for q in range(4):
            out = b.claim(pe, f"y{q}")
            for n in range(4):
                t, kk = q // 2, (q % 2) * 4 + n
                last = pe.transpose(out[:, n * P:(n + 1) * P], k.x[:, kk, t * P:(t + 1) * P], k.ident)
            b.filled(last, f"y{q}")

    def dve(self, dve):
        k, b = self.k, self.k.banks
        for q in range(4):
            src = b.wait(dve, f"y{q}")
            b.read(dve.tensor_copy(self.y[:, q // 2, (q % 2) * 512:(q % 2 + 1) * 512], src), f"y{q}")

    def sp(self, eng):
        k, b = self.k, self.k.banks
        for q in range(4):
            b.wait_read(eng, f"y{q}")
            eng.dma_start(k.a["out"][0, (q // 2) * P:(q // 2 + 1) * P, (q % 2) * 512:(q % 2 + 1) * 512],
                          self.y[:, q // 2, (q % 2) * 512:(q % 2 + 1) * 512]).then_inc(self.stored, 16)
        eng.wait_ge(self.stored, 64)


class Mixer:

    def plan_blocks(self, blocks, per_fill=3):
        self.block_fill = {}
        for at in range(0, len(blocks), per_fill):
            some = blocks[at:at + per_fill]
            n = self.k.ring.plan(len(some))
            for i, (name, src) in enumerate(some):
                self.block_fill[name] = (n, i, src)

    def sp_blocks(self, eng):
        k, last = self.k, None
        for n, i, src in self.block_fill.values():
            if n != last:
                k.ring.wait_free(eng, n)
                last = n
            width = src.shape[1]
            eng.dma_start(k.ring.slot(n)[:, i * 2048:i * 2048 + KD * width].rearrange("p (k n) -> p k n", k=KD),
                          src.rearrange("(k p) n -> p k n", p=P)).then_inc(k.ring.full[n % SLOTS], 16)

    def block(self, name):
        n, i, src = self.block_fill[name]
        width = src.shape[1]
        return n, self.k.ring.slot(n)[:, i * 2048:i * 2048 + KD * width].rearrange("p (k n) -> p k n", k=KD)

    def project(self, pe, out, w, moving, start=True):
        for kk in range(KD):
            last = pe.matmul(out, w(kk), moving[:, kk], start=kk == 0, stop=kk == KD - 1)
        return last

    def release(self, eng, fill):
        eng.sem_inc(self.k.ring.free[fill % SLOTS], 1)

    def plan_out(self, name, w_out):
        k = self.k
        self.w_out, self.out_fills = w_out, [k.ring.plan(1), k.ring.plan(1)]
        self.out_ready = k.s(name + "_out_ready")
        self.turn = k.x_turns
        k.x_turns += 1

    def sp_out(self, eng):
        k = self.k
        for half, n in enumerate(self.out_fills):
            k.ring.wait_free(eng, n)
            eng.dma_start(k.ring.slot(n)[:, 0:4096].rearrange("p (k n) -> p k n", k=KD),
                          self.w_out[:, half * 512:(half + 1) * 512].rearrange("(k p) n -> p k n", p=P)
                          ).then_inc(k.ring.full[n % SLOTS], 16)

    def pe_out(self, pe):
        k = self.k
        for n in range(KD):
            fill = self.out_fills[n // 4]
            if n % 4 == 0:
                k.ring.wait_full(pe, fill)
            w = k.ring.slot(fill)
            last = self.project(pe, k.acc[:, n], lambda kk: w[:, kk * 512 + (n % 4) * P:kk * 512 + (n % 4 + 1) * P], k.cat)
            if n % 2:
                last.then_inc(self.out_ready, 1)

    def dve_out(self, dve, scale=1.0):
        k = self.k
        for c in range(4):
            dve.wait_ge(self.out_ready, c + 1)
            if c % 2:
                self.release(dve, self.out_fills[c // 2])
            dve.scalar_tensor_tensor(out=k.x[:, 2 * c:2 * c + 2], in0=k.x[:, 2 * c:2 * c + 2], scalar=scale,
                                     in1=k.acc[:, 2 * c:2 * c + 2], op0=ALU.mult, op1=ALU.add).then_inc(k.x_ready, 1)


class Hgrn2(Mixer):

    def __init__(self, k, norm):
        self.k, self.norm = k, norm
        a = k.a
        w = a["hg_w_in"][0]
        cols = lambda part, n: w[:, part * D + n * 256:part * D + (n + 1) * 256]
        self.plan_blocks([(f"z{n}", cols(1, n)) for n in range(4)] + [(f"q{n}", cols(0, n)) for n in range(4)]
                         + [(f"g{n}", cols(3, n)) for n in range(4)])
        self.v_fills = [k.ring.plan(1), k.ring.plan(1)]
        self.plan_out("hg", a["hg_w_out"][0])
        k.banks.plan(*[f"hg_{p}{n}" for p in "zqg" for n in range(4)])
        k.banks.plan(*[f"hg_v{h}{t}" for h in range(2) for t in range(TT)])
        k.banks.plan(*[f"hg_s{n}_{g}" for n in [7, 0, 1, 2, 3, 4, 5, 6] for g in range(4)], "hg_x0", "hg_x1")
        k.banks.plan(*[f"hg_n{n}" for n in range(4)])
        ar = k.arena
        part = lambda n: ar[:, n * 2048:(n + 1) * 2048].rearrange("p (h t) -> p h t", h=HG_H)
        self.q, self.kk, self.b, self.g, self.e = part(0), part(1), part(2), part(3), [part(4), part(5)]
        self.v = ar[:, 6 * 2048:7 * 2048].rearrange("p (t d) -> p t d", t=TT)
        self.score = ar[:, 7 * 2048:7 * 2048 + 2048].rearrange("p (m t) -> p m t", m=16)
        self.cross = ar[:, 8 * 2048:8 * 2048 + 1024].rearrange("p (h t) -> p h t", h=HG_H)
        self.std = self.e[0]
        s = lambda n: k.s("hg_" + n)
        self.sig, self.qg, self.f_ready, self.ln_ready, self.b_ready = s("sig"), s("qg"), s("f"), s("ln"), s("b")
        self.diff, self.exped, self.scaled = s("diff"), s("exped"), s("scaled")
        self.o_ready, self.o_sq, self.o_rstd, self.o_normed, self.cat_ready = s("o"), s("o_sq"), s("o_rstd"), s("o_normed"), s("cat")

    def sp(self, eng):
        k = self.k
        self.sp_blocks(eng)
        for half, n in enumerate(self.v_fills):
            k.ring.wait_free(eng, n)
            eng.dma_start(k.ring.slot(n)[:, 0:4096].rearrange("p (k n) -> p k n", k=KD),
                          k.a["hg_w_in"][0][:, 2 * D + half * 512:2 * D + (half + 1) * 512].rearrange("(k p) n -> p k n", p=P)
                          ).then_inc(k.ring.full[n % SLOTS], 16)
        self.sp_out(eng)

    def pe(self, pe):
        k, b = self.k, self.k.banks
        self.norm.pe(pe)
        self.norm.wait_xn(pe)
        for part in "zqg":
            for n in range(4):
                fill, w = self.block(f"{part}{n}")
                k.ring.wait_full(pe, fill)
                out = b.claim(pe, f"hg_{part}{n}")
                for h in range(2):
                    last = self.project(pe, out[:, h * T:(h + 1) * T], lambda kk: w[:, kk, h * P:(h + 1) * P], k.xn)
                b.filled(last, f"hg_{part}{n}")
        for half, n in enumerate(self.v_fills):
            k.ring.wait_full(pe, n)
            w = k.ring.slot(n)[:, 0:4096].rearrange("p (k n) -> p k n", k=KD)
            for t in range(TT):
                out = b.claim(pe, f"hg_v{half}{t}")
                b.filled(self.project(pe, out, lambda kk: k.xn[:, kk, t * P:(t + 1) * P], w), f"hg_v{half}{t}")
        for i, n in enumerate([7, 0, 1, 2, 3, 4, 5, 6]):
            if n == 7:
                pe.wait_ge(self.qg, 4)
            else:
                pe.wait_ge(self.scaled, 2 * (n + 1))
            e = self.e[n % 2]
            for g in range(4):
                out = b.claim(pe, f"hg_s{n}_{g}")
                for m in range(4 * g, 4 * g + 4):
                    h, t = m // 2, slice(m % 2 * P, (m % 2 + 1) * P)
                    left, right = (self.kk, self.q) if n == 7 else (e, e)
                    last = pe.matmul(out[:, (m % 4) * P:(m % 4 + 1) * P], left[:, h, t], right[:, h, t], start=True, stop=True)
                b.filled(last, f"hg_s{n}_{g}")
        pe.wait_ge(self.scaled, 16)
        for g in range(2):
            out = b.claim(pe, f"hg_x{g}")
            for h in range(4 * g, 4 * g + 4):
                last = pe.matmul(out[:, (h % 4) * P:(h % 4 + 1) * P], self.e[1][:, h, 0:P], self.e[1][:, h, P:T], start=True, stop=True)
            b.filled(last, f"hg_x{g}")
        b.wait_read(pe, "hg_v11")
        b.wait_read(pe, "hg_s6_3")
        b.wait_read(pe, "hg_x1")
        for h in range(HG_H):
            v = [self.v[:, t, h * P:(h + 1) * P] for t in range(TT)]
            pe.matmul(k.acc[:, h, 0:P], v[0], self.score[:, 2 * h], start=True, stop=True)
            pe.matmul(k.acc[:, h, P:T], v[0], self.cross[:, h], start=True, stop=False)
            last = pe.matmul(k.acc[:, h, P:T], v[1], self.score[:, 2 * h + 1], start=False, stop=True)
            if h % 2:
                last.then_inc(self.o_ready, 1)
        for n in range(4):
            pe.wait_ge(self.o_sq, n + 1)
            out = b.claim(pe, f"hg_n{n}")
            b.filled(pe.matmul(out, k.ones, k.sq[:, 2 * n:2 * n + 2], start=True, stop=True), f"hg_n{n}")
        pe.wait_ge(self.cat_ready, 4)
        self.pe_out(pe)

    def act(self, act):
        k, b = self.k, self.k.banks
        self.norm.act_squares(act)
        self.norm.act_std(act)
        for n in range(4):
            src = b.wait(act, f"hg_z{n}").rearrange("p (h t) -> p h t", h=2)
            act.activation(self.b[:, 2 * n:2 * n + 2], src, ACT.Sigmoid).then_inc(self.sig, 1)
            b.read(act.activation(self.kk[:, 2 * n:2 * n + 2], src, ACT.Sigmoid, scale=-1.0), f"hg_z{n}")
        for part, to in (("q", self.q), ("g", self.g)):
            for n in range(4):
                src = b.wait(act, f"hg_{part}{n}").rearrange("p (h t) -> p h t", h=2)
                act.activation(to[:, 2 * n:2 * n + 2], src, ACT.Sigmoid).then_inc(self.sig, 1)
        act.wait_ge(self.f_ready, 4)
        act.activation(self.e[0], self.e[0], ACT.Ln).then_inc(self.ln_ready, 1)
        for half in range(2):
            for t in range(TT):
                src = b.wait(act, f"hg_v{half}{t}")
                b.read(act.activation(self.v[:, t, half * 512:(half + 1) * 512], src, ACT.Copy), f"hg_v{half}{t}")
            self.release(act, self.v_fills[half])
        for n in range(8):
            act.wait_ge(self.diff, self.diffs[n])
            act.activation(self.e[n % 2], self.e[n % 2], ACT.Exp).then_inc(self.exped, 1)
        for g in range(2):
            src = b.wait(act, f"hg_x{g}").rearrange("p (h t) -> p h t", h=4)
            b.read(act.activation(self.cross[:, 4 * g:4 * g + 4], src, ACT.Copy), f"hg_x{g}")
        for n in range(4):
            act.wait_ge(self.o_ready, n + 1)
            act.activation(k.sq[:, 2 * n:2 * n + 2], k.acc[:, 2 * n:2 * n + 2], ACT.Square).then_inc(self.o_sq, 1)
        for n in range(4):
            src = b.wait(act, f"hg_n{n}").rearrange("p (h t) -> p h t", h=2)
            b.read(act.activation(self.std[:, 2 * n:2 * n + 2], src, ACT.Sqrt, bias=k.const(C_EPS, 1), scale=1.0 / P), f"hg_n{n}")

    def level(self, t, L):
        return t.rearrange("p h t -> p (h t)").rearrange("p (n a l) -> p n a l", a=2, l=L)

    diffs = [2, 4, 6, 8, 10, 12, 14, 18]

    def pool(self, pool):
        k, b, seq = self.k, self.k.banks, self.k.pool_seq
        ends = self.b.rearrange("p h (c l) -> p h c l", l=HG_CHUNK)[:, :, :, HG_CHUNK - 1]
        pool.wait_ge(self.b_ready, 8)
        seq.inc(pool.tensor_tensor(k.ends01[:], ends[:, :, 0], ends[:, :, 1], ALU.add))
        for n in range(7):
            L = 1 << n
            if n >= 2:
                b.wait(pool, f"hg_s{n - 2}_3")
            e, c = self.level(self.e[n % 2], L), self.level(self.b, L)
            mid = c[:, :, 0, L - 1:L].to_broadcast([P, c.shape[1], L])
            pool.tensor_tensor(e[:, :, 0, :], mid, c[:, :, 0, :], ALU.subtract).then_inc(self.diff, 1)
            if L < HG_CHUNK:
                pool.tensor_tensor(e[:, :, 1, :], c[:, :, 1, :], mid, ALU.subtract).then_inc(self.diff, 1)
            else:
                pool.tensor_copy(e[:, :, 1, :], c[:, :, 1, :]).then_inc(self.diff, 1)
        b.wait(pool, "hg_s5_3")
        seq.wait(pool)
        chunk = lambda t, c: t[:, :, c * HG_CHUNK:(c + 1) * HG_CHUNK]
        wide = lambda col: col.to_broadcast([P, HG_H, HG_CHUNK])
        e, c = self.e[1], self.b
        pool.tensor_tensor(chunk(e, 0), wide(k.ends01[:].unsqueeze(2)), chunk(c, 0), ALU.subtract).then_inc(self.diff, 1)
        pool.tensor_tensor(chunk(e, 1), wide(c[:, :, 127:128]), chunk(c, 1), ALU.subtract).then_inc(self.diff, 1)
        pool.tensor_copy(chunk(e, 2), chunk(c, 2)).then_inc(self.diff, 1)
        pool.tensor_tensor(chunk(e, 3), chunk(c, 3), wide(c[:, :, 191:192]), ALU.add).then_inc(self.diff, 1)

    def dve(self, dve):
        k, b, seq = self.k, self.k.banks, self.k.dve_seq
        l, w, r = k.param[:, R_LB:R_LB + 8], k.lb_e[:], k.lb_r[:]
        for ins in (lambda: dve.tensor_tensor(w, l, l, ALU.subtract),
                    lambda: dve.tensor_scalar(w, w, 1.0, None, ALU.add),
                    lambda: dve.reciprocal(r, w),
                    lambda: dve.tensor_tensor(r, w, r, ALU.mult),
                    lambda: dve.tensor_tensor(k.lb[:], r, r, ALU.subtract),
                    lambda: dve.tensor_scalar(k.omlb[:], k.lb[:], -1.0, 1.0, ALU.mult, ALU.add)):
            seq.inc(ins())
            seq.wait(dve)
        self.norm.dve(dve)
        seq.inc(dve.memset(self.score, 0.0))
        f, up, off = self.b, self.e[0], self.e[1]
        for h in range(HG_H):
            if h % 2 == 0:
                b.wait_read(dve, f"hg_z{h // 2}")
            if h == 4:
                self.release(dve, self.block_fill["z2"][0])
            seq.inc(dve.tensor_scalar(f[:, h], f[:, h], k.omlb[:, h:h + 1], k.lb[:, h:h + 1], ALU.mult, ALU.add))
            seq.inc(dve.tensor_scalar(self.kk[:, h], self.kk[:, h], k.omlb[:, h:h + 1], None, ALU.mult))
        seq.wait(dve)
        seq.inc(dve.tensor_scalar(f, f, 1e-30, None, ALU.max))
        seq.wait(dve)
        small = 2.0 ** -60
        seq.inc(dve.tensor_scalar(up, f, small, 2.0 ** 36 - 1.0, ALU.is_lt, ALU.mult))
        seq.inc(dve.tensor_scalar(off, f, small, 36.0 * float(np.log(2.0)), ALU.is_lt, ALU.mult))
        seq.wait(dve)
        for c in range(4):
            hs = slice(2 * c, 2 * c + 2)
            dve.scalar_tensor_tensor(out=up[:, hs], in0=up[:, hs], scalar=1.0, in1=f[:, hs], op0=ALU.add, op1=ALU.mult).then_inc(self.f_ready, 1)
        for part, to, at, last in (("q", self.q, 4, "q1"), ("g", self.g, 8, "g0")):
            for n in range(4):
                dve.wait_ge(self.sig, at + n + 1)
                if f"{part}{n}" in ("q1", "g0", "g3"):
                    self.release(dve, self.block_fill[f"{part}{n}"][0])
                src = b.at(f"hg_{part}{n}").rearrange("p (h t) -> p h t", h=2)
                dve.tensor_tensor(to[:, 2 * n:2 * n + 2], to[:, 2 * n:2 * n + 2], src, ALU.mult).then_inc(self.qg, 1)
                if n:
                    dve.wait_ge(self.qg, at - 4 + n)
                    b.release(dve, f"hg_{part}{n - 1}")
            dve.wait_ge(self.qg, at)
            b.release(dve, f"hg_{part}3")
        dve.wait_ge(self.ln_ready, 1)
        seq.inc(dve.tensor_tensor(up, up, off, ALU.subtract))
        seq.wait(dve)
        for h in range(HG_H):
            dve.tensor_tensor_scan(f[:, h], k.const(C_RESET, T), up[:, h], 0.0, ALU.mult, ALU.add).then_inc(self.b_ready, 1)

        def place(n):
            mask = k.const(C_LEVEL + n * P, P).bitcast(U32).unsqueeze(1).to_broadcast([P, 4, P])
            for g in range(4):
                src = b.wait(dve, f"hg_s{n}_{g}").rearrange("p (m t) -> p m t", m=4)
                b.read(dve.copy_predicated(self.score[:, 4 * g:4 * g + 4], mask, src), f"hg_s{n}_{g}")

        for n in range(8):
            dve.wait_ge(self.exped, n + 1)
            e = self.level(self.e[n % 2], 1 << n)
            for half, by in enumerate((self.kk, self.q)):
                dve.tensor_tensor(e[:, :, half, :], e[:, :, half, :], self.level(by, 1 << n)[:, :, half, :],
                                  ALU.mult).then_inc(self.scaled, 1)
            place(n - 1 if n else 7)
        for n in range(4):
            hs = slice(2 * n, 2 * n + 2)
            b.wait_read(dve, f"hg_n{n}")
            dve.reciprocal(self.std[:, hs], self.std[:, hs]).then_inc(self.o_rstd, 1)
            dve.wait_ge(self.o_rstd, n + 1)
            dve.scalar_tensor_tensor(out=self.e[1][:, hs], in0=k.acc[:, hs], scalar=k.param[:, R_HGN:R_HGN + 1],
                                     in1=self.std[:, hs], op0=ALU.mult, op1=ALU.mult).then_inc(self.o_normed, 1)
            dve.wait_ge(self.o_normed, n + 1)
            dve.tensor_tensor(k.cat[:, hs], self.e[1][:, hs], self.g[:, hs], ALU.mult).then_inc(self.cat_ready, 1)
        self.dve_out(dve)


class Attention(Mixer):

    def plan_units(self, name, units, at):
        k = self.k
        self.units, self.u0, self.name = units, k.att_units, name
        k.att_units += len(units)
        n = len(units)
        for i in range(n + 3):
            if i < n:
                k.banks.plan(f"{name}_s{i}")
            if 2 <= i < n + 2:
                k.banks.plan(f"{name}_t{i - 2}")
        part = lambda j: at[:, j * 768:(j + 1) * 768].rearrange("p (r t) -> p r t", r=3)
        self.sc, self.pr, self.pt = part(0), part(1), part(2)
        self.acc_out = {}
        for i, u in enumerate(units):
            self.acc_out[u["out"][0]] = self.u0 + i + 1

    def pe_unit(self, pe, i):
        k, b, n = self.k, self.k.banks, len(self.units)
        if i < n:
            u = self.units[i]
            out = b.claim(pe, f"{self.name}_s{i}")[:, 0:u["n"]]
            pairs = [(u["q"], u["keys"])] + u.get("bias", [])
            for m, (left, right) in enumerate(pairs):
                last = pe.matmul(out, left, right, start=m == 0, stop=m == len(pairs) - 1)
            b.filled(last, f"{self.name}_s{i}")
        if 2 <= i < n + 2:
            u, j = self.units[i - 2], i - 2
            pe.wait_ge(k.att_norm, self.u0 + j + 1)
            out = b.claim(pe, f"{self.name}_t{j}")
            for m, (rows, _) in enumerate(u["values"]):
                last = pe.transpose(out[0:rows, m * P:(m + 1) * P], self.pr[:, j % 3, m * P:m * P + rows], k.ident)
            b.filled(last, f"{self.name}_t{j}")
        if i >= 3:
            u, j = self.units[i - 3], i - 3
            b.wait_read(pe, f"{self.name}_t{j}")
            pair, half, qt = u["out"]
            out = k.acc[half * HD:(half + 1) * HD, pair, qt * P:(qt + 1) * P]
            for m, (rows, v) in enumerate(u["values"]):
                last = pe.matmul(out, v, self.pt[0:rows, j % 3, m * P:(m + 1) * P],
                                 start=u["first"] and m == 0, stop=u["last"] and m == len(u["values"]) - 1)
            last.then_inc(k.att_out, 1)

    def act_unit(self, act, i):
        k, b, n = self.k, self.k.banks, len(self.units)
        if i < n:
            u, c = self.units[i], (self.u0 + i) % 8
            act.wait_ge(k.att_max, self.u0 + i + 1)
            act.activation(self.pr[:, i % 3, 0:u["n"]], self.sc[:, i % 3, 0:u["n"]], ACT.Exp, scale=-1.0,
                           bias=k.att_cols[:, 0, c:c + 1], accum_out=k.att_cols[:, 1, c:c + 1]).then_inc(k.att_exp, 1)
        if 2 <= i < n + 2:
            u, j = self.units[i - 2], i - 2
            src = b.wait(act, f"{self.name}_t{j}")
            if self.u0 + j >= 3:
                act.wait_ge(k.att_out, self.u0 + j - 2)
            rows, w = u["values"][0][0], len(u["values"]) * P
            b.read(act.activation(self.pt[0:rows, j % 3, 0:w], src[0:rows, 0:w], ACT.Copy), f"{self.name}_t{j}")

    def dve_unit(self, dve, i):
        k, b, seq, n = self.k, self.k.banks, self.k.dve_seq, len(self.units)
        if i < n:
            u, c = self.units[i], (self.u0 + i) % 8
            if self.u0 + i >= 3:
                dve.wait_ge(k.att_exp, self.u0 + i - 2)
            src = b.wait(dve, f"{self.name}_s{i}")[:, 0:u["n"]]
            dve.tensor_tensor_reduce(self.sc[:, i % 3, 0:u["n"]], src, u["mask"], -u["scale"], -NEG_BIG, ALU.add, ALU.min,
                                     k.att_cols[:, 0, c:c + 1]).then_inc(k.att_max, 1)
            dve.wait_ge(k.att_max, self.u0 + i + 1)
            b.release(dve, f"{self.name}_s{i}")
        if i >= 1 and i - 1 < n:
            u, j = self.units[i - 1], i - 1
            c = (self.u0 + j) % 8
            total, weight = k.att_cols[:, 1, c:c + 1], k.att_cols[:, 2, c:c + 1]
            dve.wait_ge(k.att_exp, self.u0 + j + 1)
            if u["seen"] is not None:
                pr = self.pr[:, j % 3, 0:u["n"]]
                seq.inc(dve.tensor_tensor_reduce(pr, pr, u["seen"], 1.0, 0.0, ALU.mult, ALU.add, total))
                seq.wait(dve)
                seq.inc(dve.tensor_scalar(total, total, 1e-30, None, ALU.max))
                seq.wait(dve)
            if u["gate"] is None:
                dve.reciprocal(weight, total).then_inc(k.att_sum, 1)
            else:
                seq.inc(dve.reciprocal(total, total))
                seq.wait(dve)
                dve.tensor_tensor(weight, total, u["gate"], ALU.mult).then_inc(k.att_sum, 1)

    def pool_units(self, pool):
        k = self.k
        for j, u in enumerate(self.units):
            c, pr = (self.u0 + j) % 8, self.pr[:, j % 3, 0:u["n"]]
            pool.wait_ge(k.att_sum, self.u0 + j + 1)
            pool.tensor_scalar(pr, pr, k.att_cols[:, 2, c:c + 1], None, ALU.mult).then_inc(k.att_norm, 1)

    def run(self, eng, unit):
        for i in range(len(self.units) + 3):
            unit(eng, i)


class Fox(Attention):

    def __init__(self, k, norm):
        self.k, self.norm = k, norm
        a, ar, b = k.a, k.arena, k.banks
        w = a["fox_w_in"][0]
        cols = lambda part, n: w[:, part * D + n * 256:part * D + (n + 1) * 256]
        self.normed = [f"k{n}" for n in range(4)] + [f"q{n}" for n in range(4)]
        self.plan_blocks([(f"k{n}", cols(1, n)) for n in range(4)] + [(f"q{n}", cols(0, n)) for n in range(4)]
                         + [(f"g{n}", cols(3, n)) for n in range(4)])
        self.v_fills = [k.ring.plan(1), k.ring.plan(1)]
        self.plan_out("fox", a["fox_w_out"][0])
        b.plan("fox_z")
        for i, name in enumerate(self.normed):
            b.plan("fox_" + name)
            if i:
                b.plan("fox_n" + self.normed[i - 1])
        b.plan("fox_n" + self.normed[-1])
        b.plan(*[f"fox_g{n}" for n in range(4)], *[f"fox_v{h}{t}" for h in range(2) for t in range(TT)])
        part = lambda n: ar[:, n * 2048:(n + 1) * 2048].rearrange("p (h t) -> p h t", h=8)
        self.q, self.kk, self.g, self.bq, self.bk = part(0), part(1), part(2), part(4), part(5)
        self.v = ar[:, 3 * 2048:4 * 2048].rearrange("p (t d) -> p t d", t=TT)
        self.std = ar[:, 14592:15616].rearrange("p (r h t) -> p r h t", r=2, h=2)
        self.zb, self.ez, self.lf, self.cc, self.nc_ = (ar[0:FOX_H, 15616 + n * T:15616 + (n + 1) * T] for n in range(5))
        s = lambda n: k.s("fox_" + n)
        self.sq_ready, self.rstd_ready, self.gate_ready = s("sq"), s("rstd"), s("gate")
        self.z_step, self.c_ready, self.bias_ready, self.bias_rows, self.cat_ready = s("z"), s("c"), s("bias"), s("bias_rows"), s("cat")
        units = []
        for h in range(FOX_H):
            pair, half = divmod(h, 2)
            at = slice(half * HD, (half + 1) * HD)
            for t in range(TT):
                n, tok = (t + 1) * P, slice(t * P, (t + 1) * P)
                units.append(dict(
                    q=self.q[at, pair, tok], keys=self.kk[at, pair, 0:n], bias=[(self.bq[at, pair, tok], self.bk[at, pair, 0:n])],
                    n=n, mask=k.const(C_CAUSAL + 384 - n, n), seen=None, scale=HD ** -0.5, gate=None,
                    values=[(P, self.v[:, m, h * HD:(h + 1) * HD]) for m in range(t + 1)],
                    out=(pair, half, t), first=True, last=True))
        self.plan_units("fox", units, ar[:, 12288:14592])

    def sp(self, eng):
        k = self.k
        self.sp_blocks(eng)
        for half, n in enumerate(self.v_fills):
            k.ring.wait_free(eng, n)
            eng.dma_start(k.ring.slot(n)[:, 0:4096].rearrange("p (k n) -> p k n", k=KD),
                          k.a["fox_w_in"][0][:, 2 * D + half * 512:2 * D + (half + 1) * 512].rearrange("(k p) n -> p k n", p=P)
                          ).then_inc(k.ring.full[n % SLOTS], 16)
        self.sp_out(eng)

    def pe(self, pe):
        k, b = self.k, self.k.banks
        self.norm.pe(pe)
        self.norm.wait_xn(pe)
        pe.wait_ge(k.small_ready, k.small_all)
        b.filled(self.project(pe, b.claim(pe, "fox_z")[0:FOX_H, 0:T], lambda kk: k.wz[:, kk], k.xn), "fox_z")

        def blocks(name):
            fill, w = self.block(name)
            k.ring.wait_full(pe, fill)
            out = b.claim(pe, "fox_" + name)
            for h in range(2):
                last = self.project(pe, out[:, h * T:(h + 1) * T], lambda kk: w[:, kk, h * P:(h + 1) * P], k.xn)
            b.filled(last, "fox_" + name)

        def stat(i):
            pe.wait_ge(self.sq_ready, i + 1)
            at = 2 * (i % 4)
            b.filled(pe.matmul(b.claim(pe, "fox_n" + self.normed[i]), k.const(C_BLK, P), k.sq[:, at:at + 2],
                               start=True, stop=True), "fox_n" + self.normed[i])

        for i, name in enumerate(self.normed):
            blocks(name)
            if i:
                stat(i - 1)
        stat(len(self.normed) - 1)
        for n in range(4):
            blocks(f"g{n}")
        for half, n in enumerate(self.v_fills):
            k.ring.wait_full(pe, n)
            w = k.ring.slot(n)[:, 0:4096].rearrange("p (k n) -> p k n", k=KD)
            for t in range(TT):
                out = b.claim(pe, f"fox_v{half}{t}")
                b.filled(self.project(pe, out, lambda kk: k.xn[:, kk, t * P:(t + 1) * P], w), f"fox_v{half}{t}")
        b.wait_read(pe, "fox_q3")
        b.wait_read(pe, "fox_v11")
        pe.wait_ge(self.bias_ready, 4)
        pe.wait_ge(self.bias_rows, 64)
        self.run(pe, self.pe_unit)
        pe.wait_ge(self.cat_ready, 4)
        self.pe_out(pe)

    def act(self, act):
        k, b = self.k, self.k.banks
        self.norm.act_squares(act)
        self.norm.act_std(act)

        def square(i):
            src = b.wait(act, "fox_" + self.normed[i]).rearrange("p (h t) -> p h t", h=2)
            at = 2 * (i % 4)
            act.activation(k.sq[:, at:at + 2], src, ACT.Square).then_inc(self.sq_ready, 1)

        def root(i):
            name = "fox_n" + self.normed[i]
            src = b.wait(act, name).rearrange("p (h t) -> p h t", h=2)
            if i >= 2:
                b.wait_read(act, "fox_" + self.normed[i - 2])
            b.read(act.activation(self.std[:, i % 2], src, ACT.Sqrt, bias=k.const(C_EPS, 1), scale=1.0 / HD), name)

        for i in range(len(self.normed)):
            square(i)
            if i:
                root(i - 1)
        root(len(self.normed) - 1)
        act.wait_ge(self.z_step, 1)
        act.activation(self.ez, self.zb, ACT.Abs).then_inc(self.z_step, 1)
        act.wait_ge(self.z_step, 2)
        act.activation(self.ez, self.ez, ACT.Exp, scale=-1.0).then_inc(self.z_step, 1)
        act.wait_ge(self.z_step, 3)
        act.activation(self.ez, self.ez, ACT.Ln, bias=k.const(C_ONES, 1, FOX_H)).then_inc(self.z_step, 1)
        for n in range(4):
            src = b.wait(act, f"fox_g{n}").rearrange("p (h t) -> p h t", h=2)
            if n in (0, 3):
                self.release(act, self.block_fill[f"g{n}"][0])
            b.read(act.activation(self.g[:, 2 * n:2 * n + 2], src, ACT.Sigmoid), f"fox_g{n}")
        for half in range(2):
            for t in range(TT):
                src = b.wait(act, f"fox_v{half}{t}")
                b.read(act.activation(self.v[:, t, half * 512:(half + 1) * 512], src, ACT.Copy), f"fox_v{half}{t}")
            self.release(act, self.v_fills[half])
        act.wait_ge(self.c_ready, 2)
        act.wait_ge(self.bias_ready, 4)
        for half in range(2):
            act.dma_start(self.bq[half * HD:half * HD + 1], self.cc[half:FOX_H:2, :]).then_inc(self.bias_rows, 16)
            act.dma_start(self.bk[half * HD + 32:half * HD + 33], self.nc_[half:FOX_H:2, :]).then_inc(self.bias_rows, 16)
        self.run(act, self.act_unit)

    def dve(self, dve):
        k, b, seq = self.k, self.k.banks, self.k.dve_seq
        self.norm.dve(dve)
        src = b.wait(dve, "fox_z")[0:FOX_H, 0:T]
        dve.tensor_scalar(self.zb, src, k.bf[0:FOX_H, 0:1], None, ALU.add).then_inc(self.z_step, 1)
        dve.wait_ge(self.z_step, 1)
        b.release(dve, "fox_z")
        for i, name in enumerate(self.normed):
            std = self.std[:, i % 2]
            b.wait_read(dve, "fox_n" + name)
            if name in ("k2", "q1"):
                self.release(dve, self.block_fill[name][0])
            dve.reciprocal(std, std).then_inc(self.rstd_ready, 1)
            dve.wait_ge(self.rstd_ready, i + 1)
            to, row = (self.kk, R_FK) if name[0] == "k" else (self.q, R_FQ)
            n = int(name[1])
            src = b.at("fox_" + name).rearrange("p (h t) -> p h t", h=2)
            b.read(dve.scalar_tensor_tensor(out=to[:, 2 * n:2 * n + 2], in0=src, scalar=k.param[:, row:row + 1], in1=std,
                                            op0=ALU.mult, op1=ALU.mult), "fox_" + name)
        dve.wait_ge(self.z_step, 4)
        seq.inc(dve.scalar_tensor_tensor(out=self.lf, in0=self.zb, scalar=0.0, in1=self.ez, op0=ALU.min, op1=ALU.subtract))
        seq.wait(dve)
        seq.inc(dve.tensor_scalar(self.lf, self.lf, HD ** 0.5, None, ALU.mult))
        seq.wait(dve)
        dve.tensor_tensor_scan(self.cc, k.const(C_CAUSAL, T, FOX_H), self.lf, 0.0, ALU.add, ALU.add).then_inc(self.c_ready, 1)
        dve.wait_ge(self.c_ready, 1)
        dve.tensor_scalar(self.nc_, self.cc, -1.0, None, ALU.mult).then_inc(self.c_ready, 1)
        n_units = len(self.units)
        for i in range(n_units + 3):
            self.dve_unit(dve, i)
            if i >= 12 and (i - 12) % 8 == 0:
                self.dve_gate(dve, (i - 12) // 8)
        self.dve_gate(dve, 3)
        self.dve_out(dve)

    def dve_gate(self, dve, bank):
        k, pairs = self.k, slice(2 * bank, 2 * bank + 2)
        dve.wait_ge(k.att_out, self.acc_out[2 * bank + 1])
        dve.tensor_tensor(k.cat[:, pairs], k.acc[:, pairs], self.g[:, pairs], ALU.mult).then_inc(self.cat_ready, 1)

    def pool(self, pool):
        k, seq = self.k, self.k.pool_seq
        self.norm.wait_xn(pool)
        seq.inc(pool.memset(self.bq, 0.0))
        seq.inc(pool.memset(self.bk, 0.0))
        seq.wait(pool)
        for half in range(2):
            pool.memset(self.bq[half * HD + 32:half * HD + 33], 1.0).then_inc(self.bias_ready, 1)
            pool.memset(self.bk[half * HD:half * HD + 1], 1.0).then_inc(self.bias_ready, 1)
        self.pool_units(pool)


class Rope:

    C1, MAGIC = 6.28125, 12582912.0
    C2 = 2 * float(np.pi) - C1

    def __init__(self, k):
        self.k, self.turn = k, k.x_turns
        self.sined = k.s("rope_sined")
        self.angle, self.turns, self.half = (k.arena[:, n * 512:(n + 1) * 512].rearrange("p (r t) -> p r t", r=2) for n in range(3))
        self.reduced = k.s("rope_reduced")

    def sp(self, eng):
        pass

    def pool(self, pool):
        pass

    def pe(self, pe):
        pass

    def act(self, act):
        k = self.k
        act.wait_ge(self.reduced, 1)
        act.activation(k.rope[:, 1], self.angle, ACT.Sin).then_inc(self.sined, 1)
        act.activation(self.half, self.angle, ACT.Sin, scale=0.5).then_inc(self.sined, 1)

    def dve(self, dve):
        k, seq = self.k, self.k.dve_seq
        dve.wait_ge(k.small_ready, k.small_all)
        dve.wait_ge(k.x_ready, 4 * self.turn)
        seq.inc(dve.tensor_copy(self.turns[:, 0], k.pos[:]))
        seq.wait(dve)
        for r, col in ((0, C_INVN), (1, C_INVM)):
            seq.inc(dve.tensor_scalar(self.angle[:, r], self.turns[:, 0], k.const(col, 1), None, ALU.mult))
        seq.wait(dve)
        steps = [
            lambda: dve.tensor_scalar(self.turns, self.angle, 1.0 / (2 * float(np.pi)), self.MAGIC, ALU.mult, ALU.add),
            lambda: dve.tensor_scalar(self.turns, self.turns, self.MAGIC, None, ALU.subtract),
            lambda: dve.scalar_tensor_tensor(out=self.angle, in0=self.turns, scalar=-self.C1, in1=self.angle, op0=ALU.mult, op1=ALU.add),
            lambda: dve.scalar_tensor_tensor(out=self.angle, in0=self.turns, scalar=-self.C2, in1=self.angle, op0=ALU.mult, op1=ALU.add),
        ]
        for step in steps:
            seq.inc(step())
            seq.wait(dve)
        dve.tensor_scalar(self.angle, self.angle, 3.1415925, -3.1415925, ALU.min, ALU.max).then_inc(self.reduced, 1)
        dve.wait_ge(self.sined, 2)
        seq.inc(dve.tensor_tensor(self.half, self.half, self.half, ALU.mult))
        seq.wait(dve)
        dve.tensor_scalar(k.rope[:, 0], self.half, -2.0, 1.0, ALU.mult, ALU.add).then_inc(k.rope_ready, 1)


class LayerNorm:

    def __init__(self, k, row):
        self.k, self.row, self.i = k, row, k.layer_norms
        k.layer_norms += 1
        self.before = k.x_turns
        k.x_turns += 1
        k.banks.plan(f"ln_m{self.i}", f"ln_v{self.i}")

    def sp(self, eng):
        pass

    def pool(self, pool):
        pass

    def pe(self, pe):
        k, b, i = self.k, self.k.banks, self.i
        out = b.claim(pe, f"ln_m{i}")[:, 0:T]
        for kk in range(KD):
            if kk % 2 == 0:
                pe.wait_ge(k.x_ready, 4 * (self.before - 1) + kk // 2 + 1)
            last = pe.matmul(out, k.ones, k.x[:, kk], start=kk == 0, stop=kk == KD - 1)
        b.filled(last, f"ln_m{i}")
        out = b.claim(pe, f"ln_v{i}")[:, 0:T]
        for kk in range(KD):
            if kk % 2 == 0:
                pe.wait_ge(k.ln_sq, 4 * i + kk // 2 + 1)
            last = pe.matmul(out, k.ones, k.sq[:, kk], start=kk == 0, stop=kk == KD - 1)
        b.filled(last, f"ln_v{i}")

    def act(self, act):
        k, b, i = self.k, self.k.banks, self.i
        for c in range(4):
            act.wait_ge(k.ln_centred, 4 * i + c + 1)
            act.activation(k.sq[:, 2 * c:2 * c + 2], k.xn[:, 2 * c:2 * c + 2], ACT.Square).then_inc(k.ln_sq, 1)
        src = b.wait(act, f"ln_v{i}")[:, 0:T]
        b.read(act.activation(k.std[:], src, ACT.Sqrt, bias=k.const(C_LNEPS, 1), scale=1.0 / D), f"ln_v{i}")

    def dve(self, dve):
        k, b, i = self.k, self.k.banks, self.i
        total = b.wait(dve, f"ln_m{i}")[:, 0:T].unsqueeze(1).to_broadcast([P, 2, T])
        for c in range(4):
            cs = slice(2 * c, 2 * c + 2)
            dve.scalar_tensor_tensor(out=k.xn[:, cs], in0=total, scalar=-1.0 / D, in1=k.x[:, cs],
                                     op0=ALU.mult, op1=ALU.add).then_inc(k.ln_centred, 1)
        dve.wait_ge(k.ln_centred, 4 * i + 4)
        b.release(dve, f"ln_m{i}")
        b.wait_read(dve, f"ln_v{i}")
        dve.reciprocal(k.rstd[:], k.std[:]).then_inc(k.ln_rstd, 1)
        dve.wait_ge(k.ln_rstd, i + 1)
        for c in range(4):
            cs = slice(2 * c, 2 * c + 2)
            dve.tensor_tensor(k.xn[:, cs], k.xn[:, cs], k.rstd[:].unsqueeze(1).to_broadcast([P, 2, T]), ALU.mult).then_inc(k.ln_scaled, 1)
        for c in range(4):
            dve.wait_ge(k.ln_scaled, 4 * i + c + 1)
            for kk in (2 * c, 2 * c + 1):
                g = k.param[:, R_LNG + self.row * KD + kk:R_LNG + self.row * KD + kk + 1]
                bb = k.param[:, R_LNB + self.row * KD + kk:R_LNB + self.row * KD + kk + 1]
                ins = dve.tensor_scalar(k.x[:, kk], k.xn[:, kk], g, bb, ALU.mult, ALU.add)
            ins.then_inc(k.x_ready, 1)


class Memory(Attention):

    def plan_memory(self, layer, name, xq, mk, mv, mem_t):
        self.mem_name, self.xq, self.mk, self.mv, self.mem_t = name, xq, mk, mv, mem_t
        self.mem_layer = layer
        self.mem_fill = self.k.ring.plan(2)
        self.k.banks.plan(*[f"{name}_mt{n}" for n in range(4)], f"{name}_mk", f"{name}_mv")

    def sp_memory(self, eng):
        k, n = self.k, self.mem_fill
        k.ring.wait_free(eng, n)
        slot, full = k.ring.slot(n), k.ring.full[n % SLOTS]
        eng.dma_start(slot[:, 0:2048].rearrange("p (t d) -> p t d", t=TT), k.a["mem_2"].rearrange("o (t p) d -> p (o t) d", p=P)).then_inc(full, 16)
        eng.dma_start(slot[:, 2048:6144].rearrange("p (k n) -> p k n", k=KD),
                      k.a["mem_w_kv_2"][self.mem_layer].rearrange("(k p) n -> p k n", p=P)).then_inc(full, 16)

    def pe_memory(self, pe):
        k, b, name = self.k, self.k.banks, self.mem_name
        k.ring.wait_full(pe, self.mem_fill)
        slot = k.ring.slot(self.mem_fill)
        w = slot[:, 2048:6144].rearrange("p (k n) -> p k n", k=KD)
        for q in range(4):
            out = b.claim(pe, f"{name}_mt{q}")
            for n in range(4):
                kk, t = 2 * q + n // 2, n % 2
                last = pe.transpose(out[:, n * P:(n + 1) * P], slot[:, t * D + kk * P:t * D + (kk + 1) * P], k.ident)
            b.filled(last, f"{name}_mt{q}")
        for q in range(4):
            b.wait_read(pe, f"{name}_mt{q}")
        out = b.claim(pe, f"{name}_mk")
        for h in range(2):
            last = self.project(pe, out[:, h * T:(h + 1) * T], lambda kk: w[:, kk, h * P:(h + 1) * P], self.mem_t)
        b.filled(last, f"{name}_mk")
        out = b.claim(pe, f"{name}_mv")
        for t in range(TT):
            last = self.project(pe, out[:, t * T:(t + 1) * T], lambda kk: self.mem_t[:, kk, t * P:(t + 1) * P], w[:, :, 256:512])
        b.filled(last, f"{name}_mv")

    def act_memory(self, act):
        k, b, name = self.k, self.k.banks, self.mem_name
        for q in range(4):
            src = b.wait(act, f"{name}_mt{q}").rearrange("p (k t) -> p k t", k=2)
            b.read(act.activation(self.mem_t[:, 2 * q:2 * q + 2], src, ACT.Copy), f"{name}_mt{q}")
        for part, to in (("mk", self.mk), ("mv", self.mv)):
            src = b.wait(act, f"{name}_{part}").rearrange("p (k t) -> p k t", k=2)
            b.read(act.activation(to, src, ACT.Copy), f"{name}_{part}")
        self.release(act, self.mem_fill)

    def memory_units(self):
        k, units = self.k, []
        for h in range(XA_H):
            pair, half = divmod(h, 2)
            at = slice(half * HD, (half + 1) * HD)
            for t in range(TT):
                units.append(dict(
                    q=self.xq[at, pair, t * P:(t + 1) * P], keys=self.mk[at, pair, :], n=T, mask=k.const(C_CAUSAL, T),
                    seen=None, scale=HD ** -0.5, gate=None, values=[(P, self.mv[:, m, h * HD:(h + 1) * HD]) for m in range(TT)],
                    out=(6 + pair, half, t), first=True, last=True))
        return units

    def dve_collect(self, dve, bank):
        k, pairs = self.k, slice(2 * bank, 2 * bank + 2)
        dve.wait_ge(k.att_out, self.acc_out[2 * bank + 1])
        dve.tensor_copy(k.cat[:, pairs], k.acc[:, pairs]).then_inc(self.cat_ready, 1)

    def dve_units(self, dve):
        bank = 0
        for i in range(len(self.units) + 3):
            self.dve_unit(dve, i)
            while bank < 3 and self.u0 + i - 4 >= self.acc_out[2 * bank + 1]:
                self.dve_collect(dve, bank)
                bank += 1
        while bank < 4:
            self.dve_collect(dve, bank)
            bank += 1

    def pe_rotate(self, pe, name, raw, matrix, shape):
        k, b = self.k, self.k.banks
        b.wait_read(pe, name)
        out = b.claim(pe, name + "_r")
        b.filled(pe.matmul(out[0:shape[0], 0:shape[1]], matrix, raw, start=True, stop=True), name + "_r")

    def dve_rotate(self, dve, name, raw, out, cos, sin, shape):
        k, b, seq = self.k, self.k.banks, self.k.dve_seq
        wide = lambda t: t.unsqueeze(1).to_broadcast(list(shape))
        rot = b.wait(dve, name + "_r")[raw.start_partition():raw.start_partition() + shape[0], 0:shape[1] * shape[2]]
        rot = rot.rearrange("p (m n) -> p m n", m=shape[1])
        seq.inc(dve.tensor_tensor(out, rot, wide(sin), ALU.mult))
        first = seq.n
        seq.inc(dve.tensor_tensor(raw, raw, wide(cos), ALU.mult))
        seq.wait(dve)
        b.read(dve.tensor_tensor(out, out, raw, ALU.add), name + "_r")


class Nsa(Memory):

    def __init__(self, k):
        self.k = k
        a, ar, b = k.a, k.arena, k.banks
        w = a["nsa_w_in_2"][0]
        offs = dict(q0=0, q1=256, q2=512, kc=768, vc=1024, ks=1280, vs=1536, kw=1792, vw=2048)
        col = lambda at, n=256: w[:, at:at + n]
        cut = lambda at, p, *s: ar[:p, at:at + int(np.prod(s))].rearrange(
            "p (a b) -> p a b", a=s[0])
        self.q, self.ks, self.kw = cut(0, P, 6, T), cut(1536, P, 4, T), cut(2560, P, 4, T)
        self.kc2, self.vc2 = cut(3584, P, 4, T), cut(4608, P, 4, T)
        self.vs, self.vw = cut(5632, P, 2, T), cut(6144, P, 2, T)
        self.kc, self.vc, self.ks_once, self.kw_once = (cut(10240 + n * 512, P, 2, T) for n in range(4))
        self.raw = [cut(12544 + n * 512, P, 2, T) for n in range(3)]
        self.hid = [cut(14080 + n * 64, P, 4, N_CMP) for n in range(2)]
        self.kcmp, self.kcmp_raw = cut(14208, P, 4, N_CMP), cut(14272, P, 4, N_CMP)
        self.vcmp = ar[0:N_CMP, 14336:14336 + T]
        self.gates = cut(14592, P, 2, 36)
        self.pe_bias = ar[:, 14664:14666]
        self.plan_memory(0, "nsa", cut(6656, P, 2, T), cut(7168, P, 2, T), cut(7680, P, 2, T), cut(8192, P, 8, T))
        self.plan_blocks([(n, col(offs[n])) for n in ("kc", "vc", "ks", "kw", "vs", "vw", "q0", "q1", "q2")]
                         + [("xq", col(2340)), ("gt", col(2304, 36))])
        self.w1_fill = k.ring.plan(1)
        self.plan_out("nsa", a["w_out_2"][0])
        b.plan("nsa_kc", "nsa_vc")
        self.rotated = ["ks", "kw", "q0", "q1", "q2"]
        for i, n in enumerate(self.rotated):
            b.plan("nsa_" + n)
            if i:
                b.plan("nsa_" + self.rotated[i - 1] + "_r")
            if n == "kw":
                b.plan("nsa_vs", "nsa_vw")
        b.plan("nsa_q2_r", "nsa_xq", "nsa_gt", "nsa_hk", "nsa_hv", "nsa_kcmp", "nsa_vcmp", "nsa_kcmp_r")
        s = lambda n: k.s("nsa_" + n)
        self.cat_ready, self.pe_ready, self.hid_ready = s("cat"), s("pe"), s("hid")
        self.pairs_placed, self.keys_placed = s("pairs_placed"), s("keys_placed")
        units = []
        for h in range(NSA_H):
            pair, half, kv = h // 2, h % 2, h // GROUP
            at = slice(half * HD, (half + 1) * HD)
            vcol = slice(kv * HD, (kv + 1) * HD)
            for t in range(TT):
                n = (t + 1) * P
                base = dict(q=self.q[at, pair, t * P:(t + 1) * P], scale=HD ** -0.5, out=(pair, half, t))
                gate = lambda j: self.gates[:, t, 3 * h + j:3 * h + j + 1]
                units.append(dict(base, keys=self.kcmp[at, kv, :], n=N_CMP, mask=k.const(C_CMPADD + t * N_CMP, N_CMP),
                                  seen=k.const(C_CMPMUL + t * N_CMP, N_CMP), gate=gate(0),
                                  values=[(N_CMP, self.vcmp[:, vcol])], first=True, last=False))
                for j, keys, v in ((1, self.ks, self.vs), (2, self.kw, self.vw)):
                    units.append(dict(base, keys=keys[at, kv, 0:n], n=n, mask=k.const(C_CAUSAL + 384 - n, n), seen=None,
                                      gate=gate(j), values=[(P, v[:, m, vcol]) for m in range(t + 1)], first=False, last=j == 2))
        self.plan_units("nsa", units + self.memory_units(), ar[:, 10240:12544])

    def sp(self, eng):
        k = self.k
        self.sp_memory(eng)
        self.sp_blocks(eng)
        n = self.w1_fill
        k.ring.wait_free(eng, n)
        eng.dma_start(k.ring.slot(n)[:, 0:4096].rearrange("p (v l n) -> p v l n", v=2, l=16),
                      k.a["nsa_cmp_w1_2"][0].rearrange("v (l p) n -> p v l n", p=P)).then_inc(k.ring.full[n % SLOTS], 16)
        self.sp_out(eng)

    def pe(self, pe):
        k, b = self.k, self.k.banks
        pe.wait_ge(k.x_ready, 4 * self.turn)
        pe.wait_ge(k.rope_ready, 1)
        self.pe_memory(pe)

        def tiles(name):
            fill, w = self.block(name)
            k.ring.wait_full(pe, fill)
            out = b.claim(pe, "nsa_" + name)
            for h in range(2):
                last = self.project(pe, out[:, h * T:(h + 1) * T], lambda kk: w[:, kk, h * P:(h + 1) * P], k.x)
            b.filled(last, "nsa_" + name)

        def rows(name, n):
            fill, w = self.block(name)
            k.ring.wait_full(pe, fill)
            out = b.claim(pe, "nsa_" + name)
            for t in range(TT):
                last = self.project(pe, out[:, t * n:(t + 1) * n], lambda kk: k.x[:, kk, t * P:(t + 1) * P], w)
            b.filled(last, "nsa_" + name)

        for name in ("kc", "vc"):
            tiles(name)
        for i, name in enumerate(self.rotated):
            tiles(name)
            if i:
                self.rotate(pe, i - 1)
            if name == "kw":
                rows("vs", T)
                rows("vw", T)
        self.rotate(pe, len(self.rotated) - 1)
        tiles("xq")
        rows("gt", 36)
        k.ring.wait_full(pe, self.w1_fill)
        w1 = k.ring.slot(self.w1_fill)[:, 0:4096].rearrange("p (v l n) -> p v l n", v=2, l=16)
        pe.wait_ge(self.pairs_placed, 128)
        for v, (name, src) in enumerate((("nsa_hk", self.kc2), ("nsa_hv", self.vc2))):
            out = b.claim(pe, name)
            for l in range(16):
                pe.matmul(out[:, 64:65], w1[:, v, l], k.pe_cols[:, v * 16 + l:v * 16 + l + 1], start=l == 0, stop=l == 15)
            for l in range(16):
                last = pe.matmul(out[:, 0:4 * N_CMP], w1[:, v, l], src[:, :, 2 * l:2 * l + 225:CMP_STRIDE], start=l == 0, stop=l == 15)
            b.filled(last, name)
        pe.wait_ge(self.hid_ready, 1)
        pe.wait_ge(k.small_ready, k.small_all)
        flat = lambda t: t.rearrange("p h n -> p (h n)")
        out = b.claim(pe, "nsa_kcmp")
        for half in range(2):
            last = pe.matmul(out[half * HD:(half + 1) * HD, 0:4 * N_CMP], k.cmp_w2[:, 0], flat(self.hid[0]), start=True, stop=True)
        b.filled(last, "nsa_kcmp")
        pe.wait_ge(self.hid_ready, 2)
        out = b.claim(pe, "nsa_vcmp")
        for h in range(NSA_KV):
            last = pe.matmul(out[0:N_CMP, h * HD:(h + 1) * HD], self.hid[1][:, h], k.cmp_w2[:, 1], start=True, stop=True)
        b.filled(last, "nsa_vcmp")
        self.pe_rotate(pe, "nsa_kcmp", flat(self.kcmp_raw), k.const(C_ROTN, P), (P, 4 * N_CMP))
        b.wait_read(pe, "nsa_q2_r")
        b.wait_read(pe, "nsa_gt")
        b.wait_read(pe, "nsa_vcmp")
        b.wait_read(pe, "nsa_kcmp_r")
        pe.wait_ge(self.keys_placed, 128)
        self.run(pe, self.pe_unit)
        pe.wait_ge(self.cat_ready, 4)
        self.pe_out(pe)

    def rotate(self, pe, i):
        k = self.k
        raw = self.raw[i % 3].rearrange("p m t -> p (m t)")
        self.pe_rotate(pe, "nsa_" + self.rotated[i], raw, k.const(C_ROTN, P), (P, 2 * T))

    def act(self, act):
        k, b = self.k, self.k.banks
        act.wait_ge(k.x_ready, 4 * self.turn)
        act.wait_ge(k.rope_ready, 1)
        self.act_memory(act)
        for name, once, pairs in (("kc", self.kc, self.kc2), ("vc", self.vc, self.vc2)):
            src = b.wait(act, "nsa_" + name).rearrange("p (m t) -> p m t", m=2)
            b.read(act.activation(once, src, ACT.Copy), "nsa_" + name)
            b.wait_read(act, "nsa_" + name)
            for j in range(2):
                src = once[j * HD:(j + 1) * HD]
                act.dma_start(pairs[0:HD, j:NSA_KV:2], src).then_inc(self.pairs_placed, 16)
                act.dma_start(pairs[HD:P, j:NSA_KV:2, 0:T - 1], src[:, :, 1:T]).then_inc(self.pairs_placed, 16)
        copies = {"vs": self.vs, "vw": self.vw}
        for i, name in enumerate(self.rotated):
            if i >= 3:
                b.wait_read(act, "nsa_" + self.rotated[i - 3] + "_r")
            src = b.wait(act, "nsa_" + name).rearrange("p (m t) -> p m t", m=2)
            if name in ("ks", "q2"):
                self.release(act, self.block_fill[name][0])
            b.read(act.activation(self.raw[i % 3], src, ACT.Copy), "nsa_" + name)
            if name == "kw":
                for n, to in copies.items():
                    src = b.wait(act, "nsa_" + n).rearrange("p (m t) -> p m t", m=2)
                    b.read(act.activation(to, src, ACT.Copy), "nsa_" + n)
                self.release(act, self.block_fill["vw"][0])
        for name, once, keys in (("ks", self.ks_once, self.ks), ("kw", self.kw_once, self.kw)):
            b.wait_read(act, f"nsa_{name}_r")
            for j in range(2):
                for half in range(2):
                    act.dma_start(keys[half * HD:(half + 1) * HD, j:NSA_KV:2], once[j * HD:(j + 1) * HD]).then_inc(self.keys_placed, 16)
        src = b.wait(act, "nsa_xq").rearrange("p (m t) -> p m t", m=2)
        b.read(act.activation(self.xq, src, ACT.Copy), "nsa_xq")
        src = b.wait(act, "nsa_gt")[:, 0:72].rearrange("p (m t) -> p m t", m=2)
        self.release(act, self.block_fill["gt"][0])
        b.read(act.activation(self.gates, src, ACT.Sigmoid), "nsa_gt")
        for v, name in enumerate(("nsa_hk", "nsa_hv")):
            act.wait_ge(self.pe_ready, v + 1)
            src = b.at(name)[:, 0:4 * N_CMP].rearrange("p (h n) -> p h n", h=4)
            act.activation(self.hid[v], src, ACT.Silu, bias=self.pe_bias[:, v:v + 1]).then_inc(self.hid_ready, 1)
            act.wait_ge(self.hid_ready, v + 1)
            b.release(act, name)
        self.release(act, self.w1_fill)
        src = b.wait(act, "nsa_kcmp")[:, 0:4 * N_CMP].rearrange("p (h n) -> p h n", h=4)
        b.read(act.activation(self.kcmp_raw, src, ACT.Copy), "nsa_kcmp")
        src = b.wait(act, "nsa_vcmp")[0:N_CMP, 0:T]
        b.read(act.activation(self.vcmp, src, ACT.Copy), "nsa_vcmp")
        self.run(act, self.act_unit)

    def dve(self, dve):
        k, b = self.k, self.k.banks
        cos, sin = k.rope[:, 0, 0, :], k.rope[:, 1, 0, :]
        outs = [self.ks_once, self.kw_once] + [self.q[:, 2 * n:2 * n + 2] for n in range(3)]
        for i, name in enumerate(self.rotated):
            self.dve_rotate(dve, "nsa_" + name, self.raw[i % 3], outs[i], cos, sin, (P, 2, T))
        for v, name in enumerate(("nsa_hk", "nsa_hv")):
            src = b.wait(dve, name)
            dve.tensor_copy(self.pe_bias[:, v:v + 1], src[:, 64:65]).then_inc(self.pe_ready, 1)
        ends = slice(CMP_LEN - 1, T, CMP_STRIDE)
        self.dve_rotate(dve, "nsa_kcmp", self.kcmp_raw, self.kcmp, cos[:, ends], sin[:, ends], (P, 4, N_CMP))
        self.dve_units(dve)
        self.dve_out(dve, ALPHA)

    def pool(self, pool):
        self.pool_units(pool)


class Mla(Memory):

    def __init__(self, k):
        self.k = k
        a, ar, b = k.a, k.arena, k.banks
        cut = lambda at, p, *s: ar[:p, at:at + int(np.prod(s))].rearrange("p (a b) -> p a b", a=s[0])
        self.q, self.kk, self.v = cut(0, P, MLA_H, T), cut(3072, P, MLA_H, T), cut(6144, P, TT, MLA_H * HD)
        self.cq, self.ckv = cut(7680, P, 2, T), ar[:, 8192:8192 + T]
        self.kr_raw, self.kr = cut(8448, MLA_K, 1, T), cut(8704, MLA_K, 1, T)
        self.raw = [cut(8960 + n * 512, MLA_K, 2, T) for n in range(3)]
        self.std = cut(10496, P, 2, T)
        self.plan_memory(1, "mla", cut(11008, P, 2, T), cut(11520, P, 2, T), cut(12032, P, 2, T), cut(12544, P, 8, T))
        self.in_fill, self.up_fill = k.ring.plan(1), k.ring.plan(2)
        self.plan_out("mla", a["w_out_2"][1])
        b.plan("mla_cq", "mla_ckv", "mla_xq", "mla_n", "mla_kr_r")
        for i in range(6):
            b.plan(f"mla_q{i}", f"mla_k{i}")
            if i:
                b.plan(f"mla_q{i - 1}_r")
        b.plan("mla_q5_r", *[f"mla_v{t}{half}" for t in range(TT) for half in range(2)])
        s = lambda n: k.s("mla_" + n)
        self.sq_ready, self.std_ready, self.rstd_ready = s("sq"), s("std"), s("rstd")
        self.kr_copied, self.kr_ready, self.kr_placed = s("kr_copied"), s("kr"), s("kr_placed")
        self.latent_ready, self.cat_ready = s("latent"), s("cat")
        units = []
        for h in range(MLA_H):
            for t in range(TT):
                n = (t + 1) * P
                units.append(dict(
                    q=self.q[0:MLA_K, h, t * P:n], keys=self.kk[0:MLA_K, h, 0:n], n=n, mask=k.const(C_CAUSAL + 384 - n, n),
                    seen=None, scale=MLA_K ** -0.5, gate=None, out=(h // 2, h % 2, t), first=True, last=True,
                    values=[(P, self.v[:, m, h * HD:(h + 1) * HD]) for m in range(t + 1)]))
        self.plan_units("mla", units + self.memory_units(), ar[:, 14592:16896])

    def sp(self, eng):
        k, r, a = self.k, self.k.ring, self.k.a
        self.sp_memory(eng)
        r.wait_free(eng, self.in_fill)
        eng.dma_start(r.slot(self.in_fill)[:, 0:KD * 672].rearrange("p (k n) -> p k n", k=KD),
                      a["mla_w_in_2"][0].rearrange("(k p) n -> p k n", p=P)).then_inc(r.full[self.in_fill % SLOTS], 16)
        r.wait_free(eng, self.up_fill)
        slot, full = r.slot(self.up_fill), r.full[self.up_fill % SLOTS]
        eng.dma_start(slot[:, 0:2304].rearrange("p (k n) -> p k n", k=2),
                      a["mla_w_uq_2"][0].rearrange("(k p) n -> p k n", p=P)).then_inc(full, 16)
        eng.dma_start(slot[:, 2304:3840], a["mla_w_ukv_2"][0]).then_inc(full, 16)
        self.sp_out(eng)

    def pe(self, pe):
        k, b = self.k, self.k.banks
        pe.wait_ge(k.x_ready, 4 * self.turn)
        self.pe_memory(pe)
        k.ring.wait_full(pe, self.in_fill)
        w = k.ring.slot(self.in_fill)[:, 0:KD * 672].rearrange("p (k n) -> p k n", k=KD)

        def columns(out, at, n):
            return self.project(pe, out, lambda kk: w[:, kk, at:at + n], k.x)

        out = b.claim(pe, "mla_cq")
        columns(out[:, 0:T], 0, P)
        b.filled(columns(out[:, T:2 * T], P, P), "mla_cq")
        out = b.claim(pe, "mla_ckv")
        columns(out[:, 0:T], 256, P)
        b.filled(columns(out[0:MLA_K, T:2 * T], 320, MLA_K), "mla_ckv")
        out = b.claim(pe, "mla_xq")
        columns(out[:, 0:T], 416, P)
        b.filled(columns(out[:, T:2 * T], 416 + P, P), "mla_xq")
        pe.wait_ge(self.sq_ready, 2)
        out = b.claim(pe, "mla_n")
        pe.matmul(out[:, 0:T], k.ones, k.sq[:, 0], start=True, stop=False)
        pe.matmul(out[:, 0:T], k.ones, k.sq[:, 1], start=False, stop=True)
        b.filled(pe.matmul(out[:, T:2 * T], k.ones, k.sq[:, 2], start=True, stop=True), "mla_n")
        rot = k.c[0:MLA_K, C_ROTM:C_ROTM + MLA_K]
        pe.wait_ge(self.kr_copied, 1)
        b.filled(pe.matmul(b.claim(pe, "mla_kr_r")[0:MLA_K, 0:T], rot, self.kr_raw[:, 0], start=True, stop=True), "mla_kr_r")
        k.ring.wait_full(pe, self.up_fill)
        slot = k.ring.slot(self.up_fill)
        uq = slot[:, 0:2304].rearrange("p (k n) -> p k n", k=2)
        ukv = slot[:, 2304:3840].rearrange("p (h n) -> p h n", h=MLA_H)
        pe.wait_ge(self.latent_ready, 3)

        def rotate(i):
            self.pe_rotate(pe, f"mla_q{i}", self.raw[i % 3].rearrange("p m t -> p (m t)"), rot, (MLA_K, 2 * T))

        for i in range(6):
            out = b.claim(pe, f"mla_q{i}")
            for j in range(2):
                at = (2 * i + j) * MLA_K
                for kk in range(2):
                    last = pe.matmul(out[0:MLA_K, j * T:(j + 1) * T], uq[:, kk, at:at + MLA_K], self.cq[:, kk], start=kk == 0, stop=kk == 1)
            b.filled(last, f"mla_q{i}")
            out = b.claim(pe, f"mla_k{i}")
            for j in range(2):
                last = pe.matmul(out[0:HD, j * T:(j + 1) * T], ukv[:, 2 * i + j, 0:HD], self.ckv, start=True, stop=True)
            b.filled(last, f"mla_k{i}")
            if i:
                rotate(i - 1)
        rotate(5)
        for t in range(TT):
            for half in range(2):
                out = b.claim(pe, f"mla_v{t}{half}")[:, 0:6 * HD]
                b.filled(pe.matmul(out.rearrange("p (h n) -> p h n", h=6), self.ckv[:, t * P:(t + 1) * P],
                                   ukv[:, 6 * half:6 * half + 6, HD:2 * HD], start=True, stop=True), f"mla_v{t}{half}")
        b.wait_read(pe, "mla_q5_r")
        b.wait_read(pe, "mla_v11")
        pe.wait_ge(self.kr_placed, 1)
        self.run(pe, self.pe_unit)
        pe.wait_ge(self.cat_ready, 4)
        self.pe_out(pe)

    def act(self, act):
        k, b = self.k, self.k.banks
        act.wait_ge(k.x_ready, 4 * self.turn)
        self.act_memory(act)
        src = b.wait(act, "mla_cq").rearrange("p (m t) -> p m t", m=2)
        act.activation(k.sq[:, 0:2], src, ACT.Square).then_inc(self.sq_ready, 1)
        src = b.wait(act, "mla_ckv")
        act.activation(k.sq[:, 2], src[:, 0:T], ACT.Square).then_inc(self.sq_ready, 1)
        act.activation(self.kr_raw[:, 0], src[0:MLA_K, T:2 * T], ACT.Copy).then_inc(self.kr_copied, 1)
        src = b.wait(act, "mla_xq").rearrange("p (m t) -> p m t", m=2)
        self.release(act, self.in_fill)
        b.read(act.activation(self.xq, src, ACT.Copy), "mla_xq")
        src = b.wait(act, "mla_n")
        act.activation(self.std[:, 0], src[:, 0:T], ACT.Sqrt, bias=k.const(C_EPS, 1), scale=1.0 / 256).then_inc(self.std_ready, 1)
        act.activation(self.std[:, 1], src[:, T:2 * T], ACT.Sqrt, bias=k.const(C_EPS, 1), scale=1.0 / P).then_inc(self.std_ready, 1)
        act.wait_ge(self.std_ready, 2)
        b.release(act, "mla_n")
        for i in range(6):
            if i >= 3:
                b.wait_read(act, f"mla_q{i - 3}_r")
            src = b.wait(act, f"mla_q{i}")[0:MLA_K].rearrange("p (m t) -> p m t", m=2)
            b.read(act.activation(self.raw[i % 3], src, ACT.Copy), f"mla_q{i}")
            src = b.wait(act, f"mla_k{i}")[0:HD].rearrange("p (m t) -> p m t", m=2)
            b.read(act.activation(self.kk[0:HD, 2 * i:2 * i + 2], src, ACT.Copy), f"mla_k{i}")
        for t in range(TT):
            for half in range(2):
                src = b.wait(act, f"mla_v{t}{half}")[:, 0:6 * HD]
                b.read(act.activation(self.v[:, t, half * 384:(half + 1) * 384], src, ACT.Copy), f"mla_v{t}{half}")
        self.release(act, self.up_fill)
        self.run(act, self.act_unit)

    def dve(self, dve):
        k, b = self.k, self.k.banks
        cos, sin = k.rope[0:MLA_K, 0, 1, :], k.rope[0:MLA_K, 1, 1, :]
        dve.wait_ge(self.std_ready, 2)
        dve.reciprocal(self.std, self.std).then_inc(self.rstd_ready, 1)
        dve.wait_ge(self.rstd_ready, 1)
        cq, ckv = b.at("mla_cq"), b.at("mla_ckv")
        for out, src, row, std in ((self.cq[:, 0], cq[:, 0:T], R_MQ, 0), (self.cq[:, 1], cq[:, T:2 * T], R_MQ + 1, 0),
                                   (self.ckv, ckv[:, 0:T], R_MKV, 1)):
            dve.scalar_tensor_tensor(out=out, in0=src, scalar=k.param[:, row:row + 1], in1=self.std[:, std],
                                     op0=ALU.mult, op1=ALU.mult).then_inc(self.latent_ready, 1)
        dve.wait_ge(self.latent_ready, 3)
        b.release(dve, "mla_cq")
        b.release(dve, "mla_ckv")
        self.dve_rotate(dve, "mla_kr", self.kr_raw, self.kr, cos, sin, (MLA_K, 1, T))
        b.wait_read(dve, "mla_kr_r")
        dve.sem_inc(self.kr_ready, 1)
        for i in range(6):
            self.dve_rotate(dve, f"mla_q{i}", self.raw[i % 3], self.q[0:MLA_K, 2 * i:2 * i + 2], cos, sin, (MLA_K, 2, T))
        self.dve_units(dve)
        self.dve_out(dve, ALPHA)

    def pool(self, pool):
        pool.wait_ge(self.kr_ready, 1)
        pool.tensor_copy(self.kk[HD:MLA_K], self.kr[HD:MLA_K].to_broadcast([MLA_ROPE, MLA_H, T])).then_inc(self.kr_placed, 1)
        self.pool_units(pool)


class Moe:

    GROUPS, SLOTS_N, STEPS, TURN = G_N, G_N + 1, 2 * E_G, 9

    def __init__(self, k, layer):
        self.k, self.layer, self.turn = k, layer, k.x_turns
        k.x_turns += 1
        self.fills = [k.ring.plan(3) for _ in range(self.SLOTS_N * self.TURN)]
        self.slot0, self.step0, self.gather0 = (layer * n for n in (self.SLOTS_N, self.SLOTS_N * self.STEPS, self.SLOTS_N + 1))
        name = f"moe{layer}_"
        self.name = name
        k.banks.plan(*[name + n for n in ("lg", "x0", "x1", "x2", "x3", "rank", "st0", "st1", "st2", "gates")])
        if layer == 0:
            s = lambda n: k.s("moe_" + n)
            k.moe = dict((n, s(n)) for n in (
                "gu_used", "dn_used", "gu_hi", "dn_hi", "gu_lo", "dn_lo", "silu", "hidden", "turned", "ht_hi", "ht_lo",
                "gathered", "xs_hi", "xs_lo", "y_ready", "scattered", "added", "gate_copied",
                "grouped", "shifted", "exped", "placed", "gates", "planned", "scaled"))
        self.sem = k.moe
        flat = lambda t: t.rearrange("p k t -> p (k t)")
        sq, wide = flat(k.sq[:]), flat(k.wide[:, 1])
        cut = lambda at, n: sq[:, at:at + 2 * n].rearrange("p (t n) -> p t n", t=2)
        self.logits, self.group, self.chosen, self.first = cut(0, 20), cut(40, 4), cut(48, 4), cut(56, 4)
        self.exp_g, self.exp_e, self.best, self.rank1 = cut(64, 4), cut(72, 4), cut(80, 4), cut(88, 4)
        self.picked = sq[:, 96:128].rearrange("p (t g j) -> p t g j", t=2, g=4)
        self.cols = [cut(128 + 2 * n, 1) for n in range(8)]
        self.pos = cut(144, self.SLOTS_N + 1)
        self.over, self.over_n = sq[0:1, 160:164], sq[0:1, 164:166]
        self.place_t = sq[:, 512:512 + self.SLOTS_N * T]
        self.place = wide[:, 0:2 * 6 * P].rearrange("p (t n) -> p t n", t=2)
        self.gates = wide[:, 1536:1536 + 20].rearrange("p (i e) -> p i e", e=E_G)
        self.gate4 = wide[:, 1560:1564]
        self.tok = k.wide[:, 0].rearrange("p k t -> p (k t)").rearrange("p (t d) -> p t d", t=TT)
        pieces = lambda t: t[:].rearrange("p a n -> p (a n)").rearrange("p (m n) -> p m n", n=1024)
        self.w_hi, self.w_lo = pieces(k.w_hi), pieces(k.w_lo)
        x = lambda t: flat(t[:])[:, 0:D].rearrange("p (k n) -> p k n", n=P)
        self.x_hi, self.x_lo = x(k.x_hi), x(k.x_lo)

    def load(self, eng, f, e, more):
        k, r, n = self.k, self.k.ring, self.fills[f]
        r.wait_free(eng, n, more)
        slot, full, half, layer = r.slot(n), r.full[n % SLOTS], f % 2, self.layer
        for at, w in ((0, k.a["moe_w_gate_2"]), (1, k.a["moe_w_up_2"])):
            eng.dma_start(slot[:, at * 2048:(at + 1) * 2048].rearrange("p (k n) -> p k n", k=KD),
                          w[layer][e, :, half * 256:(half + 1) * 256].rearrange("o (k q) n -> q (o k) n", q=P)).then_inc(full, 16)
        eng.dma_start(slot[:, 4096:6144].rearrange("p (j n) -> p j n", j=2),
                      k.a["moe_w_down_2"][layer][e, half * 256:(half + 1) * 256, :].rearrange("o (j q) n -> q (o j) n", q=P)
                      ).then_inc(full, 16)

    def sp(self, eng):
        k, r = self.k, self.k.ring
        last = self.STEPS

        def empty(f, more):
            n = self.fills[f]
            r.wait_free(eng, n, more)
            eng.sem_inc(r.full[n % SLOTS], 48)

        with eng.Fori(0, self.GROUPS) as i:
            for f in range(self.STEPS):
                self.load(eng, f, ds(i * E_G + f // 2, 1), i * 3)
            empty(last, i * 3)
        count = self.load_plan(eng)
        group = eng.value_load(k.plan[0:1, 1:2], min_val=0, max_val=G_N - 1)
        at = self.GROUPS * self.TURN
        with eng.If(count > self.GROUPS):
            for f in range(self.STEPS):
                self.load(eng, at + f, ds(group * E_G + f // 2, 1), 0)
            empty(at + last, 0)
        with eng.If(count <= self.GROUPS):
            for s in range(SLOTS):
                n = self.fills[at - SLOTS + s]
                r.wait_full(eng, n)
                eng.sem_inc(r.full[n % SLOTS], 3 * 48)

    def load_plan(self, eng):
        k = self.k
        eng.wait_ge(self.sem["planned"], self.layer + 1)
        return eng.value_load(k.plan[0:1, 0:1], min_val=self.GROUPS, max_val=self.SLOTS_N)

    def slots(self, eng, work, skip):
        count = self.load_plan(eng)
        with eng.Fori(0, self.SLOTS_N) as i:
            with eng.If(i < count):
                work(eng, i)
            with eng.If(i >= count):
                skip(eng, i)

    def step(self, i, s):
        return i * self.STEPS + (self.step0 + s)

    def pe(self, pe):
        k, b, name, sem = self.k, self.k.banks, self.name, self.sem
        pe.wait_ge(k.x_ready, 4 * self.turn)
        pe.wait_ge(k.small_ready, k.small_all)
        out = b.claim(pe, name + "lg")
        for t in range(TT):
            for kk in range(KD):
                last = pe.matmul(out[:, t * 20:(t + 1) * 20], k.x[:, kk, t * P:(t + 1) * P], k.w_route[:, self.layer, kk],
                                 start=kk == 0, stop=kk == KD - 1)
        b.filled(last, name + "lg")
        for q in range(4):
            out = b.claim(pe, f"{name}x{q}")
            for n in range(4):
                t, kk = q // 2, (q % 2) * 4 + n
                last = pe.transpose(out[:, n * P:(n + 1) * P], k.x[:, kk, t * P:(t + 1) * P], k.ident)
            b.filled(last, f"{name}x{q}")
        pe.wait_ge(sem["grouped"], self.layer + 1)
        out = b.claim(pe, name + "rank")
        before = k.const(C_BEFORE, P)
        pe.matmul(out[:, 0:4], before, self.group[:, 0], start=True, stop=True)
        pe.matmul(out[:, 4:8], before, self.group[:, 1], start=True, stop=False)
        pe.matmul(out[:, 4:8], k.ones, self.group[:, 0], start=False, stop=True)
        pe.matmul(out[:, 8:12], k.ones, self.group[:, 0], start=True, stop=False)
        b.filled(pe.matmul(out[:, 8:12], k.ones, self.group[:, 1], start=False, stop=True), name + "rank")
        pe.wait_ge(sem["placed"], self.layer + 1)
        b.wait_read(pe, name + "x3")
        self.pe_gather(pe, 0)
        for q in range(3):
            out = b.claim(pe, f"{name}st{q}")
            for n in range(4 * q, min(4 * q + 4, 2 * self.SLOTS_N)):
                i, t = n // 2, n % 2
                last = pe.transpose(out[:, (n % 4) * P:(n % 4 + 1) * P], self.place[:, t, i * P:(i + 1) * P], k.ident)
            b.filled(last, f"{name}st{q}")
        pe.wait_ge(sem["gates"], self.layer + 1)
        out = b.claim(pe, name + "gates")
        for i in range(self.SLOTS_N):
            for t in range(TT):
                last = pe.matmul(out[:, i * E_G:(i + 1) * E_G], self.place[:, t, i * P:(i + 1) * P], self.best[:, t], start=t == 0, stop=t == 1)
        b.filled(last, name + "gates")
        for n in ("st0", "st1", "st2", "gates"):
            b.wait_read(pe, name + n)
        self.slots(pe, self.pe_slot, self.pe_skip)

    def pe_gather(self, pe, slot):
        k = self.k
        at = slice(0, P) if isinstance(slot, int) else ds(slot * P, P)
        for kk in range(KD):
            out = k.psum[:, 2 + kk // 4, (kk % 4) * P:(kk % 4 + 1) * P]
            for t in range(TT):
                last = pe.matmul(out, self.tok[:, t, kk * P:(kk + 1) * P], self.place[:, t, at], start=t == 0, stop=t == 1)
            if kk % 4 == 3:
                last.then_inc(self.sem["gathered"], 1)

    def pe_three(self, pe, out, m_hi, m_lo, w_hi, w_lo, start, stop):
        pe.matmul(out, m_hi, w_hi, start=start, stop=False, skip_group_check=True)
        pe.matmul(out, m_lo, w_hi, start=False, stop=False, skip_group_check=True)
        return pe.matmul(out, m_hi, w_lo, start=False, stop=stop, skip_group_check=True)

    def pe_gate_up(self, pe, s, p, n):
        pe.wait_ge(self.sem["gu_lo"], n * 4 + (p + 1))
        for kk in (2 * p, 2 * p + 1):
            at = slice((kk % 2) * 512, (kk % 2 + 1) * 512)
            last = self.pe_three(pe, self.k.psum[:, 4 + s % 2, :], self.x_hi[:, kk], self.x_lo[:, kk],
                                 self.w_hi[:, p, at], self.w_lo[:, p, at], kk == 0, kk == KD - 1)
        last.then_inc(self.sem["gu_used"], 1)

    def pe_turn(self, pe, s, n):
        k, sem = self.k, self.sem
        pe.wait_ge(sem["hidden"], n + 3)
        pe.wait_ge(sem["ht_lo"], n + 1)
        for j in range(2):
            last = pe.transpose(k.psum[:, 6 + s % 2, j * P:(j + 1) * P], k.h32[:, s % 2, j * P:(j + 1) * P], k.ident)
        last.then_inc(sem["turned"], 1)

    def pe_down(self, pe, s, n):
        k, sem = self.k, self.sem
        pe.wait_ge(sem["ht_lo"], n + 3)
        for j in range(2):
            pe.wait_ge(sem["dn_lo"], n * 2 + (j + 1))
            for c in range(2):
                at, h = slice(c * 512, (c + 1) * 512), slice(j * P, (j + 1) * P)
                last = self.pe_three(pe, k.psum[:, c, :], k.h_hi[:, s % 2, h], k.h_lo[:, s % 2, h],
                                     self.w_hi[:, 4 + j, at], self.w_lo[:, 4 + j, at],
                                     s == 0 and j == 0, s == self.STEPS - 1 and j == 1)
            last.then_inc(sem["dn_used"], 1)

    def pe_slot(self, pe, i):
        k, sem = self.k, self.sem
        end = self.STEPS - 1
        pe.wait_ge(sem["xs_lo"], i * 2 + (2 * self.gather0 + 2))
        for s in range(self.STEPS):
            pe.wait_ge(sem["hidden"], self.step(i, s) + 1)
            for p in range(4):
                self.pe_gate_up(pe, s, p, self.step(i, s))
                if s and p == 1:
                    if s == 1:
                        pe.wait_ge(sem["added"], i * 4 + (4 * self.slot0 + 4))
                    self.pe_turn(pe, s - 1, self.step(i, s - 1))
            if s:
                self.pe_down(pe, s - 1, self.step(i, s - 1))
        self.pe_gather(pe, i + 1)
        self.pe_turn(pe, end, self.step(i, end))
        self.pe_down(pe, end, self.step(i, end))
        pe.wait_ge(sem["xs_lo"], i * 2 + (2 * self.gather0 + 4))
        pe.wait_ge(sem["y_ready"], i * 2 + (2 * self.slot0 + 2))
        for kk in range(KD):
            last = pe.matmul(self.scatter_bank(kk // 2)[:, (kk % 2) * T:(kk % 2 + 1) * T], k.y[:, kk * P:(kk + 1) * P],
                             self.place_t[:, ds(i * T, T)], start=True, stop=True)
            if kk % 2:
                last.then_inc(sem["scattered"], 1)

    def scatter_bank(self, c):
        return self.k.psum[:, (2, 3, 6, 7)[c], :]

    def pe_skip(self, pe, i):
        sem = self.sem
        pe.wait_ge(sem["scattered"], i * 4 + 4 * self.slot0)
        for n, by in (("gu_used", 32), ("dn_used", 16), ("turned", 8), ("gathered", 2), ("scattered", 4)):
            pe.sem_inc(sem[n], by)

    def act(self, act):
        k, b, name, sem = self.k, self.k.banks, self.name, self.sem
        for q in range(4):
            src = b.wait(act, f"{name}x{q}")
            b.read(act.activation(self.tok[:, q // 2, (q % 2) * 512:(q % 2 + 1) * 512], src, ACT.Copy), f"{name}x{q}")
        for n, to in enumerate((self.exp_g, self.exp_e)):
            act.wait_ge(sem["shifted"], 2 * self.layer + n + 1)
            act.activation(to, to, ACT.Exp).then_inc(sem["exped"], 1)
        self.act_tokens(act, 0)
        for q in range(3):
            w = min(512, self.SLOTS_N * T - q * 512)
            src = b.wait(act, f"{name}st{q}")
            b.read(act.activation(self.place_t[:, q * 512:q * 512 + w], src[:, 0:w], ACT.Copy), f"{name}st{q}")
        src = b.wait(act, name + "gates")[:, 0:20].rearrange("p (i e) -> p i e", e=E_G)
        b.read(act.activation(self.gates, src, ACT.Copy), name + "gates")
        self.slots(act, self.act_slot, self.act_skip)

    def act_tokens(self, act, gather):
        k, sem = self.k, self.sem
        for c in range(2):
            act.wait_ge(sem["gathered"], gather * 2 + (2 * self.gather0 + c + 1))
            act.activation(self.x_hi[:, 4 * c:4 * c + 4], k.psum[:, 2 + c, :].rearrange("p (k n) -> p k n", n=P),
                           ACT.Copy).then_inc(sem["xs_hi"], 1)

    def piece(self, s, p, w=None):
        raw = self.k.ring.slot(self.fills[s])
        if p < 4:
            if w is not None:
                return w[:, p].rearrange("p (k u n) -> p k u n", k=2, u=2)
            return raw[:, 0:4096].rearrange("p (u k n) -> p k u n", u=2, k=KD)[:, 2 * p:2 * p + 2]
        return raw[:, p * 1024:(p + 1) * 1024] if w is None else w[:, p]

    def act_piece(self, act, s, p, n):
        sem = self.sem
        kind, j, per = ("gu", p, 4) if p < 4 else ("dn", p - 4, 2)
        act.wait_ge(sem[kind + "_used"], n * per + (j + 1))
        act.activation(self.piece(s, p, self.w_hi), self.piece(s, p), ACT.Copy).then_inc(sem[kind + "_hi"], 1)

    def act_silu(self, act, s, n):
        k, sem = self.k, self.sem
        act.wait_ge(sem["gu_used"], n * 4 + 8)
        act.wait_ge(sem["hidden"], n + 1)
        act.activation(k.sg[:, s % 2], k.psum[:, 4 + s % 2, 0:T], ACT.Silu).then_inc(sem["silu"], 1)

    def act_turned(self, act, s, n):
        k, sem = self.k, self.sem
        act.wait_ge(sem["turned"], n + 3)
        act.activation(k.h_hi[:, s % 2], k.psum[:, 6 + s % 2, 0:T], ACT.Copy).then_inc(sem["ht_hi"], 1)

    def act_slot(self, act, i):
        k, sem, end = self.k, self.sem, self.STEPS - 1
        for s in range(self.STEPS):
            k.ring.wait_full(act, self.fills[s], i * (3 * 48))
            for p in range(4):
                if s and p == 2:
                    self.act_silu(act, s - 1, self.step(i, s - 1))
                self.act_piece(act, s, p, self.step(i, s))
            if s:
                for p in (4, 5):
                    self.act_piece(act, s - 1, p, self.step(i, s - 1))
                self.act_turned(act, s - 1, self.step(i, s - 1))
        self.act_silu(act, end, self.step(i, end))
        for p in (4, 5):
            self.act_piece(act, end, p, self.step(i, end))
        self.act_tokens(act, i + 1)
        self.act_turned(act, end, self.step(i, end))
        act.wait_ge(sem["dn_used"], self.step(i, end) * 2 + 4)
        act.activation(k.y[:, 0:512], k.psum[:, 0, :], ACT.Copy).then_inc(sem["y_ready"], 1)

    def act_skip(self, act, i):
        sem = self.sem
        act.wait_ge(sem["y_ready"], i * 2 + 2 * self.slot0)
        for n, by in (("gu_hi", 32), ("dn_hi", 16), ("silu", 8), ("ht_hi", 8), ("xs_hi", 2), ("y_ready", 1)):
            act.sem_inc(sem[n], by)

    def dve(self, dve):
        k = self.k
        self.dve_route(dve)
        self.slots(dve, self.dve_slot, self.dve_skip)
        dve.wait_ge(self.sem["added"], 4 * (self.slot0 + self.SLOTS_N) + 4)
        dve.sem_inc(k.x_ready, 4)

    def dve_route(self, dve):
        k, b, seq, sem, name = self.k, self.k.banks, self.k.dve_seq, self.sem, self.name

        def do(ins):
            seq.inc(ins)
            seq.wait(dve)

        def best(of, top, onehot):
            do(dve.tensor_reduce(top, of, X_AXIS, ALU.max))
            do(dve.tensor_tensor(self.first, of, wide(top), ALU.is_equal))
            do(dve.tensor_tensor(self.first, self.first, k.const(C_FIRST, 4).unsqueeze(1).to_broadcast([P, TT, 4]), ALU.mult))
            do(dve.tensor_reduce(self.cols[7], self.first, X_AXIS, ALU.max))
            return dve.tensor_tensor(onehot, self.first, wide(self.cols[7]), ALU.is_equal)

        top, total, top_e, one, two, both = self.cols[0:6]
        wide = lambda t: t.to_broadcast([P, TT, 4])
        src = b.wait(dve, name + "lg")[:, 0:40].rearrange("p (t n) -> p t n", t=2)
        do(dve.tensor_tensor(self.logits, src, k.b_route[:, self.layer].unsqueeze(1).to_broadcast([P, TT, 20]), ALU.add))
        b.release(dve, name + "lg")
        groups = self.logits[:, :, 0:4]
        best(groups, top, self.group).then_inc(sem["grouped"], 1)
        dve.wait_ge(sem["grouped"], self.layer + 1)
        dve.tensor_tensor(self.exp_g, groups, wide(top), ALU.subtract).then_inc(sem["shifted"], 1)
        experts = self.logits[:, :, 4:20].rearrange("p t (g j) -> p t g j", g=4)
        do(dve.tensor_tensor(self.picked, experts, self.group.unsqueeze(3).to_broadcast([P, TT, 4, 4]), ALU.mult))
        do(dve.tensor_reduce(self.chosen, self.picked.rearrange("p t g j -> p t j g"), X_AXIS, ALU.add))
        do(dve.tensor_reduce(top_e, self.chosen, X_AXIS, ALU.max))
        dve.tensor_tensor(self.exp_e, self.chosen, wide(top_e), ALU.subtract).then_inc(sem["shifted"], 1)
        do(dve.memset(self.pos, -1.0))
        src = b.wait(dve, name + "rank")
        ranks = src[:, 0:8].rearrange("p (t g) -> p t g", t=2)
        do(dve.scalar_tensor_tensor(out=self.rank1, in0=ranks, scalar=1.0, in1=self.group, op0=ALU.add, op1=ALU.mult))
        do(dve.tensor_scalar(self.pos[:, :, 0:4], self.rank1, -1.0, None, ALU.add))
        do(dve.tensor_reduce(self.cols[6], self.rank1, X_AXIS, ALU.add))
        do(dve.tensor_scalar(self.pos[:, :, 4:5], self.cols[6], -1.0 - P, None, ALU.add))
        for t in range(TT):
            ins = dve.tensor_tensor(self.place[:, t].rearrange("p (i n) -> p i n", n=P),
                                    k.const(C_IOTA, P).unsqueeze(1).to_broadcast([P, 6, P]),
                                    self.pos[:, t].unsqueeze(2).to_broadcast([P, 6, P]), ALU.is_equal)
            seq.inc(ins)
        seq.wait(dve)
        dve.sem_inc(sem["placed"], 1)
        do(dve.tensor_scalar(self.over, src[0:1, 8:12], float(P), None, ALU.is_gt))
        b.release(dve, name + "rank")
        do(dve.tensor_tensor(self.over, self.over, k.const(C_FIRST, 4, 1), ALU.mult))
        do(dve.tensor_reduce(self.over[:, 0:1], self.over, X_AXIS, ALU.max))
        do(dve.tensor_scalar(self.over_n[:, 0:1], self.over[:, 0:1], 1.0, float(G_N), ALU.min, ALU.add))
        do(dve.tensor_scalar(self.over_n[:, 1:2], self.over[:, 0:1], -1.0, float(G_N), ALU.mult, ALU.add))
        do(dve.tensor_scalar(self.over_n[:, 1:2], self.over_n[:, 1:2], float(G_N - 1), None, ALU.min))
        dve.tensor_copy(k.plan[:], self.over_n).then_inc(sem["planned"], 1)
        dve.wait_ge(sem["exped"], 2 * self.layer + 2)
        do(dve.tensor_reduce(total, self.exp_g, X_AXIS, ALU.add))
        do(best(self.exp_e, one, self.best))
        do(dve.scalar_tensor_tensor(out=self.chosen, in0=self.best, scalar=-2.0, in1=self.exp_e, op0=ALU.mult, op1=ALU.add))
        do(best(self.chosen, two, self.first))
        do(dve.tensor_tensor(self.best, self.best, self.first, ALU.add))
        do(dve.tensor_tensor(self.best, self.best, self.exp_e, ALU.mult))
        do(dve.tensor_tensor(both, one, two, ALU.add))
        do(dve.tensor_tensor(both, both, total, ALU.mult))
        do(dve.reciprocal(both, both))
        dve.tensor_tensor(self.best, self.best, wide(both), ALU.mult).then_inc(sem["gates"], 1)
        self.dve_tokens(dve, 0)
        b.wait_read(dve, name + "gates")

    def dve_tokens(self, dve, gather):
        k, sem = self.k, self.sem
        for c in range(2):
            dve.wait_ge(sem["xs_hi"], gather * 2 + (2 * self.gather0 + c + 1))
            dve.tensor_tensor(self.x_lo[:, 4 * c:4 * c + 4], k.psum[:, 2 + c, :].rearrange("p (k n) -> p k n", n=P),
                              self.x_hi[:, 4 * c:4 * c + 4].bitcast(F32), ALU.subtract).then_inc(sem["xs_lo"], 1)

    def dve_piece(self, dve, s, p, n):
        sem = self.sem
        kind, j, per = ("gu", p, 4) if p < 4 else ("dn", p - 4, 2)
        dve.wait_ge(sem[kind + "_hi"], n * per + (j + 1))
        dve.tensor_tensor(self.piece(s, p, self.w_lo), self.piece(s, p), self.piece(s, p, self.w_hi.bitcast(F32)),
                          ALU.subtract).then_inc(sem[kind + "_lo"], 1)

    def dve_hidden(self, dve, s, n):
        k, sem = self.k, self.sem
        dve.wait_ge(sem["silu"], n + 1)
        dve.wait_ge(sem["turned"], n + 1)
        dve.scalar_tensor_tensor(out=k.h32[:, s % 2], in0=k.psum[:, 4 + s % 2, T:2 * T], scalar=self.gate4[:, s // 2:s // 2 + 1],
                                 in1=k.sg[:, s % 2], op0=ALU.mult, op1=ALU.mult).then_inc(sem["hidden"], 1)

    def dve_turned(self, dve, s, n):
        k, sem = self.k, self.sem
        dve.wait_ge(sem["ht_hi"], n + 1)
        dve.tensor_tensor(k.h_lo[:, s % 2], k.psum[:, 6 + s % 2, 0:T], k.h_hi[:, s % 2].bitcast(F32), ALU.subtract).then_inc(sem["ht_lo"], 1)

    def dve_release(self, dve, s, n):
        dve.wait_ge(self.sem["dn_lo"], n * 2 + 2)
        dve.sem_inc(self.k.ring.free[self.fills[s] % SLOTS], 1)

    def dve_slot(self, dve, i):
        k, sem, end = self.k, self.sem, self.STEPS - 1
        dve.tensor_tensor(self.gate4.unsqueeze(1), self.gates[:, ds(i, 1), :], k.const(C_ONES, E_G).unsqueeze(1),
                          ALU.mult).then_inc(sem["gate_copied"], 1)
        dve.wait_ge(sem["gate_copied"], i + (self.slot0 + 1))
        for s in range(self.STEPS):
            for p in range(4):
                if s and p == 2:
                    self.dve_hidden(dve, s - 1, self.step(i, s - 1))
                self.dve_piece(dve, s, p, self.step(i, s))
            if s:
                for p in (4, 5):
                    self.dve_piece(dve, s - 1, p, self.step(i, s - 1))
                self.dve_release(dve, s - 1, self.step(i, s - 1))
                self.dve_turned(dve, s - 1, self.step(i, s - 1))
        self.dve_hidden(dve, end, self.step(i, end))
        for p in (4, 5):
            self.dve_piece(dve, end, p, self.step(i, end))
        self.dve_release(dve, end, self.step(i, end))
        empty = self.fills[self.STEPS]
        k.ring.wait_full(dve, empty, i * (3 * 48))
        dve.sem_inc(k.ring.free[empty % SLOTS], 1)
        self.dve_tokens(dve, i + 1)
        self.dve_turned(dve, end, self.step(i, end))
        dve.wait_ge(sem["dn_used"], self.step(i, end) * 2 + 4)
        dve.tensor_copy(k.y[:, 512:1024], k.psum[:, 1, :]).then_inc(sem["y_ready"], 1)
        dve.wait_ge(sem["scaled"], self.layer + 1)
        for c in range(4):
            cs = slice(2 * c, 2 * c + 2)
            dve.wait_ge(sem["scattered"], i * 4 + (4 * self.slot0 + c + 1))
            dve.wait_ge(sem["added"], i * 4 + (4 * self.slot0 + c + 1))
            dve.tensor_tensor(k.x[:, cs], k.x[:, cs], self.scatter_bank(c).rearrange("p (k t) -> p k t", t=T), ALU.add).then_inc(sem["added"], 1)

    def dve_skip(self, dve, i):
        k, sem = self.k, self.sem
        dve.wait_ge(sem["added"], i * 4 + (4 * self.slot0 + 4))
        for n, by in (("gu_lo", 32), ("dn_lo", 16), ("hidden", 8), ("ht_lo", 8), ("xs_lo", 2), ("y_ready", 1), ("added", 4),
                      ("gate_copied", 1)):
            dve.sem_inc(sem[n], by)
        for free in k.ring.free:
            dve.sem_inc(free, 3)

    def pool(self, pool):
        k, b = self.k, self.k.banks
        b.wait(pool, self.name + "x3")
        pool.tensor_scalar(k.x[:], k.x[:], ALPHA, None, ALU.mult).then_inc(self.sem["scaled"], 1)


def make_stages(k, stages):
    a = k.a
    made = []
    order = [
        lambda: Ffn(k, FF // P, swiglu_sources(a, 0, 0), RmsNorm(k, 0)),
        lambda: Hgrn2(k, RmsNorm(k, 1)),
        lambda: Ffn(k, FF // P, swiglu_sources(a, 0, 1), RmsNorm(k, 2)),
        lambda: Ffn(k, FF // P, swiglu_sources(a, 1, 0), RmsNorm(k, 3)),
        lambda: Fox(k, RmsNorm(k, 4)),
        lambda: Ffn(k, FF // P, swiglu_sources(a, 1, 1), RmsNorm(k, 5)),
        lambda: Rope(k),
        lambda: Nsa(k),
        lambda: LayerNorm(k, 0),
        lambda: Moe(k, 0),
        lambda: LayerNorm(k, 1),
        lambda: Mla(k),
        lambda: LayerNorm(k, 2),
        lambda: Moe(k, 1),
        lambda: LayerNorm(k, 3),
    ]
    for n, make in enumerate(order[:stages]):
        made.append(make())
    return made


NAMES = ['x', 'norm_g', 'ffn_w_in', 'ffn_w_out', 'hg_w_in', 'hg_lb_logits', 'hg_out_norm_g', 'hg_w_out', 'fox_w_in',
         'fox_b_f', 'fox_q_norm_g', 'fox_k_norm_g', 'fox_w_out', 'mem_2', 'positions_2', 'nsa_w_in_2',
         'nsa_cmp_pe_2', 'nsa_cmp_w1_2', 'nsa_cmp_w2_2', 'mla_w_in_2', 'mla_q_norm_2', 'mla_w_uq_2',
         'mla_kv_norm_2', 'mla_w_ukv_2', 'mem_w_kv_2', 'w_out_2', 'ln_g_2', 'ln_b_2', 'moe_w_grp_2', 'moe_b_grp_2',
         'moe_w_exp_2', 'moe_b_exp_2', 'moe_w_gate_2', 'moe_w_up_2', 'moe_w_down_2']


def build(nc, a, stages=99):
    with ExitStack() as ctx:
        k = Core(ctx, nc, a)
        start = Start(k)
        made = make_stages(k, stages)
        finish = Finish(k)
        block = ctx.enter_context(nc.Block())

        @block.sync
        def _(sp):
            start.sp(sp)
            for stage in made:
                stage.sp(sp)
            finish.sp(sp)

        @block.scalar
        def _(act):
            start.act_dma(act)
            act.wait_ge(k.const_ready, 16)
            for stage in made:
                stage.act(act)

        @block.vector
        def _(dve):
            for sem in k.ring.free:
                dve.sem_inc(sem, 1)
            dve.sem_inc(k.gu_ready, 2)
            dve.sem_inc(k.out_used, 2)
            dve.sem_inc(k.h_ready, 2)
            for name, free in (("gu_used", 4), ("dn_used", 2), ("hidden", 2), ("turned", 2), ("ht_lo", 2), ("added", 4)):
                dve.sem_inc(k.moe[name], free)
            start.dve(dve)
            for stage in made:
                stage.dve(dve)
            finish.dve(dve)

        @block.gpsimd
        def _(pool):
            start.pool(pool)
            for stage in made:
                stage.pool(pool)

        @block.tensor
        def _(pe):
            pe.wait_ge(k.zero_ready, 1)
            start.pe(pe)
            for stage in made:
                stage.pe(pe)
            finish.pe(pe)


def kernel(**inputs):
    import concourse.bacc as bacc
    from concourse.bass_utils import run_bass_kernel_spmd

    nc = bacc.Bacc("TRN2", target_bir_lowering=False, num_devices=1)
    arrays = {"in_" + n: np.ascontiguousarray(inputs[n]) for n in NAMES}
    arrays["in_consts"] = constants()
    a = {n[3:]: nc.dram_tensor(n, v.shape, mybir.dt.from_np(v.dtype), kind="ExternalInput").ap()
         for n, v in arrays.items()}
    a["out"] = nc.dram_tensor("out_x", (1, T, D), F32, kind="ExternalOutput").ap()
    build(nc, a)
    return run_bass_kernel_spmd(nc, [arrays], core_ids=[0]).results[0]["out_x"]
```

```python
from contextlib import ExitStack

import numpy as np

import concourse.bass as bass
from concourse import mybir

F32 = mybir.dt.float32
F32R = mybir.dt.float32r
BF16 = mybir.dt.bfloat16
I32 = mybir.dt.int32
U32 = mybir.dt.uint32
ALU = mybir.AluOpType
ACT = mybir.ActivationFunctionType
X_AXIS = mybir.AxisListType.X
ds = bass.ds

P = 128
D = 1024
KD = D // P
T = 256
TT = T // P
FF = 2816
HG_H, HG_CHUNK = 8, 64
FOX_H, HD = 16, 64
NSA_H, NSA_KV, GROUP = 12, 4, 3
N_CMP, CMP_STRIDE, CMP_LEN = 15, 16, 32
XA_H = 4
MLA_H, MLA_K, MLA_NOPE, MLA_ROPE = 12, 96, 64, 32
E_N, E_FF, G_N, E_G = 16, 512, 4, 4
EPS = 1e-6
LN_EPS = 1e-5
ALPHA = (2.0 * 2) ** 0.25
MASKED = -1e30
NEG_BIG = -3e38

SLOTS = 3
SLOT = 6144
PIECES, PIECE = 3, 512
ARENA = 17408

NSA_ROT, NSA_THETA = 16, 500000.0
MLA_THETA = 10000.0
C_IDENT, C_ONES, C_EPS, C_LNEPS = 0, 128, 256, 257
C_ROTN, C_ROTM = 258, 386
C_CAUSAL = 514
C_CMPADD, C_CMPMUL = 898, 928
C_LEVEL = 958
C_RESET = C_LEVEL + 1024
C_INVN, C_INVM = C_RESET + 256, C_RESET + 257
C_FIRST = C_RESET + 258
C_BEFORE, C_IOTA = C_FIRST + 4, C_FIRST + 4 + P
C_HEADS = C_IOTA + P
C_ROW = C_HEADS + 30
N_CONST = C_ROW + 15


def constants():
    c = np.zeros((P, N_CONST), np.float32)
    i = np.arange(P)
    c[:, C_IDENT:C_IDENT + P] = np.eye(P)
    c[:, C_ONES:C_ONES + P] = 1.0
    for first, half, at in [(0, 8, C_ROTN), (64, 8, C_ROTN), (64, 16, C_ROTM)]:
        for d in range(half):
            c[first + half + d, at + first + d] = -1.0
            c[first + d, at + first + half + d] = 1.0
    t = np.arange(P)
    c[:, C_CAUSAL + 256:C_CAUSAL + 384] = np.where(t[None, :] <= t[:, None], 0.0, MASKED)
    for q in range(TT):
        seen = (np.arange(N_CMP)[None, :] * CMP_STRIDE + CMP_LEN - 1) <= (q * P + t)[:, None]
        c[:, C_CMPADD + q * N_CMP:C_CMPADD + (q + 1) * N_CMP] = np.where(seen, 0.0, MASKED)
        c[:, C_CMPMUL + q * N_CMP:C_CMPMUL + (q + 1) * N_CMP] = seen
    for n in range(7):
        L = 1 << n
        s, u = t[:, None], t[None, :]
        c[:, C_LEVEL + n * P:C_LEVEL + (n + 1) * P] = (
            (s // (2 * L) == u // (2 * L)) & (s // L % 2 == 0) & (u // L % 2 == 1))
    c[:, C_LEVEL + 7 * P:C_LEVEL + 8 * P] = np.eye(P)
    c[:, C_RESET:C_RESET + T] = (np.arange(T) % HG_CHUNK != 0)
    inv = lambda theta, dim: np.float32(theta) ** (-np.arange(0, dim, 2, dtype=np.float32) / np.float32(dim))
    for first in (0, 64):
        c[first:first + NSA_ROT, C_INVN] = np.tile(inv(NSA_THETA, NSA_ROT), 2)
    c[64:64 + MLA_ROPE, C_INVM] = np.tile(inv(MLA_THETA, MLA_ROPE), 2)
    c[:, C_FIRST:C_FIRST + 4] = [4, 3, 2, 1]
    c[:, C_EPS], c[:, C_LNEPS] = EPS, LN_EPS
    c[0:HD, C_HEADS + 14] = c[HD:P, C_HEADS + 15] = 1.0
    c[:, C_ROW + 7] = 1.0
    c[:, C_BEFORE:C_BEFORE + P] = i[:, None] < i[None, :]
    c[:, C_IOTA:C_IOTA + P] = i[None, :]
    return c


class Counted:

    def __init__(self, sem):
        self.sem, self.n = sem, 0

    def inc(self, ins):
        ins.then_inc(self.sem, 1)
        self.n += 1
        return self.n

    def wait(self, eng, n=None):
        eng.wait_ge(self.sem, self.n if n is None else n)


class Ring:

    def __init__(self, ctx, nc, slots):
        self.slots = slots
        self.full = [ctx.enter_context(nc.semaphore(f"slot_full_{s}")) for s in range(SLOTS)]
        self.free = [ctx.enter_context(nc.semaphore(f"slot_free_{s}")) for s in range(SLOTS)]
        self.targets, self.landed = [], [0] * SLOTS

    def plan(self, dmas):
        n = len(self.targets)
        self.landed[n % SLOTS] += 16 * dmas
        self.targets.append(self.landed[n % SLOTS])
        return n

    def slot(self, n):
        return self.slots[:, n % SLOTS, :]

    def wait_free(self, eng, n, turns=0):
        eng.wait_ge(self.free[n % SLOTS], n // SLOTS + 1 + turns)

    def wait_full(self, eng, n, more=0):
        eng.wait_ge(self.full[n % SLOTS], self.targets[n] + more)


class Banks:

    def __init__(self, ctx, nc, psum):
        self.psum = psum
        self.ready = [ctx.enter_context(nc.semaphore(f"bank_ready_{b}")) for b in range(4)]
        self.free = [ctx.enter_context(nc.semaphore(f"bank_free_{b}")) for b in range(4)]
        self.number, self.done_at, self.own = {}, {}, [0] * 4

    def plan(self, *names):
        for name in names:
            b = len(self.number) % 4
            self.own[b] += 1
            self.plan_by(name, self.ready[b], self.own[b])

    def plan_by(self, name, sem, value):
        assert name not in self.number, name
        self.number[name], self.done_at[name] = len(self.number), (sem, value)

    def at(self, name):
        return self.psum[:, 4 + self.number[name] % 4, :]

    def claim(self, pe, name):
        n = self.number[name]
        if n >= 4:
            pe.wait_ge(self.free[n % 4], n // 4)
        return self.at(name)

    def filled(self, ins, name):
        ins.then_inc(self.ready[self.number[name] % 4], 1)

    def wait(self, eng, name):
        eng.wait_ge(*self.done_at[name])
        return self.at(name)

    def read(self, ins, name):
        ins.then_inc(self.free[self.number[name] % 4], 1)

    def release(self, eng, name):
        eng.sem_inc(self.free[self.number[name] % 4], 1)

    def wait_read(self, eng, name):
        n = self.number[name]
        eng.wait_ge(self.free[n % 4], n // 4 + 1)


R_NORM, R_LB, R_HGN, R_LNG, R_LNB, R_FQ, R_FK, R_MQ, R_MKV, N_ROWS = 0, 48, 56, 57, 89, 121, 122, 123, 125, 126


class Core:

    def __init__(self, ctx, nc, a):
        self.ctx, self.nc, self.a = ctx, nc, a
        f32 = lambda n, s, d=F32: ctx.enter_context(nc.sbuf_tensor(n, s, d))
        self.ring = Ring(ctx, nc, f32("weight_ring", [P, SLOTS, SLOT]))
        with ExitStack() as split:
            fr = lambda n, s: split.enter_context(nc.sbuf_tensor(n, s, F32R))
            self.w_hi, self.w_lo = fr("w_hi", [P, 2, SLOT // 2]), fr("w_lo", [P, 2, SLOT // 2])
            self.x_hi, self.x_lo = fr("x_hi", [P, KD, T]), fr("x_lo", [P, KD, T])
            self.h_hi, self.h_lo = fr("h_hi", [P, 2, T]), fr("h_lo", [P, 2, T])
        with ExitStack() as split:
            fr = lambda n, s: split.enter_context(nc.sbuf_tensor(n, s, F32R))
            fr("before_pieces", [P, ARENA - PIECES * 2 * PIECE])
            self.pieces = fr("pieces", [P, PIECES, 2, PIECE])
            self.half = [fr("split_0", [P, KD, T]), fr("split_1", [P, KD, T])]
        self.arena = f32("arena", [P, ARENA])
        self.wide = f32("wide", [P, 2, KD, T])
        self.xn, self.cat = self.wide[:, 0], self.wide[:, 1]
        self.x = f32("x_res", [P, KD, T])
        self.sq = f32("squares", [P, KD, T])
        self.sg = f32("silu_gate", [P, 2, T])
        self.h32 = f32("hidden", [P, 2, T])
        self.y = f32("slot_out", [P, D])
        self.normed = self.y[:].rearrange("p (u b t) -> p u b t", u=2, b=2)
        self.plan = f32("moe_plan", [1, 2], I32)
        self.std, self.rstd = f32("std", [P, T]), f32("rstd", [P, T])
        self.c = f32("consts", [P, N_CONST])
        self.param = f32("params", [P, P])
        self.pe_cols = f32("cmp_pe_cols", [P, 32])
        self.lb, self.omlb, self.lb_e, self.lb_r, self.ends01 = (f32(n, [P, 8]) for n in ("lb", "omlb", "lb_e", "lb_r", "ends01"))
        self.zeros = f32("zeros", [P, 512], BF16)
        self.psum = ctx.enter_context(nc.psum_tensor("banks", [P, 8, 512], F32))
        self.acc = self.psum[:, 0:4, :].rearrange("p b (h t) -> p (b h) t", h=2)
        self.banks = Banks(ctx, nc, self.psum)
        s = lambda n: ctx.enter_context(nc.semaphore(n))
        self.s = s
        self.ident_ready = s("ident_ready")
        self.const_ready, self.zero_ready, self.rows_ready = s("const_ready"), s("zero_ready"), s("rows_ready")
        self.x_ready = s("x_ready")
        self.x_turns = 0
        self.norm_sq, self.xn_ready, self.norm_rstd = s("norm_sq"), s("xn_ready"), s("norm_rstd")
        self.xs_hi, self.xs_lo = s("xs_hi"), s("xs_lo")
        self.norms, self.splits, self.xn_tiles, self.ffns, self.his = 0, 0, 0, 0, 0
        self.norm_sum, self.norm_std = s("norm_sum"), s("norm_std")
        self.piece_hi, self.piece_lo, self.piece_used = s("piece_hi"), s("piece_lo"), s("piece_used")
        self.n_pieces = 0
        self.gu_hi, self.gu_lo, self.out_hi, self.out_lo = s("gu_hi"), s("gu_lo"), s("out_hi"), s("out_lo")
        self.gu_ready, self.out_used, self.h_ready = s("gu_ready"), s("out_used"), s("h_ready")
        self.gu_normed = s("gu_normed")
        self.sg_ready, self.h_prod = s("sg_ready"), s("h_prod")
        self.steps = 0
        self.moe = dict((n, s("moe_" + n)) for n in (
            "gu_used", "dn_used", "gu_hi", "dn_hi", "gu_lo", "dn_lo", "silu", "hidden", "turned", "ht_hi", "ht_lo",
            "gathered", "xs_hi", "xs_lo", "y_ready", "scattered", "added", "gate_copied",
            "logits", "grouped", "shifted", "exped", "placed", "gates", "planned", "scaled"))
        self.att_exp, self.att_sum, self.att_out, self.att_done = (s("att_" + n) for n in ("exp", "sum", "out", "done"))
        self.att_units = 0
        self.att_cols = f32("att_cols", [P, 3, 8])
        self.ln_sq, self.ln_centred, self.ln_rstd, self.ln_scaled = (s("ln_" + n) for n in ("sq", "centred", "rstd", "scaled"))
        self.layer_norms = 0
        self.rope = f32("rope", [P, 2, 2, T])
        self.rope_ready = s("rope_ready")
        self.pos = f32("positions", [P, T], I32)
        self.cmp_w2 = f32("cmp_w2", [P, 2, HD])
        self.w_route = f32("w_route", [P, 2, KD, G_N + E_N])
        self.b_route = f32("b_route", [P, 2, G_N + E_N])
        self.wz, self.bf = f32("fox_w_z", [P, KD, FOX_H]), f32("fox_b_f", [FOX_H, 1])
        self.small_ready = s("small_ready")
        self.small_loads()
        self.act_seq, self.dve_seq, self.pool_seq = Counted(s("act_seq")), Counted(s("dve_seq")), Counted(s("pool_seq"))

    def small_loads(self):
        a = self.a
        loads = [
            (self.wz[:], a["fox_w_in"][0][:, 4 * D:4 * D + FOX_H].rearrange("(k p) n -> p k n", p=P)),
            (self.bf[:], a["fox_b_f"].rearrange("o h -> h o")),
            (self.pos[:], a["positions_2"].partition_broadcast(P)),
            (self.cmp_w2[:], a["nsa_cmp_w2_2"][0].rearrange("v p n -> p v n")),
        ]
        for layer in range(2):
            loads += [
                (self.w_route[:, layer, :, 0:G_N], a["moe_w_grp_2"][layer].rearrange("(k p) n -> p k n", p=P)),
                (self.w_route[:, layer, :, G_N:G_N + E_N], a["moe_w_exp_2"][layer].rearrange("(k p) n -> p k n", p=P)),
                (self.b_route[:, layer, 0:G_N], a["moe_b_grp_2"][layer:layer + 1, :].partition_broadcast(P)),
                (self.b_route[:, layer, G_N:G_N + E_N], a["moe_b_exp_2"][layer:layer + 1, :].partition_broadcast(P)),
            ]
        loads += [
        ]
        self.small_all = 16 * len(loads)
        return loads

    def const(self, at, n, p=P):
        return self.c[0:p, at:at + n]

    @property
    def ident(self):
        return self.const(C_IDENT, P)

    @property
    def ones(self):
        return self.const(C_ONES, P)


class Start:

    def __init__(self, k):
        self.k = k
        self.fill = k.ring.plan(1)
        self.rows = k.sq[:].rearrange("p k t -> p (k t)")[:, 0:P]
        self.pe_rows = k.sq[:].rearrange("p k t -> p (k t)")[0:32, P:2 * P]
        k.banks.plan("params", "x0", "x1", "x2", "x3")
        self.turn = k.x_turns
        k.x_turns += 1

    def sp(self, eng):
        k, r = self.k, self.k.ring
        r.wait_free(eng, self.fill)
        xt = r.slot(self.fill)[:, 0:TT * D].rearrange("p (t d) -> p t d", t=TT)
        eng.dma_start(xt, k.a["x"].rearrange("o (t p) d -> p (o t) d", p=P)).then_inc(r.full[self.fill % SLOTS], 16)
        eng.wait_ge(k.rows_ready, 12 * 16)

    def act_dma(self, eng):
        k, a = self.k, self.k.a
        eng.dma_start(k.c[:, 0:C_ROTN], a["consts"][:, 0:C_ROTN]).then_inc(k.ident_ready, 16)
        rows = self.rows
        for at, n, src in [
            (R_NORM, 48, a["norm_g"].rearrange("l n (k p) -> (l n k) p", p=P)),
            (R_LB, 8, a["hg_lb_logits"].rearrange("l (k p) -> (l k) p", p=P)),
            (R_HGN, 1, a["hg_out_norm_g"]),
            (R_LNG, 32, a["ln_g_2"].rearrange("l n (k p) -> (l n k) p", p=P)),
            (R_LNB, 32, a["ln_b_2"].rearrange("l n (k p) -> (l n k) p", p=P)),
            (R_MQ, 2, a["mla_q_norm_2"].rearrange("l (k p) -> (l k) p", p=P)),
            (R_MKV, 1, a["mla_kv_norm_2"]),
        ]:
            eng.dma_start(rows[at:at + n, :], src).then_inc(k.rows_ready, 16)
        for half in (0, HD):
            eng.dma_start(rows[R_FQ:R_FQ + 1, half:half + HD], a["fox_q_norm_g"]).then_inc(k.rows_ready, 16)
            eng.dma_start(rows[R_FK:R_FK + 1, half:half + HD], a["fox_k_norm_g"]).then_inc(k.rows_ready, 16)
        eng.dma_start(self.pe_rows, a["nsa_cmp_pe_2"].rearrange("o v (l e) d -> (o v l) (e d)", e=2)).then_inc(k.rows_ready, 16)

    def pool(self, eng):
        k = self.k
        eng.memset(k.zeros[:], 0.0).then_inc(k.zero_ready, 1)
        eng.wait_ge(k.x_ready, 4)
        eng.dma_start(k.c[:, C_ROTN:N_CONST], k.a["consts"][:, C_ROTN:N_CONST]).then_inc(k.const_ready, 16)
        for dst, src in k.small_loads():
            eng.dma_start(dst, src, allow_slow_non_contiguous=True).then_inc(k.small_ready, 16)

    def pe(self, pe):
        k, b = self.k, self.k.banks
        pe.wait_ge(k.ident_ready, 16)
        k.ring.wait_full(pe, self.fill)
        xt = k.ring.slot(self.fill)
        for q in range(4):
            out = b.claim(pe, f"x{q}") if q else None
            if q == 0:
                pe.wait_ge(k.rows_ready, 12 * 16)
                out = b.claim(pe, "params")
                pe.transpose(out[:, 0:N_ROWS], self.rows[0:N_ROWS, :], k.ident[0:N_ROWS, 0:N_ROWS])
                b.filled(pe.transpose(out[:, P:P + 32], self.pe_rows, k.ident[0:32, 0:32]), "params")
                out = b.claim(pe, "x0")
            for n in range(4):
                kk, t = 2 * q + n // 2, n % 2
                last = pe.transpose(out[:, n * P:(n + 1) * P], xt[:, t * D + kk * P:t * D + (kk + 1) * P], k.ident)
            b.filled(last, f"x{q}")

    def dve(self, dve):
        k, b = self.k, self.k.banks
        src = b.wait(dve, "params")
        dve.tensor_copy(k.param[:, 0:N_ROWS], src[:, 0:N_ROWS])
        b.read(dve.tensor_copy(k.pe_cols[:], src[:, P:P + 32]), "params")
        for q in range(4):
            src = b.wait(dve, f"x{q}")
            ins = dve.tensor_copy(k.x[:, 2 * q:2 * q + 2, :].rearrange("p k t -> p (k t)"), src)
            ins.then_inc(k.x_ready, 1)
        dve.wait_ge(k.x_ready, 4)
        for q in range(4):
            b.release(dve, f"x{q}")
        dve.sem_inc(k.ring.free[self.fill % SLOTS], 1)


class RmsNorm:

    def __init__(self, k, row):
        self.k, self.row, self.i, self.turn, self.first = k, row, k.norms, k.x_turns, k.xn_tiles
        k.norms += 1
        k.xn_tiles += KD
        k.banks.plan(f"norm{self.i}")

    def act_squares(self, act):
        k = self.k
        for c in range(4):
            act.wait_ge(k.x_ready, 4 * (self.turn - 1) + c + 1)
            act.activation(k.sq[:, 2 * c:2 * c + 2], k.x[:, 2 * c:2 * c + 2], ACT.Square).then_inc(k.norm_sq, 1)

    def pe(self, pe):
        k = self.k
        out = k.banks.claim(pe, f"norm{self.i}")[:, 0:T]
        for kk in range(KD):
            if kk % 2 == 0:
                pe.wait_ge(k.norm_sq, 4 * self.i + kk // 2 + 1)
            last = pe.matmul(out, k.ones, k.sq[:, kk], start=kk == 0, stop=kk == KD - 1)
        k.banks.filled(last, f"norm{self.i}")

    def act_std(self, act):
        k = self.k
        src = k.banks.wait(act, f"norm{self.i}")[:, 0:T]
        k.banks.read(act.activation(k.std[:], src, ACT.Sqrt, bias=k.const(C_EPS, 1), scale=1.0 / D), f"norm{self.i}")

    def dve(self, dve):
        k = self.k
        k.banks.wait_read(dve, f"norm{self.i}")
        dve.reciprocal(k.rstd[:], k.std[:]).then_inc(k.norm_rstd, 1)
        dve.wait_ge(k.norm_rstd, self.i + 1)
        for kk in range(KD):
            g = k.param[:, R_NORM + self.row * KD + kk:R_NORM + self.row * KD + kk + 1]
            dve.scalar_tensor_tensor(out=k.xn[:, kk], in0=k.x[:, kk], scalar=g, in1=k.rstd[:],
                                     op0=ALU.mult, op1=ALU.mult).then_inc(k.xn_ready, 1)

    def wait_xn(self, eng, tiles=KD):
        eng.wait_ge(self.k.xn_ready, self.first + tiles)


class Ffn:

    PARTS = 3

    def __init__(self, k, steps, sources, row):
        self.k, self.steps, self.sources, self.row = k, steps, sources, row
        self.j0, self.split, self.norm, self.turn = k.steps, k.splits, k.norms, k.x_turns
        k.norms += 1
        k.steps += steps
        k.splits += 1
        self.ffn, self.hi0 = k.ffns, k.his
        k.ffns += 1
        k.his += KD
        self.fills = [k.ring.plan(3) for _ in range(steps // 2)]
        self.body = 2 * SLOTS
        self.turns = (steps - 1) // self.body
        self.rest = steps - 1 - self.turns * self.body
        k.x_turns += 1

    def fill_more(self, i):
        return i * (48 * self.body // 6)

    def sp(self, eng):
        k, r, half = self.k, self.k.ring, self.body // 2
        turns = (self.steps // 2) // half

        def load(f, i, more):
            n = self.fills[f]
            r.wait_free(eng, n, more)
            slot, full = r.slot(n), r.full[n % SLOTS]
            wg, wu, wd = self.sources(i, f)
            for at, src in ((0, wg), (1, wu)):
                eng.dma_start(slot[:, at * 2048:(at + 1) * 2048].rearrange("p (k n) -> p k n", k=KD),
                              src).then_inc(full, 16)
            eng.dma_start(slot[:, 4096:6144].rearrange("p (j n) -> p j n", j=2), wd).then_inc(full, 16)

        with eng.Fori(0, turns) as i:
            for f in range(half):
                load(f, i, i * (half // SLOTS))
        for f in range(turns * half, self.steps // 2):
            load(f, 0, 0)

    def act_split(self, act, j, base, more):
        k, n = self.k, self.fills[j // 2]
        b, jj, raw = j % 2, j % 2, k.ring.slot(n)
        k.ring.wait_full(act, n, more)
        act.wait_ge(k.gu_ready, base + 1)
        act.activation(k.w_hi[:, b, 0:2048].rearrange("p (k n) -> p k n", n=P),
                       raw[:, 0:4096].rearrange("p (k n) -> p k n", n=256)[:, :, jj * P:(jj + 1) * P],
                       ACT.Copy).then_inc(k.gu_hi, 1)
        act.wait_ge(k.out_used, base + 1)
        act.activation(k.w_hi[:, b, 2048:3072], raw[:, 4096 + jj * D:4096 + (jj + 1) * D],
                       ACT.Copy).then_inc(k.out_hi, 1)

    def dve_split_gu(self, dve, j, base):
        k, n = self.k, self.fills[j // 2]
        b, jj, raw = j % 2, j % 2, k.ring.slot(n)
        dve.wait_ge(k.gu_hi, base + 1)
        dve.tensor_tensor(k.w_lo[:, b, 0:2048].rearrange("p (k n) -> p k n", n=P),
                          raw[:, 0:4096].rearrange("p (k n) -> p k n", n=256)[:, :, jj * P:(jj + 1) * P],
                          k.w_hi[:, b, 0:2048].bitcast(F32).rearrange("p (k n) -> p k n", n=P),
                          ALU.subtract).then_inc(k.gu_lo, 1)

    def dve_split_out(self, dve, j, base):
        k, n = self.k, self.fills[j // 2]
        b, jj, raw = j % 2, j % 2, k.ring.slot(n)
        dve.wait_ge(k.out_hi, base + 1)
        dve.tensor_tensor(k.w_lo[:, b, 2048:3072], raw[:, 4096 + jj * D:4096 + (jj + 1) * D],
                          k.w_hi[:, b, 2048:3072].bitcast(F32), ALU.subtract).then_inc(k.out_lo, 1)

    def dve_release(self, dve, j, base):
        if j % 2 == 1:
            dve.wait_ge(self.k.out_lo, base + 1)
            dve.sem_inc(self.k.ring.free[self.fills[j // 2] % SLOTS], 1)

    def dve_normed(self, dve, j, base):
        k, b = self.k, j % 2
        dve.wait_ge(k.gu_ready, base + 3)
        for part in range(2):
            dve.tensor_tensor(k.normed[:, part, b], k.psum[:, 4 + b, part * T:(part + 1) * T], k.rstd[:], ALU.mult).then_inc(k.gu_normed, 1)

    def act_silu(self, act, j, base):
        k, b = self.k, j % 2
        act.wait_ge(k.h_ready, base + 1)
        act.wait_ge(k.gu_normed, 2 * base + 1)
        act.activation(k.sg[:, b], k.normed[:, 0, b], ACT.Silu).then_inc(k.sg_ready, 1)

    def dve_hidden(self, dve, j, base):
        k, b = self.k, j % 2
        dve.wait_ge(k.sg_ready, base + 1)
        dve.wait_ge(k.gu_normed, 2 * base + 2)
        left, right = k.sg[:, b], k.normed[:, 1, b]
        dve.tensor_tensor(k.h32[:, b], left, right, ALU.mult).then_inc(k.h_prod, 1)
        dve.wait_ge(k.out_used, base + 1)
        dve.tensor_tensor(k.h_hi[:, b], left, right, ALU.mult).then_inc(k.h_prod, 1)
        dve.wait_ge(k.h_prod, 2 * base + 2)
        dve.tensor_tensor(k.h_lo[:, b], k.h32[:, b], k.h_hi[:, b].bitcast(F32), ALU.subtract).then_inc(k.h_ready, 1)

    def pool(self, pool):
        pass

    def pe_three(self, pe, out, w_hi, w_lo, m_hi, m_lo, start, stop):
        pe.matmul(out, w_hi, m_hi, start=start, stop=False, skip_group_check=True)
        pe.matmul(out, w_hi, m_lo, start=False, stop=False, skip_group_check=True)
        return pe.matmul(out, w_lo, m_hi, start=False, stop=stop, skip_group_check=True)

    def pe_gate_up(self, pe, b, base, first=False):
        k = self.k
        pe.wait_ge(k.gu_lo, base + 1)
        pe.wait_ge(k.h_ready, base + 1)
        for part in range(2):
            for kk in range(KD):
                if first and part == 0 and kk % 2 == 0:
                    pe.wait_ge(k.xs_lo, 4 * self.split + kk // 2 + 1)
                at = (part * KD + kk) * P
                last = self.pe_three(pe, k.psum[:, 4 + b, part * T:(part + 1) * T],
                                     k.w_hi[:, b, at:at + P], k.w_lo[:, b, at:at + P],
                                     k.x_hi[:, kk], k.x_lo[:, kk], kk == 0, kk == KD - 1)
        last.then_inc(k.gu_ready, 1)

    def pe_down(self, pe, b, base):
        k = self.k
        pe.wait_ge(k.out_lo, base + 1)
        pe.wait_ge(k.h_ready, base + 3)
        for n in range(KD):
            at = 2048 + n * P
            last = self.pe_three(pe, k.acc[:, n], k.w_hi[:, b, at:at + P], k.w_lo[:, b, at:at + P],
                                 k.h_hi[:, b], k.h_lo[:, b], False, True)
        last.then_inc(k.out_used, 1)

    def pe(self, pe):
        k = self.k
        out = k.psum[:, 0, 0:T]
        for kk in range(KD):
            if kk % 2 == 0:
                pe.wait_ge(k.norm_sq, 4 * self.norm + kk // 2 + 1)
            last = pe.matmul(out, k.ones, k.sq[:, kk], start=kk == 0, stop=kk == KD - 1)
        last.then_inc(k.norm_sum, 1)
        self.pe_gate_up(pe, 0, self.j0, first=True)
        pe.wait_ge(k.norm_std, self.ffn + 1)
        for bank in range(4):
            pe.matmul(k.psum[:, bank, :], k.zeros[:, 0:P], k.zeros[:], start=True, stop=True, skip_group_check=True)
        turns, rest = divmod(self.steps - 1, 2)
        with pe.Fori(0, turns) as i:
            for t in range(2):
                self.pe_gate_up(pe, (t + 1) % 2, i * 2 + (self.j0 + t + 1))
                self.pe_down(pe, t % 2, i * 2 + (self.j0 + t))
        for j in range(2 * turns, self.steps - 1):
            self.pe_gate_up(pe, (j + 1) % 2, self.j0 + j + 1)
            self.pe_down(pe, j % 2, self.j0 + j)
        self.pe_down(pe, (self.steps - 1) % 2, self.j0 + self.steps - 1)

    def gain(self, kk):
        return self.k.param[:, R_NORM + self.row * KD + kk:R_NORM + self.row * KD + kk + 1]

    def act_input(self, act):
        k = self.k
        for c in range(4):
            tiles = slice(2 * c, 2 * c + 2)
            act.wait_ge(k.x_ready, 4 * (self.turn - 1) + c + 1)
            act.activation(k.sq[:, tiles], k.x[:, tiles], ACT.Square).then_inc(k.norm_sq, 1)
            for kk in (2 * c, 2 * c + 1):
                act.activation(k.x_hi[:, kk], k.x[:, kk], ACT.Copy, scale=self.gain(kk)).then_inc(k.xs_hi, 1)

    def dve_input(self, dve):
        k = self.k
        for c in range(4):
            for kk in (2 * c, 2 * c + 1):
                dve.wait_ge(k.xs_hi, self.hi0 + kk + 1)
                ins = dve.scalar_tensor_tensor(out=k.x_lo[:, kk], in0=k.x[:, kk], scalar=self.gain(kk),
                                               in1=k.x_hi[:, kk].bitcast(F32), op0=ALU.mult, op1=ALU.subtract)
            ins.then_inc(k.xs_lo, 1)

    def act_std(self, act):
        k = self.k
        act.wait_ge(k.norm_sum, self.ffn + 1)
        act.activation(k.std[:], k.psum[:, 0, 0:T], ACT.Sqrt, bias=k.const(C_EPS, 1), scale=1.0 / D).then_inc(k.norm_std, 1)

    def act(self, act):
        if self.j0:
            self.act_split(act, 0, self.j0, 0)
        self.act_input(act)
        if not self.j0:
            self.act_split(act, 0, self.j0, 0)
        self.act_std(act)
        with act.Fori(0, self.turns) as i:
            for t in range(self.body):
                self.act_split(act, t + 1, i * self.body + (self.j0 + t + 1), self.fill_more(i))
                self.act_silu(act, t, i * self.body + (self.j0 + t))
        for j in range(self.turns * self.body, self.steps - 1):
            self.act_split(act, j + 1, self.j0 + j + 1, 0)
            self.act_silu(act, j, self.j0 + j)
        self.act_silu(act, self.steps - 1, self.j0 + self.steps - 1)

    def dve_step(self, dve, j, base):
        self.dve_split_gu(dve, j + 1, base + 1)
        self.dve_normed(dve, j, base)
        self.dve_split_out(dve, j + 1, base + 1)
        self.dve_hidden(dve, j, base)
        self.dve_release(dve, j + 1, base + 1)

    def dve(self, dve):
        k = self.k
        if self.j0:
            self.dve_split_gu(dve, 0, self.j0)
            self.dve_split_out(dve, 0, self.j0)
        self.dve_input(dve)
        if not self.j0:
            self.dve_split_gu(dve, 0, self.j0)
            self.dve_split_out(dve, 0, self.j0)
        dve.wait_ge(k.norm_std, self.ffn + 1)
        dve.reciprocal(k.rstd[:], k.std[:]).then_inc(k.norm_rstd, 1)
        dve.wait_ge(k.norm_rstd, self.norm + 1)
        with dve.Fori(0, self.turns) as i:
            for t in range(self.body):
                self.dve_step(dve, t, i * self.body + (self.j0 + t))
        for j in range(self.turns * self.body, self.steps - 1):
            self.dve_step(dve, j, self.j0 + j)
        j = self.steps - 1
        self.dve_normed(dve, j, self.j0 + j)
        self.dve_hidden(dve, j, self.j0 + j)
        dve.wait_ge(k.out_used, self.j0 + self.steps + 2)
        self.dve_residual(dve)

    def dve_residual(self, dve):
        k = self.k
        for c in range(4):
            dve.scalar_tensor_tensor(out=k.x[:, 2 * c:2 * c + 2], in0=k.acc[:, 2 * c:2 * c + 2], scalar=0.5,
                                     in1=k.x[:, 2 * c:2 * c + 2], op0=ALU.mult, op1=ALU.add).then_inc(k.x_ready, 1)


def swiglu_sources(a, layer, half):
    w_in, w_out = a["ffn_w_in"][layer, half], a["ffn_w_out"][layer, half]

    def sources(i, f):
        p = i * 3 + f
        cols = lambda at: w_in[:, ds(p * 256 + at, 256)].rearrange("(k q) n -> q k n", q=P)
        return cols(0), cols(FF), w_out[ds(p * 256, 256), :].rearrange("(j q) n -> q j n", q=P)
    return sources


class Finish:

    def __init__(self, k):
        self.k = k
        self.turn = k.x_turns
        k.banks.plan("y0", "y1", "y2", "y3")
        self.stored, self.turned = k.s("stored"), k.s("turned")
        self.y = k.arena[:, 0:TT * D].rearrange("p (t d) -> p t d", t=TT)

    def pe(self, pe):
        k, b = self.k, self.k.banks
        pe.wait_ge(k.x_ready, 4 * self.turn)
        for q in range(4):
            out = b.claim(pe, f"y{q}")
            for n in range(4):
                t, kk = q // 2, (q % 2) * 4 + n
                last = pe.transpose(out[:, n * P:(n + 1) * P], k.x[:, kk, t * P:(t + 1) * P], k.ident)
            b.filled(last, f"y{q}")

    def dve(self, dve):
        k, b = self.k, self.k.banks
        for q in range(4):
            src = b.wait(dve, f"y{q}")
            b.read(dve.tensor_copy(self.y[:, q // 2, (q % 2) * 512:(q % 2 + 1) * 512], src), f"y{q}")

    def sp(self, eng):
        k, b = self.k, self.k.banks
        for q in range(4):
            b.wait_read(eng, f"y{q}")
            eng.dma_start(k.a["out"][0, (q // 2) * P:(q // 2 + 1) * P, (q % 2) * 512:(q % 2 + 1) * 512],
                          self.y[:, q // 2, (q % 2) * 512:(q % 2 + 1) * 512]).then_inc(self.stored, 16)
        eng.wait_ge(self.stored, 64)


class Mixer:

    block_fill = None

    def plan_blocks(self, blocks, per_fill=3):
        self.block_fill = self.block_fill or {}
        for at in range(0, len(blocks), per_fill):
            some = blocks[at:at + per_fill]
            n = self.k.ring.plan(len(some))
            for i, (name, src) in enumerate(some):
                self.block_fill[name] = (n, i, src)

    def sp_blocks(self, eng, names=None):
        k, last = self.k, None
        for n, i, src in [self.block_fill[name] for name in names or self.block_fill]:
            if n != last:
                k.ring.wait_free(eng, n)
                last = n
            width = src.shape[1]
            eng.dma_start(k.ring.slot(n)[:, i * 2048:i * 2048 + KD * width].rearrange("p (k n) -> p k n", k=KD),
                          src.rearrange("(k p) n -> p k n", p=P)).then_inc(k.ring.full[n % SLOTS], 16)

    def block(self, name):
        n, i, src = self.block_fill[name]
        width = src.shape[1]
        return n, self.k.ring.slot(n)[:, i * 2048:i * 2048 + KD * width].rearrange("p (k n) -> p k n", k=KD)

    def project(self, pe, out, w, moving, start=True):
        for kk in range(KD):
            last = pe.matmul(out, w(kk), moving[:, kk], start=kk == 0, stop=kk == KD - 1)
        return last

    def plan_pieces(self, fill, w, cols, per):
        k, made = self.k, []
        for kk in range(0, KD, per):
            made.append(k.n_pieces)
            self.piece_list.append((k.n_pieces, fill, w[:, kk:kk + per, cols]))
            k.n_pieces += 1
        return made

    def plan_columns(self, name, source, parts):
        fill, w = source
        self.jobs[name] = [(self.plan_pieces(fill, w, slice(at, at + n), 4), n, to) for at, n, to in parts]
        self.plan_done([name], name)

    def plan_rows(self, names, fill, w, width):
        self.jobs[names[0]] = (self.plan_pieces(fill, w, slice(0, width), min(KD, PIECE // width)), width)
        self.plan_done(names, names[0])

    def plan_done(self, banks, job):
        k = self.k
        for name in banks:
            k.banks.plan_by(name, k.piece_used, PIECES + k.n_pieces)
        self.job_end[job] = len(self.piece_list)

    def plan_split(self):
        self.piece_list, self.jobs, self.job_end, self.act_at, self.dve_at = [], {}, {}, 0, 0
        self.in_split, self.cat_split, self.hi0 = self.k.splits, self.k.splits + 1, self.k.his
        self.k.splits += 2
        self.k.his += 8

    def piece_parts(self, m, per, n):
        return [self.k.pieces[:, m % PIECES, part, 0:per * n].rearrange("p (k n) -> p k n", n=n) for part in range(2)]

    def pe_wait_input(self, pe):
        pe.wait_ge(self.k.xs_lo, 4 * self.in_split + 4)

    def pe_three(self, pe, out, left, right, start, stop):
        (l_hi, l_lo), (r_hi, r_lo) = left, right
        pe.matmul(out, l_hi, r_hi, start=start, stop=False, skip_group_check=True)
        pe.matmul(out, l_hi, r_lo, start=False, stop=False, skip_group_check=True)
        return pe.matmul(out, l_lo, r_hi, start=False, stop=stop, skip_group_check=True)

    def pe_tile(self, pe, out, made, n, x, split=None):
        for i, m in enumerate(made):
            per = KD // len(made)
            hi, lo = self.piece_parts(m, per, n)
            pe.wait_ge(self.k.piece_lo, m + 1)
            for j in range(per):
                kk = i * per + j
                if split is not None and kk % 2 == 0:
                    pe.wait_ge(self.k.xs_lo, 4 * split + kk // 2 + 1)
                last = self.pe_three(pe, out, (hi[:, j], lo[:, j]), (x[0][:, kk], x[1][:, kk]), kk == 0, kk == KD - 1)
            last.then_inc(self.k.piece_used, 1)

    def pe_columns(self, pe, name, split=None):
        k = self.k
        out = k.banks.claim(pe, name)
        for made, n, to in self.jobs[name]:
            self.pe_tile(pe, out[0:n, to:to + T], made, n, (k.half[1], k.half[0]), split)

    def pe_rows(self, pe, names):
        k = self.k
        made, width = self.jobs[names[0]]
        per = KD // len(made)
        banks = [k.banks.claim(pe, name) for name in names]
        outs = [banks[0][:, 0:width], banks[1][:, 0:width] if len(names) == 2 else banks[0][:, width:2 * width]]
        assert len(names) == 2 or len(made) == 1
        for i, m in enumerate(made):
            hi, lo = self.piece_parts(m, per, width)
            pe.wait_ge(k.piece_lo, m + 1)
            for t in range(TT):
                tok = slice(t * P, (t + 1) * P)
                for j in range(per):
                    kk = i * per + j
                    last = self.pe_three(pe, outs[t], (k.half[1][:, kk, tok], k.half[0][:, kk, tok]), (hi[:, j], lo[:, j]),
                                         kk == 0, kk == KD - 1)
            last.then_inc(k.piece_used, 1)

    def ahead(self, job):
        return min(self.job_end[job] + PIECES, self.in_pieces)

    def act_pieces(self, act, upto):
        k = self.k
        end = self.job_end[upto] if isinstance(upto, str) else upto
        while self.act_at < end:
            m, fill, raw = self.piece_list[self.act_at]
            if self.act_at == 0 or self.piece_list[self.act_at - 1][1] != fill:
                k.ring.wait_full(act, fill)
            act.wait_ge(k.piece_used, m + 1)
            act.activation(self.piece_parts(m, raw.shape[1], raw.shape[2])[0], raw, ACT.Copy).then_inc(k.piece_hi, 1)
            self.act_at += 1

    def dve_pieces(self, dve, upto):
        k = self.k
        end = self.job_end[upto] if isinstance(upto, str) else upto
        while self.dve_at < end:
            m, fill, raw = self.piece_list[self.dve_at]
            hi, lo = self.piece_parts(m, raw.shape[1], raw.shape[2])
            dve.wait_ge(k.piece_hi, m + 1)
            dve.tensor_tensor(lo, raw, hi.bitcast(F32), ALU.subtract).then_inc(k.piece_lo, 1)
            self.dve_at += 1
            if self.dve_at == len(self.piece_list) or self.piece_list[self.dve_at][1] != fill:
                dve.wait_ge(k.piece_lo, m + 1)
                self.release(dve, fill)

    def act_input(self, act, src, wait):
        k = self.k
        for c in range(4):
            wait(act, c)
            act.activation(k.half[1][:, 2 * c:2 * c + 2], src[:, 2 * c:2 * c + 2], ACT.Copy).then_inc(k.xs_hi, 1)

    def dve_input(self, dve, src):
        k = self.k
        for c in range(4):
            cs = slice(2 * c, 2 * c + 2)
            dve.wait_ge(k.xs_hi, self.hi0 + c + 1)
            dve.tensor_tensor(k.half[0][:, cs], src[:, cs], k.half[1][:, cs].bitcast(F32), ALU.subtract).then_inc(k.xs_lo, 1)

    def act_out(self, act):
        k = self.k
        self.act_pieces(act, self.in_pieces + PIECES)
        for c in range(4):
            act.wait_ge(self.cat_ready, c + 1)
            act.activation(k.half[0][:, 2 * c:2 * c + 2], k.cat[:, 2 * c:2 * c + 2], ACT.Copy).then_inc(k.xs_hi, 1)
        self.act_pieces(act, "out7")

    def release(self, eng, fill):
        eng.sem_inc(self.k.ring.free[fill % SLOTS], 1)

    def plan_out(self, name, w_out):
        k = self.k
        self.w_out, self.out_fills = w_out, [k.ring.plan(1), k.ring.plan(1)]
        self.turn = k.x_turns
        k.x_turns += 1

    def plan_out_pieces(self):
        self.in_pieces = len(self.piece_list)
        for n in range(KD):
            fill = self.out_fills[n // 4]
            w = self.k.ring.slot(fill)[:, 0:4096].rearrange("p (k n) -> p k n", k=KD)
            self.jobs[f"out{n}"] = self.plan_pieces(fill, w, slice((n % 4) * P, (n % 4 + 1) * P), 4)
            self.job_end[f"out{n}"] = len(self.piece_list)

    def sp_out(self, eng):
        k = self.k
        for half, n in enumerate(self.out_fills):
            k.ring.wait_free(eng, n)
            eng.dma_start(k.ring.slot(n)[:, 0:4096].rearrange("p (k n) -> p k n", k=KD),
                          self.w_out[:, half * 512:(half + 1) * 512].rearrange("(k p) n -> p k n", p=P)
                          ).then_inc(k.ring.full[n % SLOTS], 16)

    def pe_out(self, pe):
        k = self.k
        for n in range(KD):
            self.pe_tile(pe, k.acc[:, n], self.jobs[f"out{n}"], P, (k.half[0], k.half[1]), None if n else self.cat_split)

    def dve_out(self, dve, scale=1.0):
        k = self.k
        self.dve_pieces(dve, self.in_pieces + PIECES)
        for c in range(4):
            cs = slice(2 * c, 2 * c + 2)
            dve.wait_ge(k.xs_hi, self.hi0 + 4 + c + 1)
            dve.tensor_tensor(k.half[1][:, cs], k.cat[:, cs], k.half[0][:, cs].bitcast(F32), ALU.subtract).then_inc(k.xs_lo, 1)
        for c in range(4):
            cs = slice(2 * c, 2 * c + 2)
            self.dve_pieces(dve, f"out{min(2 * c + 3, KD - 1)}")
            dve.wait_ge(k.piece_used, PIECES + self.jobs[f"out{2 * c + 1}"][-1] + 1)
            dve.scalar_tensor_tensor(out=k.x[:, cs], in0=k.x[:, cs], scalar=scale, in1=k.acc[:, cs],
                                     op0=ALU.mult, op1=ALU.add).then_inc(k.x_ready, 1)


class Hgrn2(Mixer):

    def __init__(self, k, norm):
        self.k, self.norm = k, norm
        a = k.a
        w = a["hg_w_in"][0]
        cols = lambda part, n: w[:, part * D + n * 256:part * D + (n + 1) * 256]
        self.plan_blocks([(f"z{n}", cols(1, n)) for n in range(4)] + [(f"q{n}", cols(0, n)) for n in range(4)]
                         + [(f"g{n}", cols(3, n)) for n in range(4)])
        self.v_fills = [k.ring.plan(1), k.ring.plan(1)]
        self.plan_out("hg", a["hg_w_out"][0])
        self.plan_split()
        for name in [f"{p}{n}" for p in "zqg" for n in range(4)]:
            self.plan_columns("hg_" + name, self.block(name), [(0, P, 0), (P, P, T)])
        for h, n in enumerate(self.v_fills):
            self.plan_rows([f"hg_v{h}0", f"hg_v{h}1"], n, k.ring.slot(n)[:, 0:4096].rearrange("p (k n) -> p k n", k=KD), 512)
        self.plan_out_pieces()
        self.names = [f"hg_{p}{n}" for p in "zqg" for n in range(4)] + ["hg_v00", "hg_v10"]
        k.banks.plan(*[f"hg_s{n}_{g}" for n in [7, 0, 1, 2, 3, 4, 5, 6] for g in range(4)], "hg_x0", "hg_x1")
        k.banks.plan("hg_n", *[f"hg_r{n}" for n in range(4)])
        ar = k.arena
        part = lambda n: ar[:, n * 2048:(n + 1) * 2048].rearrange("p (h t) -> p h t", h=HG_H)
        self.q, self.kk, self.b, self.g = part(0), part(1), part(2), part(3)
        self.e = [part(4), part(5), k.wide[:, 0], k.wide[:, 1]]
        self.v = ar[:, 6 * 2048:7 * 2048].rearrange("p (t d) -> p t d", t=TT)
        self.score = ar[:, 7 * 2048:7 * 2048 + 2048].rearrange("p (m t) -> p m t", m=16)
        self.cross = ar[:, 8 * 2048:8 * 2048 + 1024].rearrange("p (h t) -> p h t", h=HG_H)
        self.root = k.std[0:HG_H]
        s = lambda n: k.s("hg_" + n)
        self.sig, self.qg, self.f_ready, self.ln_ready, self.b_ready = s("sig"), s("qg"), s("f"), s("ln"), s("b")
        self.diff, self.exped, self.scaled = s("diff"), s("exped"), s("scaled")
        self.o_ready, self.o_sq, self.root_ready, self.cat_ready = s("o"), s("o_sq"), s("root"), s("cat")

    def sp(self, eng):
        k = self.k
        self.sp_blocks(eng)
        for half, n in enumerate(self.v_fills):
            k.ring.wait_free(eng, n)
            eng.dma_start(k.ring.slot(n)[:, 0:4096].rearrange("p (k n) -> p k n", k=KD),
                          k.a["hg_w_in"][0][:, 2 * D + half * 512:2 * D + (half + 1) * 512].rearrange("(k p) n -> p k n", p=P)
                          ).then_inc(k.ring.full[n % SLOTS], 16)
        self.sp_out(eng)

    def pe(self, pe):
        k, b = self.k, self.k.banks
        self.norm.pe(pe)
        self.pe_wait_input(pe)
        for part in "zqg":
            for n in range(4):
                self.pe_columns(pe, f"hg_{part}{n}")
        for half in range(2):
            self.pe_rows(pe, [f"hg_v{half}0", f"hg_v{half}1"])
        for i, n in enumerate([7, 0, 1, 2, 3, 4, 5, 6]):
            if n == 7:
                pe.wait_ge(self.qg, 4)
            else:
                pe.wait_ge(self.scaled, 2 * (n + 1))
            e = self.e[n % 4]
            for g in range(4):
                out = b.claim(pe, f"hg_s{n}_{g}")
                for m in range(4 * g, 4 * g + 4):
                    h, t = m // 2, slice(m % 2 * P, (m % 2 + 1) * P)
                    left, right = (self.kk, self.q) if n == 7 else (e, e)
                    last = pe.matmul(out[:, (m % 4) * P:(m % 4 + 1) * P], left[:, h, t], right[:, h, t], start=True, stop=True)
                b.filled(last, f"hg_s{n}_{g}")
        pe.wait_ge(self.scaled, 16)
        for g in range(2):
            out = b.claim(pe, f"hg_x{g}")
            for h in range(4 * g, 4 * g + 4):
                last = pe.matmul(out[:, (h % 4) * P:(h % 4 + 1) * P], self.e[3][:, h, 0:P], self.e[3][:, h, P:T], start=True, stop=True)
            b.filled(last, f"hg_x{g}")
        b.wait_read(pe, "hg_v11")
        b.wait_read(pe, "hg_s6_3")
        b.wait_read(pe, "hg_x1")
        for h in range(HG_H):
            v = [self.v[:, t, h * P:(h + 1) * P] for t in range(TT)]
            pe.matmul(k.acc[:, h, 0:P], v[0], self.score[:, 2 * h], start=True, stop=True)
            pe.matmul(k.acc[:, h, P:T], v[0], self.cross[:, h], start=True, stop=False)
            last = pe.matmul(k.acc[:, h, P:T], v[1], self.score[:, 2 * h + 1], start=False, stop=True)
            if h % 2:
                last.then_inc(self.o_ready, 1)
        out = b.claim(pe, "hg_n")[0:HG_H, 0:T]
        for h in range(HG_H):
            pe.wait_ge(self.o_sq, h // 2 + 1)
            last = pe.matmul(out, k.const(C_ROW + 7 - h, HG_H), k.sq[:, h], start=h == 0, stop=h == HG_H - 1)
        b.filled(last, "hg_n")
        pe.wait_ge(self.root_ready, 1)
        for n in range(4):
            out = b.claim(pe, f"hg_r{n}")
            for h in (2 * n, 2 * n + 1):
                last = pe.matmul(out[:, (h % 2) * T:(h % 2 + 1) * T], k.c[0:HG_H, C_IDENT + h:C_IDENT + h + 1].to_broadcast([HG_H, P]),
                                 self.root, start=True, stop=True)
            b.filled(last, f"hg_r{n}")
        self.pe_out(pe)

    def act(self, act):
        k, b = self.k, self.k.banks
        act.wait_ge(k.const_ready, 16)
        self.norm.act_squares(act)
        self.norm.act_std(act)
        self.act_input(act, k.xn, lambda eng, c: self.norm.wait_xn(eng, 2 * c + 2))
        self.act_pieces(act, "hg_z0")
        for name in self.names:
            self.act_pieces(act, self.ahead(name))
            part, n = name[3], int(name[4])
            if part == "v":
                for t in range(TT):
                    src = b.wait(act, f"hg_v{n}{t}")
                    b.read(act.activation(self.v[:, t, n * 512:(n + 1) * 512], src, ACT.Copy), f"hg_v{n}{t}")
                continue
            src = b.wait(act, name).rearrange("p (h t) -> p h t", h=2)
            to = {"z": self.b, "q": self.q, "g": self.g}[part]
            act.activation(to[:, 2 * n:2 * n + 2], src, ACT.Sigmoid).then_inc(self.sig, 1)
            if part == "z":
                b.read(act.activation(self.kk[:, 2 * n:2 * n + 2], src, ACT.Sigmoid, scale=-1.0), name)
            if name == "hg_g3":
                act.wait_ge(self.f_ready, 4)
                act.activation(self.e[0], self.e[0], ACT.Ln).then_inc(self.ln_ready, 1)
        for n in range(8):
            act.wait_ge(self.diff, self.diffs[n])
            e = self.e[n % 4]
            act.activation(e, e, ACT.Exp).then_inc(self.exped, 1)
        for g in range(2):
            src = b.wait(act, f"hg_x{g}").rearrange("p (h t) -> p h t", h=4)
            b.read(act.activation(self.cross[:, 4 * g:4 * g + 4], src, ACT.Copy), f"hg_x{g}")
        for n in range(4):
            act.wait_ge(self.o_ready, n + 1)
            act.activation(k.sq[:, 2 * n:2 * n + 2], k.acc[:, 2 * n:2 * n + 2], ACT.Square).then_inc(self.o_sq, 1)
        src = b.wait(act, "hg_n")[0:HG_H, 0:T]
        b.read(act.activation(self.root, src, ACT.Sqrt, bias=k.const(C_EPS, 1, HG_H), scale=1.0 / P), "hg_n")
        self.act_out(act)

    def level(self, t, L):
        return t.rearrange("p h t -> p (h t)").rearrange("p (n a l) -> p n a l", a=2, l=L)

    diffs = [2, 4, 6, 8, 10, 12, 14, 18]

    def pool(self, pool):
        k, b, seq = self.k, self.k.banks, self.k.pool_seq
        ends = self.b.rearrange("p h (c l) -> p h c l", l=HG_CHUNK)[:, :, :, HG_CHUNK - 1]
        pool.wait_ge(self.b_ready, 8)
        seq.inc(pool.tensor_tensor(k.ends01[:], ends[:, :, 0], ends[:, :, 1], ALU.add))
        b.wait(pool, "hg_v11")
        for n in range(7):
            L = 1 << n
            if n >= 4:
                b.wait(pool, f"hg_s{n - 4}_3")
            e, c = self.level(self.e[n % 4], L), self.level(self.b, L)
            mid = c[:, :, 0, L - 1:L].to_broadcast([P, c.shape[1], L])
            pool.tensor_tensor(e[:, :, 0, :], mid, c[:, :, 0, :], ALU.subtract).then_inc(self.diff, 1)
            if L < HG_CHUNK:
                pool.tensor_tensor(e[:, :, 1, :], c[:, :, 1, :], mid, ALU.subtract).then_inc(self.diff, 1)
            else:
                pool.tensor_copy(e[:, :, 1, :], c[:, :, 1, :]).then_inc(self.diff, 1)
        b.wait(pool, "hg_s3_3")
        seq.wait(pool)
        chunk = lambda t, c: t[:, :, c * HG_CHUNK:(c + 1) * HG_CHUNK]
        wide = lambda col: col.to_broadcast([P, HG_H, HG_CHUNK])
        e, c = self.e[3], self.b
        pool.tensor_tensor(chunk(e, 0), wide(k.ends01[:].unsqueeze(2)), chunk(c, 0), ALU.subtract).then_inc(self.diff, 1)
        pool.tensor_tensor(chunk(e, 1), wide(c[:, :, 127:128]), chunk(c, 1), ALU.subtract).then_inc(self.diff, 1)
        pool.tensor_copy(chunk(e, 2), chunk(c, 2)).then_inc(self.diff, 1)
        pool.tensor_tensor(chunk(e, 3), chunk(c, 3), wide(c[:, :, 191:192]), ALU.add).then_inc(self.diff, 1)

    def dve(self, dve):
        k, b, seq = self.k, self.k.banks, self.k.dve_seq
        dve.wait_ge(k.const_ready, 16)
        l, w, r = k.param[:, R_LB:R_LB + 8], k.lb_e[:], k.lb_r[:]
        for ins in (lambda: dve.tensor_tensor(w, l, l, ALU.subtract),
                    lambda: dve.tensor_scalar(w, w, 1.0, None, ALU.add),
                    lambda: dve.reciprocal(r, w),
                    lambda: dve.tensor_tensor(r, w, r, ALU.mult),
                    lambda: dve.tensor_tensor(k.lb[:], r, r, ALU.subtract),
                    lambda: dve.tensor_scalar(k.omlb[:], k.lb[:], -1.0, 1.0, ALU.mult, ALU.add)):
            seq.inc(ins())
            seq.wait(dve)
        self.norm.dve(dve)
        self.dve_input(dve, k.xn)
        f, up, off, small = self.b, self.e[0], self.e[1], 2.0 ** -60

        def forget(n):
            b.wait_read(dve, f"hg_z{n}")
            for h in (2 * n, 2 * n + 1):
                seq.inc(dve.tensor_scalar(f[:, h], f[:, h], k.omlb[:, h:h + 1], k.lb[:, h:h + 1], ALU.mult, ALU.add))
                seq.inc(dve.tensor_scalar(self.kk[:, h], self.kk[:, h], k.omlb[:, h:h + 1], None, ALU.mult))

        def clamp(n):
            hs = slice(2 * n, 2 * n + 2)
            seq.wait(dve)
            seq.inc(dve.tensor_scalar(f[:, hs], f[:, hs], 1e-30, None, ALU.max))
            seq.wait(dve)
            seq.inc(dve.tensor_scalar(up[:, hs], f[:, hs], small, 2.0 ** 36 - 1.0, ALU.is_lt, ALU.mult))
            seq.inc(dve.tensor_scalar(off[:, hs], f[:, hs], small, 36.0 * float(np.log(2.0)), ALU.is_lt, ALU.mult))
            seq.wait(dve)
            dve.scalar_tensor_tensor(out=up[:, hs], in0=up[:, hs], scalar=1.0, in1=f[:, hs], op0=ALU.add, op1=ALU.mult).then_inc(self.f_ready, 1)

        def gated(name, to, at, n, gain):
            dve.wait_ge(self.sig, at + n + 1)
            src = b.at(name).rearrange("p (h t) -> p h t", h=2)
            dve.scalar_tensor_tensor(out=to[:, 2 * n:2 * n + 2], in0=src, scalar=gain, in1=to[:, 2 * n:2 * n + 2],
                                     op0=ALU.mult, op1=ALU.mult).then_inc(self.qg, 1)
            dve.wait_ge(self.qg, at - 4 + n + 1)
            b.release(dve, name)

        self.dve_pieces(dve, "hg_z0")
        for name in self.names[:12]:
            self.dve_pieces(dve, self.ahead(name))
            part, n = name[3], int(name[4])
            if part == "z":
                forget(n)
            elif part == "q":
                gated(name, self.q, 4, n, 1.0)
                clamp(n)
            else:
                gated(name, self.g, 8, n, k.param[:, R_HGN:R_HGN + 1])
        dve.wait_ge(self.ln_ready, 1)
        for h in range(HG_H):
            self.dve_pieces(dve, self.dve_at + 1)
            seq.inc(dve.tensor_tensor(up[:, h], up[:, h], off[:, h], ALU.subtract))
            seq.wait(dve)
            dve.tensor_tensor_scan(f[:, h], k.const(C_RESET, T), up[:, h], 0.0, ALU.mult, ALU.add).then_inc(self.b_ready, 1)
        self.dve_pieces(dve, "hg_v10")
        b.wait(dve, "hg_v11")
        seq.inc(dve.memset(self.score, 0.0))
        seq.wait(dve)

        def place(n):
            mask = k.const(C_LEVEL + n * P, P).bitcast(U32).unsqueeze(1).to_broadcast([P, 4, P])
            for g in range(4):
                src = b.wait(dve, f"hg_s{n}_{g}").rearrange("p (m t) -> p m t", m=4)
                b.read(dve.copy_predicated(self.score[:, 4 * g:4 * g + 4], mask, src), f"hg_s{n}_{g}")

        for n in range(8):
            dve.wait_ge(self.exped, n + 1)
            e = self.level(self.e[n % 4], 1 << n)
            for half, by in enumerate((self.kk, self.q)):
                dve.tensor_tensor(e[:, :, half, :], e[:, :, half, :], self.level(by, 1 << n)[:, :, half, :],
                                  ALU.mult).then_inc(self.scaled, 1)
            place(n - 1 if n else 7)
        og = self.e[0]
        for n in range(4):
            hs = slice(2 * n, 2 * n + 2)
            dve.wait_ge(self.o_sq, n + 1)
            seq.inc(dve.tensor_tensor(og[:, hs], k.acc[:, hs], self.g[:, hs], ALU.mult))
        b.wait_read(dve, "hg_n")
        dve.reciprocal(self.root, self.root).then_inc(self.root_ready, 1)
        seq.wait(dve)
        for n in range(4):
            hs = slice(2 * n, 2 * n + 2)
            src = b.wait(dve, f"hg_r{n}").rearrange("p (h t) -> p h t", h=2)
            dve.tensor_tensor(k.cat[:, hs], og[:, hs], src, ALU.mult).then_inc(self.cat_ready, 1)
            dve.wait_ge(self.cat_ready, n + 1)
            b.release(dve, f"hg_r{n}")
        self.dve_out(dve)


class Attention(Mixer):

    LAG = 3
    DEEP = 4

    def plan_units(self, name, units, at):
        k, n = self.k, len(units)
        self.units, self.u0, self.name = units, k.att_units, name
        k.att_units += n
        part = lambda t: t.rearrange("p (r t) -> p r t", r=self.DEEP)
        self.sc, self.pr, self.pt = part(at[:, 0:1024]), part(at[:, 1024:2048]), part(k.sq[:].rearrange("p k t -> p (k t)")[:, 0:1024])
        self.tok = k.wide[:, 0].rearrange("p k t -> p (k t)").rearrange("p (t d) -> p t d", t=TT)
        last = [max(i for i, u in enumerate(units) if u["head"] // 4 == q) for q in range(4)]
        self.quarter_units = [self.u0 + i + 1 for i in last]
        self.schedule, q = [], 0
        for i in range(n + self.LAG + 4):
            jobs = []
            if i < n:
                jobs.append(("score", i))
                k.banks.plan(f"{name}_s{i}")
            if self.LAG <= i < n + self.LAG:
                jobs.append(("turn", i - self.LAG))
                k.banks.plan(f"{name}_t{i - self.LAG}")
            if self.LAG + 1 <= i < n + self.LAG + 1:
                jobs.append(("value", i - self.LAG - 1))
            if q < 4 and i >= last[q] + self.LAG + 3:
                jobs.append(("quarter", q))
                k.banks.plan(f"{name}_o{q}")
                q += 1
            self.schedule.append(jobs)
        assert q == 4

    def pe_units(self, pe):
        for jobs in self.schedule:
            for job, j in jobs:
                (self.pe_score if job == "score" else self.pe_turn if job == "turn" else
                 self.pe_value if job == "value" else self.pe_quarter)(pe, j)

    def pe_score(self, pe, i):
        u, name = self.units[i], f"{self.name}_s{i}"
        out = self.k.banks.claim(pe, name)[:, 0:u["n"]]
        pairs = [(u["q"], u["keys"])] + u.get("bias", [])
        for m, (left, right) in enumerate(pairs):
            last = pe.matmul(out, left, right, start=m == 0, stop=m == len(pairs) - 1)
        self.k.banks.filled(last, name)

    def pe_turn(self, pe, j):
        k, u, name = self.k, self.units[j], f"{self.name}_t{j}"
        out = k.banks.claim(pe, name)
        pe.wait_ge(k.att_exp if u["seen"] is None else k.att_sum, self.u0 + j + 1)
        for m, (rows, _) in enumerate(u["values"]):
            last = pe.transpose(out[0:rows, m * P:(m + 1) * P], self.pr[:, j % self.DEEP, m * P:m * P + rows], k.ident)
        k.banks.filled(last, name)

    def pe_value(self, pe, j):
        k, u = self.k, self.units[j]
        k.banks.wait_read(pe, f"{self.name}_t{j}")
        if self.u0 + j >= 4:
            pe.wait_ge(k.att_done, self.u0 + j - 3)
        for m, (rows, v) in enumerate(u["values"]):
            last = pe.matmul(k.psum[:, (self.u0 + j) % 4, 0:HD], self.pt[0:rows, j % self.DEEP, m * P:(m + 1) * P], v,
                             start=m == 0, stop=m == len(u["values"]) - 1)
        last.then_inc(k.att_out, 1)

    def pe_quarter(self, pe, q):
        k, name = self.k, f"{self.name}_o{q}"
        out = k.banks.claim(pe, name)
        pe.wait_ge(k.att_done, self.quarter_units[q])
        for n in range(4):
            pair, t = 2 * q + n // 2, n % 2
            last = pe.transpose(out[:, n * P:(n + 1) * P], self.tok[:, t, pair * P:(pair + 1) * P], k.ident)
        k.banks.filled(last, name)

    def act_units(self, act):
        k, b, n = self.k, self.k.banks, len(self.units)
        for i in range(n + self.LAG):
            if i < n:
                u, c, r = self.units[i], (self.u0 + i) % 8, i % self.DEEP
                b.wait_read(act, f"{self.name}_s{i}")
                if self.u0 + i >= 4 and i < 4:
                    act.wait_ge(k.att_done, self.u0)
                act.activation(self.pr[:, r, 0:u["n"]], self.sc[:, r, 0:u["n"]], ACT.Exp, scale=-1.0,
                               bias=k.att_cols[:, 0, c:c + 1], accum_out=k.att_cols[:, 1, c:c + 1]).then_inc(k.att_exp, 1)
            if i >= self.LAG:
                j = i - self.LAG
                name = f"{self.name}_t{j}"
                u = self.units[j]
                src = b.wait(act, name)
                if j >= 4:
                    act.wait_ge(k.att_out, self.u0 + j - 3)
                rows, w = u["values"][0][0], len(u["values"]) * P
                b.read(act.activation(self.pt[0:rows, j % self.DEEP, 0:w], src[0:rows, 0:w], ACT.Copy), name)
        self.act_pieces(act, self.in_pieces + PIECES)
        b.wait(act, f"{self.name}_o3")

    def dve_units(self, dve):
        n, q = len(self.units), 0
        for i, jobs in enumerate(self.schedule):
            if i < n:
                self.dve_score(dve, i)
            if 1 <= i < n + 1:
                self.dve_weight(dve, i - 1)
            if self.LAG + 2 <= i < n + self.LAG + 2:
                self.dve_value(dve, i - self.LAG - 2)
            if i and any(job == "quarter" for job, _ in self.schedule[i - 1]):
                self.dve_quarter(dve, q)
                q += 1
        self.dve_pieces(dve, self.in_pieces + PIECES)
        while q < 4:
            self.dve_quarter(dve, q)
            q += 1

    def dve_score(self, dve, i):
        k, u, c, r, name = self.k, self.units[i], (self.u0 + i) % 8, i % self.DEEP, f"{self.name}_s{i}"
        if i >= 4:
            dve.wait_ge(k.att_exp, self.u0 + i - 3)
        src = k.banks.wait(dve, name)[:, 0:u["n"]]
        k.banks.read(dve.tensor_tensor_reduce(self.sc[:, r, 0:u["n"]], src, u["mask"], -u["scale"], -NEG_BIG, ALU.add, ALU.min,
                                              k.att_cols[:, 0, c:c + 1]), name)

    def dve_weight(self, dve, j):
        k, seq, u, c = self.k, self.k.dve_seq, self.units[j], (self.u0 + j) % 8
        total, weight = k.att_cols[:, 1, c:c + 1], k.att_cols[:, 2, c:c + 1]
        dve.wait_ge(k.att_exp, self.u0 + j + 1)
        if u["seen"] is not None:
            pr = self.pr[:, j % self.DEEP, 0:u["n"]]
            seq.inc(dve.tensor_tensor_reduce(pr, pr, u["seen"], 1.0, 0.0, ALU.mult, ALU.add, total))
            seq.wait(dve)
            seq.inc(dve.tensor_scalar(total, total, 1e-30, None, ALU.max))
            seq.wait(dve)
        if u["gate"] is None:
            dve.reciprocal(weight, total).then_inc(k.att_sum, 1)
        else:
            seq.inc(dve.reciprocal(total, total))
            seq.wait(dve)
            dve.tensor_tensor(weight, total, u["gate"], ALU.mult).then_inc(k.att_sum, 1)

    def dve_value(self, dve, j):
        k, u, c = self.k, self.units[j], (self.u0 + j) % 8
        weight, src = k.att_cols[:, 2, c:c + 1], k.psum[:, (self.u0 + j) % 4, 0:HD]
        out = self.tok[:, u["tile"], u["head"] * HD:(u["head"] + 1) * HD]
        dve.wait_ge(k.att_sum, self.u0 + j + 1)
        dve.wait_ge(k.att_out, self.u0 + j + 1)
        if u["first"]:
            ins = dve.tensor_scalar(out, src, weight, None, ALU.mult)
        else:
            dve.wait_ge(k.att_done, self.u0 + j - 1)
            ins = dve.scalar_tensor_tensor(out=out, in0=src, scalar=weight, in1=out, op0=ALU.mult, op1=ALU.add)
        ins.then_inc(k.att_done, 1)

    def dve_quarter(self, dve, q):
        k, name = self.k, f"{self.name}_o{q}"
        tiles = slice(2 * q, 2 * q + 2)
        src = k.banks.wait(dve, name).rearrange("p (m t) -> p m t", m=2)
        self.dve_collect(dve, k.cat[:, tiles], src, tiles).then_inc(self.cat_ready, 1)
        dve.wait_ge(self.cat_ready, q + 1)
        k.banks.release(dve, name)

    def dve_collect(self, dve, out, src, tiles):
        return dve.tensor_copy(out, src)


class Fox(Attention):

    def __init__(self, k, norm):
        self.k, self.norm = k, norm
        a, ar, b = k.a, k.arena, k.banks
        w = a["fox_w_in"][0]
        cols = lambda part, n: w[:, part * D + n * 256:part * D + (n + 1) * 256]
        self.names = [f"fox_{p}{n}" for p in "kqg" for n in range(4)]
        self.plan_blocks([(name, cols({"k": 1, "q": 0, "g": 3}[name[4]], int(name[5]))) for name in self.names])
        self.v_fills = [k.ring.plan(1), k.ring.plan(1)]
        self.plan_out("fox", a["fox_w_out"][0])
        self.plan_split()
        b.plan("fox_z")
        for name in self.names:
            self.plan_columns(name, self.block(name), [(0, P, 0), (P, P, T)])
            if name in ("fox_q1", "fox_g1"):
                b.plan(*[f"fox_b{'k' if name == 'fox_q1' else 'q'}{n}" for n in range(4)])
        for h, n in enumerate(self.v_fills):
            self.plan_rows([f"fox_v{h}0", f"fox_v{h}1"], n, k.ring.slot(n)[:, 0:4096].rearrange("p (k n) -> p k n", k=KD), 512)
        self.plan_out_pieces()
        self.names += ["fox_v00", "fox_v10"]
        part = lambda n: ar[:, n * 2048:(n + 1) * 2048].rearrange("p (h t) -> p h t", h=8)
        self.q, self.kk, self.g, self.bq, self.bk = part(0), part(1), part(2), part(4), part(5)
        self.v = ar[:, 3 * 2048:4 * 2048].rearrange("p (t d) -> p t d", t=TT)
        self.zb, self.ez, self.cc, self.nc_ = (ar[0:FOX_H, 12288 + n * T:12288 + (n + 1) * T] for n in range(4))
        self.spread = ar[0:FOX_H, 13312:14336]
        self.roots = {"k": k.std[0:FOX_H], "q": k.rstd[0:FOX_H]}
        self.sums = {"k": k.psum[0:FOX_H, 0, 0:T], "q": k.psum[0:FOX_H, 1, 0:T]}
        s = lambda n: k.s("fox_" + n)
        self.sq_ready, self.sq_used, self.root_ready, self.rroot_ready, self.spread_ready = (
            s("sq"), s("sq_used"), s("root"), s("rroot"), s("spread"))
        self.z_step, self.c_ready, self.bias_ready, self.bias_rows, self.cat_ready = s("z"), s("c"), s("bias"), s("bias_rows"), s("cat")
        self.raw_ready, self.normed = s("raw"), s("normed")
        units = []
        for h in range(FOX_H):
            pair, half = divmod(h, 2)
            at = slice(half * HD, (half + 1) * HD)
            for t in range(TT):
                n, tok = (t + 1) * P, slice(t * P, (t + 1) * P)
                units.append(dict(
                    q=self.q[at, pair, tok], keys=self.kk[at, pair, 0:n], bias=[(self.bq[at, pair, tok], self.bk[at, pair, 0:n])],
                    n=n, mask=k.const(C_CAUSAL + 384 - n, n), seen=None, scale=HD ** -0.5, gate=None,
                    values=[(P, self.v[:, m, h * HD:(h + 1) * HD]) for m in range(t + 1)], head=h, tile=t, first=True))
        self.plan_units("fox", units, ar[:, 12288:14336])

    def sp(self, eng):
        k = self.k
        self.sp_blocks(eng)
        for half, n in enumerate(self.v_fills):
            k.ring.wait_free(eng, n)
            eng.dma_start(k.ring.slot(n)[:, 0:4096].rearrange("p (k n) -> p k n", k=KD),
                          k.a["fox_w_in"][0][:, 2 * D + half * 512:2 * D + (half + 1) * 512].rearrange("(k p) n -> p k n", p=P)
                          ).then_inc(k.ring.full[n % SLOTS], 16)
        self.sp_out(eng)

    def pe(self, pe):
        k, b = self.k, self.k.banks
        self.norm.pe(pe)
        self.pe_wait_input(pe)
        pe.wait_ge(k.small_ready, k.small_all)
        out = b.claim(pe, "fox_z")[0:FOX_H, 0:T]
        for kk in range(KD):
            for part in range(2):
                last = pe.matmul(out, k.wz[:, kk], k.half[1 - part][:, kk].bitcast(F32), start=kk == 0 and part == 0,
                                 stop=kk == KD - 1 and part == 1)
        b.filled(last, "fox_z")
        for i, name in enumerate(self.names[:12]):
            self.pe_columns(pe, name)
            if 1 <= i < 9:
                kind, n = "kq"[(i - 1) // 4], (i - 1) % 4
                pe.wait_ge(self.sq_ready, i)
                for j in (2 * n, 2 * n + 1):
                    last = pe.matmul(self.sums[kind], k.const(C_HEADS + 14 - 2 * j, FOX_H), k.sq[:, j], start=j == 0, stop=j == 7)
                last.then_inc(self.sq_used, 1)
            if name in ("fox_q1", "fox_g1"):
                kind = "k" if name == "fox_q1" else "q"
                pe.wait_ge(self.spread_ready, 1)
                pe.wait_ge(self.rroot_ready, 1 if kind == "k" else 2)
                for n in range(4):
                    out = b.claim(pe, f"fox_b{kind}{n}")
                    for j in (2 * n, 2 * n + 1):
                        last = pe.matmul(out[:, (j % 2) * T:(j % 2 + 1) * T], self.spread[:, j * P:(j + 1) * P], self.roots[kind],
                                         start=True, stop=True)
                    b.filled(last, f"fox_b{kind}{n}")
        for half in range(2):
            self.pe_rows(pe, [f"fox_v{half}0", f"fox_v{half}1"])
        b.wait_read(pe, "fox_v11")
        pe.wait_ge(self.normed, 8)
        pe.wait_ge(self.bias_ready, 4)
        pe.wait_ge(self.bias_rows, 64)
        self.pe_units(pe)
        self.pe_out(pe)

    def act(self, act):
        k, b = self.k, self.k.banks
        self.norm.act_squares(act)
        self.norm.act_std(act)
        self.act_input(act, k.xn, lambda eng, c: self.norm.wait_xn(eng, 2 * c + 2))

        def root(kind):
            act.wait_ge(self.sq_used, 4 if kind == "k" else 8)
            act.activation(self.roots[kind], self.sums[kind], ACT.Sqrt, bias=k.const(C_EPS, 1, FOX_H), scale=1.0 / HD).then_inc(self.root_ready, 1)

        self.act_pieces(act, "fox_k0")
        for name in self.names:
            self.act_pieces(act, self.ahead(name))
            part, n = name[4], int(name[5])
            if part == "v":
                for t in range(TT):
                    src = b.wait(act, f"fox_v{n}{t}")
                    b.read(act.activation(self.v[:, t, n * 512:(n + 1) * 512], src, ACT.Copy), f"fox_v{n}{t}")
                continue
            hs = slice(2 * n, 2 * n + 2)
            src = b.wait(act, name).rearrange("p (h t) -> p h t", h=2)
            if part == "g":
                b.read(act.activation(self.g[:, hs], src, ACT.Sigmoid), name)
            else:
                if part == "q":
                    act.wait_ge(self.sq_used, n + 1)
                act.activation(k.sq[:, hs], src, ACT.Square).then_inc(self.sq_ready, 1)
                b.read(act.activation((self.kk if part == "k" else self.q)[:, hs], src, ACT.Copy), name)
            if name in ("fox_q0", "fox_g0"):
                root("k" if part == "q" else "q")
            if name == "fox_q2":
                act.wait_ge(self.z_step, 1)
                act.activation(self.ez, self.zb, ACT.Abs).then_inc(self.z_step, 1)
                act.wait_ge(self.z_step, 2)
                act.activation(self.ez, self.ez, ACT.Exp, scale=-1.0).then_inc(self.z_step, 1)
                act.wait_ge(self.z_step, 3)
                act.activation(self.ez, self.ez, ACT.Ln, bias=k.const(C_ONES, 1, FOX_H)).then_inc(self.z_step, 1)
            if name == "fox_g3":
                act.wait_ge(self.c_ready, 2)
                act.wait_ge(self.bias_ready, 4)
                for half in range(2):
                    act.dma_start(self.bq[half * HD:half * HD + 1], self.cc[half:FOX_H:2, :]).then_inc(self.bias_rows, 16)
                    act.dma_start(self.bk[half * HD + 32:half * HD + 33], self.nc_[half:FOX_H:2, :]).then_inc(self.bias_rows, 16)
        self.act_units(act)
        self.act_out(act)

    def dve(self, dve):
        k, b, seq = self.k, self.k.banks, self.k.dve_seq
        self.norm.dve(dve)
        self.dve_input(dve, k.xn)

        def norm(kind):
            to, row = (self.kk, R_FK) if kind == "k" else (self.q, R_FQ)
            for n in range(4):
                hs, name = slice(2 * n, 2 * n + 2), f"fox_b{kind}{n}"
                src = b.wait(dve, name).rearrange("p (h t) -> p h t", h=2)
                dve.scalar_tensor_tensor(out=to[:, hs], in0=src, scalar=k.param[:, row:row + 1], in1=to[:, hs],
                                         op0=ALU.mult, op1=ALU.mult).then_inc(self.normed, 1)
                dve.wait_ge(self.normed, n + 1 + (4 if kind == "q" else 0))
                b.release(dve, name)

        def rroot(kind):
            dve.wait_ge(self.root_ready, 1 if kind == "k" else 2)
            dve.reciprocal(self.roots[kind], self.roots[kind]).then_inc(self.rroot_ready, 1)

        self.dve_pieces(dve, "fox_k0")
        src = b.wait(dve, "fox_z")[0:FOX_H, 0:T]
        dve.tensor_scalar(self.zb, src, k.bf[0:FOX_H, 0:1], None, ALU.add).then_inc(self.z_step, 1)
        dve.wait_ge(self.z_step, 1)
        b.release(dve, "fox_z")
        for name in self.names:
            self.dve_pieces(dve, self.ahead(name))
            if name in ("fox_q0", "fox_g0"):
                rroot("k" if name == "fox_q0" else "q")
            if name in ("fox_q1", "fox_g1"):
                norm("k" if name == "fox_q1" else "q")
            if name == "fox_q3":
                dve.wait_ge(self.z_step, 4)
                seq.inc(dve.scalar_tensor_tensor(out=self.ez, in0=self.zb, scalar=0.0, in1=self.ez, op0=ALU.min, op1=ALU.subtract))
                seq.wait(dve)
                seq.inc(dve.tensor_scalar(self.ez, self.ez, HD ** 0.5, None, ALU.mult))
                seq.wait(dve)
                dve.tensor_tensor_scan(self.cc, k.const(C_CAUSAL, T, FOX_H), self.ez, 0.0, ALU.add, ALU.add).then_inc(self.c_ready, 1)
                dve.wait_ge(self.c_ready, 1)
                dve.tensor_scalar(self.nc_, self.cc, -1.0, None, ALU.mult).then_inc(self.c_ready, 1)
        self.dve_units(dve)
        self.dve_out(dve)

    def dve_collect(self, dve, out, src, tiles):
        return dve.tensor_tensor(out, src, self.g[:, tiles], ALU.mult)

    def pool(self, pool):
        k, seq = self.k, self.k.pool_seq
        self.norm.wait_xn(pool)
        seq.inc(pool.memset(self.bq, 0.0))
        seq.inc(pool.memset(self.bk, 0.0))
        seq.wait(pool)
        for half in range(2):
            pool.memset(self.bq[half * HD + 32:half * HD + 33], 1.0).then_inc(self.bias_ready, 1)
            pool.memset(self.bk[half * HD:half * HD + 1], 1.0).then_inc(self.bias_ready, 1)
        heads = k.const(C_IDENT, FOX_H, FOX_H).unsqueeze(2).to_broadcast([FOX_H, FOX_H, HD])
        pool.tensor_copy(self.spread.rearrange("p (h n) -> p h n", h=FOX_H), heads).then_inc(self.spread_ready, 1)


class Rope:

    C1, MAGIC = 6.28125, 12582912.0
    C2 = 2 * float(np.pi) - C1

    def __init__(self, k):
        self.k, self.turn = k, k.x_turns
        self.sined = k.s("rope_sined")
        self.angle, self.turns, self.half = (k.arena[:, n * 512:(n + 1) * 512].rearrange("p (r t) -> p r t", r=2) for n in range(3))
        self.reduced = k.s("rope_reduced")

    def act(self, act):
        k = self.k
        act.wait_ge(self.reduced, 1)
        act.activation(k.rope[:, 1], self.angle, ACT.Sin).then_inc(self.sined, 1)
        act.activation(self.half, self.angle, ACT.Sin, scale=0.5).then_inc(self.sined, 1)

    def dve(self, dve):
        k, seq = self.k, self.k.dve_seq
        dve.wait_ge(k.small_ready, k.small_all)
        dve.wait_ge(k.x_ready, 4 * self.turn)
        seq.inc(dve.tensor_copy(self.turns[:, 0], k.pos[:]))
        seq.wait(dve)
        for r, col in ((0, C_INVN), (1, C_INVM)):
            seq.inc(dve.tensor_scalar(self.angle[:, r], self.turns[:, 0], k.const(col, 1), None, ALU.mult))
        seq.wait(dve)
        steps = [
            lambda: dve.tensor_scalar(self.turns, self.angle, 1.0 / (2 * float(np.pi)), self.MAGIC, ALU.mult, ALU.add),
            lambda: dve.tensor_scalar(self.turns, self.turns, self.MAGIC, None, ALU.subtract),
            lambda: dve.scalar_tensor_tensor(out=self.angle, in0=self.turns, scalar=-self.C1, in1=self.angle, op0=ALU.mult, op1=ALU.add),
            lambda: dve.scalar_tensor_tensor(out=self.angle, in0=self.turns, scalar=-self.C2, in1=self.angle, op0=ALU.mult, op1=ALU.add),
        ]
        for step in steps:
            seq.inc(step())
            seq.wait(dve)
        dve.tensor_scalar(self.angle, self.angle, 3.1415925, -3.1415925, ALU.min, ALU.max).then_inc(self.reduced, 1)
        dve.wait_ge(self.sined, 2)
        seq.inc(dve.tensor_tensor(self.half, self.half, self.half, ALU.mult))
        seq.wait(dve)
        dve.tensor_scalar(k.rope[:, 0], self.half, -2.0, 1.0, ALU.mult, ALU.add).then_inc(k.rope_ready, 1)


class LayerNorm:

    def __init__(self, k, row, memory=None):
        self.k, self.row, self.i, self.memory = k, row, k.layer_norms, memory
        k.layer_norms += 1
        self.before = k.x_turns
        k.x_turns += 1
        k.banks.plan(f"ln_m{self.i}", f"ln_v{self.i}")
        if memory:
            memory.plan_turned()
            memory.plan_products()

    def sp(self, eng):
        if self.memory:
            self.memory.sp(eng)

    def pool(self, pool):
        pass

    def pe(self, pe):
        k, b, i = self.k, self.k.banks, self.i
        out = b.claim(pe, f"ln_m{i}")[:, 0:T]
        for kk in range(KD):
            if kk % 2 == 0:
                pe.wait_ge(k.x_ready, 4 * (self.before - 1) + kk // 2 + 1)
            last = pe.matmul(out, k.ones, k.x[:, kk], start=kk == 0, stop=kk == KD - 1)
        b.filled(last, f"ln_m{i}")
        out = b.claim(pe, f"ln_v{i}")[:, 0:T]
        for kk in range(KD):
            if kk % 2 == 0:
                pe.wait_ge(k.ln_sq, 4 * i + kk // 2 + 1)
            last = pe.matmul(out, k.ones, k.sq[:, kk], start=kk == 0, stop=kk == KD - 1)
        b.filled(last, f"ln_v{i}")
        if self.memory:
            self.memory.pe_turned(pe)
            self.memory.pe_products(pe)

    def act(self, act):
        k, b, i = self.k, self.k.banks, self.i
        for c in range(4):
            act.wait_ge(k.ln_centred, 4 * i + c + 1)
            act.activation(k.sq[:, 2 * c:2 * c + 2], k.xn[:, 2 * c:2 * c + 2], ACT.Square).then_inc(k.ln_sq, 1)
        src = b.wait(act, f"ln_v{i}")[:, 0:T]
        b.read(act.activation(k.std[:], src, ACT.Sqrt, bias=k.const(C_LNEPS, 1), scale=1.0 / D), f"ln_v{i}")
        if self.memory:
            act.wait_ge(k.x_ready, 4 * self.before)
            self.memory.act_turned(act)
        for c in range(4):
            act.wait_ge(k.ln_scaled, 4 * i + c + 1)
            for kk in (2 * c, 2 * c + 1):
                g = k.param[:, R_LNG + self.row * KD + kk:R_LNG + self.row * KD + kk + 1]
                bb = k.param[:, R_LNB + self.row * KD + kk:R_LNB + self.row * KD + kk + 1]
                ins = act.activation(k.x[:, kk], k.xn[:, kk], ACT.Identity, scale=g, bias=bb)
            ins.then_inc(k.x_ready, 1)

    def dve(self, dve):
        k, b, i = self.k, self.k.banks, self.i
        total = b.wait(dve, f"ln_m{i}")[:, 0:T].unsqueeze(1).to_broadcast([P, 2, T])
        for c in range(4):
            cs = slice(2 * c, 2 * c + 2)
            dve.scalar_tensor_tensor(out=k.xn[:, cs], in0=total, scalar=-1.0 / D, in1=k.x[:, cs],
                                     op0=ALU.mult, op1=ALU.add).then_inc(k.ln_centred, 1)
        dve.wait_ge(k.ln_centred, 4 * i + 4)
        b.release(dve, f"ln_m{i}")
        b.wait_read(dve, f"ln_v{i}")
        dve.reciprocal(k.rstd[:], k.std[:]).then_inc(k.ln_rstd, 1)
        dve.wait_ge(k.ln_rstd, i + 1)
        for c in range(4):
            cs = slice(2 * c, 2 * c + 2)
            dve.tensor_tensor(k.xn[:, cs], k.xn[:, cs], k.rstd[:].unsqueeze(1).to_broadcast([P, 2, T]), ALU.mult).then_inc(k.ln_scaled, 1)
        dve.wait_ge(k.x_ready, 4 * self.before + 4)


class MemoryRows:

    def __init__(self, k, layer, name, at):
        self.k, self.layer, self.name = k, layer, name
        cut = lambda a, n: k.arena[:, a:a + n * T].rearrange("p (m t) -> p m t", m=n)
        self.xq, self.mk, self.mv, self.mem_t = (cut(a, n) for a, n in zip(at, (2, 2, 2, 8)))
        self.fill = k.ring.plan(2)

    def plan_turned(self):
        self.k.banks.plan(*[f"{self.name}_mt{n}" for n in range(4)])

    def plan_products(self):
        self.k.banks.plan(f"{self.name}_mk", f"{self.name}_mv")

    def sp(self, eng):
        k, n = self.k, self.fill
        k.ring.wait_free(eng, n)
        slot, full = k.ring.slot(n), k.ring.full[n % SLOTS]
        eng.dma_start(slot[:, 0:2048].rearrange("p (t d) -> p t d", t=TT), k.a["mem_2"].rearrange("o (t p) d -> p (o t) d", p=P)).then_inc(full, 16)
        eng.dma_start(slot[:, 2048:6144].rearrange("p (k n) -> p k n", k=KD),
                      k.a["mem_w_kv_2"][self.layer].rearrange("(k p) n -> p k n", p=P)).then_inc(full, 16)

    def pe_turned(self, pe):
        k, b, name = self.k, self.k.banks, self.name
        k.ring.wait_full(pe, self.fill)
        slot = k.ring.slot(self.fill)
        for q in range(4):
            out = b.claim(pe, f"{name}_mt{q}")
            for n in range(4):
                kk, t = 2 * q + n // 2, n % 2
                last = pe.transpose(out[:, n * P:(n + 1) * P], slot[:, t * D + kk * P:t * D + (kk + 1) * P], k.ident)
            b.filled(last, f"{name}_mt{q}")

    def pe_products(self, pe):
        k, b, name = self.k, self.k.banks, self.name
        w = k.ring.slot(self.fill)[:, 2048:6144].rearrange("p (k n) -> p k n", k=KD)
        for q in range(4):
            b.wait_read(pe, f"{name}_mt{q}")
        out = b.claim(pe, f"{name}_mk")
        for h in range(2):
            for kk in range(KD):
                last = pe.matmul(out[:, h * T:(h + 1) * T], w[:, kk, h * P:(h + 1) * P], self.mem_t[:, kk], start=kk == 0, stop=kk == KD - 1)
        b.filled(last, f"{name}_mk")
        out = b.claim(pe, f"{name}_mv")
        for t in range(TT):
            for kk in range(KD):
                last = pe.matmul(out[:, t * T:(t + 1) * T], self.mem_t[:, kk, t * P:(t + 1) * P], w[:, kk, 256:512], start=kk == 0, stop=kk == KD - 1)
        b.filled(last, f"{name}_mv")

    def act_turned(self, act):
        k, b, name = self.k, self.k.banks, self.name
        for q in range(4):
            src = b.wait(act, f"{name}_mt{q}").rearrange("p (k t) -> p k t", k=2)
            b.read(act.activation(self.mem_t[:, 2 * q:2 * q + 2], src, ACT.Copy), f"{name}_mt{q}")

    def act_products(self, act):
        k, b, name = self.k, self.k.banks, self.name
        for part, to in (("mk", self.mk), ("mv", self.mv)):
            src = b.wait(act, f"{name}_{part}").rearrange("p (k t) -> p k t", k=2)
            b.read(act.activation(to, src, ACT.Copy), f"{name}_{part}")
        act.sem_inc(k.ring.free[self.fill % SLOTS], 1)


class Memory(Attention):

    def memory_units(self):
        k, m, units = self.k, self.memory, []
        for h in range(XA_H):
            pair, half = divmod(h, 2)
            at = slice(half * HD, (half + 1) * HD)
            for t in range(TT):
                units.append(dict(
                    q=m.xq[at, pair, t * P:(t + 1) * P], keys=m.mk[at, pair, :], n=T, mask=k.const(C_CAUSAL, T),
                    seen=None, scale=HD ** -0.5, gate=None, values=[(P, m.mv[:, r, h * HD:(h + 1) * HD]) for r in range(TT)],
                    head=12 + h, tile=t, first=True))
        return units

    def pe_rotate(self, pe, name, raw, matrix, shape):
        k, b = self.k, self.k.banks
        b.wait_read(pe, name)
        out = b.claim(pe, name + "_r")
        b.filled(pe.matmul(out[0:shape[0], 0:shape[1]], matrix, raw, start=True, stop=True), name + "_r")

    def dve_rotate(self, dve, name, raw, out, cos, sin, shape):
        k, b, seq = self.k, self.k.banks, self.k.dve_seq
        wide = lambda t: t.unsqueeze(1).to_broadcast(list(shape))
        rot = b.wait(dve, name + "_r")[raw.start_partition():raw.start_partition() + shape[0], 0:shape[1] * shape[2]]
        rot = rot.rearrange("p (m n) -> p m n", m=shape[1])
        seq.inc(dve.tensor_tensor(out, rot, wide(sin), ALU.mult))
        first = seq.n
        seq.inc(dve.tensor_tensor(raw, raw, wide(cos), ALU.mult))
        seq.wait(dve)
        b.read(dve.tensor_tensor(out, out, raw, ALU.add), name + "_r")


class Nsa(Memory):

    def __init__(self, k):
        self.k, self.rope = k, Rope(k)
        a, ar, b = k.a, k.arena, k.banks
        w = a["nsa_w_in_2"][0]
        offs = dict(q0=0, q1=256, q2=512, kc=768, vc=1024, ks=1280, vs=1536, kw=1792, vw=2048)
        col = lambda at, n=256: w[:, at:at + n]
        cut = lambda at, p, *s: ar[:p, at:at + int(np.prod(s))].rearrange(
            "p (a b) -> p a b", a=s[0])
        self.q, self.ks, self.kw = cut(0, P, 6, T), cut(1536, P, 4, T), cut(2560, P, 4, T)
        self.kc2, self.vc2 = cut(3584, P, NSA_KV + 1, T), cut(4864, P, NSA_KV + 1, T)
        self.vs, self.vw = cut(6144, P, 2, T), cut(8704, P, 2, T)
        self.kc, self.vc, self.ks_once, self.kw_once = (cut(10240 + n * 512, P, 2, T) for n in range(4))
        self.raw = [cut(12544 + n * 512, P, 2, T) for n in range(3)]
        self.hid = [cut(14080 + n * 64, P, 4, N_CMP) for n in range(2)]
        self.kcmp, self.kcmp_raw = cut(14208, P, 4, N_CMP), cut(14272, P, 4, N_CMP)
        self.memory = MemoryRows(k, 0, "nsa", (6656, 7168, 7680, 8192))
        self.memory.plan_turned()
        self.memory.plan_products()
        self.vcmp, self.gates, self.pe_bias = ar[0:N_CMP, 8192:8192 + T], cut(8448, P, 2, 36), ar[:, 8520:8522]
        self.first, self.then = ("kc", "vc", "ks", "kw", "vs", "vw"), ("q0", "q1", "q2", "xq", "gt")
        self.plan_blocks([(n, col(offs[n])) for n in self.first])
        self.w1_fill = k.ring.plan(1)
        self.plan_blocks([(n, col(offs[n])) for n in self.then[:3]] + [("xq", col(2340)), ("gt", col(2304, 36))])
        self.plan_out("nsa", a["w_out_2"][0])
        self.plan_split()
        columns = lambda n: self.plan_columns("nsa_" + n, self.block(n), [(0, P, 0), (P, P, T)])
        columns("kc")
        columns("vc")
        self.rotated = ["ks", "kw", "q0", "q1", "q2"]
        for i, n in enumerate(self.rotated):
            columns(n)
            if i:
                b.plan("nsa_" + self.rotated[i - 1] + "_r")
            if n == "kw":
                self.plan_rows(["nsa_vs0", "nsa_vs1"], *self.block("vs"), 256)
                self.plan_rows(["nsa_vw0", "nsa_vw1"], *self.block("vw"), 256)
                b.plan("nsa_hk", "nsa_hv")
            if n == "q1":
                b.plan("nsa_kcmp", "nsa_vcmp")
        b.plan("nsa_kcmp_r", "nsa_q2_r")
        columns("xq")
        self.plan_rows(["nsa_gt"], *self.block("gt"), 36)
        self.plan_out_pieces()
        s = lambda n: k.s("nsa_" + n)
        self.cat_ready, self.pe_ready, self.hid_ready = s("cat"), s("pe"), s("hid")
        self.pe_placed, self.pe_cleared = s("pe_placed"), s("pe_cleared")
        self.pairs_placed, self.keys_placed = s("pairs_placed"), s("keys_placed")
        units = []
        for h in range(NSA_H):
            pair, half, kv = h // 2, h % 2, h // GROUP
            at = slice(half * HD, (half + 1) * HD)
            vcol = slice(kv * HD, (kv + 1) * HD)
            def unit(t, j, **more):
                units.append(dict(more, q=self.q[at, pair, t * P:(t + 1) * P], scale=HD ** -0.5, head=h, tile=t, first=j == 0,
                                  gate=self.gates[:, t, 3 * h + j:3 * h + j + 1]))

            for t in range(TT):
                unit(t, 0, keys=self.kcmp[at, kv, :], n=N_CMP, mask=k.const(C_CMPADD + t * N_CMP, N_CMP),
                     seen=k.const(C_CMPMUL + t * N_CMP, N_CMP), values=[(N_CMP, self.vcmp[:, vcol])])
            for j, keys, v in ((1, self.ks, self.vs), (2, self.kw, self.vw)):
                for t in range(TT):
                    n = (t + 1) * P
                    unit(t, j, keys=keys[at, kv, 0:n], n=n, mask=k.const(C_CAUSAL + 384 - n, n), seen=None,
                         values=[(P, v[:, m, vcol]) for m in range(t + 1)])
        self.plan_units("nsa", units + self.memory_units(), ar[:, 10240:12288])

    def sp(self, eng):
        k = self.k
        self.memory.sp(eng)
        self.sp_blocks(eng, self.first)
        n = self.w1_fill
        k.ring.wait_free(eng, n)
        eng.dma_start(k.ring.slot(n)[:, 0:4096].rearrange("p (v l n) -> p v l n", v=2, l=16),
                      k.a["nsa_cmp_w1_2"][0].rearrange("v (l p) n -> p v l n", p=P)).then_inc(k.ring.full[n % SLOTS], 16)
        self.sp_blocks(eng, self.then)
        self.sp_out(eng)

    def pe(self, pe):
        k, b = self.k, self.k.banks
        self.memory.pe_turned(pe)
        self.memory.pe_products(pe)
        self.pe_wait_input(pe)
        self.pe_columns(pe, "nsa_kc")
        self.pe_columns(pe, "nsa_vc")
        flat = lambda t: t.rearrange("p h n -> p (h n)")

        def hidden():
            k.ring.wait_full(pe, self.w1_fill)
            w1 = k.ring.slot(self.w1_fill)[:, 0:4096].rearrange("p (v l n) -> p v l n", v=2, l=16)
            pe.wait_ge(self.pairs_placed, 128)
            pe.wait_ge(self.pe_placed, 2)
            for v, (name, src) in enumerate((("nsa_hk", self.kc2), ("nsa_hv", self.vc2))):
                out = b.claim(pe, name)
                for l in range(16):
                    last = pe.matmul(out[:, 0:(NSA_KV + 1) * N_CMP], w1[:, v, l], src[:, :, 2 * l:2 * l + 225:CMP_STRIDE], start=l == 0, stop=l == 15)
                b.filled(last, name)

        def compressed():
            pe.wait_ge(self.hid_ready, 1)
            pe.wait_ge(k.small_ready, k.small_all)
            out = b.claim(pe, "nsa_kcmp")
            for half in range(2):
                last = pe.matmul(out[half * HD:(half + 1) * HD, 0:4 * N_CMP], k.cmp_w2[:, 0], flat(self.hid[0]), start=True, stop=True)
            b.filled(last, "nsa_kcmp")
            pe.wait_ge(self.hid_ready, 2)
            out = b.claim(pe, "nsa_vcmp")
            for h in range(NSA_KV):
                last = pe.matmul(out[0:N_CMP, h * HD:(h + 1) * HD], self.hid[1][:, h], k.cmp_w2[:, 1], start=True, stop=True)
            b.filled(last, "nsa_vcmp")

        for i, name in enumerate(self.rotated):
            self.pe_columns(pe, "nsa_" + name)
            if i:
                self.rotate(pe, i - 1)
            if name == "kw":
                self.pe_rows(pe, ["nsa_vs0", "nsa_vs1"])
                self.pe_rows(pe, ["nsa_vw0", "nsa_vw1"])
                hidden()
            if name == "q1":
                compressed()
        self.pe_rotate(pe, "nsa_kcmp", flat(self.kcmp_raw), k.const(C_ROTN, P), (P, 4 * N_CMP))
        self.rotate(pe, len(self.rotated) - 1)
        self.pe_columns(pe, "nsa_xq")
        self.pe_rows(pe, ["nsa_gt"])
        b.wait_read(pe, "nsa_q2_r")
        b.wait_read(pe, "nsa_gt")
        b.wait_read(pe, "nsa_vcmp")
        b.wait_read(pe, "nsa_kcmp_r")
        pe.wait_ge(self.keys_placed, 128)
        self.pe_units(pe)
        self.pe_out(pe)

    def rotate(self, pe, i):
        k = self.k
        raw = self.raw[i % 3].rearrange("p m t -> p (m t)")
        self.pe_rotate(pe, "nsa_" + self.rotated[i], raw, k.const(C_ROTN, P), (P, 2 * T))

    def act(self, act):
        k, b = self.k, self.k.banks
        act.wait_ge(k.x_ready, 4 * self.turn)
        self.memory.act_turned(act)
        self.rope.act(act)
        self.act_input(act, k.x, lambda eng, c: None)
        self.act_pieces(act, PIECES)
        self.memory.act_products(act)
        two = lambda t: t.rearrange("p (m t) -> p m t", m=2)
        for name, once, pairs in (("nsa_kc", self.kc, self.kc2), ("nsa_vc", self.vc, self.vc2)):
            self.act_pieces(act, self.ahead(name))
            b.read(act.activation(once, two(b.wait(act, name)), ACT.Copy), name)
            b.wait_read(act, name)
            for j in range(2):
                src = once[j * HD:(j + 1) * HD]
                act.dma_start(pairs[0:HD, j:NSA_KV:2], src).then_inc(self.pairs_placed, 16)
                act.dma_start(pairs[HD:P, j:NSA_KV:2, 0:T - 1], src[:, :, 1:T]).then_inc(self.pairs_placed, 16)
        for i, name in enumerate(self.rotated):
            self.act_pieces(act, self.ahead("nsa_" + name))
            if i >= 3:
                b.wait_read(act, "nsa_" + self.rotated[i - 3] + "_r")
            b.read(act.activation(self.raw[i % 3], two(b.wait(act, "nsa_" + name)), ACT.Copy), "nsa_" + name)
            if name == "kw":
                for n, to in (("vs", self.vs), ("vw", self.vw)):
                    self.act_pieces(act, self.ahead(f"nsa_{n}0"))
                    for t in range(TT):
                        src = b.wait(act, f"nsa_{n}{t}")[:, 0:T]
                        b.read(act.activation(to[:, t], src, ACT.Copy), f"nsa_{n}{t}")
                for v, n in enumerate(("nsa_hk", "nsa_hv")):
                    act.wait_ge(self.pe_ready, v + 1)
                    src = b.at(n)[:, 0:4 * N_CMP].rearrange("p (h n) -> p h n", h=4)
                    act.activation(self.hid[v], src, ACT.Silu, bias=self.pe_bias[:, v:v + 1]).then_inc(self.hid_ready, 1)
                    act.wait_ge(self.hid_ready, v + 1)
                    b.release(act, n)
                self.release(act, self.w1_fill)
            if name == "q1":
                src = b.wait(act, "nsa_kcmp")[:, 0:4 * N_CMP].rearrange("p (h n) -> p h n", h=4)
                b.read(act.activation(self.kcmp_raw, src, ACT.Copy), "nsa_kcmp")
                src = b.wait(act, "nsa_vcmp")[0:N_CMP, 0:T]
                b.read(act.activation(self.vcmp, src, ACT.Copy), "nsa_vcmp")
                for n, once, keys in (("ks", self.ks_once, self.ks), ("kw", self.kw_once, self.kw)):
                    b.wait_read(act, f"nsa_{n}_r")
                    for j in range(2):
                        for half in range(2):
                            act.dma_start(keys[half * HD:(half + 1) * HD, j:NSA_KV:2], once[j * HD:(j + 1) * HD]).then_inc(self.keys_placed, 16)
        self.act_pieces(act, self.ahead("nsa_xq"))
        b.read(act.activation(self.memory.xq, two(b.wait(act, "nsa_xq")), ACT.Copy), "nsa_xq")
        self.act_pieces(act, "nsa_gt")
        src = two(b.wait(act, "nsa_gt")[:, 0:72])
        b.read(act.activation(self.gates, src, ACT.Sigmoid), "nsa_gt")
        self.act_units(act)
        self.act_out(act)

    def dve(self, dve):
        k, b = self.k, self.k.banks
        self.rope.dve(dve)
        self.dve_input(dve, k.x)
        cos, sin = k.rope[:, 0, 0, :], k.rope[:, 1, 0, :]
        outs = [self.ks_once, self.kw_once] + [self.q[:, 2 * n:2 * n + 2] for n in range(3)]
        after = dict(zip(("kw", "q0", "q1", "q2", "xq"), enumerate(self.rotated)))
        for job in ("kc", "vc", "ks", "kw", "vs0", "vw0", "q0", "q1", "q2", "xq", "gt"):
            self.dve_pieces(dve, self.ahead("nsa_" + job))
            if job in after:
                i, name = after[job]
                self.dve_rotate(dve, "nsa_" + name, self.raw[i % 3], outs[i], cos, sin, (P, 2, T))
            if job == "vw0":
                for v, name in enumerate(("nsa_hk", "nsa_hv")):
                    src = b.wait(dve, name)
                    dve.tensor_copy(self.pe_bias[:, v:v + 1], src[:, 4 * N_CMP:4 * N_CMP + 1]).then_inc(self.pe_ready, 1)
            if job == "q2":
                ends = slice(CMP_LEN - 1, T, CMP_STRIDE)
                self.dve_rotate(dve, "nsa_kcmp", self.kcmp_raw, self.kcmp, cos[:, ends], sin[:, ends], (P, 4, N_CMP))
        self.dve_units(dve)
        self.dve_out(dve, ALPHA)

    def pool(self, pool):
        k = self.k
        pool.wait_ge(k.x_ready, 4 * self.turn)
        for v, to in enumerate((self.kc2, self.vc2)):
            pool.memset(to[:, NSA_KV], 0.0).then_inc(self.pe_cleared, 1)
            pool.wait_ge(self.pe_cleared, v + 1)
            pool.tensor_copy(to[:, NSA_KV, 0:32:2], k.pe_cols[:, v * 16:(v + 1) * 16]).then_inc(self.pe_placed, 1)


class Mla(Memory):

    def __init__(self, k, memory):
        self.k = k
        a, ar, b = k.a, k.arena, k.banks
        cut = lambda at, p, *s: ar[:p, at:at + int(np.prod(s))].rearrange("p (a b) -> p a b", a=s[0])
        self.q, self.kk, self.v = cut(0, P, MLA_H, T), cut(3072, P, MLA_H, T), cut(6144, P, TT, MLA_H * HD)
        self.cq, self.ckv = cut(7680, P, 2, T), ar[:, 8192:8192 + T]
        self.kr_raw, self.kr = cut(8448, MLA_K, 1, T), cut(8704, MLA_K, 1, T)
        self.raw = [cut(8960 + n * 512, MLA_K, 2, T) for n in range(3)]
        self.std = cut(10496, P, 2, T)
        self.memory = memory
        self.in_fill, self.up_fill = k.ring.plan(1), k.ring.plan(2)
        self.plan_out("mla", a["w_out_2"][1])
        self.plan_split()
        source = self.in_fill, k.ring.slot(self.in_fill)[:, 0:KD * 672].rearrange("p (k n) -> p k n", k=KD)
        self.plan_columns("mla_cq", source, [(0, P, 0), (P, P, T)])
        self.plan_columns("mla_ckv", source, [(256, P, 0), (320, MLA_K, T)])
        self.plan_columns("mla_xq", source, [(416, P, 0), (416 + P, P, T)])
        self.plan_out_pieces()
        b.plan("mla_n", "mla_kr_r")
        for i in range(6):
            b.plan(f"mla_q{i}", f"mla_k{i}")
            if i:
                b.plan(f"mla_q{i - 1}_r")
        b.plan("mla_q5_r", *[f"mla_v{t}{half}" for t in range(TT) for half in range(2)])
        s = lambda n: k.s("mla_" + n)
        self.sq_ready, self.std_ready, self.rstd_ready = s("sq"), s("std"), s("rstd")
        self.kr_copied, self.kr_ready, self.kr_placed = s("kr_copied"), s("kr"), s("kr_placed")
        self.latent_ready, self.cat_ready = s("latent"), s("cat")
        units = []
        for h in range(MLA_H):
            for t in range(TT):
                n = (t + 1) * P
                units.append(dict(
                    q=self.q[0:MLA_K, h, t * P:n], keys=self.kk[0:MLA_K, h, 0:n], n=n, mask=k.const(C_CAUSAL + 384 - n, n),
                    seen=None, scale=MLA_K ** -0.5, gate=None, head=h, tile=t, first=True,
                    values=[(P, self.v[:, m, h * HD:(h + 1) * HD]) for m in range(t + 1)]))
        self.plan_units("mla", units + self.memory_units(), ar[:, 7680:9728])

    def sp(self, eng):
        k, r, a = self.k, self.k.ring, self.k.a
        r.wait_free(eng, self.in_fill)
        eng.dma_start(r.slot(self.in_fill)[:, 0:KD * 672].rearrange("p (k n) -> p k n", k=KD),
                      a["mla_w_in_2"][0].rearrange("(k p) n -> p k n", p=P)).then_inc(r.full[self.in_fill % SLOTS], 16)
        r.wait_free(eng, self.up_fill)
        slot, full = r.slot(self.up_fill), r.full[self.up_fill % SLOTS]
        eng.dma_start(slot[:, 0:2304].rearrange("p (k n) -> p k n", k=2),
                      a["mla_w_uq_2"][0].rearrange("(k p) n -> p k n", p=P)).then_inc(full, 16)
        eng.dma_start(slot[:, 2304:3840], a["mla_w_ukv_2"][0]).then_inc(full, 16)
        self.sp_out(eng)

    def pe(self, pe):
        k, b = self.k, self.k.banks
        for name in ("mla_cq", "mla_ckv", "mla_xq"):
            self.pe_columns(pe, name, self.in_split if name == "mla_cq" else None)
        pe.wait_ge(self.sq_ready, 2)
        out = b.claim(pe, "mla_n")
        pe.matmul(out[:, 0:T], k.ones, k.sq[:, 0], start=True, stop=False)
        pe.matmul(out[:, 0:T], k.ones, k.sq[:, 1], start=False, stop=True)
        b.filled(pe.matmul(out[:, T:2 * T], k.ones, k.sq[:, 2], start=True, stop=True), "mla_n")
        rot = k.c[0:MLA_K, C_ROTM:C_ROTM + MLA_K]
        pe.wait_ge(self.kr_copied, 1)
        b.filled(pe.matmul(b.claim(pe, "mla_kr_r")[0:MLA_K, 0:T], rot, self.kr_raw[:, 0], start=True, stop=True), "mla_kr_r")
        k.ring.wait_full(pe, self.up_fill)
        slot = k.ring.slot(self.up_fill)
        uq = slot[:, 0:2304].rearrange("p (k n) -> p k n", k=2)
        ukv = slot[:, 2304:3840].rearrange("p (h n) -> p h n", h=MLA_H)
        pe.wait_ge(self.latent_ready, 3)

        def rotate(i):
            self.pe_rotate(pe, f"mla_q{i}", self.raw[i % 3].rearrange("p m t -> p (m t)"), rot, (MLA_K, 2 * T))

        for i in range(6):
            out = b.claim(pe, f"mla_q{i}")
            for j in range(2):
                at = (2 * i + j) * MLA_K
                for kk in range(2):
                    last = pe.matmul(out[0:MLA_K, j * T:(j + 1) * T], uq[:, kk, at:at + MLA_K], self.cq[:, kk], start=kk == 0, stop=kk == 1)
            b.filled(last, f"mla_q{i}")
            out = b.claim(pe, f"mla_k{i}")
            for j in range(2):
                last = pe.matmul(out[0:HD, j * T:(j + 1) * T], ukv[:, 2 * i + j, 0:HD], self.ckv, start=True, stop=True)
            b.filled(last, f"mla_k{i}")
            if i:
                rotate(i - 1)
        rotate(5)
        for t in range(TT):
            for half in range(2):
                out = b.claim(pe, f"mla_v{t}{half}")[:, 0:6 * HD]
                b.filled(pe.matmul(out.rearrange("p (h n) -> p h n", h=6), self.ckv[:, t * P:(t + 1) * P],
                                   ukv[:, 6 * half:6 * half + 6, HD:2 * HD], start=True, stop=True), f"mla_v{t}{half}")
        b.wait_read(pe, "mla_q5_r")
        b.wait_read(pe, "mla_v11")
        pe.wait_ge(self.kr_placed, 1)
        self.pe_units(pe)
        self.pe_out(pe)

    def act(self, act):
        k, b = self.k, self.k.banks
        self.act_input(act, k.x, lambda eng, c: eng.wait_ge(k.x_ready, 4 * (self.turn - 1) + c + 1))
        self.act_pieces(act, self.ahead("mla_cq"))
        self.memory.act_products(act)
        src = b.wait(act, "mla_cq").rearrange("p (m t) -> p m t", m=2)
        act.activation(k.sq[:, 0:2], src, ACT.Square).then_inc(self.sq_ready, 1)
        self.act_pieces(act, self.ahead("mla_ckv"))
        src = b.wait(act, "mla_ckv")
        act.activation(k.sq[:, 2], src[:, 0:T], ACT.Square).then_inc(self.sq_ready, 1)
        act.activation(self.kr_raw[:, 0], src[0:MLA_K, T:2 * T], ACT.Copy).then_inc(self.kr_copied, 1)
        self.act_pieces(act, "mla_xq")
        src = b.wait(act, "mla_xq").rearrange("p (m t) -> p m t", m=2)
        b.read(act.activation(self.memory.xq, src, ACT.Copy), "mla_xq")
        src = b.wait(act, "mla_n")
        act.activation(self.std[:, 0], src[:, 0:T], ACT.Sqrt, bias=k.const(C_EPS, 1), scale=1.0 / 256).then_inc(self.std_ready, 1)
        act.activation(self.std[:, 1], src[:, T:2 * T], ACT.Sqrt, bias=k.const(C_EPS, 1), scale=1.0 / P).then_inc(self.std_ready, 1)
        act.wait_ge(self.std_ready, 2)
        b.release(act, "mla_n")
        for i in range(6):
            if i >= 3:
                b.wait_read(act, f"mla_q{i - 3}_r")
            src = b.wait(act, f"mla_q{i}")[0:MLA_K].rearrange("p (m t) -> p m t", m=2)
            b.read(act.activation(self.raw[i % 3], src, ACT.Copy), f"mla_q{i}")
            src = b.wait(act, f"mla_k{i}")[0:HD].rearrange("p (m t) -> p m t", m=2)
            b.read(act.activation(self.kk[0:HD, 2 * i:2 * i + 2], src, ACT.Copy), f"mla_k{i}")
        for t in range(TT):
            for half in range(2):
                src = b.wait(act, f"mla_v{t}{half}")[:, 0:6 * HD]
                b.read(act.activation(self.v[:, t, half * 384:(half + 1) * 384], src, ACT.Copy), f"mla_v{t}{half}")
        self.release(act, self.up_fill)
        self.act_units(act)
        self.act_out(act)

    def dve(self, dve):
        k, b = self.k, self.k.banks
        cos, sin = k.rope[0:MLA_K, 0, 1, :], k.rope[0:MLA_K, 1, 1, :]
        self.dve_input(dve, k.x)
        self.dve_pieces(dve, "mla_xq")
        dve.wait_ge(self.std_ready, 2)
        cq, ckv = b.at("mla_cq"), b.at("mla_ckv")
        for out, src, row, std in ((self.cq[:, 0], cq[:, 0:T], R_MQ, 0), (self.cq[:, 1], cq[:, T:2 * T], R_MQ + 1, 0),
                                   (self.ckv, ckv[:, 0:T], R_MKV, 1)):
            if row != R_MQ + 1:
                dve.reciprocal(self.std[:, std], self.std[:, std]).then_inc(self.rstd_ready, 1)
                dve.wait_ge(self.rstd_ready, std + 1)
            dve.scalar_tensor_tensor(out=out, in0=src, scalar=k.param[:, row:row + 1], in1=self.std[:, std],
                                     op0=ALU.mult, op1=ALU.mult).then_inc(self.latent_ready, 1)
        dve.wait_ge(self.latent_ready, 3)
        b.release(dve, "mla_cq")
        b.release(dve, "mla_ckv")
        self.dve_rotate(dve, "mla_kr", self.kr_raw, self.kr, cos, sin, (MLA_K, 1, T))
        b.wait_read(dve, "mla_kr_r")
        dve.sem_inc(self.kr_ready, 1)
        for i in range(6):
            self.dve_rotate(dve, f"mla_q{i}", self.raw[i % 3], self.q[0:MLA_K, 2 * i:2 * i + 2], cos, sin, (MLA_K, 2, T))
        self.dve_units(dve)
        self.dve_out(dve, ALPHA)

    def pool(self, pool):
        pool.wait_ge(self.kr_ready, 1)
        pool.tensor_copy(self.kk[HD:MLA_K], self.kr[HD:MLA_K].to_broadcast([MLA_ROPE, MLA_H, T])).then_inc(self.kr_placed, 1)


class Moe:

    GROUPS, SLOTS_N, STEPS, TURN = G_N, G_N + 1, 2 * E_G, 2 * E_G + 1

    def __init__(self, k, layer):
        self.k, self.layer, self.turn = k, layer, k.x_turns
        k.x_turns += 1
        dmas = [2] + [3] * (self.STEPS - 1) + [1]
        self.fills = [k.ring.plan(n) for n in dmas * self.SLOTS_N]
        self.landed = [16 * sum(dmas[r::SLOTS]) for r in range(SLOTS)]
        assert self.TURN % SLOTS == 0
        self.slot0, self.step0, self.gather0 = (layer * n for n in (self.SLOTS_N, self.SLOTS_N * self.STEPS, self.SLOTS_N + 1))
        name = f"moe{layer}_"
        self.name = name
        k.banks.plan(*[name + n for n in ("lg", "x0", "lt", "x1", "x2", "x3", "rank", "st0", "st1", "st2", "gates")])
        self.sem = k.moe
        flat = lambda t: t.rearrange("p k t -> p (k t)")
        sq, wide = flat(k.sq[:]), flat(k.wide[:, 1])
        cut = lambda at, n: sq[:, at:at + 2 * n].rearrange("p (t n) -> p t n", t=2)
        self.logits, self.group, self.chosen, self.first = cut(0, 20), cut(40, 4), cut(48, 4), cut(56, 4)
        self.exp_g, self.exp_e, self.best, self.rank1 = cut(64, 4), cut(72, 4), cut(80, 4), cut(88, 4)
        self.picked = sq[:, 96:128].rearrange("p (t g j) -> p t g j", t=2, g=4)
        self.cols = [cut(128 + 2 * n, 1) for n in range(8)]
        self.pos = cut(144, self.SLOTS_N + 1)
        self.over, self.over_n = sq[0:1, 160:164], sq[0:1, 164:166]
        self.place_t = sq[:, 512:512 + self.SLOTS_N * T]
        self.logits_t = sq[0:G_N + E_N, 512 + self.SLOTS_N * T:512 + self.SLOTS_N * T + T]
        self.place = wide[:, 0:2 * 6 * P].rearrange("p (t n) -> p t n", t=2)
        self.gates = wide[:, 1536:1536 + 20].rearrange("p (i e) -> p i e", e=E_G)
        self.gate4 = wide[:, 1560:1564]
        self.tok = k.wide[:, 0].rearrange("p k t -> p (k t)").rearrange("p (t d) -> p t d", t=TT)
        pieces = lambda t: t[:].rearrange("p a n -> p (a n)").rearrange("p (m n) -> p m n", n=1024)
        self.w_hi, self.w_lo = pieces(k.w_hi), pieces(k.w_lo)
        x = lambda t: flat(t[:])[:, 0:D].rearrange("p (k n) -> p k n", n=P)
        self.x_hi, self.x_lo = x(k.x_hi), x(k.x_lo)

    def load(self, eng, base, group, i):
        k, r, layer = self.k, self.k.ring, self.layer
        rows = lambda s: (ds(group * E_G + s // 2, 1), slice(s % 2 * 256, (s % 2 + 1) * 256))
        for f in range(self.TURN):
            n = self.fills[base + f]
            slot, full = r.slot(n), r.full[n % SLOTS]
            r.wait_free(eng, n, i * (self.TURN // SLOTS))
            if f < self.STEPS:
                e, cols = rows(f)
                for at, w in ((0, k.a["moe_w_gate_2"]), (1, k.a["moe_w_up_2"])):
                    eng.dma_start(slot[:, at * 2048:(at + 1) * 2048].rearrange("p (k n) -> p k n", k=KD),
                                  w[layer][e, :, cols].rearrange("o (k q) n -> q (o k) n", q=P)).then_inc(full, 16)
            if f:
                e, cols = rows(f - 1)
                eng.dma_start(slot[:, 4096:6144].rearrange("p (j n) -> p j n", j=2),
                              k.a["moe_w_down_2"][layer][e, cols, :].rearrange("o (j q) n -> q (o j) n", q=P)).then_inc(full, 16)

    def sp(self, eng):
        k, r = self.k, self.k.ring
        with eng.Fori(0, self.GROUPS) as i:
            self.load(eng, 0, i, i)
        count = self.load_plan(eng)
        group = eng.value_load(k.plan[0:1, 1:2], min_val=0, max_val=G_N - 1)
        at = self.GROUPS * self.TURN
        with eng.If(count > self.GROUPS):
            self.load(eng, at, group, 0)
        with eng.If(count <= self.GROUPS):
            for s in range(SLOTS):
                n = self.fills[at - SLOTS + s]
                r.wait_full(eng, n)
                eng.sem_inc(r.full[n % SLOTS], self.landed[s])

    def wait_full(self, eng, f, i):
        self.k.ring.wait_full(eng, self.fills[f], i * self.landed[f % SLOTS])

    def load_plan(self, eng):
        k = self.k
        eng.wait_ge(self.sem["planned"], self.layer + 1)
        return eng.value_load(k.plan[0:1, 0:1], min_val=self.GROUPS, max_val=self.SLOTS_N)

    def slots(self, eng, count, work, skip):
        with eng.Fori(0, self.SLOTS_N) as i:
            with eng.If(i < count):
                work(eng, i, count)
            with eng.If(i >= count):
                skip(eng, i)

    def step(self, i, s):
        return i * self.STEPS + (self.step0 + s)

    def pe(self, pe):
        k, b, name, sem = self.k, self.k.banks, self.name, self.sem
        pe.wait_ge(k.small_ready, k.small_all)
        out = b.claim(pe, name + "lg")[0:G_N + E_N, 0:T]
        for kk in range(KD):
            if kk % 2 == 0:
                pe.wait_ge(k.x_ready, 4 * (self.turn - 1) + kk // 2 + 1)
            last = pe.matmul(out, k.w_route[:, self.layer, kk], k.x[:, kk], start=kk == 0, stop=kk == KD - 1)
        b.filled(last, name + "lg")
        self.pe_x_turned(pe, 0)
        pe.wait_ge(sem["logits"], self.layer + 1)
        out = b.claim(pe, name + "lt")
        for t in range(TT):
            last = pe.transpose(out[:, t * 20:(t + 1) * 20], self.logits_t[:, t * P:(t + 1) * P], k.ident[0:G_N + E_N, 0:G_N + E_N])
        b.filled(last, name + "lt")
        for q in (1, 2, 3):
            self.pe_x_turned(pe, q)
        pe.wait_ge(sem["grouped"], self.layer + 1)
        out = b.claim(pe, name + "rank")
        before = k.const(C_BEFORE, P)
        pe.matmul(out[:, 0:4], before, self.group[:, 0], start=True, stop=True)
        pe.matmul(out[:, 4:8], before, self.group[:, 1], start=True, stop=False)
        pe.matmul(out[:, 4:8], k.ones, self.group[:, 0], start=False, stop=True)
        pe.matmul(out[:, 8:12], k.ones, self.group[:, 0], start=True, stop=False)
        b.filled(pe.matmul(out[:, 8:12], k.ones, self.group[:, 1], start=False, stop=True), name + "rank")
        pe.wait_ge(sem["placed"], self.layer + 1)
        b.wait_read(pe, name + "x3")
        for q in range(3):
            out = b.claim(pe, f"{name}st{q}")
            for n in range(4 * q, min(4 * q + 4, 2 * self.SLOTS_N)):
                i, t = n // 2, n % 2
                last = pe.transpose(out[:, (n % 4) * P:(n % 4 + 1) * P], self.place[:, t, i * P:(i + 1) * P], k.ident)
            b.filled(last, f"{name}st{q}")
        self.pe_gather(pe, 0)
        count = self.load_plan(pe)
        pe.wait_ge(sem["gates"], self.layer + 1)
        out = b.claim(pe, name + "gates")
        for i in range(self.SLOTS_N):
            for t in range(TT):
                last = pe.matmul(out[:, i * E_G:(i + 1) * E_G], self.place[:, t, i * P:(i + 1) * P], self.best[:, t], start=t == 0, stop=t == 1)
        b.filled(last, name + "gates")
        for n in ("st0", "st1", "st2", "gates"):
            b.wait_read(pe, name + n)
        self.slots(pe, count, self.pe_slot, self.pe_skip)

    def pe_x_turned(self, pe, q):
        k, b = self.k, self.k.banks
        out = b.claim(pe, f"{self.name}x{q}")
        for n in range(4):
            t, kk = q // 2, (q % 2) * 4 + n
            last = pe.transpose(out[:, n * P:(n + 1) * P], k.x[:, kk, t * P:(t + 1) * P], k.ident)
        b.filled(last, f"{self.name}x{q}")

    def pe_gather(self, pe, slot):
        k = self.k
        at = slice(0, P) if isinstance(slot, int) else ds(slot * P, P)
        for kk in range(KD):
            out = k.psum[:, 2 + kk // 4, (kk % 4) * P:(kk % 4 + 1) * P]
            for t in range(TT):
                last = pe.matmul(out, self.tok[:, t, kk * P:(kk + 1) * P], self.place[:, t, at], start=t == 0, stop=t == 1)
            if kk % 4 == 3:
                last.then_inc(self.sem["gathered"], 1)

    def pe_three(self, pe, out, m_hi, m_lo, w_hi, w_lo, start, stop):
        pe.matmul(out, m_hi, w_hi, start=start, stop=False, skip_group_check=True)
        pe.matmul(out, m_lo, w_hi, start=False, stop=False, skip_group_check=True)
        return pe.matmul(out, m_hi, w_lo, start=False, stop=stop, skip_group_check=True)

    def pe_gate_up(self, pe, s, p, n):
        pe.wait_ge(self.sem["gu_lo"], n * 4 + (p + 1))
        for kk in (2 * p, 2 * p + 1):
            at = slice((kk % 2) * 512, (kk % 2 + 1) * 512)
            last = self.pe_three(pe, self.k.psum[:, 4 + s % 2, :], self.x_hi[:, kk], self.x_lo[:, kk],
                                 self.w_hi[:, p, at], self.w_lo[:, p, at], kk == 0, kk == KD - 1)
        last.then_inc(self.sem["gu_used"], 1)

    def pe_turn(self, pe, s, n):
        k, sem = self.k, self.sem
        pe.wait_ge(sem["hidden"], n + 3)
        pe.wait_ge(sem["ht_lo"], n + 1)
        for j in range(2):
            last = pe.transpose(k.psum[:, 6 + s % 2, j * P:(j + 1) * P], k.h32[:, s % 2, j * P:(j + 1) * P], k.ident)
        last.then_inc(sem["turned"], 1)

    def pe_down(self, pe, s, n):
        k, sem = self.k, self.sem
        pe.wait_ge(sem["ht_lo"], n + 3)
        for j in range(2):
            pe.wait_ge(sem["dn_lo"], n * 2 + (j + 1))
            for c in range(2):
                at, h = slice(c * 512, (c + 1) * 512), slice(j * P, (j + 1) * P)
                last = self.pe_three(pe, k.psum[:, c, :], k.h_hi[:, s % 2, h], k.h_lo[:, s % 2, h],
                                     self.w_hi[:, 4 + j, at], self.w_lo[:, 4 + j, at],
                                     s == 0 and j == 0, s == self.STEPS - 1 and j == 1)
            last.then_inc(sem["dn_used"], 1)

    def pe_slot(self, pe, i, count):
        k, sem = self.k, self.sem
        end = self.STEPS - 1
        pe.wait_ge(sem["xs_lo"], i * 2 + (2 * self.gather0 + 2))
        for s in range(self.STEPS):
            pe.wait_ge(sem["hidden"], self.step(i, s) + 1)
            for p in range(4):
                self.pe_gate_up(pe, s, p, self.step(i, s))
                if s and p == 1:
                    if s == 1:
                        pe.wait_ge(sem["added"], i * 4 + (4 * self.slot0 + 4))
                    self.pe_turn(pe, s - 1, self.step(i, s - 1))
            if s:
                self.pe_down(pe, s - 1, self.step(i, s - 1))
        self.pe_turn(pe, end, self.step(i, end))
        self.pe_gather(pe, i + 1)
        self.pe_down(pe, end, self.step(i, end))
        pe.wait_ge(sem["xs_lo"], i * 2 + (2 * self.gather0 + 4))
        pe.wait_ge(sem["y_ready"], i * 2 + (2 * self.slot0 + 2))
        for kk in range(KD):
            last = pe.matmul(self.scatter_bank(kk // 2)[:, (kk % 2) * T:(kk % 2 + 1) * T], k.y[:, kk * P:(kk + 1) * P],
                             self.place_t[:, ds(i * T, T)], start=True, stop=True)
            if kk % 2:
                last.then_inc(sem["scattered"], 1)

    def scatter_bank(self, c):
        return self.k.psum[:, (2, 3, 6, 7)[c], :]

    def pe_skip(self, pe, i):
        sem = self.sem
        pe.wait_ge(sem["scattered"], i * 4 + 4 * self.slot0)
        for n, by in (("gu_used", 32), ("dn_used", 16), ("turned", 8), ("gathered", 2), ("scattered", 4)):
            pe.sem_inc(sem[n], by)

    def act(self, act):
        k, b, name, sem = self.k, self.k.banks, self.name, self.sem
        self.act_first(act)
        for q in range(4):
            src = b.wait(act, f"{name}x{q}")
            b.read(act.activation(self.tok[:, q // 2, (q % 2) * 512:(q % 2 + 1) * 512], src, ACT.Copy), f"{name}x{q}")
        for n, to in enumerate((self.exp_g, self.exp_e)):
            act.wait_ge(sem["shifted"], 2 * self.layer + n + 1)
            act.activation(to, to, ACT.Exp).then_inc(sem["exped"], 1)
        for q in range(3):
            w = min(512, self.SLOTS_N * T - q * 512)
            src = b.wait(act, f"{name}st{q}")
            b.read(act.activation(self.place_t[:, q * 512:q * 512 + w], src[:, 0:w], ACT.Copy), f"{name}st{q}")
        self.act_tokens(act, 0)
        count = self.load_plan(act)
        src = b.wait(act, name + "gates")[:, 0:20].rearrange("p (i e) -> p i e", e=E_G)
        b.read(act.activation(self.gates, src, ACT.Copy), name + "gates")
        self.slots(act, count, self.act_slot, self.act_skip)

    def act_first(self, act):
        self.wait_full(act, 0, 0)
        for p in range(4):
            self.act_piece(act, 0, p, self.step0)

    def act_tokens(self, act, gather):
        k, sem = self.k, self.sem
        for c in range(2):
            act.wait_ge(sem["gathered"], gather * 2 + (2 * self.gather0 + c + 1))
            act.activation(self.x_hi[:, 4 * c:4 * c + 4], k.psum[:, 2 + c, :].rearrange("p (k n) -> p k n", n=P),
                           ACT.Copy).then_inc(sem["xs_hi"], 1)

    def piece(self, s, p, w=None):
        raw = self.k.ring.slot(self.fills[s if p < 4 else s + 1])
        if p < 4:
            if w is not None:
                return w[:, p].rearrange("p (k u n) -> p k u n", k=2, u=2)
            return raw[:, 0:4096].rearrange("p (u k n) -> p k u n", u=2, k=KD)[:, 2 * p:2 * p + 2]
        return raw[:, p * 1024:(p + 1) * 1024] if w is None else w[:, p]

    def act_piece(self, act, s, p, n):
        sem = self.sem
        kind, j, per = ("gu", p, 4) if p < 4 else ("dn", p - 4, 2)
        act.wait_ge(sem[kind + "_used"], n * per + (j + 1))
        act.activation(self.piece(s, p, self.w_hi), self.piece(s, p), ACT.Copy).then_inc(sem[kind + "_hi"], 1)

    def act_silu(self, act, s, n):
        k, sem = self.k, self.sem
        act.wait_ge(sem["gu_used"], n * 4 + 8)
        act.wait_ge(sem["hidden"], n + 1)
        act.activation(k.sg[:, s % 2], k.psum[:, 4 + s % 2, 0:T], ACT.Silu).then_inc(sem["silu"], 1)

    def act_turned(self, act, s, n):
        k, sem = self.k, self.sem
        act.wait_ge(sem["turned"], n + 3)
        act.activation(k.h_hi[:, s % 2], k.psum[:, 6 + s % 2, 0:T], ACT.Copy).then_inc(sem["ht_hi"], 1)

    def act_slot(self, act, i, count):
        k, end = self.k, self.STEPS - 1
        for s in range(1, self.STEPS):
            self.wait_full(act, s, i)
            for p in range(4):
                if p == 2:
                    self.act_silu(act, s - 1, self.step(i, s - 1))
                self.act_piece(act, s, p, self.step(i, s))
            for p in (4, 5):
                self.act_piece(act, s - 1, p, self.step(i, s - 1))
            self.act_turned(act, s - 1, self.step(i, s - 1))
        self.act_silu(act, end, self.step(i, end))
        self.wait_full(act, end + 1, i)
        for p in (4, 5):
            self.act_piece(act, end, p, self.step(i, end))
        self.act_turned(act, end, self.step(i, end))
        with act.If(i + 1 < count):
            self.act_end(act, i, True)
        with act.If(i + 1 >= count):
            self.act_end(act, i, False)

    def act_end(self, act, i, ahead):
        k, sem, end = self.k, self.sem, self.STEPS - 1
        if ahead:
            self.wait_full(act, 0, i + 1)
            self.act_piece(act, 0, 0, self.step(i + 1, 0))
        self.act_tokens(act, i + 1)
        if ahead:
            self.act_piece(act, 0, 1, self.step(i + 1, 0))
        act.wait_ge(sem["dn_used"], self.step(i, end) * 2 + 4)
        act.activation(k.y[:, 0:512], k.psum[:, 0, :], ACT.Copy).then_inc(sem["y_ready"], 1)
        if ahead:
            for p in (2, 3):
                self.act_piece(act, 0, p, self.step(i + 1, 0))

    def act_skip(self, act, i):
        sem = self.sem
        act.wait_ge(sem["y_ready"], i * 2 + 2 * self.slot0)
        for n, by in (("gu_hi", 32), ("dn_hi", 16), ("silu", 8), ("ht_hi", 8), ("xs_hi", 2), ("y_ready", 1)):
            act.sem_inc(sem[n], by)

    def dve(self, dve):
        k = self.k
        self.dve_piece(dve, 0, 0, self.step0)
        self.dve_route(dve)
        count = self.load_plan(dve)
        self.slots(dve, count, self.dve_slot, self.dve_skip)
        dve.wait_ge(self.sem["added"], 4 * (self.slot0 + self.SLOTS_N) + 4)
        dve.sem_inc(k.x_ready, 4)

    def dve_route(self, dve):
        k, b, seq, sem, name = self.k, self.k.banks, self.k.dve_seq, self.sem, self.name

        def do(ins):
            seq.inc(ins)
            seq.wait(dve)

        def best(of, top, onehot):
            do(dve.tensor_reduce(top, of, X_AXIS, ALU.max))
            do(dve.tensor_tensor(self.first, of, wide(top), ALU.is_equal))
            do(dve.tensor_tensor(self.first, self.first, k.const(C_FIRST, 4).unsqueeze(1).to_broadcast([P, TT, 4]), ALU.mult))
            do(dve.tensor_reduce(self.cols[7], self.first, X_AXIS, ALU.max))
            return dve.tensor_tensor(onehot, self.first, wide(self.cols[7]), ALU.is_equal)

        top, total, top_e, one, two, both = self.cols[0:6]
        wide = lambda t: t.to_broadcast([P, TT, 4])
        src = b.wait(dve, name + "lg")[0:G_N + E_N, 0:T]
        dve.tensor_copy(self.logits_t, src).then_inc(sem["logits"], 1)
        dve.wait_ge(sem["logits"], self.layer + 1)
        b.release(dve, name + "lg")
        self.dve_piece(dve, 0, 1, self.step0)
        src = b.wait(dve, name + "lt")[:, 0:40].rearrange("p (t n) -> p t n", t=2)
        do(dve.tensor_tensor(self.logits, src, k.b_route[:, self.layer].unsqueeze(1).to_broadcast([P, TT, 20]), ALU.add))
        b.release(dve, name + "lt")
        groups = self.logits[:, :, 0:4]
        best(groups, top, self.group).then_inc(sem["grouped"], 1)
        dve.wait_ge(sem["grouped"], self.layer + 1)
        dve.tensor_tensor(self.exp_g, groups, wide(top), ALU.subtract).then_inc(sem["shifted"], 1)
        experts = self.logits[:, :, 4:20].rearrange("p t (g j) -> p t g j", g=4)
        do(dve.tensor_tensor(self.picked, experts, self.group.unsqueeze(3).to_broadcast([P, TT, 4, 4]), ALU.mult))
        do(dve.tensor_reduce(self.chosen, self.picked.rearrange("p t g j -> p t j g"), X_AXIS, ALU.add))
        do(dve.tensor_reduce(top_e, self.chosen, X_AXIS, ALU.max))
        dve.tensor_tensor(self.exp_e, self.chosen, wide(top_e), ALU.subtract).then_inc(sem["shifted"], 1)
        self.dve_piece(dve, 0, 2, self.step0)
        do(dve.memset(self.pos, -1.0))
        src = b.wait(dve, name + "rank")
        ranks = src[:, 0:8].rearrange("p (t g) -> p t g", t=2)
        do(dve.scalar_tensor_tensor(out=self.rank1, in0=ranks, scalar=1.0, in1=self.group, op0=ALU.add, op1=ALU.mult))
        do(dve.tensor_scalar(self.pos[:, :, 0:4], self.rank1, -1.0, None, ALU.add))
        do(dve.tensor_reduce(self.cols[6], self.rank1, X_AXIS, ALU.add))
        do(dve.tensor_scalar(self.pos[:, :, 4:5], self.cols[6], -1.0 - P, None, ALU.add))
        for t in range(TT):
            ins = dve.tensor_tensor(self.place[:, t].rearrange("p (i n) -> p i n", n=P),
                                    k.const(C_IOTA, P).unsqueeze(1).to_broadcast([P, 6, P]),
                                    self.pos[:, t].unsqueeze(2).to_broadcast([P, 6, P]), ALU.is_equal)
            seq.inc(ins)
        seq.wait(dve)
        dve.sem_inc(sem["placed"], 1)
        self.dve_piece(dve, 0, 3, self.step0)
        dve.wait_ge(sem["gu_lo"], self.step0 * 4 + 4)
        self.dve_release(dve, 0)
        do(dve.tensor_scalar(self.over, src[0:1, 8:12], float(P), None, ALU.is_gt))
        b.release(dve, name + "rank")
        do(dve.tensor_tensor(self.over, self.over, k.const(C_FIRST, 4, 1), ALU.mult))
        do(dve.tensor_reduce(self.over[:, 0:1], self.over, X_AXIS, ALU.max))
        do(dve.tensor_scalar(self.over_n[:, 0:1], self.over[:, 0:1], 1.0, float(G_N), ALU.min, ALU.add))
        do(dve.tensor_scalar(self.over_n[:, 1:2], self.over[:, 0:1], -1.0, float(G_N), ALU.mult, ALU.add))
        do(dve.tensor_scalar(self.over_n[:, 1:2], self.over_n[:, 1:2], float(G_N - 1), None, ALU.min))
        dve.tensor_copy(k.plan[:], self.over_n).then_inc(sem["planned"], 1)
        dve.wait_ge(sem["exped"], 2 * self.layer + 2)
        do(dve.tensor_reduce(total, self.exp_g, X_AXIS, ALU.add))
        do(best(self.exp_e, one, self.best))
        do(dve.scalar_tensor_tensor(out=self.chosen, in0=self.best, scalar=-2.0, in1=self.exp_e, op0=ALU.mult, op1=ALU.add))
        do(best(self.chosen, two, self.first))
        do(dve.tensor_tensor(self.best, self.best, self.first, ALU.add))
        do(dve.tensor_tensor(self.best, self.best, self.exp_e, ALU.mult))
        do(dve.tensor_tensor(both, one, two, ALU.add))
        do(dve.tensor_tensor(both, both, total, ALU.mult))
        do(dve.reciprocal(both, both))
        dve.tensor_tensor(self.best, self.best, wide(both), ALU.mult).then_inc(sem["gates"], 1)
        self.dve_tokens(dve, 0)
        b.wait_read(dve, name + "gates")

    def dve_tokens(self, dve, gather):
        k, sem = self.k, self.sem
        for c in range(2):
            dve.wait_ge(sem["xs_hi"], gather * 2 + (2 * self.gather0 + c + 1))
            dve.tensor_tensor(self.x_lo[:, 4 * c:4 * c + 4], k.psum[:, 2 + c, :].rearrange("p (k n) -> p k n", n=P),
                              self.x_hi[:, 4 * c:4 * c + 4].bitcast(F32), ALU.subtract).then_inc(sem["xs_lo"], 1)

    def dve_piece(self, dve, s, p, n):
        sem = self.sem
        kind, j, per = ("gu", p, 4) if p < 4 else ("dn", p - 4, 2)
        dve.wait_ge(sem[kind + "_hi"], n * per + (j + 1))
        dve.tensor_tensor(self.piece(s, p, self.w_lo), self.piece(s, p), self.piece(s, p, self.w_hi.bitcast(F32)),
                          ALU.subtract).then_inc(sem[kind + "_lo"], 1)

    def dve_hidden(self, dve, s, n):
        k, sem = self.k, self.sem
        dve.wait_ge(sem["silu"], n + 1)
        dve.wait_ge(sem["turned"], n + 1)
        dve.scalar_tensor_tensor(out=k.h32[:, s % 2], in0=k.psum[:, 4 + s % 2, T:2 * T], scalar=self.gate4[:, s // 2:s // 2 + 1],
                                 in1=k.sg[:, s % 2], op0=ALU.mult, op1=ALU.mult).then_inc(sem["hidden"], 1)

    def dve_turned(self, dve, s, n):
        k, sem = self.k, self.sem
        dve.wait_ge(sem["ht_hi"], n + 1)
        dve.tensor_tensor(k.h_lo[:, s % 2], k.psum[:, 6 + s % 2, 0:T], k.h_hi[:, s % 2].bitcast(F32), ALU.subtract).then_inc(sem["ht_lo"], 1)

    def dve_release(self, dve, f):
        dve.sem_inc(self.k.ring.free[self.fills[f] % SLOTS], 1)

    def dve_slot(self, dve, i, count):
        k, sem, end = self.k, self.sem, self.STEPS - 1
        dve.tensor_tensor(self.gate4.unsqueeze(1), self.gates[:, ds(i, 1), :], k.const(C_ONES, E_G).unsqueeze(1),
                          ALU.mult).then_inc(sem["gate_copied"], 1)
        dve.wait_ge(sem["gate_copied"], i + (self.slot0 + 1))
        for s in range(1, self.STEPS):
            for p in range(4):
                if p == 2:
                    self.dve_hidden(dve, s - 1, self.step(i, s - 1))
                self.dve_piece(dve, s, p, self.step(i, s))
            for p in (4, 5):
                self.dve_piece(dve, s - 1, p, self.step(i, s - 1))
            dve.wait_ge(sem["dn_lo"], self.step(i, s - 1) * 2 + 2)
            self.dve_release(dve, s)
            self.dve_turned(dve, s - 1, self.step(i, s - 1))
        self.dve_hidden(dve, end, self.step(i, end))
        for p in (4, 5):
            self.dve_piece(dve, end, p, self.step(i, end))
        dve.wait_ge(sem["dn_lo"], self.step(i, end) * 2 + 2)
        self.dve_release(dve, end + 1)
        self.dve_turned(dve, end, self.step(i, end))
        with dve.If(i + 1 < count):
            self.dve_end(dve, i, True)
        with dve.If(i + 1 >= count):
            self.dve_end(dve, i, False)

    def dve_end(self, dve, i, ahead):
        k, sem, end = self.k, self.sem, self.STEPS - 1
        if ahead:
            self.dve_piece(dve, 0, 0, self.step(i + 1, 0))
        self.dve_tokens(dve, i + 1)
        if ahead:
            self.dve_piece(dve, 0, 1, self.step(i + 1, 0))
        dve.wait_ge(sem["dn_used"], self.step(i, end) * 2 + 4)
        dve.tensor_copy(k.y[:, 512:1024], k.psum[:, 1, :]).then_inc(sem["y_ready"], 1)
        if ahead:
            for p in (2, 3):
                self.dve_piece(dve, 0, p, self.step(i + 1, 0))
            dve.wait_ge(sem["gu_lo"], self.step(i + 1, 0) * 4 + 4)
            self.dve_release(dve, 0)
        dve.wait_ge(sem["scaled"], self.layer + 1)
        for c in range(4):
            cs = slice(2 * c, 2 * c + 2)
            dve.wait_ge(sem["scattered"], i * 4 + (4 * self.slot0 + c + 1))
            dve.wait_ge(sem["added"], i * 4 + (4 * self.slot0 + c + 1))
            dve.tensor_tensor(k.x[:, cs], k.x[:, cs], self.scatter_bank(c).rearrange("p (k t) -> p k t", t=T), ALU.add).then_inc(sem["added"], 1)

    def dve_skip(self, dve, i):
        k, sem = self.k, self.sem
        dve.wait_ge(sem["added"], i * 4 + (4 * self.slot0 + 4))
        for n, by in (("gu_lo", 32), ("dn_lo", 16), ("hidden", 8), ("ht_lo", 8), ("xs_lo", 2), ("y_ready", 1), ("added", 4),
                      ("gate_copied", 1)):
            dve.sem_inc(sem[n], by)
        for free in k.ring.free:
            dve.sem_inc(free, self.TURN // SLOTS)

    def pool(self, pool):
        k, b = self.k, self.k.banks
        b.wait(pool, self.name + "x3")
        pool.tensor_scalar(k.x[:], k.x[:], ALPHA, None, ALU.mult).then_inc(self.sem["scaled"], 1)


def make_stages(k, stages):
    a = k.a
    made = []
    order = [
        lambda: Ffn(k, FF // P, swiglu_sources(a, 0, 0), 0),
        lambda: Hgrn2(k, RmsNorm(k, 1)),
        lambda: Ffn(k, FF // P, swiglu_sources(a, 0, 1), 2),
        lambda: Ffn(k, FF // P, swiglu_sources(a, 1, 0), 3),
        lambda: Fox(k, RmsNorm(k, 4)),
        lambda: Ffn(k, FF // P, swiglu_sources(a, 1, 1), 5),
        lambda: Nsa(k),
        lambda: LayerNorm(k, 0),
        lambda: Moe(k, 0),
        lambda: LayerNorm(k, 1, MemoryRows(k, 1, "mla", (11008, 11520, 12032, 0))),
        lambda: Mla(k, made[-1].memory),
        lambda: LayerNorm(k, 2),
        lambda: Moe(k, 1),
        lambda: LayerNorm(k, 3),
    ]
    for n, make in enumerate(order[:stages]):
        made.append(make())
    return made


NAMES = ['x', 'norm_g', 'ffn_w_in', 'ffn_w_out', 'hg_w_in', 'hg_lb_logits', 'hg_out_norm_g', 'hg_w_out', 'fox_w_in',
         'fox_b_f', 'fox_q_norm_g', 'fox_k_norm_g', 'fox_w_out', 'mem_2', 'positions_2', 'nsa_w_in_2',
         'nsa_cmp_pe_2', 'nsa_cmp_w1_2', 'nsa_cmp_w2_2', 'mla_w_in_2', 'mla_q_norm_2', 'mla_w_uq_2',
         'mla_kv_norm_2', 'mla_w_ukv_2', 'mem_w_kv_2', 'w_out_2', 'ln_g_2', 'ln_b_2', 'moe_w_grp_2', 'moe_b_grp_2',
         'moe_w_exp_2', 'moe_b_exp_2', 'moe_w_gate_2', 'moe_w_up_2', 'moe_w_down_2']


def build(nc, a, stages=99):
    with ExitStack() as ctx:
        k = Core(ctx, nc, a)
        start = Start(k)
        made = make_stages(k, stages)
        finish = Finish(k)
        block = ctx.enter_context(nc.Block())

        @block.sync
        def _(sp):
            start.sp(sp)
            for stage in made:
                stage.sp(sp)
            finish.sp(sp)

        @block.scalar
        def _(act):
            start.act_dma(act)
            act.wait_ge(k.ident_ready, 16)
            for stage in made:
                stage.act(act)

        @block.vector
        def _(dve):
            for sem in k.ring.free:
                dve.sem_inc(sem, 1)
            dve.sem_inc(k.gu_ready, 2)
            dve.sem_inc(k.out_used, 2)
            dve.sem_inc(k.h_ready, 2)
            dve.sem_inc(k.piece_used, PIECES)
            for name, free in (("gu_used", 4), ("dn_used", 2), ("hidden", 2), ("turned", 2), ("ht_lo", 2), ("added", 4)):
                dve.sem_inc(k.moe[name], free)
            start.dve(dve)
            for stage in made:
                stage.dve(dve)
            finish.dve(dve)

        @block.gpsimd
        def _(pool):
            start.pool(pool)
            for stage in made:
                stage.pool(pool)

        @block.tensor
        def _(pe):
            pe.wait_ge(k.zero_ready, 1)
            start.pe(pe)
            for stage in made:
                stage.pe(pe)
            finish.pe(pe)


def kernel(**inputs):
    import concourse.bacc as bacc
    from concourse.bass_utils import run_bass_kernel_spmd

    nc = bacc.Bacc("TRN2", target_bir_lowering=False, num_devices=1)
    arrays = {"in_" + n: np.ascontiguousarray(inputs[n]) for n in NAMES}
    arrays["in_consts"] = constants()
    a = {n[3:]: nc.dram_tensor(n, v.shape, mybir.dt.from_np(v.dtype), kind="ExternalInput").ap()
         for n, v in arrays.items()}
    a["out"] = nc.dram_tensor("out_x", (1, T, D), F32, kind="ExternalOutput").ap()
    build(nc, a)
    return run_bass_kernel_spmd(nc, [arrays], core_ids=[0]).results[0]["out_x"]
```
